# Optimizing a Trainium2 kernel written in Bass

```python
import math
import jax, jax.numpy as jnp
from jax import lax
import numpy as np

D_MODEL = 1024
BATCH = 1
SEQ = 512
DEPTH = 1

D_MIX = D_MODEL
HEAD_SIZE = 64
RWKV_DIM = D_MIX // 2
RWKV_HEADS = RWKV_DIM // HEAD_SIZE
POOL_DIM = D_MIX - RWKV_DIM
POOL_WINDOWS = (2, 4, 8, 16)
POOL_GROUPS = len(POOL_WINDOWS)
POOL_GROUP_DIM = POOL_DIM // POOL_GROUPS

DECAY_LORA = max(32, int(round(1.8 * D_MODEL ** 0.5 / 32)) * 32)
AAA_LORA = max(32, int(round(1.8 * D_MODEL ** 0.5 / 32)) * 32)
GATE_LORA = max(32, int(round(0.6 * D_MODEL ** 0.8 / 32)) * 32)
N_DIR = 2
RWKV_IN = 3 * RWKV_DIM + N_DIR * DECAY_LORA + N_DIR * AAA_LORA + GATE_LORA
D_IN = RWKV_IN + POOL_DIM
RWKV_SPLITS = (RWKV_DIM, 2 * RWKV_DIM, 3 * RWKV_DIM,
               3 * RWKV_DIM + N_DIR * DECAY_LORA,
               3 * RWKV_DIM + N_DIR * DECAY_LORA + N_DIR * AAA_LORA)
GN_EPS = 64e-5
RMS_EPS = 1e-5

N_KEYS = 128
N_EXPERTS = N_KEYS * N_KEYS
PEER_HEADS = 8
PEER_TOPK = 16
PEER_QDIM = 256
PEER_KHALF = PEER_QDIM // 2
PEER_BLOCK = 128


def rmsnorm(x, w):
    xf = x.astype(jnp.float32)
    y = xf * lax.rsqrt(jnp.mean(xf * xf, axis=-1, keepdims=True) + RMS_EPS)
    return (y * w.astype(jnp.float32)).astype(x.dtype)

def bi_token_shift(p, mu):
    prev = jnp.pad(p[:, :-1], ((0, 0), (1, 0), (0, 0)))
    nxt = jnp.pad(p[:, 1:], ((0, 0), (0, 1), (0, 0)))
    return p + mu[0] * (prev - p) + mu[1] * (nxt - p)

def wkv7_scan(r, w, k, v, kk, a, reverse):
    B, S, H, N = r.shape

    def step(state, inp):
        r_t, w_t, k_t, v_t, kk_t, a_t = inp
        sa = jnp.einsum('bhvk,bhk->bhv', state, -kk_t)
        state = (state * w_t[:, :, None, :]
                 + sa[..., :, None] * (kk_t * a_t)[..., None, :]
                 + v_t[..., :, None] * k_t[..., None, :])
        out = jnp.einsum('bhvk,bhk->bhv', state, r_t)
        return state, out

    xs = tuple(jnp.moveaxis(t, 1, 0) for t in (r, w, k, v, kk, a))
    state0 = jnp.zeros((B, H, N, N), jnp.float32)
    _, out = lax.scan(step, state0, xs, reverse=reverse)
    return jnp.moveaxis(out, 0, 1)

def multiscale_pool(p, pool_w, pool_scale):
    B, S, _ = p.shape
    pg = p.reshape(B, S, POOL_GROUPS, POOL_GROUP_DIM).astype(jnp.float32)
    cs = jnp.concatenate([jnp.zeros((B, 1, POOL_GROUPS, POOL_GROUP_DIM), jnp.float32),
                          jnp.cumsum(pg, axis=1)], axis=1)
    t = jnp.arange(S)
    outs = []
    for gi, win in enumerate(POOL_WINDOWS):
        half = win // 2
        lo = jnp.clip(t - half, 0, S)
        hi = jnp.clip(t + half, 0, S)
        cnt = (hi - lo).astype(jnp.float32)[None, :, None]
        cs_g = cs[:, :, gi]
        mean = (jnp.take(cs_g, hi, axis=1) - jnp.take(cs_g, lo, axis=1)) / cnt
        outs.append(mean - pg[:, :, gi])
    pooled = jnp.stack(outs, axis=2)
    mixed = jnp.einsum('bsgc,gcd->bsgd', pooled, pool_w.astype(jnp.float32))
    return (mixed.reshape(B, S, POOL_DIM) * pool_scale.astype(jnp.float32)).astype(p.dtype)

def hybrid_mixer(h, w_in, shift_mu, w0, w_up, a0, a_up, g_up, k_k, k_a, r_k,
                 ln_x_w, ln_x_b, pool_w, pool_scale, w_out):
    B, S, _ = h.shape
    f32 = jnp.float32
    p = h @ w_in
    p_rw = bi_token_shift(p[..., :RWKV_IN], shift_mu)
    p_pool = p[..., RWKV_IN:]

    r, k, v, wd, ad, gd = jnp.split(p_rw, RWKV_SPLITS, axis=-1)
    wd = wd.reshape(B, S, N_DIR, DECAY_LORA)
    ad = ad.reshape(B, S, N_DIR, AAA_LORA)

    def heads(t):
        return t.reshape(B, S, RWKV_HEADS, HEAD_SIZE).astype(f32)

    rh = heads(r)
    vh = heads(v)
    kk = heads(k * k_k)
    kk = kk / jnp.maximum(jnp.sqrt(jnp.sum(kk * kk, axis=-1, keepdims=True)), 1e-12)
    g = jax.nn.sigmoid(gd) @ g_up

    o = jnp.zeros((B, S, RWKV_HEADS, HEAD_SIZE), f32)
    bonus = jnp.zeros((B, S, RWKV_HEADS, HEAD_SIZE), f32)
    for d in range(N_DIR):
        wlog = -jax.nn.softplus(-(w0[d] + jnp.tanh(wd[:, :, d]) @ w_up[d])) - 0.5
        decay = jnp.exp(-jnp.exp(wlog.astype(f32)))
        a = jax.nn.sigmoid(a0[d] + ad[:, :, d] @ a_up[d])
        kd = heads(k * (1 + (a - 1) * k_a))
        o = o + wkv7_scan(rh, heads(decay), kd, vh, kk, heads(a), reverse=(d == 1))
        bonus = bonus + jnp.sum(rh * kd * r_k.astype(f32), axis=-1, keepdims=True) * vh

    mu = jnp.mean(o, axis=-1, keepdims=True)
    var = jnp.mean(jnp.square(o - mu), axis=-1, keepdims=True)
    o = ((o - mu) * lax.rsqrt(var + GN_EPS)).reshape(B, S, RWKV_DIM)
    o = o * ln_x_w.astype(f32) + ln_x_b.astype(f32) + bonus.reshape(B, S, RWKV_DIM)
    y_rwkv = (o * g.astype(f32)).astype(h.dtype)

    y_pool = multiscale_pool(p_pool, pool_w, pool_scale)
    return jnp.concatenate([y_rwkv, y_pool], axis=-1) @ w_out

def peer_ffn(h, wq, keys, u_tab, v_tab):
    B, S, D = h.shape
    hb = h.reshape(-1, PEER_BLOCK, D)

    def block_fn(xb):
        T = xb.shape[0]
        q = (xb @ wq).reshape(T, PEER_HEADS, 2, PEER_KHALF)
        s = jnp.einsum('thpc,hpnc->thpn', q.astype(jnp.float32), keys.astype(jnp.float32))
        v1, i1 = lax.top_k(s[:, :, 0], PEER_TOPK)
        v2, i2 = lax.top_k(s[:, :, 1], PEER_TOPK)
        cand = (v1[..., :, None] + v2[..., None, :]).reshape(T, PEER_HEADS, PEER_TOPK * PEER_TOPK)
        cidx = (i1[..., :, None] * N_KEYS + i2[..., None, :]).reshape(T, PEER_HEADS, PEER_TOPK * PEER_TOPK)
        sc, pos = lax.top_k(cand, PEER_TOPK)
        idx = jnp.take_along_axis(cidx, pos, axis=-1)
        gate = jax.nn.softmax(sc, axis=-1)
        ug = jnp.take(u_tab, idx, axis=0)
        act = jax.nn.gelu(jnp.einsum('td,thkd->thk', xb, ug).astype(jnp.float32), approximate=False)
        vg = jnp.take(v_tab, idx, axis=0)
        return jnp.einsum('thk,thkd->td', (gate * act).astype(xb.dtype), vg)

    return lax.map(block_fn, hb).reshape(B, S, D)

def first_inputs(seed: int = 0) -> dict:
    key = jax.random.key(seed)
    ks = jax.random.split(key, 24)
    L = DEPTH
    nrm = lambda k, shape, s: jax.random.normal(k, shape, jnp.float32) * s
    return {
        "x": nrm(ks[0], (BATCH, SEQ, D_MODEL), 1.0),
        "norm1_w": 1.0 + nrm(ks[1], (L, D_MODEL), 0.02),
        "w_in": nrm(ks[2], (L, D_MODEL, D_IN), D_MODEL ** -0.5),
        "shift_mu": jax.random.uniform(ks[3], (L, 2, RWKV_IN), jnp.float32, 0.0, 0.5),
        "w0": nrm(ks[4], (L, N_DIR, RWKV_DIM), 0.5) - 1.0,
        "w_up": nrm(ks[5], (L, N_DIR, DECAY_LORA, RWKV_DIM), 0.1),
        "a0": nrm(ks[6], (L, N_DIR, RWKV_DIM), 0.5),
        "a_up": nrm(ks[7], (L, N_DIR, AAA_LORA, RWKV_DIM), 0.1),
        "g_up": nrm(ks[8], (L, GATE_LORA, RWKV_DIM), GATE_LORA ** -0.5),
        "k_k": 0.85 + nrm(ks[9], (L, RWKV_DIM), 0.05),
        "k_a": 1.0 + nrm(ks[10], (L, RWKV_DIM), 0.05),
        "r_k": nrm(ks[11], (L, RWKV_HEADS, HEAD_SIZE), 0.1),
        "ln_x_w": 1.0 + nrm(ks[12], (L, RWKV_DIM), 0.02),
        "ln_x_b": nrm(ks[13], (L, RWKV_DIM), 0.02),
        "pool_w": nrm(ks[14], (L, POOL_GROUPS, POOL_GROUP_DIM, POOL_GROUP_DIM), POOL_GROUP_DIM ** -0.5),
        "pool_scale": 1.0 + nrm(ks[15], (L, POOL_DIM), 0.1),
        "w_out": nrm(ks[16], (L, D_MIX, D_MODEL), D_MIX ** -0.5),
        "norm2_w": 1.0 + nrm(ks[17], (L, D_MODEL), 0.02),
        "peer_wq": nrm(ks[18], (L, D_MODEL, PEER_HEADS * PEER_QDIM), D_MODEL ** -0.5),
        "peer_keys": nrm(ks[19], (L, PEER_HEADS, 2, N_KEYS, PEER_KHALF), PEER_KHALF ** -0.5),
        "peer_u": nrm(ks[20], (L, N_EXPERTS, D_MODEL), D_MODEL ** -0.5),
        "peer_v": nrm(ks[21], (L, N_EXPERTS, D_MODEL), PEER_HEADS ** -0.5),
        "norm_f_w": 1.0 + nrm(ks[22], (D_MODEL,), 0.02),
    }

def first_block(x, norm1_w, w_in, shift_mu, w0, w_up, a0, a_up, g_up, k_k, k_a, r_k,
              ln_x_w, ln_x_b, pool_w, pool_scale, w_out, norm2_w, peer_wq, peer_keys,
              peer_u, peer_v, norm_f_w):
    for l in range(DEPTH):
        h = rmsnorm(x, norm1_w[l])
        x = x + hybrid_mixer(h, w_in[l], shift_mu[l], w0[l], w_up[l], a0[l], a_up[l], g_up[l],
                             k_k[l], k_a[l], r_k[l], ln_x_w[l], ln_x_b[l], pool_w[l],
                             pool_scale[l], w_out[l])
        h = rmsnorm(x, norm2_w[l])
        x = x + peer_ffn(h, peer_wq[l], peer_keys[l], peer_u[l], peer_v[l])
    return rmsnorm(x, norm_f_w)


DEPTH_2 = 2

HEAD_DIM = 64
BLOCK_Q = 128
NORM_EPS = 1e-6
MLA_HEADS = 8
MLA_Q_RANK = 256
MLA_KV_RANK = 128
MLA_NOPE = 64
MLA_ROPE = 32
MLA_V = 64
ROPE_BASE = 10000.0
DIFF_HEADS = 4
DIFF_QK = 64
DIFF_V = 2 * DIFF_QK
DIL_CONFIGS = ((128, 1), (512, 4), (2048, 16))
DIL_GROUPS = len(DIL_CONFIGS)
DIL_HEADS_PER_GROUP = 4
SB_HEADS = 4
D_FF = 2816
CONV_WIDTH = 3

EVEN_SPLITS = (MLA_Q_RANK, MLA_KV_RANK, MLA_ROPE,
               DIFF_HEADS * 2 * DIFF_QK, DIFF_HEADS * 2 * DIFF_QK, DIFF_HEADS * DIFF_V)
EVEN_IN = sum(EVEN_SPLITS)
EVEN_OUT = MLA_HEADS * MLA_V + DIFF_HEADS * DIFF_V
DIL_QKV = DIL_GROUPS * DIL_HEADS_PER_GROUP * HEAD_DIM
SB_QKV = SB_HEADS * HEAD_DIM
ODD_SPLITS = (DIL_QKV, DIL_QKV, DIL_QKV, SB_QKV, SB_QKV, SB_QKV)
ODD_IN = sum(ODD_SPLITS)
ODD_OUT = DIL_HEADS_PER_GROUP * HEAD_DIM + SB_QKV
N_EVEN = (DEPTH_2 + 1) // 2
N_ODD = DEPTH_2 // 2


def rms_norm(x, g):
    xf = x.astype(jnp.float32)
    y = xf * lax.rsqrt(jnp.mean(xf * xf, axis=-1, keepdims=True) + NORM_EPS)
    return (y * g.astype(jnp.float32)).astype(x.dtype)

def alibi_slopes(n):
    return jnp.asarray(2.0 ** (-8.0 * np.arange(1, n + 1) / n), dtype=jnp.float32)

def split_cols(p, sizes):
    return jnp.split(p, np.cumsum(sizes)[:-1].tolist(), axis=-1)

def rope(x, pos):
    half = x.shape[-1] // 2
    inv = ROPE_BASE ** (-jnp.arange(half, dtype=jnp.float32) / half)
    ang = pos.astype(jnp.float32)[:, None] * inv
    cos, sin = jnp.cos(ang), jnp.sin(ang)
    xf = x.astype(jnp.float32)
    x1, x2 = xf[..., :half], xf[..., half:]
    return jnp.concatenate([x1 * cos - x2 * sin, x2 * cos + x1 * sin], axis=-1).astype(x.dtype)

def to_blocks(t):
    b, h, s, d = t.shape
    return t.reshape(b, h, s // BLOCK_Q, BLOCK_Q, d).transpose(2, 0, 1, 3, 4)

def from_blocks(t):
    nb, b, h, bq, d = t.shape
    return t.transpose(1, 2, 0, 3, 4).reshape(b, h, nb * bq, d)

def heads_first(t, n_heads):
    b, s, _ = t.shape
    return t.reshape(b, s, n_heads, -1).transpose(0, 2, 1, 3)

def heads_last(t):
    b, h, s, d = t.shape
    return t.transpose(0, 2, 1, 3).reshape(b, s, h * d)

def mla_attention(q_nope, q_rope, k_nope, k_rope, v):
    s_len = v.shape[2]
    scale = (MLA_NOPE + MLA_ROPE) ** -0.5
    kpos = jnp.arange(s_len)

    def block(args):
        i, qn, qr = args
        qpos = i * BLOCK_Q + jnp.arange(BLOCK_Q)
        s = (jnp.einsum('bhqd,bhkd->bhqk', qn, k_nope)
             + jnp.einsum('bhqr,bkr->bhqk', qr, k_rope)).astype(jnp.float32) * scale
        s = jnp.where(kpos[None, :] <= qpos[:, None], s, -jnp.inf)
        p = jax.nn.softmax(s, axis=-1)
        return jnp.einsum('bhqk,bhkd->bhqd', p.astype(v.dtype), v)

    out = lax.map(block, (jnp.arange(s_len // BLOCK_Q), to_blocks(q_nope), to_blocks(q_rope)))
    return from_blocks(out)

def diff_attention(q1, q2, k1, k2, v, lam, slopes):
    s_len = v.shape[2]
    scale = DIFF_QK ** -0.5
    kpos = jnp.arange(s_len)

    def block(args):
        i, a1, a2 = args
        qpos = i * BLOCK_Q + jnp.arange(BLOCK_Q)
        dist = (qpos[:, None] - kpos[None, :]).astype(jnp.float32)
        causal = dist >= 0
        bias = -slopes[:, None, None] * dist

        def probs(qb, kf):
            s = jnp.einsum('bhqd,bhkd->bhqk', qb, kf).astype(jnp.float32) * scale + bias
            return jax.nn.softmax(jnp.where(causal, s, -jnp.inf), axis=-1)

        p = probs(a1, k1) - lam * probs(a2, k2)
        return jnp.einsum('bhqk,bhkd->bhqd', p.astype(v.dtype), v)

    out = lax.map(block, (jnp.arange(s_len // BLOCK_Q), to_blocks(q1), to_blocks(q2)))
    return from_blocks(out)

def dilated_attention(q, k, v, slopes):
    b, g_n, hg, s_len, d = q.shape
    nb = s_len // BLOCK_Q
    scale = d ** -0.5
    qb = q.reshape(b, g_n, hg, nb, BLOCK_Q, d).transpose(3, 0, 1, 2, 4, 5)
    padded = []
    for g, (w, dil) in enumerate(DIL_CONFIGS):
        pad = ((0, 0), (0, 0), (w, 0), (0, 0))
        padded.append((jnp.pad(k[:, g], pad), jnp.pad(v[:, g], pad)))

    def block(args):
        i, qblk = args
        qpos = i * BLOCK_Q + jnp.arange(BLOCK_Q)
        outs, lses = [], []
        for g, (w, dil) in enumerate(DIL_CONFIGS):
            steps = np.arange(w // dil + 1) * dil
            local = np.arange(BLOCK_Q)[:, None] + w - steps[None, :]
            kp, vp = padded[g]
            kb = lax.dynamic_slice_in_dim(kp, i * BLOCK_Q, BLOCK_Q + w, axis=2)
            vb = lax.dynamic_slice_in_dim(vp, i * BLOCK_Q, BLOCK_Q + w, axis=2)
            kg = kb[:, :, local]
            vg = vb[:, :, local]
            steps_f = jnp.asarray(steps, dtype=jnp.float32)
            s = (jnp.einsum('bhqd,bhqnd->bhqn', qblk[:, g], kg).astype(jnp.float32) * scale
                 - slopes[g][:, None, None] * steps_f[None, None, :])
            valid = (qpos[:, None] - jnp.asarray(steps)[None, :]) >= 0
            s = jnp.where(valid, s, -jnp.inf)
            m = jnp.max(s, axis=-1, keepdims=True)
            e = jnp.exp(s - m)
            den = jnp.sum(e, axis=-1, keepdims=True)
            o = jnp.einsum('bhqn,bhqnd->bhqd', (e / den).astype(v.dtype), vg)
            outs.append(o.astype(jnp.float32))
            lses.append((m + jnp.log(den))[..., 0])
        wts = jax.nn.softmax(jnp.stack(lses, axis=0), axis=0)
        o = jnp.einsum('gbhq,gbhqd->bhqd', wts, jnp.stack(outs, axis=0))
        return o.astype(v.dtype)

    out = lax.map(block, (jnp.arange(nb), qb))
    return from_blocks(out)

def stick_breaking_attention(q, k, v):
    s_len = v.shape[2]
    scale = q.shape[-1] ** -0.5
    kpos = jnp.arange(s_len)

    def block(args):
        i, qblk = args
        qpos = i * BLOCK_Q + jnp.arange(BLOCK_Q)
        strict = kpos[None, :] < qpos[:, None]
        z = jnp.einsum('bhqd,bhkd->bhqk', qblk, k).astype(jnp.float32) * scale
        log_beta = jax.nn.log_sigmoid(z)
        log_keep = jnp.where(strict, jax.nn.log_sigmoid(-z), 0.0)
        after = lax.cumsum(log_keep, axis=3, reverse=True) - log_keep
        a = jnp.where(strict, jnp.exp(log_beta + after), 0.0)
        return jnp.einsum('bhqk,bhkd->bhqd', a.astype(v.dtype), v)

    out = lax.map(block, (jnp.arange(s_len // BLOCK_Q), to_blocks(q)))
    return from_blocks(out)

def causal_dwconv(h, w, b):
    c = h.shape[-1]
    y = lax.conv_general_dilated(h, w[:, None, :].astype(h.dtype), (1,), [(CONV_WIDTH - 1, 0)],
                                 dimension_numbers=('NWC', 'WIO', 'NWC'), feature_group_count=c)
    return y + b

def conv_ffn(h, w_up, conv_w, conv_b, w_down):
    u = causal_dwconv(h @ w_up, conv_w, conv_b)
    gate, up = jnp.split(u, 2, axis=-1)
    return (jax.nn.silu(gate) * up) @ w_down

def even_mixer(h, w_in, cq_g, w_uq, ckv_g, w_ukv, lam_q1, lam_k1, lam_q2, lam_k2,
               subln_g, w_out, layer_idx):
    b, s_len, _ = h.shape
    c_q, c_kv, k_rope, dq, dk, dv = split_cols(h @ w_in, EVEN_SPLITS)
    pos = jnp.arange(s_len)
    q = heads_first(rms_norm(c_q, cq_g) @ w_uq, MLA_HEADS)
    q_nope, q_rope = q[..., :MLA_NOPE], rope(q[..., MLA_NOPE:], pos)
    kv = heads_first(rms_norm(c_kv, ckv_g) @ w_ukv, MLA_HEADS)
    k_nope, v_mla = kv[..., :MLA_NOPE], kv[..., MLA_NOPE:]
    o_mla = mla_attention(q_nope, q_rope, k_nope, rope(k_rope, pos), v_mla)
    dq = dq.reshape(b, s_len, DIFF_HEADS, 2, DIFF_QK).transpose(0, 2, 3, 1, 4)
    dk = dk.reshape(b, s_len, DIFF_HEADS, 2, DIFF_QK).transpose(0, 2, 3, 1, 4)
    dv = heads_first(dv, DIFF_HEADS)
    lam_init = 0.8 - 0.6 * math.exp(-0.3 * layer_idx)
    f32 = jnp.float32
    lam = (jnp.exp(jnp.sum(lam_q1.astype(f32) * lam_k1.astype(f32)))
           - jnp.exp(jnp.sum(lam_q2.astype(f32) * lam_k2.astype(f32))) + lam_init)
    o_diff = diff_attention(dq[:, :, 0], dq[:, :, 1], dk[:, :, 0], dk[:, :, 1], dv, lam,
                            alibi_slopes(DIFF_HEADS))
    o_diff = rms_norm(o_diff, subln_g) * (1.0 - lam_init)
    return jnp.concatenate([heads_last(o_mla), heads_last(o_diff)], axis=-1) @ w_out

def odd_mixer(h, w_in, w_out):
    b, s_len, _ = h.shape
    cq, ck, cv, sq, sk, sv = split_cols(h @ w_in, ODD_SPLITS)

    def groups(t):
        return t.reshape(b, s_len, DIL_GROUPS, DIL_HEADS_PER_GROUP, HEAD_DIM).transpose(0, 2, 3, 1, 4)

    slopes = alibi_slopes(DIL_GROUPS * DIL_HEADS_PER_GROUP).reshape(DIL_GROUPS, DIL_HEADS_PER_GROUP)
    o_dil = dilated_attention(groups(cq), groups(ck), groups(cv), slopes)
    o_sb = stick_breaking_attention(heads_first(sq, SB_HEADS), heads_first(sk, SB_HEADS),
                                    heads_first(sv, SB_HEADS))
    return jnp.concatenate([heads_last(o_dil), heads_last(o_sb)], axis=-1) @ w_out

def second_inputs(seed: int = 0) -> dict:
    key = jax.random.key(seed)
    ks = iter(jax.random.split(key, 32))

    def nrm(shape, scale):
        return jax.random.normal(next(ks), shape, jnp.float32) * scale

    def gain(shape):
        return 1.0 + nrm(shape, 0.05)

    D = D_MODEL
    return {
        "x": nrm((BATCH, SEQ, D), 1.0),
        "ev_pre_g": gain((N_EVEN, D)),
        "ev_w_in": nrm((N_EVEN, D, EVEN_IN), D ** -0.5),
        "ev_cq_g": gain((N_EVEN, MLA_Q_RANK)),
        "ev_w_uq": nrm((N_EVEN, MLA_Q_RANK, MLA_HEADS * (MLA_NOPE + MLA_ROPE)), MLA_Q_RANK ** -0.5),
        "ev_ckv_g": gain((N_EVEN, MLA_KV_RANK)),
        "ev_w_ukv": nrm((N_EVEN, MLA_KV_RANK, MLA_HEADS * (MLA_NOPE + MLA_V)), MLA_KV_RANK ** -0.5),
        "ev_lam_q1": nrm((N_EVEN, DIFF_QK), 0.1),
        "ev_lam_k1": nrm((N_EVEN, DIFF_QK), 0.1),
        "ev_lam_q2": nrm((N_EVEN, DIFF_QK), 0.1),
        "ev_lam_k2": nrm((N_EVEN, DIFF_QK), 0.1),
        "ev_subln_g": gain((N_EVEN, DIFF_V)),
        "ev_w_out": nrm((N_EVEN, EVEN_OUT, D), EVEN_OUT ** -0.5),
        "ev_post_g": gain((N_EVEN, D)),
        "od_pre_g": gain((N_ODD, D)),
        "od_w_in": nrm((N_ODD, D, ODD_IN), D ** -0.5),
        "od_w_out": nrm((N_ODD, ODD_OUT, D), ODD_OUT ** -0.5),
        "od_post_g": gain((N_ODD, D)),
        "ffn_pre_g": gain((DEPTH_2, D)),
        "ffn_w_up": nrm((DEPTH_2, D, 2 * D_FF), D ** -0.5),
        "ffn_conv_w": nrm((DEPTH_2, CONV_WIDTH, 2 * D_FF), CONV_WIDTH ** -0.5),
        "ffn_conv_b": nrm((DEPTH_2, 2 * D_FF), 0.01),
        "ffn_w_down": nrm((DEPTH_2, D_FF, D), D_FF ** -0.5),
        "ffn_post_g": gain((DEPTH_2, D)),
    }

def second_block(x, ev_pre_g, ev_w_in, ev_cq_g, ev_w_uq, ev_ckv_g, ev_w_ukv, ev_lam_q1, ev_lam_k1,
              ev_lam_q2, ev_lam_k2, ev_subln_g, ev_w_out, ev_post_g, od_pre_g, od_w_in, od_w_out,
              od_post_g, ffn_pre_g, ffn_w_up, ffn_conv_w, ffn_conv_b, ffn_w_down, ffn_post_g):
    for i in range(DEPTH_2):
        j = i // 2
        if i % 2 == 0:
            h = rms_norm(x, ev_pre_g[j])
            h = even_mixer(h, ev_w_in[j], ev_cq_g[j], ev_w_uq[j], ev_ckv_g[j], ev_w_ukv[j],
                           ev_lam_q1[j], ev_lam_k1[j], ev_lam_q2[j], ev_lam_k2[j],
                           ev_subln_g[j], ev_w_out[j], i)
            x = x + rms_norm(h, ev_post_g[j])
        else:
            h = rms_norm(x, od_pre_g[j])
            h = odd_mixer(h, od_w_in[j], od_w_out[j])
            x = x + rms_norm(h, od_post_g[j])
        h = conv_ffn(rms_norm(x, ffn_pre_g[i]), ffn_w_up[i], ffn_conv_w[i], ffn_conv_b[i], ffn_w_down[i])
        x = x + rms_norm(h, ffn_post_g[i])
    return x


def setup_inputs(seed=0):
    out = dict(first_inputs(seed))
    for name, value in second_inputs(seed + 1).items():
        if name != "x":
            out[name + "_2"] = value
    return out


def reference(
    x, norm1_w, w_in, shift_mu, w0, w_up, a0, a_up, g_up, k_k, k_a, r_k, ln_x_w, ln_x_b, pool_w,
    pool_scale, w_out, norm2_w, peer_wq, peer_keys, peer_u, peer_v, norm_f_w, ev_pre_g_2,
    ev_w_in_2, ev_cq_g_2, ev_w_uq_2, ev_ckv_g_2, ev_w_ukv_2, ev_lam_q1_2, ev_lam_k1_2,
    ev_lam_q2_2, ev_lam_k2_2, ev_subln_g_2, ev_w_out_2, ev_post_g_2, od_pre_g_2, od_w_in_2,
    od_w_out_2, od_post_g_2, ffn_pre_g_2, ffn_w_up_2, ffn_conv_w_2, ffn_conv_b_2, ffn_w_down_2,
    ffn_post_g_2,
):
    x = first_block(
        x, norm1_w, w_in, shift_mu, w0, w_up, a0, a_up, g_up, k_k, k_a, r_k, ln_x_w, ln_x_b,
        pool_w, pool_scale, w_out, norm2_w, peer_wq, peer_keys, peer_u, peer_v, norm_f_w,
    )
    return second_block(
        x, ev_pre_g_2, ev_w_in_2, ev_cq_g_2, ev_w_uq_2, ev_ckv_g_2, ev_w_ukv_2, ev_lam_q1_2,
        ev_lam_k1_2, ev_lam_q2_2, ev_lam_k2_2, ev_subln_g_2, ev_w_out_2, ev_post_g_2,
        od_pre_g_2, od_w_in_2, od_w_out_2, od_post_g_2, ffn_pre_g_2, ffn_w_up_2, ffn_conv_w_2,
        ffn_conv_b_2, ffn_w_down_2, ffn_post_g_2,
    )


_drawn_inputs = setup_inputs


def setup_inputs(seed=0):
    import zlib

    import numpy as np

    out = dict(_drawn_inputs(seed))
    spreads = {}
    factors = {'ev_cq_g_2': 6.48,
     'ev_ckv_g_2': 3.655,
     'ev_lam_k2_2': 17.234,
     'ffn_conv_b_2': 4.902,
     'ev_lam_q1_2': 5.434,
     'ev_lam_k1_2': 4.279,
     'ev_subln_g_2': 4.522}
    for name, (base, spread) in spreads.items():
        noise = np.random.default_rng([zlib.crc32(name.encode()), seed]).standard_normal(out[name].shape)
        drawn = base * np.exp(spread * noise) if base else spread * noise
        out[name] = __import__('jax').numpy.asarray(drawn.astype(out[name].dtype))
    for name, factor in factors.items():
        out[name] = (out[name] * factor).astype(out[name].dtype)
    return out
```

```python
from contextlib import ExitStack, contextmanager

import numpy as np
import concourse.bass as bass
from concourse import mybir

F32 = mybir.dt.float32
U32 = mybir.dt.uint32
ALU = mybir.AluOpType
ACT = mybir.ActivationFunctionType
AX = mybir.AxisListType

P = 128
S = 512
TT = S // P
D = 1024
KD = D // P
RD = 512
PR = RD // P
HS = 64
LORA = 64
C = 64
NCH = S // C
DECAY = float(np.exp(-0.5))
GN_EPS = 64e-5
RMS_EPS = 1e-5
NORM_EPS = 1e-6
NEG = -1e30
IN1_TILES = 20
SHIFTED = 16


def buffer(nc, name, shape, dt=F32):
    return nc.sbuf_tensor(f"{name}_{len(STAGES)}", shape, dt)


class Steps:

    def __init__(self, eng, sem, base=0):
        self.eng, self.sem, self.n, self.base = eng, sem, 0, base

    def __call__(self, ins):
        self.n += 1
        ins.then_inc(self.sem, 1)
        return self.n

    def wait(self):
        self.eng.wait_ge(self.sem, self.base + self.n)


STAGES = []


@contextmanager
def stage(nc, *names):
    STAGES.append(names)
    sems = [nc.alloc_semaphore(f"s{len(STAGES)}_{n}") for n in names]
    yield sems
    nc.clear_and_free_semaphores(sems)
    nc.all_engine_barrier()


COLS = {}


def _cols():
    at = 0
    for name, n in (("norm1_w", 8), ("mu0", SHIFTED), ("mu1", SHIFTED), ("w0", 8), ("a0", 8), ("k_k", 4),
                    ("k_a", 4), ("r_k", 4), ("ln_x_w", 4), ("ln_x_b", 4), ("pool_scale", 4),
                    ("norm2_w", 8), ("ev_pre", 8), ("cq_g", 2), ("ckv_g", 1), ("subln_g", 1),
                    ("od_pre", 8), ("ffn_pre", 16), ("conv_w", 2 * 3 * 44), ("conv_b", 2 * 44)):
        COLS[name] = (at, n)
        at += n
    return at


NCOLS = _cols()


class Chip:

    def __init__(self, nc, ctx):
        sb = lambda name, shape, dt=F32: ctx.enter_context(buffer(nc, name, shape, dt))
        self.x = sb("x_res", [P, TT, D])
        self.hT = sb("hT", [P, KD, S])
        self.cols = sb("cols", [P, NCOLS])
        self.ident = sb("ident", [P, P])
        self.stack2 = sb("stack2", [P, HS])
        self.ps = ctx.enter_context(nc.psum_tensor("ps", [P, 8, 512], F32))

    def col(self, name, i=0, n=1):
        at, _ = COLS[name]
        return self.cols[:, at + i:at + i + n]


def load_constants(nc, chip, A):
    with stage(nc, "constants_loaded", "constants_step") as (loaded, step):
        with nc.Block() as block:
            @block.sync
            def _(sp):
                sp.dma_start(chip.x[:], A["x"].rearrange("(t p) d -> p t d", p=P)).then_inc(loaded, 16)
                sp.dma_start(chip.cols[:], A["cols"]).then_inc(loaded, 16)
                sp.wait_ge(loaded, 32)

            @block.gpsimd
            def _(pool):
                done = Steps(pool, step)
                done(pool.memset(chip.ident[:], 0.0))
                done(pool.memset(chip.stack2[:], 0.0))
                done.wait()
                done(pool.affine_select(out=chip.ident[:], in_=chip.ident[:], compare_op=ALU.not_equal, fill=1.0,
                                        base=0, pattern=[[-1, P]], channel_multiplier=1))
                done(pool.affine_select(out=chip.stack2[:], in_=chip.stack2[:], compare_op=ALU.not_equal,
                                        fill=1.0, base=0, pattern=[[-1, HS]], channel_multiplier=1))
                done.wait()
                done(pool.affine_select(out=chip.stack2[:], in_=chip.stack2[:], compare_op=ALU.not_equal,
                                        fill=1.0, base=-HS, pattern=[[-1, HS]], channel_multiplier=1))
                done.wait()


def norm_transpose(nc, chip, eps, gain, gain_at, keep=None):
    with ExitStack() as ctx:
        h = keep if keep is not None else ctx.enter_context(buffer(nc, "norm_h", [P, TT, D], F32))
        junk = ctx.enter_context(buffer(nc, "norm_squares", [P, D], F32))
        st = ctx.enter_context(buffer(nc, "norm_stats", [P, 4, TT], F32))
        with stage(nc, "squares", "mean_ready", "root_ready", "v_step", "normed", "turned", "emptied_act",
                   "emptied_vec") as (squares, mean_ready, root_ready, v_step, normed, turned, em_a, em_v):
            with nc.Block() as block:
                @block.scalar
                def _(act):
                    for t in range(TT):
                        if t:
                            act.wait_ge(squares, t)
                        act.activation(junk[:], chip.x[:, t, :], ACT.Square,
                                       accum_out=st[:, 0, t:t + 1]).then_inc(squares, 1)
                    act.wait_ge(mean_ready, 1)
                    act.activation(st[:, 2, :], st[:, 1, :], ACT.Sqrt).then_inc(root_ready, 1)
                    for k in range(0, KD, 2):
                        act.wait_ge(turned, k + 1)
                        act.activation(chip.hT[:, k, :], chip.ps[:, k, :], ACT.Copy,
                                       scale=chip.col(gain, gain_at + k)).then_inc(em_a, 1)
                    act.wait_ge(em_a, KD // 2)

                @block.vector
                def _(dve):
                    done = Steps(dve, v_step)
                    dve.wait_ge(squares, TT)
                    dve.tensor_scalar(st[:, 1, :], st[:, 0, :], 1.0 / D, eps, ALU.mult,
                                      ALU.add).then_inc(mean_ready, 1)
                    dve.wait_ge(root_ready, 1)
                    done(dve.reciprocal(st[:, 3, :], st[:, 2, :]))
                    done.wait()
                    for t in range(TT):
                        dve.tensor_scalar(h[:, t, :], chip.x[:, t, :], st[:, 3, t:t + 1], None,
                                          ALU.mult).then_inc(normed, 1)
                    for k in range(1, KD, 2):
                        dve.wait_ge(turned, k + 1)
                        dve.tensor_scalar(chip.hT[:, k, :], chip.ps[:, k, :], chip.col(gain, gain_at + k), None,
                                          ALU.mult).then_inc(em_v, 1)
                    dve.wait_ge(em_v, KD // 2)

                @block.tensor
                def _(pe):
                    pe.wait_ge(normed, TT)
                    for k in range(KD):
                        for t in range(TT):
                            last = pe.transpose(chip.ps[:, k, t * P:(t + 1) * P], h[:, t, k * P:(k + 1) * P],
                                                chip.ident[:])
                        last.then_inc(turned, 1)


def project_in_1(nc, chip, A, b):
    RING = 5
    with ExitStack() as ctx:
        ring = ctx.enter_context(buffer(nc, "w_in_ring", [P, RING, KD, P], F32))
        rest = ctx.enter_context(buffer(nc, "mu_rest", [P, SHIFTED], F32))
        dst = ([b.rT[:, i, :] for i in range(4)] + [b.kT[:, i, :] for i in range(4)]
               + [b.vT[:, i, :] for i in range(4)] + [b.loraT[:, i, :] for i in range(4)])
        with stage(nc, *[f"w{i}" for i in range(RING)], "rest_ready", "product", "scaled", "shifted", "prev",
                   "pooled") as (*w, rest_ready, product, scaled, shifted, prev, pooled):
            with nc.Block() as block:
                @block.sync
                def _(sp):
                    for m in range(IN1_TILES):
                        if m >= RING:
                            sp.wait_ge(product, m - RING + 1)
                        sp.dma_start(ring[:, m % RING], A["w_in"][m]).then_inc(w[m % RING], 16)

                @block.tensor
                def _(pe):
                    for m in range(IN1_TILES):
                        pe.wait_ge(w[m % RING], 16 * (m // RING + 1))
                        if m >= 8:
                            if m - 8 < SHIFTED:
                                pe.wait_ge(shifted, m - 7)
                            else:
                                pe.wait_ge(pooled, m - 7 - SHIFTED)
                        for k in range(KD):
                            last = pe.matmul(chip.ps[:, m % 8, :], ring[:, m % RING, k, :], chip.hT[:, k, :],
                                             start=k == 0, stop=k == KD - 1)
                        last.then_inc(product, 1)

                @block.scalar
                def _(act):
                    act.wait_ge(rest_ready, 2)
                    for m in range(SHIFTED):
                        act.wait_ge(product, m + 1)
                        act.activation(dst[m], chip.ps[:, m % 8, :], ACT.Copy,
                                       scale=rest[:, m:m + 1]).then_inc(scaled, 1)
                    for g in range(4):
                        act.wait_ge(product, SHIFTED + g + 1)
                        act.activation(b.poolT[:, g, 8:8 + S], chip.ps[:, (SHIFTED + g) % 8, :],
                                       ACT.Copy).then_inc(pooled, 1)
                    act.wait_ge(pooled, 4)

                @block.vector
                def _(dve):
                    dve.tensor_tensor(rest[:], chip.col("mu0", 0, SHIFTED), chip.col("mu1", 0, SHIFTED),
                                      ALU.add).then_inc(rest_ready, 1)
                    dve.wait_ge(rest_ready, 1)
                    dve.tensor_scalar(rest[:], rest[:], -1.0, 1.0, ALU.mult, ALU.add).then_inc(rest_ready, 1)
                    for m in range(SHIFTED):
                        o, ps = dst[m], chip.ps[:, m % 8, :]
                        dve.wait_ge(scaled, m + 1)
                        dve.scalar_tensor_tensor(out=o[:, 1:S], in0=ps[:, 0:S - 1], scalar=chip.col("mu0", m),
                                                 in1=o[:, 1:S], op0=ALU.mult, op1=ALU.add).then_inc(prev, 1)
                        dve.wait_ge(prev, m + 1)
                        dve.scalar_tensor_tensor(out=o[:, 0:S - 1], in0=ps[:, 1:S], scalar=chip.col("mu1", m),
                                                 in1=o[:, 0:S - 1], op0=ALU.mult, op1=ALU.add).then_inc(shifted, 1)
                    dve.wait_ge(shifted, SHIFTED)


def rwkv_inputs(nc, chip, A, b):
    with ExitStack() as ctx:
        sb = lambda name, shape: ctx.enter_context(buffer(nc, name, shape, F32))
        ups = sb("ups", [P, 2, RD])
        gup = sb("gup", [P, 2, RD])
        sq = sb("kk_square", [P, PR, S])
        rr = sb("r_rk", [P, PR, S])
        oma = sb("one_less_ka", [P, PR])
        halves = sb("halves", [P, P])
        with stage(nc, "loras_loaded", "a_step", "v_step", "squared", "summed", "rooted", "low_ready", "up_done",
                   "sig_done", "gate_done", "gate_out", "bonus_in", "bonus_sum", "kept", "spilled", "halves_ready") as \
                (loaded, a_step, v_step, squared, summed, rooted, low_ready, up_done, sig_done, gate_done,
                 gate_out, bonus_in, bonus_sum, kept, spilled, halves_ready):
            with nc.Block() as block:
                @block.sync
                def _(sp):
                    sp.dma_start(ups[:, 0, :], A["w_up"]).then_inc(loaded, 16)
                    sp.dma_start(ups[:, 1, :], A["a_up"]).then_inc(loaded, 16)
                    sp.dma_start(gup[:, 0, :], A["g_up"][0:P]).then_inc(loaded, 16)
                    sp.dma_start(gup[0:32, 1, :], A["g_up"][P:P + 32]).then_inc(loaded, 16)
                    sp.wait_ge(kept, 1)
                    for n, t in enumerate((b.decay, b.a, b.kd)):
                        sp.dma_start(A["scratch"][:, n].rearrange("d p s -> p d s"), t[:]).then_inc(spilled, 16)
                    sp.wait_ge(spilled, 48)

                @block.scalar
                def _(act):
                    act.activation(b.loraT[:, 0, :], b.loraT[:, 0, :], ACT.Tanh).then_inc(low_ready, 1)
                    act.activation(b.loraT[:, 2:4, :], b.loraT[:, 2:4, :], ACT.Sigmoid).then_inc(low_ready, 1)
                    for n in range(16):
                        act.wait_ge(up_done, n + 1)
                        out = (b.decay if n < 8 else b.a)[:, n % 8, :]
                        act.activation(out, chip.ps[:, n % 4, :], ACT.Sigmoid,
                                       bias=chip.col("w0" if n < 8 else "a0", n % 8)).then_inc(sig_done, 1)
                    for i in range(PR):
                        act.wait_ge(gate_done, i + 1)
                        act.activation(b.gateT[:, i, :], chip.ps[:, i, :], ACT.Copy).then_inc(gate_out, 1)
                    act.wait_ge(squared, PR)
                    for i in range(PR):
                        act.wait_ge(summed, i + 1)
                        act.activation(sq[:, i, :], chip.ps[:, 4 + i, :], ACT.Sqrt).then_inc(rooted, 1)
                    act.wait_ge(rooted, PR)

                @block.gpsimd
                def _(pool):
                    pool.memset(halves[0:HS, 0:HS], 1.0).then_inc(halves_ready, 1)
                    pool.memset(halves[HS:P, HS:P], 1.0).then_inc(halves_ready, 1)
                    pool.memset(halves[0:HS, HS:P], 0.0).then_inc(halves_ready, 1)
                    pool.memset(halves[HS:P, 0:HS], 0.0).then_inc(halves_ready, 1)

                @block.tensor
                def _(pe):
                    pe.wait_ge(halves_ready, 4)
                    for i in range(PR):
                        pe.wait_ge(squared, i + 1)
                        pe.matmul(chip.ps[:, 4 + i, :], halves[:], sq[:, i, :], start=True,
                                  stop=True).then_inc(summed, 1)
                    pe.wait_ge(loaded, 64)
                    pe.wait_ge(low_ready, 2)
                    for n in range(16):
                        d, i = n // 4 % 2, n % 4
                        if n >= 4:
                            pe.wait_ge(sig_done, n - 3)
                        pe.matmul(chip.ps[:, n % 4, :], ups[d * LORA:(d + 1) * LORA, n // 8, i * P:(i + 1) * P],
                                  b.loraT[d * LORA:(d + 1) * LORA, n // 8, :], start=True,
                                  stop=True).then_inc(up_done, 1)
                    pe.wait_ge(sig_done, 16)
                    for i in range(PR):
                        pe.matmul(chip.ps[:, i, :], gup[:, 0, i * P:(i + 1) * P], b.loraT[:, 2, :], start=True,
                                  stop=False)
                        pe.matmul(chip.ps[:, i, :], gup[0:32, 1, i * P:(i + 1) * P], b.loraT[0:32, 3, :],
                                  start=False, stop=True).then_inc(gate_done, 1)
                    pe.wait_ge(rooted, PR)
                    for i in range(PR):
                        pe.wait_ge(bonus_in, i + 1)
                        pe.matmul(chip.ps[:, 4 + i, :], halves[:], rr[:, i, :], start=True,
                                  stop=True).then_inc(bonus_sum, 1)

                @block.vector
                def _(dve):
                    done = Steps(dve, v_step)
                    for i in range(PR):
                        done(dve.tensor_scalar(b.kk[:, i, :], b.kT[:, i, :], chip.col("k_k", i), None, ALU.mult))
                    done(dve.tensor_scalar(oma[:], chip.col("k_a", 0, 4), -1.0, 1.0, ALU.mult, ALU.add))
                    done.wait()
                    for i in range(PR):
                        dve.tensor_tensor(sq[:, i, :], b.kk[:, i, :], b.kk[:, i, :], ALU.mult).then_inc(squared, 1)
                    for i in range(PR):
                        done(dve.tensor_scalar(rr[:, i, :], b.rT[:, i, :], chip.col("r_k", i), None, ALU.mult))
                    dve.wait_ge(sig_done, 16)
                    for n in range(8):
                        done(dve.tensor_scalar(b.kd[:, n, :], b.a[:, n, :], chip.col("k_a", n % 4),
                                               oma[:, n % 4:n % 4 + 1], ALU.mult, ALU.add))
                        done.wait()
                        done(dve.tensor_tensor(b.kd[:, n, :], b.kd[:, n, :], b.kT[:, n % 4, :], ALU.mult))
                    dve.wait_ge(rooted, PR)
                    done(dve.tensor_scalar(sq[:], sq[:], 1e-12, None, ALU.max))
                    done.wait()
                    done(dve.reciprocal(sq[:], sq[:]))
                    done.wait()
                    done(dve.tensor_tensor(b.kk[:], b.kk[:], sq[:], ALU.mult))
                    done.wait()
                    for i in range(PR):
                        done(dve.tensor_tensor(sq[:, i, :], b.kd[:, i, :], b.kd[:, 4 + i, :], ALU.add))
                        done.wait()
                        dve.tensor_tensor(rr[:, i, :], rr[:, i, :], sq[:, i, :], ALU.mult).then_inc(bonus_in, 1)
                    for i in range(PR):
                        dve.wait_ge(bonus_sum, i + 1)
                        done(dve.tensor_tensor(b.bonusT[:, i, :], chip.ps[:, 4 + i, :], b.vT[:, i, :], ALU.mult))
                    done.wait()
                    for n in range(8):
                        done(dve.tensor_tensor(b.a[:, n, :], b.a[:, n, :], b.kk[:, n % 4, :], ALU.mult))
                    done.wait()
                    dve.memset(oma[:], 0.0).then_inc(kept, 1)


def recurrence(nc, chip, b, A, rev):
    with ExitStack() as ctx:
        sb = lambda name, shape: ctx.enter_context(buffer(nc, name, shape, F32))
        M1 = sb("M1", [P, PR, NCH, P])
        M2 = sb("M2", [P, PR, NCH, P])
        C1 = sb("C1", [P, NCH, PR, HS])
        C2 = sb("C2", [P, NCH, PR, HS])
        with ExitStack() as inner:
            _chunks(nc, chip, b, A, rev, M1, M2, C1, C2, lambda n, s: inner.enter_context(buffer(nc, n, s, F32)))
        _chain(nc, chip, b, rev, M1, M2, C1, C2, sb)


ROUNDS = 14
DVE_IDLE = (8, 10)
ACT_IDLE = (6, 11, 12, 13)


def signals(idle, n):
    whole, part = divmod(n + 1, 2 * ROUNDS)
    return whole * 2 * (ROUNDS - len(idle)) + sum(m // 2 not in idle for m in range(part))


def _chunks(nc, chip, b, A, rev, M1, M2, C1, C2, sb):
    E = {n: sb("E" + n, [P, NCH, P]) for n in ("alpha", "beta", "kappa", "rho", "beta_end", "kappa_end", "v")}
    cum = sb("cum", [P, S])
    grow = sb("grow", [P, 3, S])
    start = sb("chunk_start", [P, S])
    strict = sb("strict", [P, P])
    incl = sb("incl", [P, P])
    near = sb("near", [P, 2, P])
    far = sb("far", [P, 2, P])
    blk = M1[:, 0, 0, :]
    fed = sb("fed", [P, 2, 3, S])
    B = []
    for i in range(2):
        B.append({n: sb(f"{n}{i}", [P, 4, w]) for n, w in (
            ("DD", 2 * P), ("Fn", P), ("Fm", P), ("QB", 2 * P), ("BT", P), ("Qv", P), ("kT_", P),
            ("V", HS), ("XA", HS + P), ("R", P))})
        w = B[-1]
        whole = w["DD"][:].rearrange("p u f -> p (u f)")
        w["Dn"] = whole[:, 0:4 * P].rearrange("p (u f) -> p u f", u=4)
        w["Dm"] = whole[:, 4 * P:8 * P].rearrange("p (u f) -> p u f", u=4)
        w["WA"] = whole[:, 0:4 * (HS + P)].rearrange("p (u f) -> p u f", u=4)
        w["RT"] = w["BT"]
    ps = chip.ps
    with stage(nc, "mask_step", "e_step_v", "e_step_a", "e_step_p", "masks_ready", "pe_round", "dve_round",
               "act_round", "v_step", "fed0", "fed1") as (mask_step, e_v, e_a, e_p, masks_ready, pe_round, dve_round, act_round,
                                          v_step, fed0, fed1):
        def bc(m):
            return m.rearrange("p (o f) -> p o f", o=1).to_broadcast([P, 4, P])

        def banks(i, k, w=P):
            if w == P:
                return ps[:, 4 * i + k, :].rearrange("p (u f) -> p u f", u=4)
            return ps[:, 4 * i + k:4 * i + k + 2, :].rearrange("p b (u f) -> p (b u) f", u=2)

        def quad(i, k, u, w):
            if w == P:
                return ps[:, 4 * i + k, u * P:(u + 1) * P]
            return ps[:, 4 * i + k + u // 2, (u % 2) * 2 * P:(u % 2) * 2 * P + w]

        with nc.Block() as block:
            @block.gpsimd
            def _(pool):
                done = Steps(pool, mask_step)
                for n in E:
                    done(pool.memset(E[n][:], 0.0))
                done(pool.memset(start[:], 1.0))
                done(pool.memset(strict[:], 1.0))
                done(pool.memset(incl[:], 1.0))
                done(pool.memset(far[:, 1, :], 1.0))
                done(pool.memset(blk, 1.0))
                done.wait()
                edge = C - 1 if rev else 0
                done(pool.memset(start[:, edge:S:C], 0.0))
                sg = -1 if rev else 1
                for m, op, s_ in ((strict[:], ALU.is_gt, sg), (incl[:], ALU.is_ge, sg), (far[:, 1, :], ALU.is_gt, -sg)):
                    done(pool.affine_select(out=m, in_=m, compare_op=op, fill=0.0, base=0, pattern=[[s_, P]],
                                            channel_multiplier=-s_))
                v = blk.rearrange("p (g f) -> p g f", f=16)
                done(pool.affine_select(out=v, in_=v, compare_op=ALU.is_ge, fill=0.0, base=0,
                                        pattern=[[-16, 8], [0, 16]], channel_multiplier=1))
                done.wait()
                done(pool.affine_select(out=v, in_=v, compare_op=ALU.is_ge, fill=0.0, base=15,
                                        pattern=[[16, 8], [0, 16]], channel_multiplier=-1))
                done.wait()
                done(pool.tensor_tensor(near[:, 0, :], strict[:], blk, ALU.mult))
                done(pool.tensor_tensor(near[:, 1, :], far[:, 1, :], blk, ALU.mult))
                done.wait()
                done(pool.tensor_tensor(far[:, 0, :], strict[:], near[:, 0, :], ALU.subtract))
                done(pool.tensor_tensor(far[:, 1, :], far[:, 1, :], near[:, 1, :], ALU.subtract))
                done.wait()
                pool.memset(cum[:, 0:1], 0.0).then_inc(masks_ready, 1)

            def chunked(ap):
                return ap.rearrange("p (c t) -> p c t", t=C)

            @block.sync
            def _(sp):
                for g in range(PR):
                    if g >= 2:
                        sp.wait_ge(e_v, 2 * g - 2)
                    sp.dma_start(fed[:, g % 2], A["scratch"][(4 if rev else 0) + g].rearrange("n p s -> p n s"))\
                        .then_inc((fed0, fed1)[g % 2], 16)

            @block.vector
            def _(dve):
                done = Steps(dve, v_step)
                dve.wait_ge(masks_ready, 1)
                for g in range(PR):
                    if g:
                        dve.wait_ge(pe_round, 2 * ROUNDS * g)
                    dve.wait_ge((fed0, fed1)[g % 2], 16 * (g // 2 + 1))
                    decay, bb, kd = (fed[:, g % 2, n, :] for n in range(3))
                    flip = slice(None, None, -1) if rev else slice(None)
                    done(dve.tensor_tensor_scan(cum[:, flip], start[:, flip], decay[:, flip], 0.0, ALU.mult,
                                                ALU.add))
                    done.wait()
                    dve.tensor_tensor(grow[:, 2, :], cum[:], decay, ALU.subtract).then_inc(e_v, 1)
                    dve.wait_ge(e_a, g + 1)
                    src = {"alpha": (b.kk[:, g, :], 2), "beta": (bb, 1), "kappa": (kd, 1),
                           "rho": (b.rT[:, g, :], 0)}
                    for n, (s_, w) in src.items():
                        for h in range(2):
                            r = slice(h * HS, (h + 1) * HS)
                            done(dve.tensor_tensor(E[n][r, :, r], chunked(s_[r]), chunked(grow[r, w, :]), ALU.mult))
                    for h in range(2):
                        r = slice(h * HS, (h + 1) * HS)
                        done(dve.tensor_copy(E["v"][r, :, r], chunked(b.vT[r, g, :])))
                    done.wait()
                    at = 0 if rev else C - 1
                    pend = grow[:, 0, at:S:C].rearrange("p (c o) -> p c o", o=1).to_broadcast([P, NCH, P])
                    done(dve.tensor_tensor(E["beta_end"][:], E["beta"][:], pend, ALU.mult))
                    dve.tensor_tensor(E["kappa_end"][:], E["kappa"][:], pend, ALU.mult).then_inc(e_v, 1)
                    done.wait()
                    dve.wait_ge(e_v, 2 * g + 2)
                    for r in range(ROUNDS):
                        for i in range(2):
                            n = (g * ROUNDS + r) * 2 + i
                            dve.wait_ge(pe_round, n + 1)
                            w, c0 = B[i], 4 * i
                            fin = None
                            if r == 0:
                                done(dve.tensor_tensor(w["Dn"][:], banks(i, 0, 256)[:, :, 0:P], bc(near[:, 0, :]), ALU.mult))
                                done(dve.tensor_tensor(w["Fn"][:], banks(i, 0, 256)[:, :, 0:P], bc(far[:, 0, :]), ALU.mult))
                                done(dve.tensor_tensor(w["Dm"][:], banks(i, 2), bc(near[:, 1, :]), ALU.mult))
                                done(dve.tensor_tensor(w["Fm"][:], banks(i, 2), bc(far[:, 1, :]), ALU.mult))
                                done.wait()
                                done(dve.tensor_tensor(w["R"][:], bc(chip.ident[:]), w["Dn"][:], ALU.subtract))
                                fin = dve.tensor_tensor(w["QB"][:, :, 0:P], banks(i, 0, 256)[:, :, P:256], bc(incl[:]), ALU.mult)
                            elif r == 1:
                                done(dve.tensor_tensor(w["BT"][:], banks(i, 0, 256)[:, :, 0:P], bc(strict[:]), ALU.mult))
                                fin = dve.tensor_tensor(w["Qv"][:], banks(i, 0, 256)[:, :, P:256], bc(incl[:]), ALU.mult)
                            elif r == 2:
                                fin = dve.tensor_copy(w["V"][:], ps[:, 4 * i + 1, 0:4 * HS].rearrange("p (u f) -> p u f", u=4))
                            elif r == 3:
                                fin = dve.tensor_copy(w["Dn"][:], banks(i, 0))
                            elif r in (4, 5):
                                done(dve.tensor_tensor(w["R"][:], w["R"][:], banks(i, 2), ALU.add))
                                if r == 4:
                                    fin = dve.tensor_copy(w["Dn"][:], banks(i, 0))
                                else:
                                    fin = dve.tensor_copy(w["XA"][:, :, 0:HS], ps[:, 4 * i + 3, 0:4 * HS].rearrange("p (u f) -> p u f", u=4))
                            elif r == 6:
                                fin = dve.tensor_tensor(w["R"][:], w["R"][:], banks(i, 2), ALU.add)
                            elif r == 7:
                                done(dve.tensor_copy(w["Dn"][:], banks(i, 0)))
                                fin = dve.tensor_tensor(w["Fn"][:], bc(chip.ident[:]), banks(i, 0), ALU.subtract)
                            elif r == 9:
                                fin = dve.tensor_tensor(w["Fn"][:], w["Fn"][:], banks(i, 0), ALU.add)
                            elif r == 11:
                                fin = dve.tensor_scalar(w["WA"][:], banks(i, 0, 256)[:, :, 0:HS + P], -1.0, None, ALU.mult)
                            elif r == 12:
                                done(dve.tensor_tensor(M1[:, g, c0:c0 + 4, :], banks(i, 0, 256)[:, :, 0:P],
                                                       E["rho"][:, c0:c0 + 4, :], ALU.add))
                                for u in range(4):
                                    pe_col = grow[:, 0, (c0 + u) * C + at:(c0 + u) * C + at + 1]
                                    fin = dve.scalar_tensor_tensor(
                                        out=M2[:, g, c0 + u, :], in0=chip.ident[:], scalar=pe_col,
                                        in1=quad(i, 0, u, 256)[:, P:256], op0=ALU.mult, op1=ALU.add)
                                    if u < 3:
                                        done(fin)
                            elif r == 13:
                                done(dve.tensor_copy(C1[:, c0:c0 + 4, g, :], ps[:, 4 * i, 0:256].rearrange("p (u f) -> p u f", u=4)))
                                fin = dve.tensor_copy(C2[:, c0:c0 + 4, g, :], ps[:, 4 * i + 1, 0:256].rearrange("p (u f) -> p u f", u=4))
                            if r not in DVE_IDLE:
                                fin.then_inc(dve_round, 1)

            @block.scalar
            def _(act):
                for g in range(PR):
                    act.wait_ge(e_v, 2 * g + 1)
                    if g:
                        act.wait_ge(dve_round, signals(DVE_IDLE, 2 * ROUNDS * g - 1))
                    act.activation(grow[:, 0, :], cum[:], ACT.Exp, scale=-DECAY).then_inc(e_p, 1)
                    act.activation(grow[:, 1, :], cum[:], ACT.Exp, scale=DECAY).then_inc(e_p, 1)
                    act.wait_ge(e_p, 2 * g + 2)
                    act.activation(grow[:, 2, :], grow[:, 2, :], ACT.Exp, scale=-DECAY).then_inc(e_a, 1)
                    for r in range(ROUNDS):
                        for i in range(2):
                            n = (g * ROUNDS + r) * 2 + i
                            act.wait_ge(pe_round, n + 1)
                            w = B[i]
                            cp = lambda o, s_: act.activation(o, s_, ACT.Copy)
                            if r == 0:
                                fin = cp(w["XA"][:, :, HS:HS + P], banks(i, 3))
                            elif r == 1:
                                fin = cp(w["QB"][:, :, P:2 * P], banks(i, 2))
                            elif r == 2:
                                fin = cp(w["kT_"][:], banks(i, 0))
                            elif r == 3:
                                fin = cp(w["Dm"][:], banks(i, 1))
                            elif r in (4, 5):
                                fin = cp(w["Dm"][:], banks(i, 1))
                            elif r == 7:
                                fin = cp(w["Dm"][:], banks(i, 1))
                            elif r == 8:
                                fin = cp(w["Fm"][:], banks(i, 0))
                            elif r == 9:
                                fin = cp(w["RT"][:], banks(i, 1))
                            elif r == 10:
                                fin = cp(w["R"][:], banks(i, 0))
                            if r not in ACT_IDLE:
                                fin.then_inc(act_round, 1)

            @block.tensor
            def _(pe):
                for g in range(PR):
                    pe.wait_ge(e_v, 2 * g + 2)
                    for r in range(ROUNDS):
                        for i in range(2):
                            n = (g * ROUNDS + r) * 2 + i
                            if n >= 2:
                                pe.wait_ge(dve_round, signals(DVE_IDLE, n - 2))
                                pe.wait_ge(act_round, signals(ACT_IDLE, n - 2))
                            w = B[i]
                            last = None
                            for u in range(4):
                                c = 4 * i + u
                                al, be, ka, rh = (E[x][:, c, :] for x in ("alpha", "beta", "kappa", "rho"))

                                def mm(dst, lhsT, rhs, start=True, stop=True):
                                    return pe.matmul(dst, lhsT, rhs, start=start, stop=stop)

                                def q(k, width=P):
                                    return quad(i, k, u, width)

                                X = lambda name: w[name][:, u, :]
                                if r == 0:
                                    mm(quad(i, 0, u, 256)[:, 0:P], be, al)
                                    mm(quad(i, 0, u, 256)[:, P:256], be, rh)
                                    mm(q(2), al, be)
                                    last = pe.transpose(q(3), al, chip.ident[:])
                                elif r == 1:
                                    mm(quad(i, 0, u, 256)[:, 0:P], ka, al)
                                    mm(quad(i, 0, u, 256)[:, P:256], ka, rh)
                                    last = pe.transpose(q(2), E["beta_end"][:, c, :], chip.ident[:])
                                elif r == 2:
                                    pe.transpose(q(0), E["kappa_end"][:, c, :], chip.ident[:])
                                    last = mm(ps[:, 4 * i + 1, u * HS:(u + 1) * HS], E["v"][:, c, :], chip.stack2[:])
                                elif r == 3:
                                    mm(q(0), X("Dm"), X("Dn"))
                                    last = mm(q(1), X("Dn"), X("Dm"))
                                elif r == 4:
                                    mm(q(0), X("Dm"), X("Dn"))
                                    mm(q(1), X("Dn"), X("Dm"))
                                    last = mm(q(2), X("Dm"), X("R"))
                                elif r == 5:
                                    mm(ps[:, 4 * i + 3, u * HS:(u + 1) * HS], X("BT"), X("V"))
                                    mm(q(1), X("Dn"), X("Dm"))
                                    last = mm(q(2), X("Dm"), X("R"))
                                elif r == 6:
                                    last = mm(q(2), X("Dm"), X("R"))
                                elif r == 7:
                                    mm(q(0), X("Fm"), X("R"))
                                    last = mm(q(1), X("R"), X("Fm"))
                                elif r == 8:
                                    last = mm(q(0), X("Dn"), X("Dm"))
                                elif r == 9:
                                    mm(q(0), X("Fm"), X("Fn"))
                                    last = pe.transpose(q(1), X("R"), chip.ident[:])
                                elif r == 10:
                                    last = mm(q(0), X("RT"), X("Fn"))
                                elif r == 11:
                                    last = mm(quad(i, 0, u, 256)[:, 0:HS + P], X("R"), X("XA"))
                                elif r == 12:
                                    last = mm(quad(i, 0, u, 256), w["WA"][:, u, HS:HS + P], X("QB"))
                                elif r == 13:
                                    o1 = ps[:, 4 * i, u * HS:(u + 1) * HS]
                                    mm(o1, X("Qv"), X("V"), stop=False)
                                    mm(o1, w["QB"][:, u, 0:P], w["WA"][:, u, 0:HS], start=False)
                                    o2 = ps[:, 4 * i + 1, u * HS:(u + 1) * HS]
                                    mm(o2, X("kT_"), X("V"), stop=False)
                                    last = mm(o2, w["QB"][:, u, P:2 * P], w["WA"][:, u, 0:HS], start=False)
                            last.then_inc(pe_round, 1)


def _chain(nc, chip, b, rev, M1, M2, C1, C2, sb):
    st = sb("states", [P, NCH + 1, PR, HS])
    order = list(range(NCH))[::-1] if rev else list(range(NCH))
    with stage(nc, "stepped", "state_ready", "out_ready", "v_step") as (stepped, state_ready, out_ready, v_step):
        with nc.Block() as block:
            @block.tensor
            def _(pe):
                for n, c in enumerate(order[:-1]):
                    pe.wait_ge(state_ready, n + 1)
                    for g in range(PR):
                        last = pe.matmul(chip.ps[:, n % 2, g * HS:(g + 1) * HS], M2[:, g, c, :], st[:, n, g, :],
                                         start=True, stop=True)
                    last.then_inc(stepped, 1)
                pe.wait_ge(state_ready, NCH)
                for n, c in enumerate(order):
                    for g in range(PR):
                        u = c * PR + g
                        last = pe.matmul(chip.ps[:, 4 + u // 8, (u % 8) * HS:(u % 8 + 1) * HS], M1[:, g, c, :],
                                         st[:, n, g, :], start=True, stop=True)
                last.then_inc(out_ready, 1)

            @block.vector
            def _(dve):
                done = Steps(dve, v_step)
                dve.memset(st[:, 0], 0.0).then_inc(state_ready, 1)
                for n, c in enumerate(order[:-1]):
                    dve.wait_ge(stepped, n + 1)
                    dve.tensor_tensor(st[:, n + 1], chip.ps[:, n % 2, 0:PR * HS].rearrange("p (g v) -> p g v", g=PR),
                                      C2[:, c], ALU.add).then_inc(state_ready, 1)
                if rev:
                    done(dve.tensor_tensor(C1[:], C1[:], b.out, ALU.add))
                dve.wait_ge(out_ready, 1)
                done.wait()
                done(dve.tensor_tensor(b.out.rearrange("p c g v -> p (c g v)"),
                                       chip.ps[:, 4:8, :].rearrange("p b n -> p (b n)"),
                                       C1[:].rearrange("p c g v -> p (c g v)"), ALU.add))
                done.wait()


def rwkv_output(nc, chip, A, b, yT):
    NU = NCH * PR
    with ExitStack() as ctx:
        sb = lambda name, shape: ctx.enter_context(buffer(nc, name, shape, F32))
        sq = sb("out_sq", [P, NU, HS])
        OE = sb("out_E", [P, NU, P])
        st = sb("out_stats", [P, 4, NU])
        with stage(nc, "v_step", "var_ready", "root_ready", "zeroed", "normed", "turned", "affine", "gated") as \
                (v_step, var_ready, root_ready, zeroed, normed, turned, affine, gated):
            with nc.Block() as block:
                @block.gpsimd
                def _(pool):
                    pool.memset(OE[0:HS, :, HS:P], 0.0).then_inc(zeroed, 1)
                    pool.memset(OE[HS:P, :, 0:HS], 0.0).then_inc(zeroed, 1)
                    pool.wait_ge(zeroed, 2)

                @block.vector
                def _(dve):
                    done = Steps(dve, v_step)
                    o = b.out.rearrange("p c g v -> p (c g) v")
                    spread = lambda r: st[:, r, :].rearrange("p (u o) -> p u o", o=1).to_broadcast([P, NU, HS])
                    done(dve.tensor_reduce(st[:, 0, :], o, AX.X, ALU.add))
                    done.wait()
                    done(dve.tensor_scalar(st[:, 0, :], st[:, 0, :], 1.0 / HS, None, ALU.mult))
                    done.wait()
                    done(dve.tensor_tensor(o, o, spread(0), ALU.subtract))
                    done.wait()
                    done(dve.tensor_tensor(sq[:], o, o, ALU.mult))
                    done.wait()
                    done(dve.tensor_reduce(st[:, 1, :], sq[:], AX.X, ALU.add))
                    done.wait()
                    dve.tensor_scalar(st[:, 2, :], st[:, 1, :], 1.0 / HS, GN_EPS, ALU.mult,
                                      ALU.add).then_inc(var_ready, 1)
                    dve.wait_ge(root_ready, 1)
                    done(dve.reciprocal(st[:, 1, :], st[:, 3, :]))
                    done.wait()
                    dve.wait_ge(zeroed, 2)
                    for h in range(2):
                        r = slice(h * HS, (h + 1) * HS)
                        dve.tensor_tensor(OE[r, :, r], o[r], spread(1)[r], ALU.mult).then_inc(normed, 1)
                    for g in range(PR):
                        dve.wait_ge(affine, g + 1)
                        done(dve.tensor_tensor(yT[:, g, :], yT[:, g, :], b.bonusT[:, g, :], ALU.add))
                        done.wait()
                        done(dve.tensor_tensor(yT[:, g, :], yT[:, g, :], b.gateT[:, g, :], ALU.mult))
                    done.wait()

                @block.scalar
                def _(act):
                    act.wait_ge(var_ready, 1)
                    act.activation(st[:, 3, :], st[:, 2, :], ACT.Sqrt).then_inc(root_ready, 1)
                    for g in range(PR):
                        act.wait_ge(turned, g + 1)
                        act.activation(yT[:, g, :], chip.ps[:, g, :], ACT.Identity, scale=chip.col("ln_x_w", g),
                                       bias=chip.col("ln_x_b", g)).then_inc(affine, 1)

                @block.tensor
                def _(pe):
                    pe.wait_ge(normed, 2)
                    for g in range(PR):
                        for c in range(NCH):
                            last = pe.matmul(chip.ps[:, g, c * C:(c + 1) * C], OE[:, c * PR + g, :], chip.stack2[:],
                                             start=True, stop=True)
                        last.then_inc(turned, 1)


def pooling(nc, chip, A, b, yT):
    W = S + 16
    with ExitStack() as ctx:
        sb = lambda name, shape: ctx.enter_context(buffer(nc, name, shape, F32))
        sums = sb("window_sums", [P, 2, W])
        inv = sb("window_inverse", [P, 4, S])
        pw = sb("pool_w", [P, 4, P])
        with stage(nc, "loaded", "v_step", "ready", "mixed", "taken") as (loaded, v_step, ready, mixed, taken):
            with nc.Block() as block:
                @block.sync
                def _(sp):
                    sp.dma_start(inv[:].rearrange("p g t -> p (g t)"), A["pool_inv"][0].partition_broadcast(P)).then_inc(loaded, 16)
                    sp.dma_start(pw[:], A["pool_w"]).then_inc(loaded, 16)

                @block.vector
                def _(dve):
                    done = Steps(dve, v_step)
                    done(dve.memset(b.poolT[:, :, 0:8], 0.0))
                    done(dve.memset(b.poolT[:, :, S + 8:W], 0.0))
                    done(dve.memset(sums[:], 0.0))
                    done.wait()
                    dve.wait_ge(loaded, 32)
                    for g in range(4):
                        src, half = b.poolT[:, g, :], 0
                        for lv in range(g + 1):
                            lo, hi = (1, 0) if lv == 0 else (1 << (lv - 1), 1 << (lv - 1))
                            dst = sums[:, lv % 2, :]
                            done(dve.tensor_tensor(dst[:, 8:8 + S] if lv == g else dst[:, lo:W - hi],
                                                   src[:, 8 - lo:8 - lo + S] if lv == g else src[:, 0:W - hi - lo],
                                                   src[:, 8 + hi:8 + hi + S] if lv == g else src[:, lo + hi:W],
                                                   ALU.add))
                            done.wait()
                            src = dst
                        done(dve.tensor_tensor(sums[:, g % 2, 8:8 + S], src[:, 8:8 + S], inv[:, g, :], ALU.mult))
                        done.wait()
                        dve.tensor_tensor(b.poolT[:, g, 8:8 + S], sums[:, g % 2, 8:8 + S], b.poolT[:, g, 8:8 + S],
                                          ALU.subtract).then_inc(ready, 1)
                        dve.wait_ge(ready, g + 1)
                        if g < 3:
                            done(dve.memset(sums[:], 0.0))
                            done.wait()

                @block.tensor
                def _(pe):
                    pe.wait_ge(loaded, 32)
                    for g in range(4):
                        pe.wait_ge(ready, g + 1)
                        pe.matmul(chip.ps[:, g, :], pw[:, g, :], b.poolT[:, g, 8:8 + S], start=True,
                                  stop=True).then_inc(mixed, 1)

                @block.scalar
                def _(act):
                    for g in range(4):
                        act.wait_ge(mixed, g + 1)
                        act.activation(yT[:, 4 + g, :], chip.ps[:, g, :], ACT.Copy,
                                       scale=chip.col("pool_scale", g)).then_inc(taken, 1)
                    act.wait_ge(taken, 4)


def project_out(nc, chip, w_dram, yT, K, out=None):
    with ExitStack() as ctx:
        w = ctx.enter_context(buffer(nc, "w_out_sb", [P, K, D], F32))
        with stage(nc, "w_loaded", "product", "taken") as (w_loaded, product, taken):
            with nc.Block() as block:
                @block.sync
                def _(sp):
                    sp.dma_start(w[:], w_dram).then_inc(w_loaded, 16)

                @block.tensor
                def _(pe):
                    pe.wait_ge(w_loaded, 16)
                    for n in range(2 * TT):
                        t, half = n // 2, n % 2
                        for k in range(K):
                            last = pe.matmul(chip.ps[:, n, :], yT[:, k, t * P:(t + 1) * P],
                                             w[:, k, half * 512:(half + 1) * 512], start=k == 0, stop=k == K - 1)
                        last.then_inc(product, 1)

                @block.vector
                def _(dve):
                    for n in range(2 * TT):
                        t, cols = n // 2, slice(n % 2 * 512, n % 2 * 512 + 512)
                        dve.wait_ge(product, n + 1)
                        if out is None:
                            ins = dve.tensor_tensor(chip.x[:, t, cols], chip.x[:, t, cols], chip.ps[:, n, :], ALU.add)
                        else:
                            ins = dve.tensor_copy(out[:, t, cols], chip.ps[:, n, :])
                        ins.then_inc(taken, 1)
                    dve.wait_ge(taken, 2 * TT)


class Obj:
    pass


def rwkv_block(nc, chip, A):
    norm_transpose(nc, chip, RMS_EPS, "norm1_w", 0)
    with ExitStack() as ctx:
        sb = lambda name, shape, c=ctx: c.enter_context(buffer(nc, name, shape, F32))
        b = Obj()
        yT = chip.hT[:]
        b.out = chip.hT[:, 0:4, :].rearrange("p k (c v) -> p (k c) v", v=HS).rearrange("p (c g) v -> p c g v", g=PR)
        spare = chip.x[:].rearrange("p t d -> p (t d)")
        b.gateT = spare[:, 0:PR * S].rearrange("p (g s) -> p g s", g=PR)
        b.bonusT = spare[:, PR * S:2 * PR * S].rearrange("p (g s) -> p g s", g=PR)
        b.rT, b.vT, b.kk = (sb(n, [P, PR, S]) for n in ("rT", "vT", "kkT"))
        with ExitStack() as early:
            b.kT, b.loraT = sb("kT", [P, PR, S], early), sb("loraT", [P, 4, S], early)
            with ExitStack() as pool_ctx:
                b.poolT = sb("poolT", [P, 4, S + 16], pool_ctx)
                project_in_1(nc, chip, A, b)
                pooling(nc, chip, A, b, yT)
            b.decay, b.a, b.kd = (sb(n, [P, 8, S], early) for n in ("decayT", "aT", "kdT"))
            rwkv_inputs(nc, chip, A, b)
        for rev in (False, True):
            recurrence(nc, chip, b, A, rev)
        rwkv_output(nc, chip, A, b, yT)
    with stage(nc, "x_again") as (x_again,):
        with nc.Block() as block:
            @block.sync
            def _(sp):
                sp.dma_start(chip.x[:], A["x"].rearrange("(t p) d -> p t d", p=P)).then_inc(x_again, 16)
                sp.wait_ge(x_again, 16)
    project_out(nc, chip, A["w_out"], yT, KD)


PH = 8
TOPK = 16
SLOTS = PH * TOPK
NKEYS = 128
RING = 16


def token_norm(nc, chip, eps, w_row, src=None, add=False, gain_out=None):
    src = chip.x if src is None else src
    with ExitStack() as ctx:
        w = ctx.enter_context(buffer(nc, "gain_row", [P, D], F32))
        junk = ctx.enter_context(buffer(nc, "squares", [P, D], F32))
        st = ctx.enter_context(buffer(nc, "tn_stats", [P, 4, TT], F32))
        with stage(nc, "w_loaded", "squares", "mean_ready", "root_ready", "v_step") as \
                (w_loaded, squares, mean_ready, root_ready, v_step):
            with nc.Block() as block:
                @block.sync
                def _(sp):
                    sp.dma_start(w[:], w_row.partition_broadcast(P)).then_inc(w_loaded, 16)

                @block.scalar
                def _(act):
                    for t in range(TT):
                        if t:
                            act.wait_ge(squares, t)
                        act.activation(junk[:], src[:, t, :], ACT.Square,
                                       accum_out=st[:, 0, t:t + 1]).then_inc(squares, 1)
                    act.wait_ge(mean_ready, 1)
                    act.activation(st[:, 2, :], st[:, 1, :], ACT.Sqrt).then_inc(root_ready, 1)

                @block.vector
                def _(dve):
                    done = Steps(dve, v_step)
                    dve.wait_ge(squares, TT)
                    dve.tensor_scalar(st[:, 1, :], st[:, 0, :], 1.0 / D, eps, ALU.mult,
                                      ALU.add).then_inc(mean_ready, 1)
                    dve.wait_ge(root_ready, 1)
                    done(dve.reciprocal(st[:, 3, :], st[:, 2, :]))
                    done.wait()
                    dve.wait_ge(w_loaded, 16)
                    dst = src if gain_out is None else gain_out
                    for t in range(TT):
                        done(dve.scalar_tensor_tensor(out=dst[:, t, :], in0=src[:, t, :], scalar=st[:, 3, t:t + 1],
                                                      in1=w[:], op0=ALU.mult, op1=ALU.mult))
                    done.wait()
                    if add:
                        for t in range(TT):
                            done(dve.tensor_tensor(chip.x[:, t, :], chip.x[:, t, :], src[:, t, :], ALU.add))
                        done.wait()


def expert_choice(nc, chip, A, idx, gate):
    WR = 4
    with ExitStack() as ctx:
        sb = lambda name, shape, dt=F32: ctx.enter_context(buffer(nc, name, shape, dt))
        ring = sb("wq_ring", [P, WR, KD, P])
        keys = sb("keys", [P, 2 * PH, NKEYS])
        qT = sb("qT", [P, 2 * PH, S])
        sc = sb("scores", [P, 2, 2 * PH, NKEYS])
        left = sb("scores_left", [P, 2 * PH, NKEYS])
        top = sb("top", [P, 2 * PH, TOPK])
        topi = sb("top_index", [P, 2 * PH, TOPK], U32)
        topf = sb("top_index_f", [P, 2 * PH, TOPK])
        cand = sb("cand", [P, PH, TOPK * TOPK])
        candl = sb("cand_left", [P, PH, TOPK * TOPK])
        best = sb("best", [P, PH, TOPK])
        pos = sb("best_pos", [P, PH, TOPK], U32)
        part = sb("pos_part", [P, 2, PH * TOPK], U32)
        partf = sb("pos_part_f", [P, 2, PH * TOPK])
        chosen = sb("chosen", [P, 2, PH * TOPK])
        iota = sb("iota16", [P, TOPK])
        sums = sb("gate_sum", [P, PH])
        with stage(nc, *[f"w{i}" for i in range(WR)], "keys_in", "iota_ready", "q_done", "q_out_a", "q_out_v",
                   "s_done", "s_out", "v_step", "shifted", "exped", "tile_done") as \
                (*w, keys_in, iota_ready, q_done, q_out_a, q_out_v, s_done, s_out, v_step, shifted, exped, tile_done):
            with nc.Block() as block:
                @block.sync
                def _(sp):
                    for m in range(2 * PH):
                        if m >= WR:
                            sp.wait_ge(q_done, m - WR + 1)
                        sp.dma_start(ring[:, m % WR], A["peer_wq"][m]).then_inc(w[m % WR], 16)
                        if m == 1:
                            sp.dma_start(keys[:], A["peer_keys"]).then_inc(keys_in, 16)

                @block.gpsimd
                def _(pool):
                    pool.iota(iota[:], pattern=[[1, TOPK]], base=0, channel_multiplier=0,
                              allow_small_or_imprecise_dtypes=True).then_inc(iota_ready, 1)

                @block.tensor
                def _(pe):
                    for m in range(2 * PH):
                        pe.wait_ge(w[m % WR], 16 * (m // WR + 1))
                        if m >= 8:
                            pe.wait_ge(q_out_v if m % 2 else q_out_a, m // 2 - 3)
                        for k in range(KD):
                            last = pe.matmul(chip.ps[:, m % 8, :], ring[:, m % WR, k, :], chip.hT[:, k, :],
                                             start=k == 0, stop=k == KD - 1)
                        last.then_inc(q_done, 1)
                    pe.wait_ge(q_out_a, PH)
                    pe.wait_ge(q_out_v, PH)
                    pe.wait_ge(keys_in, 16)
                    for t in range(TT):
                        for j in range(2 * PH):
                            if t >= 2 and j % 4 == 0:
                                pe.wait_ge(s_out, (t - 2) * 4 + j // 4 + 1)
                            last = pe.matmul(chip.ps[:, t % 2 * 4 + j // 4, j % 4 * P:(j % 4 + 1) * P],
                                             qT[:, j, t * P:(t + 1) * P], keys[:, j, :], start=True, stop=True)
                            if j % 4 == 3:
                                last.then_inc(s_done, 1)

                @block.scalar
                def _(act):
                    for m in range(0, 2 * PH, 2):
                        act.wait_ge(q_done, m + 1)
                        act.activation(qT[:, m, :], chip.ps[:, m % 8, :], ACT.Copy).then_inc(q_out_a, 1)
                    for t in range(TT):
                        if t >= 2:
                            act.wait_ge(tile_done, t - 1)
                        for j in range(4):
                            act.wait_ge(s_done, t * 4 + j + 1)
                            act.activation(sc[:, t % 2, 4 * j:4 * j + 4, :].rearrange("p a n -> p (a n)"),
                                           chip.ps[:, t % 2 * 4 + j, :], ACT.Copy).then_inc(s_out, 1)
                        if t:
                            act.wait_ge(shifted, t)
                            act.activation(gate[:, t - 1, :], gate[:, t - 1, :], ACT.Exp).then_inc(exped, 1)
                    act.wait_ge(shifted, TT)
                    act.activation(gate[:, TT - 1, :], gate[:, TT - 1, :], ACT.Exp).then_inc(exped, 1)

                @block.vector
                def _(dve):
                    done = Steps(dve, v_step)
                    for m in range(1, 2 * PH, 2):
                        dve.wait_ge(q_done, m + 1)
                        dve.tensor_copy(qT[:, m, :], chip.ps[:, m % 8, :]).then_inc(q_out_v, 1)
                    dve.wait_ge(iota_ready, 1)

                    def top16(values, rest, n, out, index):
                        for j in range(n):
                            done(dve.max(out[:, j, 0:8], values[:, j, :]))
                        done.wait()
                        for j in range(n):
                            done(dve.match_replace(rest[:, j, :], out[:, j, 0:8], values[:, j, :], -3e38))
                            done(dve.max_index(index[:, j, 0:8], out[:, j, 0:8], values[:, j, :]))
                        done.wait()
                        for j in range(n):
                            done(dve.max(out[:, j, 8:16], rest[:, j, :]))
                        done.wait()
                        for j in range(n):
                            done(dve.max_index(index[:, j, 8:16], out[:, j, 8:16], rest[:, j, :]))
                        done.wait()

                    def normalise(t):
                        g = gate[:, t, :].rearrange("p (h k) -> p h k", h=PH)
                        dve.wait_ge(exped, t + 1)
                        done(dve.tensor_reduce(sums[:], g, AX.X, ALU.add))
                        done.wait()
                        done(dve.reciprocal(sums[:], sums[:]))
                        done.wait()
                        done(dve.tensor_tensor(g, g, sums[:].rearrange("p (h o) -> p h o", o=1)
                                               .to_broadcast([P, PH, TOPK]), ALU.mult))
                        done.wait()

                    for t in range(TT):
                        dve.wait_ge(s_out, 4 * t + 4)
                        top16(sc[:, t % 2], left, 2 * PH, top, topi)
                        done(dve.tensor_copy(topf[:], topi[:]))
                        for h in range(PH):
                            a = top[:, 2 * h, :].rearrange("p (k o) -> p k o", o=1).to_broadcast([P, TOPK, TOPK])
                            c = top[:, 2 * h + 1, :].rearrange("p (o k) -> p o k", o=1).to_broadcast([P, TOPK, TOPK])
                            done(dve.tensor_tensor(cand[:, h, :].rearrange("p (a b) -> p a b", b=TOPK), a, c, ALU.add))
                        done.wait()
                        top16(cand, candl, PH, best, pos)
                        g = gate[:, t, :].rearrange("p (h k) -> p h k", h=PH)
                        dve.tensor_tensor(g, best[:], best[:, :, 0:1].to_broadcast([P, PH, TOPK]),
                                          ALU.subtract).then_inc(shifted, 1)
                        flat = pos[:].rearrange("p h k -> p (h k)")
                        done(dve.tensor_scalar(part[:, 0, :], flat, 4, None, ALU.logical_shift_right))
                        done(dve.tensor_scalar(part[:, 1, :], flat, 15, None, ALU.bitwise_and))
                        done.wait()
                        done(dve.tensor_copy(partf[:], part[:]))
                        done.wait()
                        for side in range(2):
                            for h in range(PH):
                                eq = cand[:, h, :].rearrange("p (k a) -> p k a", a=TOPK)
                                done(dve.tensor_tensor(
                                    eq, partf[:, side, h * TOPK:(h + 1) * TOPK].rearrange("p (k o) -> p k o", o=1)
                                    .to_broadcast([P, TOPK, TOPK]),
                                    iota[:].rearrange("p (o a) -> p o a", o=1).to_broadcast([P, TOPK, TOPK]),
                                    ALU.is_equal))
                            done.wait()
                            for h in range(PH):
                                eq = cand[:, h, :].rearrange("p (k a) -> p k a", a=TOPK)
                                done(dve.tensor_tensor(
                                    candl[:, h, :].rearrange("p (k a) -> p k a", a=TOPK), eq,
                                    topf[:, 2 * h + side, :].rearrange("p (o a) -> p o a", o=1)
                                    .to_broadcast([P, TOPK, TOPK]), ALU.mult))
                            done.wait()
                            done(dve.tensor_reduce(chosen[:, side, :], candl[:].rearrange("p h (k a) -> p (h k) a", a=TOPK),
                                                   AX.X, ALU.add))
                            done.wait()
                        done(dve.scalar_tensor_tensor(out=chosen[:, 0, :], in0=chosen[:, 0, :], scalar=float(NKEYS),
                                                      in1=chosen[:, 1, :], op0=ALU.mult, op1=ALU.add))
                        done.wait()
                        dve.tensor_copy(idx[:, t, :], chosen[:, 0, :]).then_inc(tile_done, 1)
                        if t:
                            normalise(t - 1)
                    normalise(TT - 1)
                    dve.wait_ge(tile_done, TT)


PASSES = (("u", 0), ("u", 1), ("v", 0), ("u", 2), ("v", 1), ("u", 3), ("v", 2), ("v", 3))
TURNS = SLOTS // RING
HALF = RING // 2


def experts(nc, chip, A, h2, idx, gate):
    with ExitStack() as ctx:
        sb = lambda name, shape, dt=F32: ctx.enter_context(buffer(nc, name, shape, dt))
        ring = sb("row_ring", [P, RING, D])
        now = sb("idx_now", [P, RING], U32)
        dots = sb("dots_now", [P, RING])
        dot = sb("dots", [P, TT, SLOTS])
        coef = sb("coef", [P, TT, SLOTS])
        diag = sb("diag", [P, RING, P])
        zero = sb("zero", [P, P])
        gatekeeper = sb("gatekeeper", [P, 1], U32)
        with stage(nc, *[f"row{i}" for i in range(RING)], "idx_now_ready", "u_used", "v_used", "dots_kept",
                   "gelu_done", "coef_ready", "diag_ready", "zeroed", "summed", "x_taken") as \
                (*row, idx_ready, u_used, v_used, dots_kept, gelu_done, coef_ready, diag_ready, zeroed, summed, x_taken):
            def before(n, kind):
                return SLOTS * sum(k == kind for k, _ in PASSES[:n])

            with nc.Block() as block:
                @block.gpsimd
                def _(pool):
                    def turn(n, i, first=False):
                        kind, t = PASSES[n]
                        used, other = (u_used, v_used) if kind == "u" else (v_used, u_used)
                        at, others = before(n, kind), before(n, "v" if kind == "u" else "u")
                        for half in range(2):
                            lo = half * HALF
                            if not first:
                                if at:
                                    pool.wait_ge(used, i * RING + (at - RING + lo + HALF))
                                elif kind == "v":
                                    if not isinstance(i, int):
                                        pool.wait_ge(used, i * RING + (lo + HALF - RING))
                                else:
                                    pool.wait_ge(used, i * RING + (lo + HALF - RING))
                                if others:
                                    pool.wait_ge(other, others - RING + lo + HALF)
                            pool.tensor_copy(now[:, lo:lo + HALF], idx[:, t, bass.ds(i * RING + lo, HALF)]) \
                                .then_inc(idx_ready, 1)
                            pool.wait_ge(idx_ready, i * 4 + (n * TURNS * 4 + half * 2 + 1))
                            pool.tensor_tensor(gatekeeper[:], now[:, lo:lo + 1], now[:, lo:lo + 1],
                                               ALU.add).then_inc(idx_ready, 1)
                            for s in range(lo, lo + HALF):
                                pool.indirect_dma_start(
                                    ring[:, s, :], None, A["peer_u"] if kind == "u" else A["peer_v"],
                                    bass.IndirectOffsetOnAxis(ap=now[:, s:s + 1], axis=0)).then_inc(row[s], 16)

                    for n, (kind, t) in enumerate(PASSES):
                        if before(n, kind) == 0:
                            turn(n, 0, first=n == 0)
                            with pool.Fori(1, TURNS) as i:
                                turn(n, i)
                        else:
                            with pool.Fori(0, TURNS) as i:
                                turn(n, i)

                @block.vector
                def _(dve):
                    kept = [0]

                    def weights(t):
                        dve.wait_ge(gelu_done, t + 1)
                        dve.tensor_tensor(coef[:, t, :], coef[:, t, :], gate[:, t, :], ALU.mult).then_inc(coef_ready, 1)

                    def take(t):
                        dve.wait_ge(summed, t + 1)
                        dve.tensor_copy(chip.x[:, t, :].rearrange("p (b n) -> p b n", b=2),
                                        chip.ps[:, t % 2 * 2:t % 2 * 2 + 2, :]).then_inc(x_taken, 1)

                    dve.memset(zero[:], 0.0).then_inc(zeroed, 1)
                    nu = 0
                    for n, (kind, t) in enumerate(PASSES):
                        if kind == "v":
                            continue
                        with dve.Fori(0, TURNS) as i:
                            for s in range(RING):
                                dve.wait_ge(row[s], i * 16 + 16 * (n * TURNS + 1))
                                dve.tensor_tensor_reduce(ring[:, s, :], ring[:, s, :], h2[:, t, :], 1.0, 0.0, ALU.mult,
                                                         ALU.add, dots[:, s:s + 1]).then_inc(u_used, 1)
                            dve.wait_ge(u_used, i * RING + (before(n, "u") + RING))
                            dve.tensor_copy(dot[:, t, bass.ds(i * RING, RING)], dots[:]).then_inc(dots_kept, 1)
                            dve.wait_ge(dots_kept, i + (nu * TURNS + 1))
                        nu += 1
                        weights(t)
                        if t >= 2:
                            take(t - 2)
                    take(TT - 2)
                    take(TT - 1)
                    dve.wait_ge(x_taken, TT)

                @block.scalar
                def _(act):
                    for n, (kind, t) in enumerate(PASSES):
                        if kind == "u":
                            act.wait_ge(dots_kept, TURNS * (t + 1))
                            act.activation(coef[:, t, :], dot[:, t, :], ACT.Gelu).then_inc(gelu_done, 1)
                            continue
                        act.wait_ge(coef_ready, t + 1)
                        at = before(n, "v")

                        def build(i, first=False):
                            for s in range(RING):
                                if not first:
                                    act.wait_ge(v_used, i * RING + (at - RING + s + 1))
                                act.activation(diag[:, s, :], chip.ident[:], ACT.Copy,
                                               scale=coef[:, t, bass.ds(i * RING + s, 1)]).then_inc(diag_ready, 1)

                        if at == 0:
                            build(0, True)
                            with act.Fori(1, TURNS) as i:
                                build(i)
                        else:
                            with act.Fori(0, TURNS) as i:
                                build(i)
                    act.wait_ge(diag_ready, SLOTS * TT)

                @block.tensor
                def _(pe):
                    for n, (kind, t) in enumerate(PASSES):
                        if kind == "u":
                            continue
                        at = before(n, "v")
                        bank = t % 2 * 2
                        if t >= 2:
                            pe.wait_ge(x_taken, t - 1)
                        for b2 in range(2):
                            pe.matmul(chip.ps[:, bank + b2, :], chip.ident[:], chip.x[:, t, b2 * 512:(b2 + 1) * 512],
                                      start=True, stop=False, skip_group_check=True)
                        with pe.Fori(0, TURNS) as i:
                            for s in range(RING):
                                pe.wait_ge(row[s], i * 16 + 16 * (n * TURNS + 1))
                                pe.wait_ge(diag_ready, i * RING + (at + s + 1))
                                for b2 in range(2):
                                    last = pe.matmul(chip.ps[:, bank + b2, :], diag[:, s, :],
                                                     ring[:, s, b2 * 512:(b2 + 1) * 512], start=False, stop=False,
                                                     skip_group_check=True)
                                last.then_inc(v_used, 1)
                        pe.wait_ge(zeroed, 1)
                        for b2 in range(2):
                            last = pe.matmul(chip.ps[:, bank + b2, :], zero[:], chip.ident[:, 0:1]
                                             .to_broadcast([P, 512]), start=False, stop=True, skip_group_check=True)
                        last.then_inc(summed, 1)


def expert_block(nc, chip, A):
    with ExitStack() as ctx:
        sb = lambda name, shape, dt=F32: ctx.enter_context(buffer(nc, name, shape, dt))
        idx = sb("expert_idx", [P, TT, SLOTS], U32)
        gate = sb("expert_gate", [P, TT, SLOTS])
        norm_transpose(nc, chip, RMS_EPS, "norm2_w", 0)
        expert_choice(nc, chip, A, idx, gate)
        h2 = sb("h2", [P, TT, D])
        token_norm(nc, chip, RMS_EPS, A["norm2_row"], gain_out=h2)
        experts(nc, chip, A, h2, idx, gate)
    token_norm(nc, chip, RMS_EPS, A["norm_f_row"])


MH, QN, QR, VH = 8, 64, 32, 64
QK = QN + QR
DH, DV = 4, 128
GROUPS, GH = 3, 4
LAM_INIT = 0.8 - 0.6
MASK, DIST, DIL0, STRICT = 0, 1, 2, 5


def feature_projection(nc, chip, w_dram, n_tiles, out_of, rows_of=lambda m: P):
    R = 4
    with ExitStack() as ctx:
        ring = ctx.enter_context(buffer(nc, "proj_ring", [P, R, KD, P], F32))
        with stage(nc, *[f"w{i}" for i in range(R)], "product", "out_a", "out_v") as (*w, product, out_a, out_v):
            with nc.Block() as block:
                @block.sync
                def _(sp):
                    for m in range(n_tiles):
                        if m >= R:
                            sp.wait_ge(product, m - R + 1)
                        sp.dma_start(ring[:, m % R], w_dram[m]).then_inc(w[m % R], 16)

                @block.tensor
                def _(pe):
                    for m in range(n_tiles):
                        pe.wait_ge(w[m % R], 16 * (m // R + 1))
                        if m >= 8:
                            pe.wait_ge(out_v if m % 2 else out_a, m // 2 - 3)
                        r = rows_of(m)
                        for k in range(KD):
                            last = pe.matmul(chip.ps[0:r, m % 8, :], ring[:, m % R, k, 0:r], chip.hT[:, k, :],
                                             start=k == 0, stop=k == KD - 1)
                        last.then_inc(product, 1)

                @block.scalar
                def _(act):
                    for m in range(0, n_tiles, 2):
                        act.wait_ge(product, m + 1)
                        act.activation(out_of(m), chip.ps[0:rows_of(m), m % 8, :], ACT.Copy).then_inc(out_a, 1)
                    act.wait_ge(out_a, (n_tiles + 1) // 2)

                @block.vector
                def _(dve):
                    for m in range(1, n_tiles, 2):
                        dve.wait_ge(product, m + 1)
                        dve.tensor_copy(out_of(m), chip.ps[0:rows_of(m), m % 8, :]).then_inc(out_v, 1)
                    dve.wait_ge(out_v, n_tiles // 2)


def token_projection(nc, chip, w_dram, width, blocks, dst_of):
    with ExitStack() as ctx:
        w = ctx.enter_context(buffer(nc, "token_w", [P, 2, KD, width], F32))
        with stage(nc, "w0", "w1", "product", "taken") as (w0, w1, product, taken):
            with nc.Block() as block:
                @block.sync
                def _(sp):
                    for m in range(blocks):
                        if m >= 2:
                            sp.wait_ge(product, TT * (m - 1))
                        sp.dma_start(w[:, m % 2], w_dram[:, :, m * width:(m + 1) * width]).then_inc((w0, w1)[m % 2], 16)

                @block.tensor
                def _(pe):
                    for m in range(blocks):
                        pe.wait_ge((w0, w1)[m % 2], 16 * (m // 2 + 1))
                        for t in range(TT):
                            n = m * TT + t
                            if n >= 8:
                                pe.wait_ge(taken, n - 7)
                            for k in range(KD):
                                last = pe.matmul(chip.ps[:, n % 8, 0:width], chip.hT[:, k, t * P:(t + 1) * P],
                                                 w[:, m % 2, k, :], start=k == 0, stop=k == KD - 1)
                            last.then_inc(product, 1)

                @block.vector
                def _(dve):
                    for n in range(blocks * TT):
                        dve.wait_ge(product, n + 1)
                        dve.tensor_copy(dst_of(n // TT, n % TT), chip.ps[:, n % 8, 0:width]).then_inc(taken, 1)
                    dve.wait_ge(taken, blocks * TT)


class Unit:

    def __init__(self, q, k, bias, values, stat):
        self.q, self.k, self.bias, self.values, self.stat = q, k, bias, values, stat
        self.width = k.shape[1]


def attend(nc, chip, units, scale, width, dst_of, low, total):
    N, G = len(units), 512 // width if len(units) % (512 // width) == 0 else 256 // width
    with ExitStack() as ctx:
        sb = lambda name, shape: ctx.enter_context(buffer(nc, name, shape, F32))
        neg = sb("neg_logits", [P, 3, S])
        prob = sb("probs", [P, 3, S])
        probT = sb("probsT", [P, 2, S])
        with stage(nc, "scored", "masked", "exped", "turned", "turned_out", "weighted", "kept") as \
                (scored, masked, exped, turned, turned_out, weighted, kept):
            with nc.Block() as block:
                @block.tensor
                def _(pe):
                    for n in range(N + 3):
                        if n < N:
                            u = units[n]
                            if n >= 3:
                                pe.wait_ge(masked, n - 2)
                            pe.matmul(chip.ps[:, n % 3, 0:u.width], u.q, u.k, start=True,
                                      stop=True).then_inc(scored, 1)
                        m = n - 2
                        if 0 <= m < N:
                            pe.wait_ge(exped, m + 1)
                            if m >= 2:
                                pe.wait_ge(turned_out, m - 1)
                            for j in range(units[m].width // P):
                                last = pe.transpose(chip.ps[:, 3 + m % 2, j * P:(j + 1) * P],
                                                    prob[:, m % 3, j * P:(j + 1) * P], chip.ident[:])
                            last.then_inc(turned, 1)
                        m = n - 3
                        if 0 <= m < N:
                            pe.wait_ge(turned_out, m + 1)
                            if m % G == 0 and m >= 2 * G:
                                pe.wait_ge(kept, m // G - 1)
                            vs = units[m].values
                            for j, v in enumerate(vs):
                                last = pe.matmul(chip.ps[:, 6 + m // G % 2, m % G * width:(m % G + 1) * width],
                                                 probT[:, m % 2, j * P:(j + 1) * P], v, start=j == 0,
                                                 stop=j == len(vs) - 1)
                            last.then_inc(weighted, 1)

                @block.vector
                def _(dve):
                    for n in range(N + 2):
                        if n < N:
                            u = units[n]
                            dve.wait_ge(scored, n + 1)
                            if n >= 3:
                                dve.wait_ge(exped, n - 2)
                            dve.tensor_tensor_reduce(neg[:, n % 3, 0:u.width], chip.ps[:, n % 3, 0:u.width], u.bias,
                                                     -scale, 3e38, ALU.add, ALU.min,
                                                     low[:, u.stat:u.stat + 1]).then_inc(masked, 1)
                        m = n - 2
                        if 0 <= m < N:
                            w = units[m].width
                            dve.wait_ge(turned, m + 1)
                            if m >= 2:
                                dve.wait_ge(weighted, m - 1)
                            dve.tensor_copy(probT[:, m % 2, 0:w], chip.ps[:, 3 + m % 2, 0:w]).then_inc(turned_out, 1)

                @block.scalar
                def _(act):
                    for n in range(N + 4):
                        if n < N:
                            u = units[n]
                            act.wait_ge(masked, n + 1)
                            if n >= 3:
                                act.wait_ge(turned, n - 2)
                            act.activation(prob[:, n % 3, 0:u.width], neg[:, n % 3, 0:u.width], ACT.Exp, scale=-1.0,
                                           bias=low[:, u.stat:u.stat + 1],
                                           accum_out=total[:, u.stat:u.stat + 1]).then_inc(exped, 1)
                        m = n - 4
                        if m >= 0 and m % G == G - 1:
                            act.wait_ge(weighted, m + 1)
                            act.activation(dst_of(m // G), chip.ps[:, 6 + m // G % 2, 0:G * width],
                                           ACT.Copy).then_inc(kept, 1)
                    act.wait_ge(kept, N // G)


def turn_tokens(nc, chip, src_of, n_tiles, dst_of, gain_of):
    with stage(nc, "turned", "out_a", "out_v") as (turned, out_a, out_v):
        with nc.Block() as block:
            @block.tensor
            def _(pe):
                for n in range(n_tiles):
                    for t in range(TT):
                        last = pe.transpose(chip.ps[:, n % 8, t * P:(t + 1) * P], src_of(n, t), chip.ident[:])
                    last.then_inc(turned, 1)

            @block.scalar
            def _(act):
                for n in range(0, n_tiles, 2):
                    act.wait_ge(turned, n + 1)
                    g = gain_of(n)
                    act.activation(dst_of(n), chip.ps[:, n % 8, :], ACT.Copy, scale=1.0 if g is None else g)\
                        .then_inc(out_a, 1)
                act.wait_ge(out_a, (n_tiles + 1) // 2)

            @block.vector
            def _(dve):
                for n in range(1, n_tiles, 2):
                    dve.wait_ge(turned, n + 1)
                    g = gain_of(n)
                    dve.tensor_scalar(dst_of(n), chip.ps[:, n % 8, :], 1.0 if g is None else g, None,
                                      ALU.mult).then_inc(out_v, 1)
                dve.wait_ge(out_v, n_tiles // 2)


def even_mixer(nc, chip, A):
    norm_transpose(nc, chip, NORM_EPS, "ev_pre", 0)
    with ExitStack() as ctx:
        sb = lambda name, shape, c=ctx: c.enter_context(buffer(nc, name, shape, F32))
        ocat = sb("ev_out", [P, TT, D])
        low, total = sb("ev_low", [P, 64]), sb("ev_total", [P, 64])
        lam = sb("ev_lam", [P, 4])
        tables = sb("ev_tables", [P, 2, S])
        dqT, dkT, dv = sb("dqT", [P, DH, S]), sb("dkT", [P, DH, S]), sb("dv", [P, TT, DH * DV])
        with ExitStack() as mla:
            c_tok = sb("c_tok", [P, TT, 384], mla)
            krT = sb("krT", [32, 2, S], mla)
            token_projection(nc, chip, A["ev_w_c"], 384, 1, lambda m, t: c_tok[:, t, :])
            token_projection(nc, chip, A["ev_w_dv"], 512, 1, lambda m, t: dv[:, t, :])
            feature_projection(nc, chip, A["ev_w_qk"], 10,
                               lambda m: (dqT, dkT)[m // 4][:, m % 4, :] if m < 8 else krT[:, m - 8, :],
                               lambda m: P if m < 8 else 32)
            _mla(nc, chip, A, mla, c_tok, krT, ocat, low, total, tables, lam)
        _diff(nc, chip, dqT, dkT, dv, ocat, low, total, tables, lam)
        turn_tokens(nc, chip, lambda n, t: ocat[:, t, n * P:(n + 1) * P], KD, lambda n: chip.hT[:, n, :],
                    lambda n: None if n < 4 else lam[:, 3:4])
    with ExitStack() as ctx:
        out = ctx.enter_context(buffer(nc, "ev_y", [P, TT, D], F32))
        project_out(nc, chip, A["ev_w_out"], chip.hT, KD, out)
        token_norm(nc, chip, NORM_EPS, A["ev_post_row"], src=out, add=True)


def _mla(nc, chip, A, ctx, c_tok, krT, ocat, low, total, tables, lam):
    sb = lambda name, shape, c=ctx: c.enter_context(buffer(nc, name, shape, F32))
    cT = sb("cT", [P, 3, S])
    v = sb("mla_v", [P, TT, MH * VH])
    qT, kT = sb("mla_qT", [QK, MH, S]), sb("mla_kT", [QK, MH, S])
    with ExitStack() as own:
        wuq = sb("w_uq", [P, 2, MH * QK], own)
        wus = sb("w_uq_swapped", [P, 2, MH * QR], own)
        wuk = sb("w_uk", [P, MH * QK], own)
        wuv = sb("w_uv", [P, MH * VH], own)
        rot = sb("rope_tables", [QR, 2, S], own)
        turn = sb("rope_turn", [QR, 2, S], own)
        kr = sb("rope_k", [QR, S], own)
        st = sb("c_stats", [P, 4, 2 * TT], own)
        junk = sb("c_junk", [P, 256], own)
        lv = sb("lam_vectors", [P, 4 * HS], own)
        lj = sb("lam_products", [P, HS], own)
        with stage(nc, "loaded", "squares", "mean_ready", "root_ready", "v_step", "lam_dots", "lam_exps") as \
                (loaded, squares, mean_ready, root_ready, v_step, lam_dots, lam_exps):
            with nc.Block() as block:
                @block.sync
                def _(sp):
                    sp.dma_start(lv[:], A["ev_lam"].partition_broadcast(P)).then_inc(loaded, 16)
                    sp.dma_start(tables[:], A["tables"][:, MASK:DIST + 1, :]).then_inc(loaded, 16)
                    sp.wait_ge(loaded, 32)

                @block.scalar
                def _(act):
                    for t in range(TT):
                        for part in range(2):
                            n = 2 * t + part
                            if n:
                                act.wait_ge(squares, n)
                            sl = slice(0, 256) if part == 0 else slice(256, 384)
                            act.activation(junk[:, 0:sl.stop - sl.start], c_tok[:, t, sl], ACT.Square,
                                           accum_out=st[:, 0, part * TT + t:part * TT + t + 1]).then_inc(squares, 1)
                    act.wait_ge(mean_ready, 2)
                    act.activation(st[:, 2, :], st[:, 1, :], ACT.Sqrt).then_inc(root_ready, 1)
                    act.wait_ge(lam_dots, 2)
                    act.activation(lam[:, 1:3], lam[:, 1:3], ACT.Exp).then_inc(lam_exps, 1)

                @block.vector
                def _(dve):
                    done = Steps(dve, v_step)
                    dve.wait_ge(squares, 2 * TT)
                    for part, n in ((0, 256), (1, 128)):
                        r = slice(part * TT, (part + 1) * TT)
                        dve.tensor_scalar(st[:, 1, r], st[:, 0, r], 1.0 / n, NORM_EPS, ALU.mult,
                                          ALU.add).then_inc(mean_ready, 1)
                    dve.wait_ge(root_ready, 1)
                    done(dve.reciprocal(st[:, 3, :], st[:, 2, :]))
                    done.wait()
                    for t in range(TT):
                        for part, sl in ((0, slice(0, 256)), (1, slice(256, 384))):
                            done(dve.tensor_scalar(c_tok[:, t, sl], c_tok[:, t, sl],
                                                   st[:, 3, part * TT + t:part * TT + t + 1], None, ALU.mult))
                    dve.wait_ge(loaded, 32)
                    for j in range(2):
                        a, c = lv[:, 2 * j * HS:(2 * j + 1) * HS], lv[:, (2 * j + 1) * HS:(2 * j + 2) * HS]
                        if j:
                            dve.wait_ge(lam_dots, j)
                        dve.tensor_tensor_reduce(lj[:], a, c, 1.0, 0.0, ALU.mult, ALU.add,
                                                 lam[:, 1 + j:2 + j]).then_inc(lam_dots, 1)
                    dve.wait_ge(lam_exps, 1)
                    done(dve.tensor_tensor(lam[:, 0:1], lam[:, 2:3], lam[:, 1:2], ALU.subtract))
                    done.wait()
                    done(dve.tensor_scalar(lam[:, 0:1], lam[:, 0:1], LAM_INIT, None, ALU.subtract))
                    done(dve.tensor_scalar(lam[:, 3:4], chip.col("subln_g"), 1.0 - LAM_INIT, None, ALU.mult))
                    done.wait()
        turn_tokens(nc, chip, lambda n, t: c_tok[:, t, n * P:(n + 1) * P], 3, lambda n: cT[:, n, :],
                    lambda n: chip.col("cq_g", n) if n < 2 else chip.col("ckv_g"))
        with stage(nc, "loaded", "product", "copied", "v_step", "key_turned", "values_out") as \
                (loaded, product, copied, v_step, key_turned, values_out):
            with nc.Block() as block:
                @block.sync
                def _(sp):
                    for dst, src in ((wuq, "ev_w_uq"), (wus, "ev_w_us"), (wuk, "ev_w_uk"), (wuv, "ev_w_uv"), (rot, "rope")):
                        sp.dma_start(dst[:], A[src]).then_inc(loaded, 16)

                @block.tensor
                def _(pe):
                    pe.wait_ge(loaded, 80)
                    for h in range(MH):
                        if h >= 2:
                            pe.wait_ge(copied, 3 * (h - 1))
                        b0 = h % 2 * 3
                        for k in range(2):
                            pe.matmul(chip.ps[0:QK, b0, :], wuq[:, k, h * QK:(h + 1) * QK], cT[:, k, :],
                                      start=k == 0, stop=k == 1)
                        for k in range(2):
                            pe.matmul(chip.ps[0:QR, b0 + 1, :], wus[:, k, h * QR:(h + 1) * QR], cT[:, k, :],
                                      start=k == 0, stop=k == 1)
                        pe.matmul(chip.ps[0:QK, b0 + 2, :], wuk[:, h * QK:(h + 1) * QK], cT[:, 2, :], start=True,
                                  stop=True).then_inc(product, 1)
                    for t in range(TT):
                        if t >= 2:
                            pe.wait_ge(values_out, t - 1)
                        pe.matmul(chip.ps[:, 6 + t % 2, :], cT[:, 2, t * P:(t + 1) * P], wuv[:], start=True,
                                  stop=True).then_inc(product, 1)

                @block.scalar
                def _(act):
                    for h in range(MH):
                        act.wait_ge(product, h + 1)
                        b0 = h % 2 * 3
                        act.activation(qT[:, h, :], chip.ps[0:QK, b0, :], ACT.Copy).then_inc(copied, 1)
                        act.activation(kT[:, h, :], chip.ps[0:QK, b0 + 2, :], ACT.Copy).then_inc(copied, 1)
                        if h >= 2:
                            act.wait_ge(v_step, 3 * (h - 1) + 3)
                        act.activation(turn[:, h % 2, :], chip.ps[0:QR, b0 + 1, :], ACT.Copy).then_inc(copied, 1)
                    for t in range(TT):
                        act.wait_ge(product, MH + t + 1)
                        act.activation(v[:, t, :], chip.ps[:, 6 + t % 2, :], ACT.Copy).then_inc(values_out, 1)
                    act.wait_ge(values_out, TT)

                @block.vector
                def _(dve):
                    done = Steps(dve, v_step)
                    dve.wait_ge(loaded, 80)
                    done(dve.tensor_tensor(krT[:, 0, :], krT[:, 0, :], rot[:, 0, :], ALU.mult))
                    done(dve.tensor_tensor(krT[:, 1, :], krT[:, 1, :], rot[:, 1, :], ALU.mult))
                    done.wait()
                    done(dve.tensor_tensor(kr[:], krT[:, 0, :], krT[:, 1, :], ALU.add))
                    for h in range(MH):
                        dve.wait_ge(copied, 3 * h + 3)
                        if h == 0:
                            done.wait()
                        done(dve.tensor_tensor(turn[:, h % 2, :], turn[:, h % 2, :], rot[:, 1, :], ALU.mult))
                        done(dve.tensor_tensor(qT[0:QR, h, :], qT[0:QR, h, :], rot[:, 0, :], ALU.mult))
                        done.wait()
                        done(dve.tensor_tensor(qT[0:QR, h, :], qT[0:QR, h, :], turn[:, h % 2, :], ALU.add))
                        dve.tensor_copy(kT[0:QR, h, :], kr[:]).then_inc(key_turned, 1)
                    done.wait()
                    dve.wait_ge(key_turned, MH)
    units = []
    for i in range(TT):
        w = (i + 1) * P
        for h in range(MH):
            units.append(Unit(qT[:, h, i * P:(i + 1) * P], kT[:, h, 0:w], tables[:, MASK, S - w:S],
                              [v[:, j, h * VH:(h + 1) * VH] for j in range(i + 1)], i * MH + h))
    attend(nc, chip, units, QK ** -0.5, VH, lambda g: ocat[:, g, 0:512], low, total)
    with stage(nc, "v_step") as (v_step,):
        with nc.Block() as block:
            @block.vector
            def _(dve):
                done = Steps(dve, v_step)
                done(dve.reciprocal(total[:, 0:TT * MH], total[:, 0:TT * MH]))
                done.wait()
                for t in range(TT):
                    o = ocat[:, t, 0:512].rearrange("p (h v) -> p h v", h=MH)
                    done(dve.tensor_tensor(o, o, total[:, t * MH:(t + 1) * MH].rearrange("p (h o) -> p h o", o=1)
                                           .to_broadcast([P, MH, VH]), ALU.mult))
                done.wait()


def _diff(nc, chip, dqT, dkT, dv, ocat, low, total, tables, lam):
    with ExitStack() as ctx:
        sb = lambda name, shape: ctx.enter_context(buffer(nc, name, shape, F32))
        bias = sb("diff_bias", [P, DH, S])
        o = sb("diff_o", [P, 2, TT, DH * DV])
        st = sb("diff_stats", [P, 4, TT * DH])
        scale = HS ** -0.5
        with stage(nc, "biased") as (biased,):
            with nc.Block() as block:
                @block.vector
                def _(dve):
                    for h in range(DH):
                        slope = 2.0 ** (-8.0 * (h + 1) / DH)
                        dve.tensor_scalar(bias[:, h, :], tables[:, DIST, :], -slope / scale, None,
                                          ALU.mult).then_inc(biased, 1)
                    dve.wait_ge(biased, DH)
        units = []
        for i in range(TT):
            w = (i + 1) * P
            for s_ in range(2):
                r = slice(s_ * HS, (s_ + 1) * HS)
                for h in range(DH):
                    units.append(Unit(dqT[r, h, i * P:(i + 1) * P], dkT[r, h, 0:w], bias[:, h, S - w:S],
                                      [dv[:, j, h * DV:(h + 1) * DV] for j in range(i + 1)],
                                      s_ * TT * DH + i * DH + h))
        attend(nc, chip, units, scale, DV, lambda g: o[:, g % 2, g // 2, :], low, total)
        n = TT * DH
        with stage(nc, "v_step", "mean_ready", "root_ready") as (v_step, mean_ready, root_ready):
            with nc.Block() as block:
                @block.scalar
                def _(act):
                    act.wait_ge(mean_ready, 1)
                    act.activation(st[:, 2, :], st[:, 1, :], ACT.Sqrt).then_inc(root_ready, 1)

                @block.vector
                def _(dve):
                    done = Steps(dve, v_step)
                    flat = lambda s_: o[:, s_].rearrange("p t (h v) -> p (t h) v", v=DV)
                    wide = lambda ap: ap.rearrange("p (n o) -> p n o", o=1).to_broadcast([P, n, DV])
                    done(dve.reciprocal(total[:, 0:2 * n], total[:, 0:2 * n]))
                    done.wait()
                    done(dve.tensor_scalar(total[:, n:2 * n], total[:, n:2 * n], lam[:, 0:1], None, ALU.mult))
                    done(dve.tensor_tensor(flat(0), flat(0), wide(total[:, 0:n]), ALU.mult))
                    done.wait()
                    done(dve.tensor_tensor(flat(1), flat(1), wide(total[:, n:2 * n]), ALU.mult))
                    done.wait()
                    done(dve.tensor_tensor(flat(0), flat(0), flat(1), ALU.add))
                    done.wait()
                    done(dve.tensor_tensor(flat(1), flat(0), flat(0), ALU.mult))
                    done.wait()
                    done(dve.tensor_reduce(st[:, 0, :], flat(1), AX.X, ALU.add))
                    done.wait()
                    dve.tensor_scalar(st[:, 1, :], st[:, 0, :], 1.0 / DV, NORM_EPS, ALU.mult,
                                      ALU.add).then_inc(mean_ready, 1)
                    dve.wait_ge(root_ready, 1)
                    done(dve.reciprocal(st[:, 3, :], st[:, 2, :]))
                    done.wait()
                    for t in range(TT):
                        done(dve.tensor_tensor(
                            ocat[:, t, 512:1024].rearrange("p (h v) -> p h v", v=DV), flat(0)[:, t * DH:(t + 1) * DH],
                            wide(st[:, 3, :])[:, t * DH:(t + 1) * DH], ALU.mult))
                    done.wait()


ND = GROUPS * GH


def odd_mixer(nc, chip, A):
    norm_transpose(nc, chip, NORM_EPS, "od_pre", 0)
    with ExitStack() as ctx:
        sb = lambda name, shape, c=ctx: c.enter_context(buffer(nc, name, shape, F32))
        ocat = sb("od_out", [P, TT, 512])
        v = sb("od_v", [P, TT, D])
        qk = sb("od_qk", [P, 16, S])
        token_projection(nc, chip, A["od_w_v"], 512, 2, lambda m, t: v[:, t, m * 512:(m + 1) * 512])
        feature_projection(nc, chip, A["od_w_qk"], 16, lambda m: qk[:, m, :])
        _dilated(nc, chip, A, qk, v, ocat)
        _stick(nc, chip, A, qk, v, ocat)
        turn_tokens(nc, chip, lambda n, t: ocat[:, t, n * P:(n + 1) * P], 4, lambda n: chip.hT[:, n, :],
                    lambda n: None)
    with ExitStack() as ctx:
        out = ctx.enter_context(buffer(nc, "od_y", [P, TT, D], F32))
        project_out(nc, chip, A["od_w_out"], chip.hT, 4, out)
        token_norm(nc, chip, NORM_EPS, A["od_post_row"], src=out, add=True)


def _dilated(nc, chip, A, qk, v, ocat):
    with ExitStack() as ctx:
        sb = lambda name, shape: ctx.enter_context(buffer(nc, name, shape, F32))
        bias = sb("dil_bias", [P, ND, S])
        tables = sb("dil_tables", [P, GROUPS, S])
        o = sb("dil_o", [P, TT, ND * HS])
        low, total = sb("dil_low", [P, TT, ND]), sb("dil_total", [P, TT, ND])
        wts = sb("dil_weights", [P, TT, ND])
        small = sb("dil_small", [P, 2, TT, GH])
        scale = HS ** -0.5
        with stage(nc, "loaded", "biased") as (loaded, biased):
            with nc.Block() as block:
                @block.sync
                def _(sp):
                    sp.dma_start(tables[:], A["tables"][:, DIL0:DIL0 + GROUPS, :]).then_inc(loaded, 16)

                @block.vector
                def _(dve):
                    dve.wait_ge(loaded, 16)
                    for n in range(ND):
                        slope = 2.0 ** (-8.0 * (n + 1) / ND)
                        dve.tensor_scalar(bias[:, n, :], tables[:, n // GH, :], -slope / scale, None,
                                          ALU.mult).then_inc(biased, 1)
                    dve.wait_ge(biased, ND)
        units = []
        for i in range(TT):
            for n in range(ND):
                first = max(0, i - 1) if n < GH else 0
                w = (i + 1 - first) * P
                r = slice(n % 2 * HS, n % 2 * HS + HS)
                units.append(Unit(qk[r, n // 2, i * P:(i + 1) * P], qk[r, 6 + n // 2, first * P:(i + 1) * P],
                                  bias[:, n, S - w:S], [v[:, j, n * HS:(n + 1) * HS] for j in range(first, i + 1)],
                                  i * ND + n))
        flat = o[:].rearrange("p t n -> p (t n)")
        attend(nc, chip, units, scale, HS, lambda g: flat[:, g * 512:(g + 1) * 512],
               low[:].rearrange("p t n -> p (t n)"), total[:].rearrange("p t n -> p (t n)"))
        with stage(nc, "v_step", "apart", "exped") as (v_step, apart, exped):
            with nc.Block() as block:
                @block.vector
                def _(dve):
                    done = Steps(dve, v_step)
                    of = lambda ap, g: ap[:, :, g * GH:(g + 1) * GH]
                    lo, den = small[:, 0], small[:, 1]
                    done(dve.tensor_tensor(lo, of(low, 0), of(low, 1), ALU.min))
                    done.wait()
                    done(dve.tensor_tensor(lo, lo, of(low, 2), ALU.min))
                    done.wait()
                    for g in range(GROUPS):
                        dve.tensor_tensor(of(wts, g), lo, of(low, g), ALU.subtract).then_inc(apart, 1)
                    dve.wait_ge(exped, 1)
                    done(dve.tensor_tensor(total[:], total[:], wts[:], ALU.mult))
                    done.wait()
                    done(dve.tensor_tensor(den, of(total, 0), of(total, 1), ALU.add))
                    done.wait()
                    done(dve.tensor_tensor(den, den, of(total, 2), ALU.add))
                    done.wait()
                    done(dve.reciprocal(den, den))
                    done.wait()
                    for g in range(GROUPS):
                        done(dve.tensor_tensor(of(wts, g), of(wts, g), den, ALU.mult))
                    done.wait()
                    for t in range(TT):
                        ot = o[:, t].rearrange("p (n v) -> p n v", v=HS)
                        done(dve.tensor_tensor(ot, ot, wts[:, t].rearrange("p (n o) -> p n o", o=1)
                                               .to_broadcast([P, ND, HS]), ALU.mult))
                    done.wait()
                    q = GH * HS
                    done(dve.tensor_tensor(ocat[:, :, 0:q], o[:, :, 0:q], o[:, :, q:2 * q], ALU.add))
                    done.wait()
                    done(dve.tensor_tensor(ocat[:, :, 0:q], ocat[:, :, 0:q], o[:, :, 2 * q:3 * q], ALU.add))
                    done.wait()

                @block.scalar
                def _(act):
                    act.wait_ge(apart, GROUPS)
                    act.activation(wts[:], wts[:], ACT.Exp).then_inc(exped, 1)


def _stick(nc, chip, A, qk, v, ocat):
    NHD = 4
    with ExitStack() as ctx:
        sb = lambda name, shape: ctx.enter_context(buffer(nc, name, shape, F32))
        strict = sb("strict_table", [P, 1, S])
        ones = sb("stick_ones", [P, S])
        z, mag, keep, after = (sb("stick_" + n, [P, NHD, S]) for n in ("z", "mag", "keep", "after"))
        probT = sb("stick_pT", [P, 2, S])
        scale = HS ** -0.5
        with stage(nc, "loaded", "scored", "z_out", "logged", "a_step", "v_step", "arg_ready", "a_exped", "masked",
                   "turned", "turned_out", "weighted", "kept") as \
                (loaded, scored, z_out, logged, a_step, v_step, arg_ready, a_exped, masked, turned, turned_out,
                 weighted, kept):
            with nc.Block() as block:
                @block.sync
                def _(sp):
                    sp.dma_start(strict[:], A["tables"][:, STRICT:STRICT + 1, :]).then_inc(loaded, 16)

                @block.tensor
                def _(pe):
                    for i in range(TT):
                        w = (i + 1) * P
                        if i:
                            pe.wait_ge(z_out, i)
                        for h in range(NHD):
                            r = slice(h % 2 * HS, h % 2 * HS + HS)
                            last = pe.matmul(chip.ps[:, h, 0:w], qk[r, 12 + h // 2, i * P:(i + 1) * P],
                                             qk[r, 14 + h // 2, 0:w], start=True, stop=True)
                        last.then_inc(scored, 1)
                        pe.wait_ge(masked, i + 1)
                        for h in range(NHD + 1):
                            if h < NHD:
                                n = i * NHD + h
                                if n >= 2:
                                    pe.wait_ge(turned_out, n - 1)
                                for j in range(i + 1):
                                    last = pe.transpose(chip.ps[:, 4 + n % 2, j * P:(j + 1) * P],
                                                        z[:, h, j * P:(j + 1) * P], chip.ident[:])
                                last.then_inc(turned, 1)
                            if h:
                                n = i * NHD + h - 1
                                pe.wait_ge(turned_out, n + 1)
                                if h == 1 and i >= 2:
                                    pe.wait_ge(kept, i - 1)
                                for j in range(i + 1):
                                    at = ND * HS + (h - 1) * HS
                                    last = pe.matmul(chip.ps[:, 6 + i % 2, (h - 1) * HS:h * HS],
                                                     probT[:, n % 2, j * P:(j + 1) * P], v[:, j, at:at + HS],
                                                     start=j == 0, stop=j == i)
                                last.then_inc(weighted, 1)

                @block.scalar
                def _(act):
                    step = Steps(act, a_step)
                    for i in range(TT):
                        w = (i + 1) * P
                        act.wait_ge(scored, i + 1)
                        if i:
                            act.wait_ge(turned, i * NHD)
                        ps = chip.ps[:, 0:NHD, 0:w]
                        step(act.activation(mag[:, :, 0:w], ps, ACT.Abs, scale=scale))
                        act.activation(z[:, :, 0:w], ps, ACT.Copy, scale=scale).then_inc(z_out, 1)
                        step.wait()
                        step(act.activation(mag[:, :, 0:w], mag[:, :, 0:w], ACT.Exp, scale=-1.0))
                        step.wait()
                        act.activation(mag[:, :, 0:w], mag[:, :, 0:w], ACT.Ln, bias=1.0).then_inc(logged, 1)
                        act.wait_ge(arg_ready, i + 1)
                        act.activation(z[:, :, 0:w], z[:, :, 0:w], ACT.Exp).then_inc(a_exped, 1)
                        act.wait_ge(weighted, (i + 1) * NHD)
                        act.activation(ocat[:, i, 256:512], chip.ps[:, 6 + i % 2, 0:256], ACT.Copy).then_inc(kept, 1)
                    act.wait_ge(kept, TT)

                @block.vector
                def _(dve):
                    done = Steps(dve, v_step)
                    done(dve.memset(ones[:], 1.0))
                    dve.wait_ge(loaded, 16)
                    for i in range(TT):
                        w = (i + 1) * P
                        zz, mm, kk, aa = z[:, :, 0:w], mag[:, :, 0:w], keep[:, :, 0:w], after[:, :, 0:w]
                        own = strict[:, :, S - w:S].to_broadcast([P, NHD, w])
                        dve.wait_ge(logged, i + 1)
                        dve.wait_ge(z_out, i + 1)
                        done(dve.scalar_tensor_tensor(out=mm, in0=zz, scalar=0.0, in1=mm, op0=ALU.max, op1=ALU.add))
                        done.wait()
                        done(dve.tensor_tensor(kk, mm, own, ALU.mult))
                        done(dve.tensor_tensor(zz, zz, mm, ALU.subtract))
                        done.wait()
                        for h in range(NHD):
                            done(dve.tensor_tensor_scan(after[:, h, 0:w][:, ::-1], ones[:, 0:w],
                                                        keep[:, h, 0:w][:, ::-1], 0.0, ALU.mult, ALU.add))
                        done(dve.tensor_tensor(zz, zz, kk, ALU.add))
                        done.wait()
                        dve.tensor_tensor(zz, zz, aa, ALU.subtract).then_inc(arg_ready, 1)
                        dve.wait_ge(a_exped, i + 1)
                        dve.tensor_tensor(zz, zz, own, ALU.mult).then_inc(masked, 1)
                        for h in range(NHD):
                            n = i * NHD + h
                            dve.wait_ge(turned, n + 1)
                            if n >= 2:
                                dve.wait_ge(weighted, n - 1)
                            dve.tensor_copy(probT[:, n % 2, 0:w], chip.ps[:, 4 + n % 2, 0:w]).then_inc(turned_out, 1)


FF = 2816
FT = FF // P
WPAIR = 2


def conv_ffn(nc, chip, A, layer):
    norm_transpose(nc, chip, NORM_EPS, "ffn_pre", 8 * layer)
    with ExitStack() as ctx:
        sb = lambda name, shape, c=ctx: c.enter_context(buffer(nc, name, shape, F32))
        out = sb("ffn_y", [P, TT, D])
        with ExitStack() as inner:
            hid = sb("hiddenT", [P, FT, S], inner)
            _ffn_up(nc, chip, A, layer, hid)
            _ffn_down(nc, chip, A, layer, hid, out)
        token_norm(nc, chip, NORM_EPS, A["ffn_post_rows"][layer], src=out, add=True)


def _ffn_up(nc, chip, A, layer, hid):
    with ExitStack() as ctx:
        sb = lambda name, shape: ctx.enter_context(buffer(nc, name, shape, F32))
        ring = sb("up_ring", [P, WPAIR, 2, KD, P])
        conv = sb("conv", [P, WPAIR, 2, S])
        with stage(nc, "w0", "w1", "product", "centre", "one_back", "two_back", "gated", "hidden") as \
                (w0, w1, product, centre, one_back, two_back, gated, hidden):
            w = (w0, w1)
            turns = FT // WPAIR

            def tap(side, f, back):
                return chip.cols[:, bass.ds(f + (COLS["conv_w"][0] + (3 * layer + 2 - back) * 2 * FT + side * FT), 1)]

            with nc.Block() as block:
                @block.sync
                def _(sp):
                    def load(i, first=False):
                        for j in range(WPAIR):
                            if not first:
                                sp.wait_ge(product, i * 2 * WPAIR + (2 * j + 2 - 2 * WPAIR))
                            sp.dma_start(ring[:, j], A["ffn_w_up"][layer, bass.ds(i * WPAIR + j, 1)]
                                         .rearrange("o p s k n -> p (o s) k n")).then_inc(w[j], 16)

                    load(0, True)
                    with sp.Fori(1, turns) as i:
                        load(i)

                @block.tensor
                def _(pe):
                    def products(i, first=False):
                        for j in range(WPAIR):
                            pe.wait_ge(w[j], i * 16 + 16)
                            if not first:
                                pe.wait_ge(two_back, i * 2 * WPAIR + (2 * j + 2 - 2 * WPAIR))
                            for side in range(2):
                                for k in range(KD):
                                    last = pe.matmul(chip.ps[:, 2 * j + side, :], ring[:, j, side, k, :],
                                                     chip.hT[:, k, :], start=k == 0, stop=k == KD - 1)
                                last.then_inc(product, 1)

                    products(0, True)
                    with pe.Fori(1, turns) as i:
                        products(i)

                @block.scalar
                def _(act):
                    def centre_and_gate(i, first=False):
                        for j in range(WPAIR):
                            f = i * WPAIR + j
                            if not first:
                                act.wait_ge(hidden, i * WPAIR + (j + 1 - WPAIR))
                            for side in range(2):
                                act.wait_ge(product, i * 2 * WPAIR + (2 * j + side + 1))
                                act.activation(conv[:, j, side, :], chip.ps[:, 2 * j + side, :], ACT.Identity,
                                               scale=tap(side, f, 0),
                                               bias=chip.cols[:, bass.ds(f + (COLS["conv_b"][0] + layer * 2 * FT
                                                                              + side * FT), 1)]).then_inc(centre, 1)
                            act.wait_ge(two_back, i * 2 * WPAIR + (2 * j + 1))
                            act.activation(conv[:, j, 0, :], conv[:, j, 0, :], ACT.Silu).then_inc(gated, 1)

                    centre_and_gate(0, True)
                    with act.Fori(1, turns) as i:
                        centre_and_gate(i)

                @block.vector
                def _(dve):
                    def taps_and_product(i):
                        for j in range(WPAIR):
                            f = i * WPAIR + j
                            for side in range(2):
                                c, ps = conv[:, j, side, :], chip.ps[:, 2 * j + side, :]
                                dve.wait_ge(centre, i * 2 * WPAIR + (2 * j + side + 1))
                                dve.scalar_tensor_tensor(out=c[:, 1:S], in0=ps[:, 0:S - 1], scalar=tap(side, f, 1),
                                                         in1=c[:, 1:S], op0=ALU.mult, op1=ALU.add).then_inc(one_back, 1)
                                dve.wait_ge(one_back, i * 2 * WPAIR + (2 * j + side + 1))
                                dve.scalar_tensor_tensor(out=c[:, 2:S], in0=ps[:, 0:S - 2], scalar=tap(side, f, 2),
                                                         in1=c[:, 2:S], op0=ALU.mult, op1=ALU.add).then_inc(two_back, 1)
                            dve.wait_ge(two_back, i * 2 * WPAIR + (2 * j + 2))
                            dve.wait_ge(gated, i * WPAIR + (j + 1))
                            dve.tensor_tensor(hid[:, bass.ds(f, 1), :].rearrange("p o s -> p (o s)"),
                                              conv[:, j, 0, :], conv[:, j, 1, :], ALU.mult).then_inc(hidden, 1)

                    with dve.Fori(0, turns) as i:
                        taps_and_product(i)
                    dve.wait_ge(hidden, FT)


def _ffn_down(nc, chip, A, layer, hid, out):
    R = 4
    with ExitStack() as ctx:
        ring = ctx.enter_context(buffer(nc, "down_ring", [P, R, D], F32))
        with stage(nc, *[f"w{i}" for i in range(R)], "product", "taken_a", "taken_v") as \
                (*w, product, taken_a, taken_v):
            with nc.Block() as block:
                @block.sync
                def _(sp):
                    for f in range(FT):
                        if f >= R:
                            sp.wait_ge(product, f - R + 1)
                        sp.dma_start(ring[:, f % R], A["ffn_w_down"][layer, f]).then_inc(w[f % R], 16)

                @block.tensor
                def _(pe):
                    for f in range(FT):
                        pe.wait_ge(w[f % R], 16 * (f // R + 1))
                        for n in range(2 * TT):
                            t, half = n // 2, n % 2
                            last = pe.matmul(chip.ps[:, n, :], hid[:, f, t * P:(t + 1) * P],
                                             ring[:, f % R, half * 512:(half + 1) * 512], start=f == 0,
                                             stop=f == FT - 1)
                        last.then_inc(product, 1)

                @block.scalar
                def _(act):
                    act.wait_ge(product, FT)
                    for t in range(TT):
                        act.activation(out[:, t, 0:512], chip.ps[:, 2 * t, :], ACT.Copy).then_inc(taken_a, 1)
                    act.wait_ge(taken_a, TT)

                @block.vector
                def _(dve):
                    dve.wait_ge(product, FT)
                    for t in range(TT):
                        dve.tensor_copy(out[:, t, 512:1024], chip.ps[:, 2 * t + 1, :]).then_inc(taken_v, 1)
                    dve.wait_ge(taken_v, TT)


UPTO = 99


def build(nc, A, out):
    STAGES.clear()
    with ExitStack() as ctx:
        chip = Chip(nc, ctx)
        load_constants(nc, chip, A)
        if UPTO not in (20, 30, 40, 50):
            rwkv_block(nc, chip, A)
        if UPTO not in (1, 30, 40, 50):
            expert_block(nc, chip, A)
        if UPTO == 30 or UPTO > 90:
            even_mixer(nc, chip, A)
        if UPTO == 40 or UPTO > 90:
            conv_ffn(nc, chip, A, 0)
        if UPTO == 50 or UPTO > 90:
            odd_mixer(nc, chip, A)
        if UPTO > 90:
            conv_ffn(nc, chip, A, 1)
        with stage(nc, "stored") as (stored,):
            with nc.Block() as block:
                @block.sync
                def _(sp):
                    sp.dma_start(out.rearrange("(t p) d -> p t d", p=P), chip.x[:]).then_inc(stored, 16)
                    sp.wait_ge(stored, 16)


def pack_columns(vectors):
    return np.concatenate([np.ascontiguousarray(v.reshape(-1, P).T) for v in vectors], axis=1)


def tiles_of_columns(w, widths):
    k = w.shape[0] // P
    out, at = np.zeros((len(widths), P, k, P), w.dtype), 0
    for i, n in enumerate(widths):
        out[i, :, :, :n] = w[:, at:at + n].reshape(k, P, n).transpose(1, 0, 2)
        at += n
    return out


def rows(w):
    return np.ascontiguousarray(w.reshape(-1, P, w.shape[1]).transpose(1, 0, 2))


def lay_out(i):
    f = lambda n: np.asarray(i[n])
    a = {}
    a["x"] = f("x")[0]
    in1 = [P] * 15 + [32] + [P] * 4
    a["w_in"] = tiles_of_columns(f("w_in")[0], in1)
    mu = np.zeros((2, SHIFTED * P), np.float32)
    mu[:, :1952] = f("shift_mu")[0]
    a["w_up"] = f("w_up")[0].reshape(P, RD)
    a["a_up"] = f("a_up")[0].reshape(P, RD)
    a["g_up"] = f("g_up")[0]
    a["pool_w"] = np.ascontiguousarray(f("pool_w")[0].transpose(1, 0, 2))
    inv = np.zeros((1, 4 * S), np.float32)
    t = np.arange(S)
    for g, win in enumerate((2, 4, 8, 16)):
        inv[0, g * S:(g + 1) * S] = 1.0 / (np.clip(t + win // 2, 0, S) - np.clip(t - win // 2, 0, S))
    a["pool_inv"] = inv
    a["w_out"] = rows(f("w_out")[0])
    a["peer_wq"] = tiles_of_columns(f("peer_wq")[0], [P] * 16)
    a["peer_keys"] = np.ascontiguousarray(f("peer_keys")[0].reshape(16, P, P).transpose(2, 0, 1))
    a["peer_u"], a["peer_v"] = f("peer_u")[0], f("peer_v")[0]
    a["norm2_row"], a["norm_f_row"] = f("norm2_w")[0], f("norm_f_w")
    a["cols"] = pack_columns([
        f("norm1_w")[0], mu[0], mu[1], f("w0")[0], f("a0")[0], f("k_k")[0], f("k_a")[0], f("r_k")[0],
        f("ln_x_w")[0], f("ln_x_b")[0], f("pool_scale")[0], f("norm2_w")[0], f("ev_pre_g_2")[0],
        f("ev_cq_g_2")[0], f("ev_ckv_g_2")[0], f("ev_subln_g_2")[0], f("od_pre_g_2")[0], f("ffn_pre_g_2"),
        f("ffn_conv_w_2"), f("ffn_conv_b_2")])
    a.update(lay_out_attention(f))
    return a


def lay_out_attention(f):
    a = {}
    w = f("ev_w_in_2")[0]
    a["ev_w_c"] = rows(w[:, 0:384])
    a["ev_w_dv"] = rows(w[:, 416 + 1024:416 + 1536])
    half = QR // 2
    swap = np.r_[half:QR, 0:half]
    kr = w[:, 384:416]
    a["ev_w_qk"] = tiles_of_columns(np.concatenate([w[:, 416:416 + 1024], kr, kr[:, swap]], axis=1), [P] * 8 + [32, 32])
    uq = f("ev_w_uq_2")[0].reshape(256, MH, QK)
    rope_cols = uq[:, :, QN:]
    a["ev_w_uq"] = rows(np.concatenate([rope_cols, uq[:, :, :QN]], axis=2).reshape(256, MH * QK))
    a["ev_w_us"] = rows(np.ascontiguousarray(rope_cols[:, :, swap]).reshape(256, MH * QR))
    ukv = f("ev_w_ukv_2")[0].reshape(P, MH, QN + VH)
    uk = np.zeros((P, MH, QK), np.float32)
    uk[:, :, QR:] = ukv[:, :, :QN]
    a["ev_w_uk"] = uk.reshape(P, MH * QK)
    a["ev_w_uv"] = np.ascontiguousarray(ukv[:, :, QN:]).reshape(P, MH * VH)
    a["ev_lam"] = np.concatenate([f(n)[0] for n in ("ev_lam_q1_2", "ev_lam_k1_2", "ev_lam_q2_2", "ev_lam_k2_2")])
    a["ev_w_out"] = rows(f("ev_w_out_2")[0])
    a["ev_post_row"] = f("ev_post_g_2")[0]
    w = f("od_w_in_2")[0]
    a["od_w_qk"] = tiles_of_columns(np.concatenate([w[:, 0:1536], w[:, 2304:2816]], axis=1), [P] * 16)
    a["od_w_v"] = rows(np.concatenate([w[:, 1536:2304], w[:, 2816:3072]], axis=1))
    a["od_w_out"] = rows(f("od_w_out_2")[0])
    a["od_post_row"] = f("od_post_g_2")[0]
    up = f("ffn_w_up_2")
    a["ffn_w_up"] = np.ascontiguousarray(up.reshape(2, KD, P, 2, FT, P).transpose(0, 4, 2, 3, 1, 5))
    a["ffn_w_down"] = f("ffn_w_down_2").reshape(2, FT, P, D)
    a["ffn_post_rows"] = f("ffn_post_g_2")
    ang = (np.arange(S, dtype=np.float32)[None, :]
           * (np.float32(10000.0) ** (-np.arange(half, dtype=np.float32) / half))[:, None]).astype(np.float32)
    cos, sin = np.cos(ang), np.sin(ang)
    a["rope"] = np.stack([np.r_[cos, cos], np.r_[-sin, sin]], axis=1).astype(np.float32)
    dist = (np.arange(P)[:, None] + (S - P) - np.arange(S)[None, :]).astype(np.float32)
    far = np.float32(1e32)
    t = [np.where(dist >= 0, 0, NEG), np.where(dist >= 0, dist, far)]
    for wdt, dil in ((128, 1), (512, 4), (2048, 16)):
        t.append(np.where((dist >= 0) & (dist <= wdt) & (dist % dil == 0), dist, far))
    t.append(dist > 0)
    a["tables"] = np.stack(t, axis=1).astype(np.float32)
    return a


def kernel(**inputs):
    import numpy as _np
    import concourse.bacc as _bacc
    from concourse import mybir as _mybir
    from concourse.bass_utils import run_bass_kernel_spmd as _run

    nc = _bacc.Bacc("TRN2", target_bir_lowering=False, num_devices=1)
    arrays, A = {}, {}
    for name, a in lay_out(inputs).items():
        arrays[f"in_{name}_dram"] = _np.ascontiguousarray(a)
        A[name] = nc.dram_tensor(f"in_{name}_dram", a.shape, _mybir.dt.from_np(a.dtype), kind="ExternalInput").ap()
    A["scratch"] = nc.dram_tensor("rwkv_scratch", (8, 3, P, S), F32, kind="Internal").ap()
    out = nc.dram_tensor("out_0_dram", (S, D), F32, kind="ExternalOutput").ap()
    build(nc, A, out)
    r = _run(nc, [arrays], core_ids=[0])
    return r.results[0]["out_0_dram"].reshape(1, S, D)
```

```python
from contextlib import ExitStack, contextmanager

import numpy as np
import concourse.bass as bass
from concourse import mybir

F32 = mybir.dt.float32
F32R = mybir.dt.float32r
U32 = mybir.dt.uint32
ALU = mybir.AluOpType
ACT = mybir.ActivationFunctionType
AX = mybir.AxisListType

P = 128
S = 512
TT = S // P
D = 1024
KD = D // P
RD = 512
PR = RD // P
HS = 64
LORA = 64
C = 64
NCH = S // C
DECAY = float(np.exp(-0.5))
GN_EPS = 64e-5
RMS_EPS = 1e-5
NORM_EPS = 1e-6
NEG = -1e30
IN1_TILES = 20
SHIFTED = 16


def buffer(nc, name, shape, dt=F32):
    return nc.sbuf_tensor(f"{name}_{len(STAGES)}", shape, dt)


class Steps:

    def __init__(self, eng, sem, base=0):
        self.eng, self.sem, self.n, self.base = eng, sem, 0, base

    def __call__(self, ins):
        self.n += 1
        ins.then_inc(self.sem, 1)
        return self.n

    def wait(self):
        self.eng.wait_ge(self.sem, self.base + self.n)


STAGES = []


@contextmanager
def stage(nc, *names):
    STAGES.append(names)
    sems = [nc.alloc_semaphore(f"s{len(STAGES)}_{n}") for n in names]
    yield sems
    nc.clear_and_free_semaphores(sems)
    nc.all_engine_barrier()


COLS = {}


def _cols():
    at = 0
    for name, n in (("mu0", SHIFTED), ("mu1", SHIFTED), ("w0", 8), ("a0", 8), ("k_k", 4),
                    ("k_a", 4), ("r_k", 4), ("ln_x_w", 4), ("ln_x_b", 4), ("pool_scale", 4),
                    ("cq_g", 2), ("ckv_g", 1), ("subln_g", 1), ("conv_w", 2 * 3 * 44), ("conv_b", 2 * 44)):
        COLS[name] = (at, n)
        at += n
    return at


NCOLS = _cols()


class Chip:

    def __init__(self, nc, ctx):
        sb = lambda name, shape, dt=F32: ctx.enter_context(buffer(nc, name, shape, dt))
        self.x = sb("x_res", [P, TT, D])
        self.hT = sb("hT", [P, KD, S])
        self.cols = sb("cols", [P, NCOLS])
        self.ident = sb("ident", [P, P])
        self.stack2 = sb("stack2", [P, HS])
        self.ps = ctx.enter_context(nc.psum_tensor("ps", [P, 8, 512], F32))

    def col(self, name, i=0, n=1):
        at, _ = COLS[name]
        return self.cols[:, at + i:at + i + n]


def load_constants(nc, chip, A):
    with stage(nc, "constants_loaded", "constants_step") as (loaded, step):
        with nc.Block() as block:
            @block.sync
            def _(sp):
                sp.dma_start(chip.x[:], A["x"].rearrange("(t p) d -> p t d", p=P)).then_inc(loaded, 16)
                sp.dma_start(chip.cols[:], A["cols"]).then_inc(loaded, 16)
                sp.wait_ge(loaded, 32)

            @block.gpsimd
            def _(pool):
                done = Steps(pool, step)
                done(pool.memset(chip.ident[:], 0.0))
                done(pool.memset(chip.stack2[:], 0.0))
                done.wait()
                done(pool.affine_select(out=chip.ident[:], in_=chip.ident[:], compare_op=ALU.not_equal, fill=1.0,
                                        base=0, pattern=[[-1, P]], channel_multiplier=1))
                done(pool.affine_select(out=chip.stack2[:], in_=chip.stack2[:], compare_op=ALU.not_equal,
                                        fill=1.0, base=0, pattern=[[-1, HS]], channel_multiplier=1))
                done.wait()
                done(pool.affine_select(out=chip.stack2[:], in_=chip.stack2[:], compare_op=ALU.not_equal,
                                        fill=1.0, base=-HS, pattern=[[-1, HS]], channel_multiplier=1))
                done.wait()


def split_product(pe, out, a, b, start, stop):
    pe.matmul(out, a[0], b[0], start=start, stop=False)
    pe.matmul(out, a[0], b[1], start=False, stop=False)
    return pe.matmul(out, a[1], b[0], start=False, stop=stop)


def large_part(act, parts, src):
    return act.activation(parts[0], src, ACT.Copy)


def small_part(dve, parts, src):
    return dve.tensor_tensor(parts[1], src, parts[0].bitcast(F32), ALU.subtract)


def norm_transpose(nc, chip, eps, gain_row, parts, keep=None):
    with ExitStack() as ctx:
        h = keep if keep is not None else ctx.enter_context(buffer(nc, "norm_h", [P, TT, D], F32))
        junk = ctx.enter_context(buffer(nc, "norm_squares", [P, D], F32))
        gain = ctx.enter_context(buffer(nc, "norm_gain", [P, D], F32))
        st = ctx.enter_context(buffer(nc, "norm_stats", [P, 4, TT], F32))
        with stage(nc, "gain_in", "squares", "mean_ready", "root_ready", "v_step", "normed", "turned", "large",
                   "small") as (gain_in, squares, mean_ready, root_ready, v_step, normed, turned, large, small):
            def turned_tile(t):
                return chip.ps[:, 2 * t:2 * t + 2, :].rearrange("p b (k n) -> p (b k) n", n=P)

            def tile_parts(t):
                return [parts[:, i, :, t * P:(t + 1) * P] for i in range(2)]

            with nc.Block() as block:
                @block.sync
                def _(sp):
                    sp.dma_start(gain[:], gain_row.partition_broadcast(P)).then_inc(gain_in, 16)

                @block.scalar
                def _(act):
                    def square(t):
                        if t:
                            act.wait_ge(squares, t)
                        act.activation(junk[:], chip.x[:, t, :], ACT.Square,
                                       accum_out=st[:, 0, t:t + 1]).then_inc(squares, 1)

                    square(0)
                    for t in range(TT):
                        if t + 1 < TT:
                            square(t + 1)
                        act.wait_ge(mean_ready, t + 1)
                        act.activation(st[:, 2, t:t + 1], st[:, 1, t:t + 1], ACT.Sqrt).then_inc(root_ready, 1)
                    for t in range(TT):
                        act.wait_ge(turned, t + 1)
                        large_part(act, tile_parts(t), turned_tile(t)).then_inc(large, 1)

                @block.vector
                def _(dve):
                    done = Steps(dve, v_step)

                    def mean(t):
                        dve.wait_ge(squares, t + 1)
                        dve.tensor_scalar(st[:, 1, t:t + 1], st[:, 0, t:t + 1], 1.0 / D, eps, ALU.mult,
                                          ALU.add).then_inc(mean_ready, 1)

                    mean(0)
                    for t in range(TT):
                        if t + 1 < TT:
                            mean(t + 1)
                        dve.wait_ge(root_ready, t + 1)
                        done(dve.reciprocal(st[:, 3, t:t + 1], st[:, 2, t:t + 1]))
                        done.wait()
                        if t == 0:
                            dve.wait_ge(gain_in, 16)
                        dve.scalar_tensor_tensor(out=h[:, t, :], in0=chip.x[:, t, :], scalar=st[:, 3, t:t + 1],
                                                 in1=gain[:], op0=ALU.mult, op1=ALU.mult).then_inc(normed, 1)
                    for t in range(TT):
                        dve.wait_ge(large, t + 1)
                        small_part(dve, tile_parts(t), turned_tile(t)).then_inc(small, 1)
                    dve.wait_ge(small, TT)

                @block.tensor
                def _(pe):
                    for t in range(TT):
                        pe.wait_ge(normed, t + 1)
                        for k in range(KD):
                            last = pe.transpose(chip.ps[:, 2 * t + k // 4, k % 4 * P:(k % 4 + 1) * P],
                                                h[:, t, k * P:(k + 1) * P], chip.ident[:])
                        last.then_inc(turned, 1)


def split_weights(nc, ctx):
    return ctx.enter_context(buffer(nc, "w_parts", [P, 2, 2, KD, P], F32R))


def project_in_1(nc, chip, A, b, parts):
    RING = 4
    with ExitStack() as ctx:
        ring = ctx.enter_context(buffer(nc, "w_in_ring", [P, RING, KD, P], F32))
        wp = split_weights(nc, ctx)
        rest = ctx.enter_context(buffer(nc, "mu_rest", [P, SHIFTED], F32))
        dst = ([b.rT[:, i, :] for i in range(4)] + [b.kT[:, i, :] for i in range(4)]
               + [b.vT[:, i, :] for i in range(4)] + [b.loraT[:, i, :] for i in range(4)])
        with stage(nc, *[f"w{i}" for i in range(RING)], "rest_ready", "large", "small", "product", "scaled", "shifted",
                   "prev", "pooled") as (*w, rest_ready, large, small, product, scaled, shifted, prev, pooled):
            def w_parts(m):
                return wp[:, m % 2, 0], wp[:, m % 2, 1]

            with nc.Block() as block:
                @block.sync
                def _(sp):
                    for m in range(IN1_TILES):
                        if m >= RING:
                            sp.wait_ge(small, m - RING + 1)
                        sp.dma_start(ring[:, m % RING], A["w_in"][m]).then_inc(w[m % RING], 16)

                @block.tensor
                def _(pe):
                    for m in range(IN1_TILES):
                        pe.wait_ge(small, m + 1)
                        if m >= 8:
                            if m - 8 < SHIFTED:
                                pe.wait_ge(shifted, m - 7)
                            else:
                                pe.wait_ge(pooled, m - 7 - SHIFTED)
                        wide = w_parts(m)
                        for k in range(KD):
                            last = split_product(pe, chip.ps[:, m % 8, :], (wide[0][:, k, :], wide[1][:, k, :]),
                                                 (parts[:, 0, k, :], parts[:, 1, k, :]), k == 0, k == KD - 1)
                        last.then_inc(product, 1)

                @block.scalar
                def _(act):
                    def split(m):
                        act.wait_ge(w[m % RING], 16 * (m // RING + 1))
                        if m >= 2:
                            act.wait_ge(product, m - 1)
                        large_part(act, w_parts(m), ring[:, m % RING]).then_inc(large, 1)

                    split(0)
                    act.wait_ge(rest_ready, 2)
                    for m in range(IN1_TILES):
                        if m + 1 < IN1_TILES:
                            split(m + 1)
                        act.wait_ge(product, m + 1)
                        if m < SHIFTED:
                            act.activation(dst[m], chip.ps[:, m % 8, :], ACT.Copy,
                                           scale=rest[:, m:m + 1]).then_inc(scaled, 1)
                        else:
                            act.activation(b.poolT[:, m - SHIFTED, 8:8 + S], chip.ps[:, m % 8, :],
                                           ACT.Copy).then_inc(pooled, 1)
                    act.wait_ge(pooled, 4)

                @block.vector
                def _(dve):
                    dve.tensor_tensor(rest[:], chip.col("mu0", 0, SHIFTED), chip.col("mu1", 0, SHIFTED),
                                      ALU.add).then_inc(rest_ready, 1)
                    dve.wait_ge(rest_ready, 1)
                    dve.tensor_scalar(rest[:], rest[:], -1.0, 1.0, ALU.mult, ALU.add).then_inc(rest_ready, 1)

                    def split(m):
                        dve.wait_ge(large, m + 1)
                        small_part(dve, w_parts(m), ring[:, m % RING]).then_inc(small, 1)

                    split(0)
                    for m in range(IN1_TILES):
                        if m + 1 < IN1_TILES:
                            split(m + 1)
                        if m >= SHIFTED:
                            continue
                        o, ps = dst[m], chip.ps[:, m % 8, :]
                        dve.wait_ge(scaled, m + 1)
                        dve.scalar_tensor_tensor(out=o[:, 1:S], in0=ps[:, 0:S - 1], scalar=chip.col("mu0", m),
                                                 in1=o[:, 1:S], op0=ALU.mult, op1=ALU.add).then_inc(prev, 1)
                        dve.wait_ge(prev, m + 1)
                        dve.scalar_tensor_tensor(out=o[:, 0:S - 1], in0=ps[:, 1:S], scalar=chip.col("mu1", m),
                                                 in1=o[:, 0:S - 1], op0=ALU.mult, op1=ALU.add).then_inc(shifted, 1)
                    dve.wait_ge(shifted, SHIFTED)


def rwkv_inputs(nc, chip, A, b, yT):
    W = S + 16
    with ExitStack() as ctx:
        sb = lambda name, shape: ctx.enter_context(buffer(nc, name, shape, F32))
        ups = sb("ups", [P, 2, RD])
        gup = sb("gup", [P, 2, RD])
        sq = sb("kk_square", [P, PR, S])
        rr = sb("r_rk", [P, PR, S])
        oma = sb("one_less_ka", [P, PR])
        halves = sb("halves", [P, P])
        sums = sb("window_sums", [P, 2, W])
        inv = sb("window_inverse", [P, 4, S])
        pw = sb("pool_w", [P, 4, P])
        cell = sb("signal_cell", [P, 1])
        with stage(nc, "loras_loaded", "a_step", "v_step", "squared", "summed", "rooted", "low_ready", "up_done",
                   "sig_done", "gate_done", "gate_out", "bonus_in", "bonus_sum", "kept", "spilled", "halves_ready",
                   "windows_loaded", "p_step", "means_ready", "mixed", "pool_taken") as \
                (loaded, a_step, v_step, squared, summed, rooted, low_ready, up_done, sig_done, gate_done,
                 gate_out, bonus_in, bonus_sum, kept, spilled, halves_ready, windows_loaded, p_step, means_ready,
                 mixed, pool_taken):
            with nc.Block() as block:
                @block.sync
                def _(sp):
                    sp.dma_start(ups[:, 0, :], A["w_up"]).then_inc(loaded, 16)
                    sp.dma_start(ups[:, 1, :], A["a_up"]).then_inc(loaded, 16)
                    sp.dma_start(gup[:, 0, :], A["g_up"][0:P]).then_inc(loaded, 16)
                    sp.dma_start(gup[0:32, 1, :], A["g_up"][P:P + 32]).then_inc(loaded, 16)
                    sp.dma_start(inv[:].rearrange("p g t -> p (g t)"),
                                 A["pool_inv"][0].partition_broadcast(P)).then_inc(windows_loaded, 16)
                    sp.dma_start(pw[:], A["pool_w"]).then_inc(windows_loaded, 16)
                    sp.wait_ge(sig_done, 8)
                    sp.dma_start(A["scratch"][:, 0].rearrange("d p s -> p d s"), b.decay[:]).then_inc(spilled, 16)
                    sp.wait_ge(kept, 1)
                    sp.dma_start(A["scratch"][:, 2].rearrange("d p s -> p d s"), b.kd[:]).then_inc(spilled, 16)
                    sp.wait_ge(kept, 2)
                    sp.dma_start(A["scratch"][:, 1].rearrange("d p s -> p d s"), b.a[:]).then_inc(spilled, 16)
                    sp.wait_ge(spilled, 48)

                @block.scalar
                def _(act):
                    act.activation(b.loraT[:, 0, :], b.loraT[:, 0, :], ACT.Tanh).then_inc(low_ready, 1)
                    act.activation(b.loraT[:, 2:4, :], b.loraT[:, 2:4, :], ACT.Sigmoid).then_inc(low_ready, 1)
                    for n in range(16):
                        act.wait_ge(up_done, n + 1)
                        out = (b.decay if n < 8 else b.a)[:, n % 8, :]
                        act.activation(out, chip.ps[:, n % 4, :], ACT.Sigmoid,
                                       bias=chip.col("w0" if n < 8 else "a0", n % 8)).then_inc(sig_done, 1)
                    for i in range(PR):
                        act.wait_ge(gate_done, i + 1)
                        act.activation(b.gateT[:, i, :], chip.ps[:, i, :], ACT.Copy).then_inc(gate_out, 1)
                    act.wait_ge(squared, PR)
                    for i in range(PR):
                        act.wait_ge(summed, i + 1)
                        act.activation(sq[:, i, :], chip.ps[:, 4 + i, :], ACT.Sqrt).then_inc(rooted, 1)
                    act.wait_ge(rooted, PR)
                    for g in range(4):
                        act.wait_ge(mixed, g + 1)
                        act.activation(yT[:, 4 + g, :], chip.ps[:, g, :], ACT.Copy,
                                       scale=chip.col("pool_scale", g)).then_inc(pool_taken, 1)
                    act.wait_ge(pool_taken, 4)

                @block.gpsimd
                def _(pool):
                    pool.memset(halves[0:HS, 0:HS], 1.0).then_inc(halves_ready, 1)
                    pool.memset(halves[HS:P, HS:P], 1.0).then_inc(halves_ready, 1)
                    pool.memset(halves[0:HS, HS:P], 0.0).then_inc(halves_ready, 1)
                    pool.memset(halves[HS:P, 0:HS], 0.0).then_inc(halves_ready, 1)
                    pool.wait_ge(halves_ready, 4)
                    done = Steps(pool, p_step)
                    done(pool.memset(b.poolT[:, :, 0:8], 0.0))
                    done(pool.memset(b.poolT[:, :, S + 8:W], 0.0))
                    done(pool.memset(sums[:], 0.0))
                    done.wait()
                    pool.wait_ge(windows_loaded, 32)
                    for g in range(4):
                        src = b.poolT[:, g, :]
                        for lv in range(g + 1):
                            lo, hi = (1, 0) if lv == 0 else (1 << (lv - 1), 1 << (lv - 1))
                            dst = sums[:, lv % 2, :]
                            done(pool.tensor_tensor(dst[:, 8:8 + S] if lv == g else dst[:, lo:W - hi],
                                                    src[:, 8 - lo:8 - lo + S] if lv == g else src[:, 0:W - hi - lo],
                                                    src[:, 8 + hi:8 + hi + S] if lv == g else src[:, lo + hi:W],
                                                    ALU.add))
                            done.wait()
                            src = dst
                        done(pool.tensor_tensor(sums[:, g % 2, 8:8 + S], src[:, 8:8 + S], inv[:, g, :], ALU.mult))
                        done.wait()
                        pool.tensor_tensor(b.poolT[:, g, 8:8 + S], sums[:, g % 2, 8:8 + S], b.poolT[:, g, 8:8 + S],
                                           ALU.subtract).then_inc(means_ready, 1)
                        pool.wait_ge(means_ready, g + 1)
                        if g < 3:
                            done(pool.memset(sums[:], 0.0))
                            done.wait()

                @block.tensor
                def _(pe):
                    pe.wait_ge(halves_ready, 4)
                    for i in range(PR):
                        pe.wait_ge(squared, i + 1)
                        pe.matmul(chip.ps[:, 4 + i, :], halves[:], sq[:, i, :], start=True,
                                  stop=True).then_inc(summed, 1)
                    pe.wait_ge(loaded, 64)
                    pe.wait_ge(low_ready, 2)
                    for n in range(16):
                        d, i = n // 4 % 2, n % 4
                        if n >= 4:
                            pe.wait_ge(sig_done, n - 3)
                        pe.matmul(chip.ps[:, n % 4, :], ups[d * LORA:(d + 1) * LORA, n // 8, i * P:(i + 1) * P],
                                  b.loraT[d * LORA:(d + 1) * LORA, n // 8, :], start=True,
                                  stop=True).then_inc(up_done, 1)
                    pe.wait_ge(sig_done, 16)
                    for i in range(PR):
                        pe.matmul(chip.ps[:, i, :], gup[:, 0, i * P:(i + 1) * P], b.loraT[:, 2, :], start=True,
                                  stop=False)
                        pe.matmul(chip.ps[:, i, :], gup[0:32, 1, i * P:(i + 1) * P], b.loraT[0:32, 3, :],
                                  start=False, stop=True).then_inc(gate_done, 1)
                    pe.wait_ge(rooted, PR)
                    for i in range(PR):
                        pe.wait_ge(bonus_in, i + 1)
                        pe.matmul(chip.ps[:, 4 + i, :], halves[:], rr[:, i, :], start=True,
                                  stop=True).then_inc(bonus_sum, 1)
                    pe.wait_ge(windows_loaded, 32)
                    pe.wait_ge(gate_out, PR)
                    for g in range(4):
                        pe.wait_ge(means_ready, g + 1)
                        pe.matmul(chip.ps[:, g, :], pw[:, g, :], b.poolT[:, g, 8:8 + S], start=True,
                                  stop=True).then_inc(mixed, 1)

                @block.vector
                def _(dve):
                    done = Steps(dve, v_step)
                    for i in range(PR):
                        done(dve.tensor_scalar(b.kk[:, i, :], b.kT[:, i, :], chip.col("k_k", i), None, ALU.mult))
                    done(dve.tensor_scalar(oma[:], chip.col("k_a", 0, 4), -1.0, 1.0, ALU.mult, ALU.add))
                    done.wait()
                    for i in range(PR):
                        dve.tensor_tensor(sq[:, i, :], b.kk[:, i, :], b.kk[:, i, :], ALU.mult).then_inc(squared, 1)
                    for i in range(PR):
                        done(dve.tensor_scalar(rr[:, i, :], b.rT[:, i, :], chip.col("r_k", i), None, ALU.mult))
                    dve.wait_ge(sig_done, 16)
                    for n in range(8):
                        done(dve.tensor_scalar(b.kd[:, n, :], b.a[:, n, :], chip.col("k_a", n % 4),
                                               oma[:, n % 4:n % 4 + 1], ALU.mult, ALU.add))
                        done.wait()
                        done(dve.tensor_tensor(b.kd[:, n, :], b.kd[:, n, :], b.kT[:, n % 4, :], ALU.mult))
                    done.wait()
                    dve.memset(cell[:], 0.0).then_inc(kept, 1)
                    dve.wait_ge(rooted, PR)
                    done(dve.tensor_scalar(sq[:], sq[:], 1e-12, None, ALU.max))
                    done.wait()
                    done(dve.reciprocal(sq[:], sq[:]))
                    done.wait()
                    done(dve.tensor_tensor(b.kk[:], b.kk[:], sq[:], ALU.mult))
                    done.wait()
                    for n in range(8):
                        done(dve.tensor_tensor(b.a[:, n, :], b.a[:, n, :], b.kk[:, n % 4, :], ALU.mult))
                    done.wait()
                    dve.memset(cell[:], 0.0).then_inc(kept, 1)
                    for i in range(PR):
                        done(dve.tensor_tensor(sq[:, i, :], b.kd[:, i, :], b.kd[:, 4 + i, :], ALU.add))
                        done.wait()
                        dve.tensor_tensor(rr[:, i, :], rr[:, i, :], sq[:, i, :], ALU.mult).then_inc(bonus_in, 1)
                    for i in range(PR):
                        dve.wait_ge(bonus_sum, i + 1)
                        done(dve.tensor_tensor(b.bonusT[:, i, :], chip.ps[:, 4 + i, :], b.vT[:, i, :], ALU.mult))
                    done.wait()


def recurrence(nc, chip, b, A, rev):
    with ExitStack() as ctx:
        sb = lambda name, shape: ctx.enter_context(buffer(nc, name, shape, F32))
        M1 = sb("M1", [P, PR, NCH, P])
        M2 = sb("M2", [P, PR, NCH, P])
        C1 = sb("C1", [P, NCH, PR, HS])
        C2 = sb("C2", [P, NCH, PR, HS])
        with ExitStack() as inner:
            _chunks(nc, chip, b, A, rev, M1, M2, C1, C2, lambda n, s: inner.enter_context(buffer(nc, n, s, F32)))
        _chain(nc, chip, b, rev, M1, M2, C1, C2, sb)


ROUNDS = 14
DVE_IDLE = (8, 10)
ACT_IDLE = (6, 11, 12, 13)


def signals(idle, n):
    whole, part = divmod(n + 1, 2 * ROUNDS)
    return whole * 2 * (ROUNDS - len(idle)) + sum(m // 2 not in idle for m in range(part))


def _chunks(nc, chip, b, A, rev, M1, M2, C1, C2, sb):
    E = {n: sb("E" + n, [P, NCH, P]) for n in ("alpha", "beta", "kappa", "beta_end", "kappa_end", "v")}
    cum = sb("cum", [P, S])
    grow = sb("grow", [P, 3, S])
    start = sb("chunk_start", [P, S])
    strict = sb("strict", [P, P])
    incl = sb("incl", [P, P])
    near = sb("near", [P, 2, P])
    far = sb("far", [P, 2, P])
    pend = sb("chunk_decay", [P, 2, NCH])
    blk = M2[:, 0, 0, :]
    fed = sb("fed", [P, 2, 3, S])
    B = []
    for i in range(2):
        B.append({n: sb(f"{n}{i}", [P, 4, w]) for n, w in (
            ("DD", 2 * P), ("Fn", P), ("Fm", P), ("QB", 2 * P), ("BT", P), ("Qv", P), ("kT_", P),
            ("V", HS), ("XA", HS + P), ("R", P))})
        w = B[-1]
        whole = w["DD"][:].rearrange("p u f -> p (u f)")
        w["Dn"] = whole[:, 0:4 * P].rearrange("p (u f) -> p u f", u=4)
        w["Dm"] = whole[:, 4 * P:8 * P].rearrange("p (u f) -> p u f", u=4)
        w["WA"] = whole[:, 0:4 * (HS + P)].rearrange("p (u f) -> p u f", u=4)
        w["RT"] = w["BT"]
    ps = chip.ps
    with stage(nc, "mask_step", "start_ready", "M1_zeroed", "masks_ready", "summed", "grown", "prepared", "pe_round",
               "dve_round", "act_round", "v_step", "fed0", "fed1") as \
            (mask_step, start_ready, M1_zeroed, masks_ready, summed, grown, prepared, pe_round, dve_round, act_round,
             v_step, fed0, fed1):
        ends = 0 if rev else C - 1

        def chunked(ap):
            return ap.rearrange("p (c t) -> p c t", t=C)

        def wait_fed(eng, g):
            eng.wait_ge((fed0, fed1)[g % 2], 16 * (g // 2 + 1))

        def bc(m):
            return m.rearrange("p (o f) -> p o f", o=1).to_broadcast([P, 4, P])

        def banks(i, k, w=P):
            if w == P:
                return ps[:, 4 * i + k, :].rearrange("p (u f) -> p u f", u=4)
            return ps[:, 4 * i + k:4 * i + k + 2, :].rearrange("p b (u f) -> p (b u) f", u=2)

        def quad(i, k, u, w):
            if w == P:
                return ps[:, 4 * i + k, u * P:(u + 1) * P]
            return ps[:, 4 * i + k + u // 2, (u % 2) * 2 * P:(u % 2) * 2 * P + w]

        with nc.Block() as block:
            @block.gpsimd
            def _(pool):
                done = Steps(pool, mask_step)
                done(pool.memset(start[:], 1.0))
                done.wait()
                pool.memset(start[:, (C - 1 if rev else 0):S:C], 0.0).then_inc(start_ready, 1)
                for n in E:
                    done(pool.memset(E[n][:], 0.0))
                done(pool.memset(strict[:], 1.0))
                done(pool.memset(incl[:], 1.0))
                done(pool.memset(far[:, 1, :], 1.0))
                done(pool.memset(blk, 1.0))
                done.wait()
                sg = -1 if rev else 1
                for m, op, s_ in ((strict[:], ALU.is_gt, sg), (incl[:], ALU.is_ge, sg), (far[:, 1, :], ALU.is_gt, -sg)):
                    done(pool.affine_select(out=m, in_=m, compare_op=op, fill=0.0, base=0, pattern=[[s_, P]],
                                            channel_multiplier=-s_))
                v = blk.rearrange("p (g f) -> p g f", f=16)
                done(pool.affine_select(out=v, in_=v, compare_op=ALU.is_ge, fill=0.0, base=0,
                                        pattern=[[-16, 8], [0, 16]], channel_multiplier=1))
                done.wait()
                done(pool.affine_select(out=v, in_=v, compare_op=ALU.is_ge, fill=0.0, base=15,
                                        pattern=[[16, 8], [0, 16]], channel_multiplier=-1))
                done.wait()
                done(pool.tensor_tensor(near[:, 0, :], strict[:], blk, ALU.mult))
                done(pool.tensor_tensor(near[:, 1, :], far[:, 1, :], blk, ALU.mult))
                done.wait()
                done(pool.tensor_tensor(far[:, 0, :], strict[:], near[:, 0, :], ALU.subtract))
                done(pool.tensor_tensor(far[:, 1, :], far[:, 1, :], near[:, 1, :], ALU.subtract))
                done.wait()
                pool.memset(pend[:], 0.0).then_inc(masks_ready, 1)
                pool.wait_ge(masks_ready, 1)
                pool.wait_ge(M1_zeroed, 1)
                for g in range(PR):
                    wait_fed(pool, g)
                    pool.wait_ge(grown, 3 * g + 3)
                    if g:
                        pool.wait_ge(pe_round, 2 * ROUNDS * (g - 1) + 6)
                        pool.wait_ge(prepared, 2 * g)
                    bb, kd = fed[:, g % 2, 1, :], fed[:, g % 2, 2, :]
                    for dst, s_, w in ((E["alpha"][:], b.kk[:, g, :], 2), (E["beta"][:], bb, 1),
                                       (E["kappa"][:], kd, 1), (M1[:, g], b.rT[:, g, :], 0)):
                        for h in range(2):
                            r = slice(h * HS, (h + 1) * HS)
                            done(pool.tensor_tensor(dst[r, :, r], chunked(s_[r]), chunked(grow[r, w, :]), ALU.mult))
                    for h in range(2):
                        r = slice(h * HS, (h + 1) * HS)
                        done(pool.tensor_copy(E["v"][r, :, r], chunked(b.vT[r, g, :])))
                    done.wait()
                    done(pool.tensor_copy(pend[:, g % 2, :], grow[:, 0, ends:S:C]))
                    done.wait()
                    end = pend[:, g % 2, :].rearrange("p (c o) -> p c o", o=1).to_broadcast([P, NCH, P])
                    pool.tensor_tensor(E["beta_end"][:], E["beta"][:], end, ALU.mult).then_inc(prepared, 1)
                    pool.tensor_tensor(E["kappa_end"][:], E["kappa"][:], end, ALU.mult).then_inc(prepared, 1)

            @block.sync
            def _(sp):
                for g in range(PR):
                    if g >= 2:
                        sp.wait_ge(prepared, 2 * (g - 1))
                    sp.dma_start(fed[:, g % 2], A["scratch"][(4 if rev else 0) + g].rearrange("n p s -> p n s"))\
                        .then_inc((fed0, fed1)[g % 2], 16)

            @block.vector
            def _(dve):
                done = Steps(dve, v_step)

                def sum_up(g):
                    wait_fed(dve, g)
                    if g:
                        dve.wait_ge(prepared, 2 * g)
                    decay = fed[:, g % 2, 0, :]
                    flip = slice(None, None, -1) if rev else slice(None)
                    dve.tensor_tensor_scan(cum[:, flip], start[:, flip], decay[:, flip], 0.0, ALU.mult,
                                           ALU.add).then_inc(summed, 1)
                    dve.wait_ge(summed, 2 * g + 1)
                    dve.tensor_tensor(grow[:, 2, :], cum[:], decay, ALU.subtract).then_inc(summed, 1)

                dve.wait_ge(start_ready, 1)
                sum_up(0)
                dve.memset(M1[:], 0.0).then_inc(M1_zeroed, 1)
                dve.wait_ge(masks_ready, 1)
                for g in range(PR):
                    for r in range(ROUNDS):
                        if r == 4 and g + 1 < PR:
                            sum_up(g + 1)
                        for i in range(2):
                            n = (g * ROUNDS + r) * 2 + i
                            dve.wait_ge(pe_round, n + 1)
                            w, c0 = B[i], 4 * i
                            fin = None
                            if r == 0:
                                done(dve.tensor_tensor(w["Dn"][:], banks(i, 0, 256)[:, :, 0:P], bc(near[:, 0, :]), ALU.mult))
                                done(dve.tensor_tensor(w["Fn"][:], banks(i, 0, 256)[:, :, 0:P], bc(far[:, 0, :]), ALU.mult))
                                done(dve.tensor_tensor(w["Dm"][:], banks(i, 2), bc(near[:, 1, :]), ALU.mult))
                                done(dve.tensor_tensor(w["Fm"][:], banks(i, 2), bc(far[:, 1, :]), ALU.mult))
                                done.wait()
                                done(dve.tensor_tensor(w["R"][:], bc(chip.ident[:]), w["Dn"][:], ALU.subtract))
                                fin = dve.tensor_tensor(w["QB"][:, :, 0:P], banks(i, 0, 256)[:, :, P:256], bc(incl[:]), ALU.mult)
                            elif r == 1:
                                done(dve.tensor_tensor(w["BT"][:], banks(i, 0, 256)[:, :, 0:P], bc(strict[:]), ALU.mult))
                                fin = dve.tensor_tensor(w["Qv"][:], banks(i, 0, 256)[:, :, P:256], bc(incl[:]), ALU.mult)
                            elif r == 2:
                                fin = dve.tensor_copy(w["V"][:], ps[:, 4 * i + 1, 0:4 * HS].rearrange("p (u f) -> p u f", u=4))
                            elif r == 3:
                                fin = dve.tensor_copy(w["Dn"][:], banks(i, 0))
                            elif r in (4, 5):
                                done(dve.tensor_tensor(w["R"][:], w["R"][:], banks(i, 2), ALU.add))
                                if r == 4:
                                    fin = dve.tensor_copy(w["Dn"][:], banks(i, 0))
                                else:
                                    fin = dve.tensor_copy(w["XA"][:, :, 0:HS], ps[:, 4 * i + 3, 0:4 * HS].rearrange("p (u f) -> p u f", u=4))
                            elif r == 6:
                                fin = dve.tensor_tensor(w["R"][:], w["R"][:], banks(i, 2), ALU.add)
                            elif r == 7:
                                done(dve.tensor_copy(w["Dn"][:], banks(i, 0)))
                                fin = dve.tensor_tensor(w["Fn"][:], bc(chip.ident[:]), banks(i, 0), ALU.subtract)
                            elif r == 9:
                                fin = dve.tensor_tensor(w["Fn"][:], w["Fn"][:], banks(i, 0), ALU.add)
                            elif r == 11:
                                fin = dve.tensor_scalar(w["WA"][:], banks(i, 0, 256)[:, :, 0:HS + P], -1.0, None, ALU.mult)
                            elif r == 12:
                                done(dve.tensor_tensor(M1[:, g, c0:c0 + 4, :], banks(i, 0, 256)[:, :, 0:P],
                                                       M1[:, g, c0:c0 + 4, :], ALU.add))
                                for u in range(4):
                                    pe_col = pend[:, g % 2, c0 + u:c0 + u + 1]
                                    fin = dve.scalar_tensor_tensor(
                                        out=M2[:, g, c0 + u, :], in0=chip.ident[:], scalar=pe_col,
                                        in1=quad(i, 0, u, 256)[:, P:256], op0=ALU.mult, op1=ALU.add)
                                    if u < 3:
                                        done(fin)
                            elif r == 13:
                                done(dve.tensor_copy(C1[:, c0:c0 + 4, g, :], ps[:, 4 * i, 0:256].rearrange("p (u f) -> p u f", u=4)))
                                fin = dve.tensor_copy(C2[:, c0:c0 + 4, g, :], ps[:, 4 * i + 1, 0:256].rearrange("p (u f) -> p u f", u=4))
                            if r not in DVE_IDLE:
                                fin.then_inc(dve_round, 1)

            @block.scalar
            def _(act):
                def grow_up(g):
                    act.wait_ge(summed, 2 * g + 2)
                    act.activation(grow[:, 0, :], cum[:], ACT.Exp, scale=-DECAY).then_inc(grown, 1)
                    act.activation(grow[:, 1, :], cum[:], ACT.Exp, scale=DECAY).then_inc(grown, 1)
                    act.activation(grow[:, 2, :], grow[:, 2, :], ACT.Exp, scale=-DECAY).then_inc(grown, 1)

                grow_up(0)
                for g in range(PR):
                    for r in range(ROUNDS):
                        if r == 5 and g + 1 < PR:
                            grow_up(g + 1)
                        for i in range(2):
                            n = (g * ROUNDS + r) * 2 + i
                            act.wait_ge(pe_round, n + 1)
                            w = B[i]
                            cp = lambda o, s_: act.activation(o, s_, ACT.Copy)
                            if r == 0:
                                fin = cp(w["XA"][:, :, HS:HS + P], banks(i, 3))
                            elif r == 1:
                                fin = cp(w["QB"][:, :, P:2 * P], banks(i, 2))
                            elif r == 2:
                                fin = cp(w["kT_"][:], banks(i, 0))
                            elif r == 3:
                                fin = cp(w["Dm"][:], banks(i, 1))
                            elif r in (4, 5):
                                fin = cp(w["Dm"][:], banks(i, 1))
                            elif r == 7:
                                fin = cp(w["Dm"][:], banks(i, 1))
                            elif r == 8:
                                fin = cp(w["Fm"][:], banks(i, 0))
                            elif r == 9:
                                fin = cp(w["RT"][:], banks(i, 1))
                            elif r == 10:
                                fin = cp(w["R"][:], banks(i, 0))
                            if r not in ACT_IDLE:
                                fin.then_inc(act_round, 1)

            @block.tensor
            def _(pe):
                for g in range(PR):
                    pe.wait_ge(prepared, 2 * g + 2)
                    for r in range(ROUNDS):
                        for i in range(2):
                            n = (g * ROUNDS + r) * 2 + i
                            if n >= 2:
                                pe.wait_ge(dve_round, signals(DVE_IDLE, n - 2))
                                pe.wait_ge(act_round, signals(ACT_IDLE, n - 2))
                            w = B[i]
                            last = None
                            for u in range(4):
                                c = 4 * i + u
                                al, be, ka, rh = E["alpha"][:, c, :], E["beta"][:, c, :], E["kappa"][:, c, :], M1[:, g, c, :]

                                def mm(dst, lhsT, rhs, start=True, stop=True):
                                    return pe.matmul(dst, lhsT, rhs, start=start, stop=stop)

                                def q(k, width=P):
                                    return quad(i, k, u, width)

                                X = lambda name: w[name][:, u, :]
                                if r == 0:
                                    mm(quad(i, 0, u, 256)[:, 0:P], be, al)
                                    mm(quad(i, 0, u, 256)[:, P:256], be, rh)
                                    mm(q(2), al, be)
                                    last = pe.transpose(q(3), al, chip.ident[:])
                                elif r == 1:
                                    mm(quad(i, 0, u, 256)[:, 0:P], ka, al)
                                    mm(quad(i, 0, u, 256)[:, P:256], ka, rh)
                                    last = pe.transpose(q(2), E["beta_end"][:, c, :], chip.ident[:])
                                elif r == 2:
                                    pe.transpose(q(0), E["kappa_end"][:, c, :], chip.ident[:])
                                    last = mm(ps[:, 4 * i + 1, u * HS:(u + 1) * HS], E["v"][:, c, :], chip.stack2[:])
                                elif r == 3:
                                    mm(q(0), X("Dm"), X("Dn"))
                                    last = mm(q(1), X("Dn"), X("Dm"))
                                elif r == 4:
                                    mm(q(0), X("Dm"), X("Dn"))
                                    mm(q(1), X("Dn"), X("Dm"))
                                    last = mm(q(2), X("Dm"), X("R"))
                                elif r == 5:
                                    mm(ps[:, 4 * i + 3, u * HS:(u + 1) * HS], X("BT"), X("V"))
                                    mm(q(1), X("Dn"), X("Dm"))
                                    last = mm(q(2), X("Dm"), X("R"))
                                elif r == 6:
                                    last = mm(q(2), X("Dm"), X("R"))
                                elif r == 7:
                                    mm(q(0), X("Fm"), X("R"))
                                    last = mm(q(1), X("R"), X("Fm"))
                                elif r == 8:
                                    last = mm(q(0), X("Dn"), X("Dm"))
                                elif r == 9:
                                    mm(q(0), X("Fm"), X("Fn"))
                                    last = pe.transpose(q(1), X("R"), chip.ident[:])
                                elif r == 10:
                                    last = mm(q(0), X("RT"), X("Fn"))
                                elif r == 11:
                                    last = mm(quad(i, 0, u, 256)[:, 0:HS + P], X("R"), X("XA"))
                                elif r == 12:
                                    last = mm(quad(i, 0, u, 256), w["WA"][:, u, HS:HS + P], X("QB"))
                                elif r == 13:
                                    o1 = ps[:, 4 * i, u * HS:(u + 1) * HS]
                                    mm(o1, X("Qv"), X("V"), stop=False)
                                    mm(o1, w["QB"][:, u, 0:P], w["WA"][:, u, 0:HS], start=False)
                                    o2 = ps[:, 4 * i + 1, u * HS:(u + 1) * HS]
                                    mm(o2, X("kT_"), X("V"), stop=False)
                                    last = mm(o2, w["QB"][:, u, P:2 * P], w["WA"][:, u, 0:HS], start=False)
                            last.then_inc(pe_round, 1)


def _chain(nc, chip, b, rev, M1, M2, C1, C2, sb):
    st = sb("states", [P, NCH + 1, PR, HS])
    order = list(range(NCH))[::-1] if rev else list(range(NCH))
    with stage(nc, "stepped", "state_ready", "out_ready", "v_step") as (stepped, state_ready, out_ready, v_step):
        with nc.Block() as block:
            @block.tensor
            def _(pe):
                for n, c in enumerate(order[:-1]):
                    pe.wait_ge(state_ready, n + 1)
                    for g in range(PR):
                        last = pe.matmul(chip.ps[:, n % 2, g * HS:(g + 1) * HS], M2[:, g, c, :], st[:, n, g, :],
                                         start=True, stop=True)
                    last.then_inc(stepped, 1)
                pe.wait_ge(state_ready, NCH)
                for n, c in enumerate(order):
                    for g in range(PR):
                        u = c * PR + g
                        last = pe.matmul(chip.ps[:, 4 + u // 8, (u % 8) * HS:(u % 8 + 1) * HS], M1[:, g, c, :],
                                         st[:, n, g, :], start=True, stop=True)
                last.then_inc(out_ready, 1)

            @block.vector
            def _(dve):
                done = Steps(dve, v_step)
                dve.memset(st[:, 0], 0.0).then_inc(state_ready, 1)
                for n, c in enumerate(order[:-1]):
                    dve.wait_ge(stepped, n + 1)
                    dve.tensor_tensor(st[:, n + 1], chip.ps[:, n % 2, 0:PR * HS].rearrange("p (g v) -> p g v", g=PR),
                                      C2[:, c], ALU.add).then_inc(state_ready, 1)
                if rev:
                    done(dve.tensor_tensor(C1[:], C1[:], b.out, ALU.add))
                dve.wait_ge(out_ready, 1)
                done.wait()
                done(dve.tensor_tensor(b.out.rearrange("p c g v -> p (c g v)"),
                                       chip.ps[:, 4:8, :].rearrange("p b n -> p (b n)"),
                                       C1[:].rearrange("p c g v -> p (c g v)"), ALU.add))
                done.wait()


def rwkv_output(nc, chip, A, b, yT):
    NU = NCH * PR
    with ExitStack() as ctx:
        sb = lambda name, shape: ctx.enter_context(buffer(nc, name, shape, F32))
        sq = sb("out_sq", [P, NU, HS])
        OE = sb("out_E", [P, NU, P])
        st = sb("out_stats", [P, 4, NU])
        with stage(nc, "v_step", "var_ready", "root_ready", "zeroed", "normed", "turned", "affine", "gated") as \
                (v_step, var_ready, root_ready, zeroed, normed, turned, affine, gated):
            with nc.Block() as block:
                @block.gpsimd
                def _(pool):
                    pool.memset(OE[0:HS, :, HS:P], 0.0).then_inc(zeroed, 1)
                    pool.memset(OE[HS:P, :, 0:HS], 0.0).then_inc(zeroed, 1)
                    pool.wait_ge(zeroed, 2)

                @block.vector
                def _(dve):
                    done = Steps(dve, v_step)
                    o = b.out.rearrange("p c g v -> p (c g) v")
                    spread = lambda r: st[:, r, :].rearrange("p (u o) -> p u o", o=1).to_broadcast([P, NU, HS])
                    done(dve.tensor_reduce(st[:, 0, :], o, AX.X, ALU.add))
                    done.wait()
                    done(dve.tensor_scalar(st[:, 0, :], st[:, 0, :], 1.0 / HS, None, ALU.mult))
                    done.wait()
                    done(dve.tensor_tensor(o, o, spread(0), ALU.subtract))
                    done.wait()
                    done(dve.tensor_tensor(sq[:], o, o, ALU.mult))
                    done.wait()
                    done(dve.tensor_reduce(st[:, 1, :], sq[:], AX.X, ALU.add))
                    done.wait()
                    dve.tensor_scalar(st[:, 2, :], st[:, 1, :], 1.0 / HS, GN_EPS, ALU.mult,
                                      ALU.add).then_inc(var_ready, 1)
                    dve.wait_ge(root_ready, 1)
                    done(dve.reciprocal(st[:, 1, :], st[:, 3, :]))
                    done.wait()
                    dve.wait_ge(zeroed, 2)
                    for h in range(2):
                        r = slice(h * HS, (h + 1) * HS)
                        dve.tensor_tensor(OE[r, :, r], o[r], spread(1)[r], ALU.mult).then_inc(normed, 1)
                    for g in range(PR):
                        dve.wait_ge(affine, g + 1)
                        done(dve.tensor_tensor(yT[:, g, :], yT[:, g, :], b.bonusT[:, g, :], ALU.add))
                        done.wait()
                        done(dve.tensor_tensor(yT[:, g, :], yT[:, g, :], b.gateT[:, g, :], ALU.mult))
                    done.wait()

                @block.scalar
                def _(act):
                    act.wait_ge(var_ready, 1)
                    act.activation(st[:, 3, :], st[:, 2, :], ACT.Sqrt).then_inc(root_ready, 1)
                    for g in range(PR):
                        act.wait_ge(turned, g + 1)
                        act.activation(yT[:, g, :], chip.ps[:, g, :], ACT.Identity, scale=chip.col("ln_x_w", g),
                                       bias=chip.col("ln_x_b", g)).then_inc(affine, 1)

                @block.tensor
                def _(pe):
                    pe.wait_ge(normed, 2)
                    for g in range(PR):
                        for c in range(NCH):
                            last = pe.matmul(chip.ps[:, g, c * C:(c + 1) * C], OE[:, c * PR + g, :], chip.stack2[:],
                                             start=True, stop=True)
                        last.then_inc(turned, 1)


def stream_product(nc, chip, w_of, n_k, halves=((0, 512), (512, 1024)), x_of=None, parts=None, out_of=None,
                   norm_row=None, x_again=None):
    width = halves[1][1]
    turns = n_k // 2
    per = 1 if parts is not None else 2
    with ExitStack() as ctx:
        raw = ctx.enter_context(buffer(nc, "stream_w", [P, 2, width], F32))
        wp = ctx.enter_context(buffer(nc, "stream_w_parts", [P, 2, 2, width], F32R))
        xp = ctx.enter_context(buffer(nc, "stream_x_parts", [P, 2, 2, S if per == 2 else 2], F32R))
        gain = ctx.enter_context(buffer(nc, "post_gain", [P, D if norm_row is not None else 2], F32))
        junk = ctx.enter_context(buffer(nc, "post_squares", [P, D if norm_row is not None else 2], F32))
        y = ctx.enter_context(buffer(nc, "post_normed", [P, 2, D if norm_row is not None else 2], F32))
        st = ctx.enter_context(buffer(nc, "post_stats", [P, 4, TT], F32))
        with stage(nc, "w0", "w1", "gain_in", "x_in", "large", "small", "product", "taken_a", "taken_v", "squares", "mean_ready",
                   "root_ready", "v_step", "normed", "added") as \
                (w0, w1, gain_in, x_in, large, small, product, taken_a, taken_v, squares, mean_ready, root_ready, v_step,
                 normed, added):
            def w_parts(j):
                return wp[:, j, 0, :], wp[:, j, 1, :]

            def x_parts(j):
                return xp[:, j, 0, :], xp[:, j, 1, :]

            def loop(eng, turn, last_apart=False):
                turn(0, first=True)
                end = turns - 1 if last_apart else turns
                if parts is not None or end < 4:
                    for i in range(1, end):
                        turn(i)
                else:
                    with eng.Fori(1, end) as i:
                        turn(i)
                if last_apart:
                    turn(turns - 1, last=True)

            with nc.Block() as block:
                @block.sync
                def _(sp):
                    def load(i, first=False):
                        for j in range(2):
                            if not first:
                                sp.wait_ge(small, i * 2 * per + (j + 1 - 2) * per)
                            sp.dma_start(raw[:, j], w_of(i * 2 + j)).then_inc((w0, w1)[j], 16)

                    load(0, True)
                    if x_again is not None:
                        sp.dma_start(chip.x[:], x_again).then_inc(x_in, 16)
                    if norm_row is not None:
                        sp.dma_start(gain[:], norm_row.partition_broadcast(P)).then_inc(gain_in, 16)
                    if parts is not None or turns < 4:
                        for i in range(1, turns):
                            load(i)
                    else:
                        with sp.Fori(1, turns) as i:
                            load(i)

                @block.tensor
                def _(pe):
                    def turn(i, first=False, last=False):
                        for j in range(2):
                            pe.wait_ge(small, i * 2 * per + (j + 1) * per)
                            for t in range(TT):
                                cols = slice(t * P, (t + 1) * P)
                                if parts is None:
                                    x = [part[:, cols] for part in x_parts(j)]
                                else:
                                    x = [parts[:, part, 2 * i + j, cols] for part in range(2)]
                                for half, (lo, hi) in enumerate(halves):
                                    ins = split_product(pe, chip.ps[:, 2 * t + half, 0:hi - lo], x,
                                                        [part[:, lo:hi] for part in w_parts(j)],
                                                        first and j == 0, last and j == 1)
                            ins.then_inc(product, 1)

                    loop(pe, turn, last_apart=True)

                @block.scalar
                def _(act):
                    def split(i, first=False):
                        for j in range(2):
                            act.wait_ge((w0, w1)[j], i * 16 + 16)
                            if not first:
                                act.wait_ge(product, i * 2 + (j + 1 - 2))
                            large_part(act, w_parts(j), raw[:, j, :]).then_inc(large, 1)
                            if per == 2:
                                large_part(act, x_parts(j), x_of(i * 2 + j)).then_inc(large, 1)

                    loop(act, split)
                    act.wait_ge(product, n_k)
                    if out_of is not None:
                        lo, hi = halves[0]
                        for t in range(TT):
                            act.activation(out_of(t, 0), chip.ps[:, 2 * t, 0:hi - lo], ACT.Copy).then_inc(taken_a, 1)
                        act.wait_ge(taken_a, TT)
                    elif norm_row is not None:
                        for t in range(TT):
                            if t:
                                act.wait_ge(squares, t)
                            act.activation(junk[:], chip.ps[:, 2 * t:2 * t + 2, :].rearrange("p b n -> p (b n)"),
                                           ACT.Square, accum_out=st[:, 0, t:t + 1]).then_inc(squares, 1)
                            if t:
                                act.wait_ge(mean_ready, t)
                                act.activation(st[:, 2, t - 1:t], st[:, 1, t - 1:t], ACT.Sqrt).then_inc(root_ready, 1)
                        act.wait_ge(mean_ready, TT)
                        act.activation(st[:, 2, TT - 1:TT], st[:, 1, TT - 1:TT], ACT.Sqrt).then_inc(root_ready, 1)

                @block.vector
                def _(dve):
                    done = Steps(dve, v_step)

                    def split(i, first=False):
                        for j in range(2):
                            dve.wait_ge(large, i * 2 * per + (j * per + 1))
                            small_part(dve, w_parts(j), raw[:, j, :]).then_inc(small, 1)
                            if per == 2:
                                dve.wait_ge(large, i * 2 * per + (j * per + 2))
                                small_part(dve, x_parts(j), x_of(i * 2 + j)).then_inc(small, 1)

                    loop(dve, split)
                    if norm_row is None:
                        dve.wait_ge(product, n_k)
                        if x_again is not None:
                            dve.wait_ge(x_in, 16)
                        lo, hi = halves[1]
                        for t in range(TT):
                            if out_of is not None:
                                dve.tensor_copy(out_of(t, 1), chip.ps[:, 2 * t + 1, 0:hi - lo]).then_inc(taken_v, 1)
                            else:
                                xt = chip.x[:, t, :].rearrange("p (b n) -> p b n", b=2)
                                dve.tensor_tensor(xt, xt, chip.ps[:, 2 * t:2 * t + 2, :], ALU.add).then_inc(taken_v, 1)
                        dve.wait_ge(taken_v, TT)
                        return

                    def mean(t):
                        dve.wait_ge(squares, t + 1)
                        dve.tensor_scalar(st[:, 1, t:t + 1], st[:, 0, t:t + 1], 1.0 / D, NORM_EPS, ALU.mult,
                                          ALU.add).then_inc(mean_ready, 1)

                    mean(0)
                    for t in range(TT):
                        if t + 1 < TT:
                            mean(t + 1)
                        dve.wait_ge(root_ready, t + 1)
                        done(dve.reciprocal(st[:, 3, t:t + 1], st[:, 2, t:t + 1]))
                        done.wait()
                        if t == 0:
                            dve.wait_ge(gain_in, 16)
                        if t >= 2:
                            dve.wait_ge(added, t - 1)
                        dve.scalar_tensor_tensor(out=y[:, t % 2, :], in0=chip.ps[:, 2 * t:2 * t + 2, :]
                                                 .rearrange("p b n -> p (b n)"), scalar=st[:, 3, t:t + 1], in1=gain[:],
                                                 op0=ALU.mult, op1=ALU.mult).then_inc(normed, 1)

                @block.gpsimd
                def _(pool):
                    if norm_row is not None:
                        for t in range(TT):
                            pool.wait_ge(normed, t + 1)
                            pool.tensor_tensor(chip.x[:, t, :], chip.x[:, t, :], y[:, t % 2, :],
                                               ALU.add).then_inc(added, 1)
                        pool.wait_ge(added, TT)


def of_rows(w, k):
    return w[bass.ds(k, 1)].rearrange("o p n -> p (o n)")


def of_tiles(xT, k):
    return xT[:, bass.ds(k, 1), :].rearrange("p o s -> p (o s)")


class Obj:
    pass


def rwkv_block(nc, chip, A):
    with ExitStack() as ctx:
        sb = lambda name, shape, c=ctx: c.enter_context(buffer(nc, name, shape, F32))
        b = Obj()
        yT = chip.hT[:]
        b.out = chip.hT[:, 0:4, :].rearrange("p k (c v) -> p (k c) v", v=HS).rearrange("p (c g) v -> p c g v", g=PR)
        spare = chip.x[:].rearrange("p t d -> p (t d)")
        b.gateT = spare[:, 0:PR * S].rearrange("p (g s) -> p g s", g=PR)
        b.bonusT = spare[:, PR * S:2 * PR * S].rearrange("p (g s) -> p g s", g=PR)
        b.rT, b.vT, b.kk = (sb(n, [P, PR, S]) for n in ("rT", "vT", "kkT"))
        with ExitStack() as early:
            b.kT, b.loraT = sb("kT", [P, PR, S], early), sb("loraT", [P, 4, S], early)
            b.poolT = sb("poolT", [P, 4, S + 16], early)
            with ExitStack() as split_ctx:
                parts = split_ctx.enter_context(buffer(nc, "h_parts", [P, 2, KD, S], F32R))
                norm_transpose(nc, chip, RMS_EPS, A["norm1_row"], parts)
                project_in_1(nc, chip, A, b, parts)
            b.decay, b.a, b.kd = (sb(n, [P, 8, S], early) for n in ("decayT", "aT", "kdT"))
            rwkv_inputs(nc, chip, A, b, yT)
        for rev in (False, True):
            recurrence(nc, chip, b, A, rev)
        rwkv_output(nc, chip, A, b, yT)
    stream_product(nc, chip, lambda k: of_rows(A["w_out"], k), KD, x_of=lambda k: of_tiles(chip.hT, k),
                   x_again=A["x"].rearrange("(t p) d -> p t d", p=P))


PH = 8
TOPK = 16
SLOTS = PH * TOPK
NKEYS = 128
RING = 16


def expert_scores(nc, chip, A, parts, scores):
    WR = 4
    with ExitStack() as ctx:
        sb = lambda name, shape, dt=F32: ctx.enter_context(buffer(nc, name, shape, dt))
        ring = sb("wq_ring", [P, WR, KD, P])
        keys = sb("keys", [P, 2 * PH, NKEYS])
        q_high = sb("q_highT", [P, PH, S])
        q = lambda m: chip.hT[:, m, :] if m < PH else q_high[:, m - PH, :]
        wp = split_weights(nc, ctx)
        with stage(nc, *[f"w{i}" for i in range(WR)], "keys_in", "large", "small", "q_done", "q_out_a", "q_out_v",
                   "s_done", "s_out_a", "s_out_v") as \
                (*w, keys_in, large, small, q_done, q_out_a, q_out_v, s_done, s_out_a, s_out_v):
            def w_parts(m):
                return wp[:, m % 2, 0], wp[:, m % 2, 1]

            with nc.Block() as block:
                @block.sync
                def _(sp):
                    for m in range(2 * PH):
                        if m >= WR:
                            sp.wait_ge(small, m - WR + 1)
                        sp.dma_start(ring[:, m % WR], A["peer_wq"][m]).then_inc(w[m % WR], 16)
                        if m == 1:
                            sp.dma_start(keys[:], A["peer_keys"]).then_inc(keys_in, 16)

                @block.tensor
                def _(pe):
                    for m in range(2 * PH):
                        pe.wait_ge(small, m + 1)
                        if m >= 8:
                            pe.wait_ge(q_out_v if m % 2 else q_out_a, m // 2 - 3)
                        wide = w_parts(m)
                        for k in range(KD):
                            last = split_product(pe, chip.ps[:, m % 8, :], (wide[0][:, k, :], wide[1][:, k, :]),
                                                 (parts[:, 0, k, :], parts[:, 1, k, :]), k == 0, k == KD - 1)
                        last.then_inc(q_done, 1)
                    pe.wait_ge(q_out_a, PH)
                    pe.wait_ge(q_out_v, PH)
                    pe.wait_ge(keys_in, 16)
                    for t in range(TT):
                        for j in range(2 * PH):
                            if t >= 2 and j % 4 == 0:
                                pe.wait_ge(s_out_v if j // 4 % 2 else s_out_a, (t - 2) * 2 + j // 8 + 1)
                            last = pe.matmul(chip.ps[:, t % 2 * 4 + j // 4, j % 4 * P:(j % 4 + 1) * P],
                                             q(j)[:, t * P:(t + 1) * P], keys[:, j, :], start=True, stop=True)
                            if j % 4 == 3:
                                last.then_inc(s_done, 1)

                @block.scalar
                def _(act):
                    for m in range(2 * PH + 1):
                        if m < 2 * PH:
                            act.wait_ge(w[m % WR], 16 * (m // WR + 1))
                            if m >= 2:
                                act.wait_ge(q_done, m - 1)
                            large_part(act, w_parts(m), ring[:, m % WR]).then_inc(large, 1)
                        if m % 2:
                            act.wait_ge(q_done, m)
                            act.activation(q(m - 1), chip.ps[:, (m - 1) % 8, :], ACT.Copy).then_inc(q_out_a, 1)
                    for t in range(TT):
                        for j in (0, 2):
                            act.wait_ge(s_done, t * 4 + j + 1)
                            act.activation(scores[:, t, j * 512:(j + 1) * 512],
                                           chip.ps[:, t % 2 * 4 + j, :], ACT.Copy).then_inc(s_out_a, 1)
                    act.wait_ge(s_out_a, 2 * TT)

                @block.vector
                def _(dve):
                    for m in range(2 * PH + 1):
                        if m < 2 * PH:
                            dve.wait_ge(large, m + 1)
                            small_part(dve, w_parts(m), ring[:, m % WR]).then_inc(small, 1)
                        if m and m % 2 == 0:
                            dve.wait_ge(q_done, m)
                            dve.tensor_copy(q(m - 1), chip.ps[:, (m - 1) % 8, :]).then_inc(q_out_v, 1)
                    for t in range(TT):
                        for j in (1, 3):
                            dve.wait_ge(s_done, t * 4 + j + 1)
                            dve.tensor_copy(scores[:, t, j * 512:(j + 1) * 512],
                                            chip.ps[:, t % 2 * 4 + j, :]).then_inc(s_out_v, 1)
                    dve.wait_ge(s_out_v, 2 * TT)


PASSES = tuple((kind, t) for t in range(TT) for kind in "uv")
TURNS = SLOTS // RING
HALF = RING // 2
ADDED = (3, 7, 11, 15)
MULTIPLIED = tuple(s for s in range(RING) if s not in ADDED)


class Choice:
    STEPS = 28

    def __init__(self, dve, sb, scores, idx, gate, iota):
        self.dve, self.scores, self.idx, self.gate, self.iota = dve, scores, idx, gate, iota
        self.mine = sb("scores_now", [P, 2, NKEYS])
        self.left = sb("scores_left", [P, 2, NKEYS])
        self.top = sb("top", [P, 2, TOPK])
        self.topi = sb("top_index", [P, 2, TOPK], U32)
        self.topf = sb("top_index_f", [P, 2, TOPK])
        self.cand = sb("cand", [P, 1, TOPK * TOPK])
        self.candl = sb("cand_left", [P, 1, TOPK * TOPK])
        self.best = sb("best", [P, 1, TOPK])
        self.pos = sb("best_pos", [P, 1, TOPK], U32)
        self.part = sb("pos_part", [P, 2, TOPK], U32)
        self.partf = sb("pos_part_f", [P, 2, TOPK])
        self.same = sb("pos_same", [P, 2, TOPK, TOPK])
        self.chosen = sb("chosen", [P, 2, TOPK])
        self.gatekeeper = sb("choice_gatekeeper", [P, 1])

    def let_through(self):
        self.dve.tensor_copy(self.gatekeeper[:], self.iota[:, 0:1])

    def top16(self, done, values, rest, n, out, index):
        dve = self.dve
        self.let_through()
        for j in range(n):
            done(dve.max(out[:, j, 0:8], values[:, j, :]))
        done.wait()
        self.let_through()
        for j in range(n):
            done(dve.match_replace(rest[:, j, :], out[:, j, 0:8], values[:, j, :], -3e38))
            done(dve.max_index(index[:, j, 0:8], out[:, j, 0:8], values[:, j, :]))
        done.wait()
        self.let_through()
        for j in range(n):
            done(dve.max(out[:, j, 8:16], rest[:, j, :]))
        done.wait()
        self.let_through()
        for j in range(n):
            done(dve.max_index(index[:, j, 8:16], out[:, j, 8:16], rest[:, j, :]))
        done.wait()

    def sides(self, done, t, h):
        done(self.dve.tensor_copy(self.mine[:].rearrange("p a n -> p (a n)"),
                                  self.scores[:, t, bass.ds(h * (2 * NKEYS), 2 * NKEYS)]))
        done.wait()
        self.top16(done, self.mine, self.left, 2, self.top, self.topi)

    def pairs(self, done, t, h):
        dve = self.dve
        done(dve.tensor_copy(self.topf[:], self.topi[:]))
        a = self.top[:, 0, :].rearrange("p (k o) -> p k o", o=1).to_broadcast([P, TOPK, TOPK])
        c = self.top[:, 1, :].rearrange("p (o k) -> p o k", o=1).to_broadcast([P, TOPK, TOPK])
        done(dve.tensor_tensor(self.cand[:, 0, :].rearrange("p (a b) -> p a b", b=TOPK), a, c, ALU.add))
        done.wait()
        self.top16(done, self.cand, self.candl, 1, self.best, self.pos)

    def names(self, done, t, h, picked):
        dve = self.dve
        done(dve.tensor_scalar(self.gate[:, t, bass.ds(h * TOPK, TOPK)], self.best[:, 0, :], self.best[:, 0, 0:1], None,
                               ALU.subtract))
        done(dve.tensor_scalar(self.part[:, 0, :], self.pos[:, 0, :], 4, None, ALU.logical_shift_right))
        done(dve.tensor_scalar(self.part[:, 1, :], self.pos[:, 0, :], 15, None, ALU.bitwise_and))
        done.wait()
        done(dve.tensor_copy(self.partf[:], self.part[:]))
        done.wait()
        for side in range(2):
            done(dve.tensor_tensor(self.same[:, side], self.partf[:, side, :].rearrange("p (k o) -> p k o", o=1)
                                   .to_broadcast([P, TOPK, TOPK]), self.iota[:].rearrange("p (o a) -> p o a", o=1)
                                   .to_broadcast([P, TOPK, TOPK]), ALU.is_equal))
        done.wait()
        for side in range(2):
            done(dve.tensor_tensor(self.same[:, side], self.same[:, side], self.topf[:, side, :]
                                   .rearrange("p (o a) -> p o a", o=1).to_broadcast([P, TOPK, TOPK]), ALU.mult))
        done.wait()
        done(dve.tensor_reduce(self.chosen[:].rearrange("p s k -> p (s k)"),
                               self.same[:].rearrange("p s k a -> p (s k) a"), AX.X, ALU.add))
        done.wait()
        done(dve.scalar_tensor_tensor(out=self.chosen[:, 0, :], in0=self.chosen[:, 0, :], scalar=float(NKEYS),
                                      in1=self.chosen[:, 1, :], op0=ALU.mult, op1=ALU.add))
        done.wait()
        dve.tensor_copy(self.idx[:, t, bass.ds(h * TOPK, TOPK)], self.chosen[:, 0, :]).then_inc(picked, 1)


def experts(nc, chip, A, h2, scores, idx, gate):
    with ExitStack() as ctx:
        sb = lambda name, shape, dt=F32: ctx.enter_context(buffer(nc, name, shape, dt))
        ring = sb("row_ring", [P, RING, D])
        now = sb("idx_now", [P, RING], U32)
        dots = sb("dots_now", [P, RING])
        dot = sb("dots", [P, TT, SLOTS])
        coef = sb("coef", [P, TT, SLOTS])
        diag = sb("diag", [P, RING, P])
        zero = sb("zero", [P, P])
        iota = sb("iota16", [P, TOPK])
        sums = sb("gate_sum", [P, PH])
        gatekeeper = sb("gatekeeper", [P, 1], U32)
        gain = sb("norm_f_gain", [P, D])
        junk = sb("norm_f_squares", [P, D])
        st = sb("norm_f_stats", [P, 4, TT])
        with stage(nc, *[f"row{i}" for i in range(RING)], "iota_ready", "picked", "v_step", "idx_now_ready", "u_used",
                   "v_multiplied", "v_added", "dots_kept", "exped", "gelu_done", "coef_ready", "diag_ready", "zeroed",
                   "summed", "x_taken", "gain_in", "squared", "mean_ready", "rooted") as \
                (*row, iota_ready, picked, v_step, idx_ready, u_used, v_multiplied, v_added, dots_kept, exped, gelu_done,
                 coef_ready, diag_ready, zeroed, summed, x_taken, gain_in, squared, mean_ready, rooted):
            users = {"u": ((u_used, RING),), "v": ((v_multiplied, len(MULTIPLIED)), (v_added, len(ADDED)))}

            with nc.Block() as block:
                @block.sync
                def _(sp):
                    sp.dma_start(gain[:], A["norm_f_row"].partition_broadcast(P)).then_inc(gain_in, 16)

                @block.gpsimd
                def _(pool):
                    def turn(n, i, first=False):
                        kind, t = PASSES[n]
                        for half in range(2):
                            lo = half * HALF
                            if not first:
                                for used, per in users[kind]:
                                    pool.wait_ge(used, i * per + (t * TURNS * per - per + (half + 1) * per // 2))
                            if n:
                                for used, per in users["v" if kind == "u" else "u"]:
                                    turns = TURNS * (t if kind == "u" else t + 1)
                                    pool.wait_ge(used, turns * per - per + (half + 1) * per // 2)
                            if kind == "u" and half == 0:
                                pool.wait_ge(picked, i + (t * PH + 1))
                            pool.tensor_copy(now[:, lo:lo + HALF], idx[:, t, bass.ds(i * RING + lo, HALF)]) \
                                .then_inc(idx_ready, 1)
                            pool.wait_ge(idx_ready, i * 4 + (n * TURNS * 4 + half * 2 + 1))
                            pool.tensor_tensor(gatekeeper[:], now[:, lo:lo + 1], now[:, lo:lo + 1],
                                               ALU.add).then_inc(idx_ready, 1)
                            for s in range(lo, lo + HALF):
                                pool.indirect_dma_start(
                                    ring[:, s, :], None, A["peer_u"] if kind == "u" else A["peer_v"],
                                    bass.IndirectOffsetOnAxis(ap=now[:, s:s + 1], axis=0)).then_inc(row[s], 16)

                    pool.iota(iota[:], pattern=[[1, TOPK]], base=0, channel_multiplier=0,
                              allow_small_or_imprecise_dtypes=True).then_inc(iota_ready, 1)
                    for n, (kind, t) in enumerate(PASSES):
                        if t == 0:
                            turn(n, 0, first=True)
                            with pool.Fori(1, TURNS) as i:
                                turn(n, i)
                        else:
                            with pool.Fori(0, TURNS) as i:
                                turn(n, i)

                @block.vector
                def _(dve):
                    choice = Choice(dve, sb, scores, idx, gate, iota)
                    steps = 0

                    def whole_choice(t, h, base):
                        done = Steps(dve, v_step, base)
                        choice.sides(done, t, h)
                        choice.pairs(done, t, h)
                        choice.names(done, t, h, picked)
                        assert done.n == Choice.STEPS

                    def dot_rows(n, t, i):
                        for s in range(RING):
                            dve.wait_ge(row[s], i * 16 + 16 * (n * TURNS + 1))
                            dve.tensor_tensor_reduce(ring[:, s, :], ring[:, s, :], h2[:, t, :], 1.0, 0.0, ALU.mult,
                                                     ALU.add, dots[:, s:s + 1]).then_inc(u_used, 1)
                        dve.wait_ge(u_used, i * RING + (t * SLOTS + RING))
                        dve.tensor_copy(dot[:, t, bass.ds(i * RING, RING)], dots[:]).then_inc(dots_kept, 1)
                        dve.wait_ge(dots_kept, i + (t * TURNS + 1))

                    def add_row(n, t, i, j):
                        s = ADDED[j]
                        dve.wait_ge(row[s], i * 16 + 16 * (n * TURNS + 1))
                        if j:
                            dve.wait_ge(v_added, i * len(ADDED) + (t * TURNS * len(ADDED) + j))
                        dve.scalar_tensor_tensor(out=chip.x[:, t, :], in0=ring[:, s, :],
                                                 scalar=coef[:, t, bass.ds(i * RING + s, 1)], in1=chip.x[:, t, :],
                                                 op0=ALU.mult, op1=ALU.add).then_inc(v_added, 1)

                    def weights(t):
                        done = Steps(dve, v_step, steps)
                        g = gate[:, t, :].rearrange("p (h k) -> p h k", h=PH)
                        dve.wait_ge(exped, t + 1)
                        done(dve.tensor_reduce(sums[:], g, AX.X, ALU.add))
                        done.wait()
                        done(dve.reciprocal(sums[:], sums[:]))
                        done.wait()
                        done(dve.tensor_tensor(g, g, sums[:].rearrange("p (h o) -> p h o", o=1)
                                               .to_broadcast([P, PH, TOPK]), ALU.mult))
                        done.wait()
                        dve.wait_ge(gelu_done, t + 1)
                        dve.tensor_tensor(coef[:, t, :], coef[:, t, :], gate[:, t, :], ALU.mult).then_inc(coef_ready, 1)
                        dve.wait_ge(coef_ready, t + 1)
                        return done.n

                    def take(t):
                        dve.wait_ge(summed, t + 1)
                        xt = chip.x[:, t, :].rearrange("p (b n) -> p b n", b=2)
                        dve.tensor_tensor(xt, xt, chip.ps[:, t % 2 * 2:t % 2 * 2 + 2, :], ALU.add).then_inc(x_taken, 1)

                    def mean(t):
                        dve.wait_ge(squared, t + 1)
                        dve.tensor_scalar(st[:, 1, t:t + 1], st[:, 0, t:t + 1], 1.0 / D, RMS_EPS, ALU.mult,
                                          ALU.add).then_inc(mean_ready, 1)

                    def norm(t):
                        done = Steps(dve, v_step, steps)
                        dve.wait_ge(rooted, t + 1)
                        done(dve.reciprocal(st[:, 3, t:t + 1], st[:, 2, t:t + 1]))
                        done.wait()
                        dve.wait_ge(gain_in, 16)
                        done(dve.scalar_tensor_tensor(out=chip.x[:, t, :], in0=chip.x[:, t, :], scalar=st[:, 3, t:t + 1],
                                                      in1=gain[:], op0=ALU.mult, op1=ALU.mult))
                        done.wait()
                        return done.n

                    dve.memset(zero[:], 0.0).then_inc(zeroed, 1)
                    dve.wait_ge(iota_ready, 1)
                    whole_choice(0, 0, 0)
                    with dve.Fori(0, TURNS - 1) as i:
                        whole_choice(0, i + 1, i * Choice.STEPS + Choice.STEPS)
                        dot_rows(0, 0, i)
                    dot_rows(0, 0, TURNS - 1)
                    steps += PH * Choice.STEPS
                    for t in range(TT):
                        if t:
                            with dve.Fori(0, TURNS) as i:
                                dot_rows(2 * t, t, i)
                        steps += weights(t)
                        if t:
                            take(t - 1)
                        if t >= 2:
                            mean(t - 2)
                        with dve.Fori(0, TURNS) as i:
                            n = 2 * t + 1
                            add_row(n, t, i, 0)
                            if t + 1 < TT:
                                done = Steps(dve, v_step, i * Choice.STEPS + steps)
                                choice.sides(done, t + 1, i)
                                add_row(n, t, i, 1)
                                choice.pairs(done, t + 1, i)
                                add_row(n, t, i, 2)
                                choice.names(done, t + 1, i, picked)
                            else:
                                add_row(n, t, i, 1)
                                add_row(n, t, i, 2)
                            add_row(n, t, i, 3)
                            dve.wait_ge(v_added, i * len(ADDED) + (t * TURNS + 1) * len(ADDED))
                        if t + 1 < TT:
                            steps += PH * Choice.STEPS
                        if t >= 3:
                            steps += norm(t - 3)
                    take(TT - 1)
                    mean(TT - 2)
                    steps += norm(TT - 3)
                    steps += norm(TT - 2)
                    mean(TT - 1)
                    steps += norm(TT - 1)

                @block.scalar
                def _(act):
                    per = len(MULTIPLIED)

                    def square(t):
                        act.wait_ge(x_taken, t + 1)
                        if t:
                            act.wait_ge(squared, t)
                        act.activation(junk[:], chip.x[:, t, :], ACT.Square, accum_out=st[:, 0, t:t + 1]).then_inc(squared, 1)

                    def root(t):
                        act.wait_ge(mean_ready, t + 1)
                        act.activation(st[:, 2, t:t + 1], st[:, 1, t:t + 1], ACT.Sqrt).then_inc(rooted, 1)

                    for n, (kind, t) in enumerate(PASSES):
                        if kind == "u" and t >= 2:
                            square(t - 2)
                            if t >= 3:
                                root(t - 3)
                        if kind == "u":
                            act.wait_ge(picked, PH * (t + 1))
                            act.activation(gate[:, t, :], gate[:, t, :], ACT.Exp).then_inc(exped, 1)
                            act.wait_ge(dots_kept, TURNS * (t + 1))
                            act.activation(coef[:, t, :], dot[:, t, :], ACT.Gelu).then_inc(gelu_done, 1)
                            continue
                        act.wait_ge(coef_ready, t + 1)

                        def build(i, first=False):
                            for j, s in enumerate(MULTIPLIED):
                                if not first:
                                    act.wait_ge(v_multiplied, i * per + (t * TURNS * per - per + j + 1))
                                act.activation(diag[:, s, :], chip.ident[:], ACT.Copy,
                                               scale=coef[:, t, bass.ds(i * RING + s, 1)]).then_inc(diag_ready, 1)

                        if t == 0:
                            build(0, True)
                            with act.Fori(1, TURNS) as i:
                                build(i)
                        else:
                            with act.Fori(0, TURNS) as i:
                                build(i)
                    act.wait_ge(diag_ready, TURNS * per * TT)
                    root(TT - 3)
                    square(TT - 2)
                    root(TT - 2)
                    square(TT - 1)
                    root(TT - 1)

                @block.tensor
                def _(pe):
                    per = len(MULTIPLIED)
                    pe.wait_ge(zeroed, 1)

                    def product_with_zero(bank, **flags):
                        for b2 in range(2):
                            last = pe.matmul(chip.ps[:, bank + b2, :], zero[:], chip.ident[:, 0:1]
                                             .to_broadcast([P, 512]), skip_group_check=True, **flags)
                        return last

                    for n, (kind, t) in enumerate(PASSES):
                        if kind == "u":
                            continue
                        bank = t % 2 * 2
                        if t >= 2:
                            pe.wait_ge(x_taken, t - 1)
                        product_with_zero(bank, start=True, stop=False)
                        with pe.Fori(0, TURNS) as i:
                            for j, s in enumerate(MULTIPLIED):
                                pe.wait_ge(row[s], i * 16 + 16 * (n * TURNS + 1))
                                pe.wait_ge(diag_ready, i * per + (t * TURNS * per + j + 1))
                                for b2 in range(2):
                                    last = pe.matmul(chip.ps[:, bank + b2, :], diag[:, s, :],
                                                     ring[:, s, b2 * 512:(b2 + 1) * 512], start=False, stop=False,
                                                     skip_group_check=True)
                                last.then_inc(v_multiplied, 1)
                        product_with_zero(bank, start=False, stop=True).then_inc(summed, 1)


def expert_block(nc, chip, A):
    with ExitStack() as ctx:
        sb = lambda name, shape, dt=F32: ctx.enter_context(buffer(nc, name, shape, dt))
        idx = sb("expert_idx", [P, TT, SLOTS], U32)
        gate = sb("expert_gate", [P, TT, SLOTS])
        h2 = sb("h2", [P, TT, D])
        scores = sb("scores", [P, TT, 2 * PH * NKEYS])
        with ExitStack() as split_ctx:
            parts = split_ctx.enter_context(buffer(nc, "h_parts", [P, 2, KD, S], F32R))
            norm_transpose(nc, chip, RMS_EPS, A["norm2_row"], parts, keep=h2)
            expert_scores(nc, chip, A, parts, scores)
        experts(nc, chip, A, h2, scores, idx, gate)


MH, QN, QR, VH = 8, 64, 32, 64
QK = QN + QR
DH, DV = 4, 128
GROUPS, GH = 3, 4
LAM_INIT = 0.8 - 0.6
MASK, DIST, DIL0, STRICT = 0, 1, 2, 5


def feature_projection(nc, chip, parts, w_dram, n_tiles, out_of, rows_of=lambda m: P):
    R = 4
    with ExitStack() as ctx:
        ring = ctx.enter_context(buffer(nc, "proj_ring", [P, R, KD, P], F32))
        wp = split_weights(nc, ctx)
        with stage(nc, *[f"w{i}" for i in range(R)], "large", "small", "product", "out_a", "out_v") as \
                (*w, large, small, product, out_a, out_v):
            def w_parts(m):
                return wp[:, m % 2, 0], wp[:, m % 2, 1]

            with nc.Block() as block:
                @block.sync
                def _(sp):
                    for m in range(n_tiles):
                        if m >= R:
                            sp.wait_ge(small, m - R + 1)
                        sp.dma_start(ring[:, m % R], w_dram[m]).then_inc(w[m % R], 16)

                @block.tensor
                def _(pe):
                    for m in range(n_tiles):
                        pe.wait_ge(small, m + 1)
                        if m >= 8:
                            pe.wait_ge(out_v if m % 2 else out_a, m // 2 - 3)
                        wide = w_parts(m)
                        for k in range(KD):
                            last = split_product(pe, chip.ps[:, m % 8, :], (wide[0][:, k, :], wide[1][:, k, :]),
                                                 (parts[:, 0, k, :], parts[:, 1, k, :]), k == 0, k == KD - 1)
                        last.then_inc(product, 1)

                @block.scalar
                def _(act):
                    for m in range(n_tiles + 1):
                        if m < n_tiles:
                            act.wait_ge(w[m % R], 16 * (m // R + 1))
                            if m >= 2:
                                act.wait_ge(product, m - 1)
                            large_part(act, w_parts(m), ring[:, m % R]).then_inc(large, 1)
                        if m % 2:
                            act.wait_ge(product, m)
                            act.activation(out_of(m - 1), chip.ps[0:rows_of(m - 1), (m - 1) % 8, :],
                                           ACT.Copy).then_inc(out_a, 1)
                    act.wait_ge(out_a, (n_tiles + 1) // 2)

                @block.vector
                def _(dve):
                    for m in range(n_tiles + 1):
                        if m < n_tiles:
                            dve.wait_ge(large, m + 1)
                            small_part(dve, w_parts(m), ring[:, m % R]).then_inc(small, 1)
                        if m and m % 2 == 0:
                            dve.wait_ge(product, m)
                            dve.tensor_copy(out_of(m - 1), chip.ps[0:rows_of(m - 1), (m - 1) % 8, :]).then_inc(out_v, 1)
                    dve.wait_ge(out_v, n_tiles // 2)


class Unit:

    def __init__(self, q, k, bias, values, stat):
        self.q, self.k, self.bias, self.values, self.stat = q, k, bias, values, stat
        self.width = k.shape[1]


def attend(nc, chip, units, scale, width, dst_of, low, total):
    N, G = len(units), 512 // width if len(units) % (512 // width) == 0 else 256 // width
    with ExitStack() as ctx:
        sb = lambda name, shape: ctx.enter_context(buffer(nc, name, shape, F32))
        neg = sb("neg_logits", [P, 3, S])
        prob = sb("probs", [P, 3, S])
        probT = sb("probsT", [P, 2, S])
        with stage(nc, "scored", "masked", "exped", "turned", "turned_out", "weighted", "kept") as \
                (scored, masked, exped, turned, turned_out, weighted, kept):
            with nc.Block() as block:
                @block.tensor
                def _(pe):
                    for n in range(N + 3):
                        if n < N:
                            u = units[n]
                            if n >= 3:
                                pe.wait_ge(masked, n - 2)
                            pe.matmul(chip.ps[:, n % 3, 0:u.width], u.q, u.k, start=True,
                                      stop=True).then_inc(scored, 1)
                        m = n - 2
                        if 0 <= m < N:
                            pe.wait_ge(exped, m + 1)
                            if m >= 2:
                                pe.wait_ge(turned_out, m - 1)
                            for j in range(units[m].width // P):
                                last = pe.transpose(chip.ps[:, 3 + m % 2, j * P:(j + 1) * P],
                                                    prob[:, m % 3, j * P:(j + 1) * P], chip.ident[:])
                            last.then_inc(turned, 1)
                        m = n - 3
                        if 0 <= m < N:
                            pe.wait_ge(turned_out, m + 1)
                            if m % G == 0 and m >= 2 * G:
                                pe.wait_ge(kept, m // G - 1)
                            vs = units[m].values
                            for j, v in enumerate(vs):
                                last = pe.matmul(chip.ps[:, 6 + m // G % 2, m % G * width:(m % G + 1) * width],
                                                 probT[:, m % 2, j * P:(j + 1) * P], v, start=j == 0,
                                                 stop=j == len(vs) - 1)
                            last.then_inc(weighted, 1)

                @block.vector
                def _(dve):
                    for n in range(N + 2):
                        if n < N:
                            u = units[n]
                            dve.wait_ge(scored, n + 1)
                            if n >= 3:
                                dve.wait_ge(exped, n - 2)
                            dve.tensor_tensor_reduce(neg[:, n % 3, 0:u.width], chip.ps[:, n % 3, 0:u.width], u.bias,
                                                     -scale, 3e38, ALU.add, ALU.min,
                                                     low[:, u.stat:u.stat + 1]).then_inc(masked, 1)
                        m = n - 2
                        if 0 <= m < N:
                            w = units[m].width
                            dve.wait_ge(turned, m + 1)
                            if m >= 2:
                                dve.wait_ge(weighted, m - 1)
                            dve.tensor_copy(probT[:, m % 2, 0:w], chip.ps[:, 3 + m % 2, 0:w]).then_inc(turned_out, 1)

                @block.scalar
                def _(act):
                    for n in range(N + 4):
                        if n < N:
                            u = units[n]
                            act.wait_ge(masked, n + 1)
                            if n >= 3:
                                act.wait_ge(turned, n - 2)
                            act.activation(prob[:, n % 3, 0:u.width], neg[:, n % 3, 0:u.width], ACT.Exp, scale=-1.0,
                                           bias=low[:, u.stat:u.stat + 1],
                                           accum_out=total[:, u.stat:u.stat + 1]).then_inc(exped, 1)
                        m = n - 4
                        if m >= 0 and m % G == G - 1:
                            act.wait_ge(weighted, m + 1)
                            act.activation(dst_of(m // G), chip.ps[:, 6 + m // G % 2, 0:G * width],
                                           ACT.Copy).then_inc(kept, 1)
                    act.wait_ge(kept, N // G)


def turn_tokens(nc, chip, src_of, n_tiles, dst_of, gain_of):
    with stage(nc, "turned", "out_a", "out_v") as (turned, out_a, out_v):
        with nc.Block() as block:
            @block.tensor
            def _(pe):
                for n in range(n_tiles):
                    for t in range(TT):
                        last = pe.transpose(chip.ps[:, n % 8, t * P:(t + 1) * P], src_of(n, t), chip.ident[:])
                    last.then_inc(turned, 1)

            @block.scalar
            def _(act):
                for n in range(0, n_tiles, 2):
                    act.wait_ge(turned, n + 1)
                    g = gain_of(n)
                    act.activation(dst_of(n), chip.ps[:, n % 8, :], ACT.Copy, scale=1.0 if g is None else g)\
                        .then_inc(out_a, 1)
                act.wait_ge(out_a, (n_tiles + 1) // 2)

            @block.vector
            def _(dve):
                for n in range(1, n_tiles, 2):
                    dve.wait_ge(turned, n + 1)
                    g = gain_of(n)
                    dve.tensor_scalar(dst_of(n), chip.ps[:, n % 8, :], 1.0 if g is None else g, None,
                                      ALU.mult).then_inc(out_v, 1)
                dve.wait_ge(out_v, n_tiles // 2)


def even_mixer(nc, chip, A):
    with ExitStack() as ctx:
        sb = lambda name, shape, c=ctx: c.enter_context(buffer(nc, name, shape, F32))
        ocat = sb("ev_out", [P, TT, D])
        low, total = sb("ev_low", [P, 64]), sb("ev_total", [P, 64])
        lam = sb("ev_lam", [P, 4])
        tables = sb("ev_tables", [P, 2, S])
        dqT, dkT, dv = sb("dqT", [P, DH, S]), sb("dkT", [P, DH, S]), sb("dv", [P, TT, DH * DV])
        with ExitStack() as mla:
            c_tok = sb("c_tok", [P, TT, 384], mla)
            krT = sb("krT", [32, 2, S], mla)
            with ExitStack() as split_ctx:
                parts = split_ctx.enter_context(buffer(nc, "h_parts", [P, 2, KD, S], F32R))
                norm_transpose(nc, chip, NORM_EPS, A["ev_pre_row"], parts)
                stream_product(nc, chip, lambda k: A["ev_w_tok"][k], KD, ((0, 384), (384, 896)), parts=parts,
                               out_of=lambda t, half: dv[:, t, :] if half else c_tok[:, t, :])
                feature_projection(nc, chip, parts, A["ev_w_qk"], 10,
                                   lambda m: (dqT, dkT)[m // 4][:, m % 4, :] if m < 8 else krT[:, m - 8, :],
                                   lambda m: P if m < 8 else 32)
            _mla(nc, chip, A, mla, c_tok, krT, ocat, low, total, tables, lam)
        _diff(nc, chip, dqT, dkT, dv, ocat, low, total, tables, lam)
        turn_tokens(nc, chip, lambda n, t: ocat[:, t, n * P:(n + 1) * P], KD, lambda n: chip.hT[:, n, :],
                    lambda n: None if n < 4 else lam[:, 3:4])
    stream_product(nc, chip, lambda k: of_rows(A["ev_w_out"], k), KD, x_of=lambda k: of_tiles(chip.hT, k),
                   norm_row=A["ev_post_row"])


def _mla(nc, chip, A, ctx, c_tok, krT, ocat, low, total, tables, lam):
    sb = lambda name, shape, c=ctx: c.enter_context(buffer(nc, name, shape, F32))
    cT = sb("cT", [P, 3, S])
    v = sb("mla_v", [P, TT, MH * VH])
    qT, kT = sb("mla_qT", [QK, MH, S]), sb("mla_kT", [QK, MH, S])
    with ExitStack() as own:
        wuq = sb("w_uq", [P, 2, MH * QK], own)
        wus = sb("w_uq_swapped", [P, 2, MH * QR], own)
        wuk = sb("w_uk", [P, MH * QK], own)
        wuv = sb("w_uv", [P, MH * VH], own)
        rot = sb("rope_tables", [QR, 2, S], own)
        turn = sb("rope_turn", [QR, 2, S], own)
        kr = sb("rope_k", [QR, S], own)
        st = sb("c_stats", [P, 4, 2 * TT], own)
        junk = sb("c_junk", [P, 256], own)
        lv = sb("lam_vectors", [P, 4 * HS], own)
        lj = sb("lam_products", [P, HS], own)
        with stage(nc, "loaded", "squares", "mean_ready", "root_ready", "v_step", "lam_dots", "lam_exps") as \
                (loaded, squares, mean_ready, root_ready, v_step, lam_dots, lam_exps):
            with nc.Block() as block:
                @block.sync
                def _(sp):
                    sp.dma_start(lv[:], A["ev_lam"].partition_broadcast(P)).then_inc(loaded, 16)
                    sp.dma_start(tables[:], A["tables"][:, MASK:DIST + 1, :]).then_inc(loaded, 16)
                    sp.wait_ge(loaded, 32)

                @block.scalar
                def _(act):
                    for t in range(TT):
                        for part in range(2):
                            n = 2 * t + part
                            if n:
                                act.wait_ge(squares, n)
                            sl = slice(0, 256) if part == 0 else slice(256, 384)
                            act.activation(junk[:, 0:sl.stop - sl.start], c_tok[:, t, sl], ACT.Square,
                                           accum_out=st[:, 0, part * TT + t:part * TT + t + 1]).then_inc(squares, 1)
                    act.wait_ge(mean_ready, 2)
                    act.activation(st[:, 2, :], st[:, 1, :], ACT.Sqrt).then_inc(root_ready, 1)
                    act.wait_ge(lam_dots, 2)
                    act.activation(lam[:, 1:3], lam[:, 1:3], ACT.Exp).then_inc(lam_exps, 1)

                @block.vector
                def _(dve):
                    done = Steps(dve, v_step)
                    dve.wait_ge(squares, 2 * TT)
                    for part, n in ((0, 256), (1, 128)):
                        r = slice(part * TT, (part + 1) * TT)
                        dve.tensor_scalar(st[:, 1, r], st[:, 0, r], 1.0 / n, NORM_EPS, ALU.mult,
                                          ALU.add).then_inc(mean_ready, 1)
                    dve.wait_ge(root_ready, 1)
                    done(dve.reciprocal(st[:, 3, :], st[:, 2, :]))
                    done.wait()
                    for t in range(TT):
                        for part, sl in ((0, slice(0, 256)), (1, slice(256, 384))):
                            done(dve.tensor_scalar(c_tok[:, t, sl], c_tok[:, t, sl],
                                                   st[:, 3, part * TT + t:part * TT + t + 1], None, ALU.mult))
                    dve.wait_ge(loaded, 32)
                    for j in range(2):
                        a, c = lv[:, 2 * j * HS:(2 * j + 1) * HS], lv[:, (2 * j + 1) * HS:(2 * j + 2) * HS]
                        if j:
                            dve.wait_ge(lam_dots, j)
                        dve.tensor_tensor_reduce(lj[:], a, c, 1.0, 0.0, ALU.mult, ALU.add,
                                                 lam[:, 1 + j:2 + j]).then_inc(lam_dots, 1)
                    dve.wait_ge(lam_exps, 1)
                    done(dve.tensor_tensor(lam[:, 0:1], lam[:, 2:3], lam[:, 1:2], ALU.subtract))
                    done.wait()
                    done(dve.tensor_scalar(lam[:, 0:1], lam[:, 0:1], LAM_INIT, None, ALU.subtract))
                    done(dve.tensor_scalar(lam[:, 3:4], chip.col("subln_g"), 1.0 - LAM_INIT, None, ALU.mult))
                    done.wait()
        turn_tokens(nc, chip, lambda n, t: c_tok[:, t, n * P:(n + 1) * P], 3, lambda n: cT[:, n, :],
                    lambda n: chip.col("cq_g", n) if n < 2 else chip.col("ckv_g"))
        with stage(nc, "loaded", "product", "copied", "v_step", "key_turned", "values_out") as \
                (loaded, product, copied, v_step, key_turned, values_out):
            with nc.Block() as block:
                @block.sync
                def _(sp):
                    for dst, src in ((wuq, "ev_w_uq"), (wus, "ev_w_us"), (wuk, "ev_w_uk"), (wuv, "ev_w_uv"), (rot, "rope")):
                        sp.dma_start(dst[:], A[src]).then_inc(loaded, 16)

                @block.tensor
                def _(pe):
                    pe.wait_ge(loaded, 80)
                    for h in range(MH):
                        if h >= 2:
                            pe.wait_ge(copied, 3 * (h - 1))
                        b0 = h % 2 * 3
                        for k in range(2):
                            pe.matmul(chip.ps[0:QK, b0, :], wuq[:, k, h * QK:(h + 1) * QK], cT[:, k, :],
                                      start=k == 0, stop=k == 1)
                        for k in range(2):
                            pe.matmul(chip.ps[0:QR, b0 + 1, :], wus[:, k, h * QR:(h + 1) * QR], cT[:, k, :],
                                      start=k == 0, stop=k == 1)
                        pe.matmul(chip.ps[0:QK, b0 + 2, :], wuk[:, h * QK:(h + 1) * QK], cT[:, 2, :], start=True,
                                  stop=True).then_inc(product, 1)
                    for t in range(TT):
                        if t >= 2:
                            pe.wait_ge(values_out, t - 1)
                        pe.matmul(chip.ps[:, 6 + t % 2, :], cT[:, 2, t * P:(t + 1) * P], wuv[:], start=True,
                                  stop=True).then_inc(product, 1)

                @block.scalar
                def _(act):
                    for h in range(MH):
                        act.wait_ge(product, h + 1)
                        b0 = h % 2 * 3
                        act.activation(qT[:, h, :], chip.ps[0:QK, b0, :], ACT.Copy).then_inc(copied, 1)
                        act.activation(kT[:, h, :], chip.ps[0:QK, b0 + 2, :], ACT.Copy).then_inc(copied, 1)
                        if h >= 2:
                            act.wait_ge(v_step, 3 * (h - 1) + 3)
                        act.activation(turn[:, h % 2, :], chip.ps[0:QR, b0 + 1, :], ACT.Copy).then_inc(copied, 1)
                    for t in range(TT):
                        act.wait_ge(product, MH + t + 1)
                        act.activation(v[:, t, :], chip.ps[:, 6 + t % 2, :], ACT.Copy).then_inc(values_out, 1)
                    act.wait_ge(values_out, TT)

                @block.vector
                def _(dve):
                    done = Steps(dve, v_step)
                    dve.wait_ge(loaded, 80)
                    done(dve.tensor_tensor(krT[:, 0, :], krT[:, 0, :], rot[:, 0, :], ALU.mult))
                    done(dve.tensor_tensor(krT[:, 1, :], krT[:, 1, :], rot[:, 1, :], ALU.mult))
                    done.wait()
                    done(dve.tensor_tensor(kr[:], krT[:, 0, :], krT[:, 1, :], ALU.add))
                    for h in range(MH):
                        dve.wait_ge(copied, 3 * h + 3)
                        if h == 0:
                            done.wait()
                        done(dve.tensor_tensor(turn[:, h % 2, :], turn[:, h % 2, :], rot[:, 1, :], ALU.mult))
                        done(dve.tensor_tensor(qT[0:QR, h, :], qT[0:QR, h, :], rot[:, 0, :], ALU.mult))
                        done.wait()
                        done(dve.tensor_tensor(qT[0:QR, h, :], qT[0:QR, h, :], turn[:, h % 2, :], ALU.add))
                        dve.tensor_copy(kT[0:QR, h, :], kr[:]).then_inc(key_turned, 1)
                    done.wait()
                    dve.wait_ge(key_turned, MH)
    units = []
    for i in range(TT):
        w = (i + 1) * P
        for h in range(MH):
            units.append(Unit(qT[:, h, i * P:(i + 1) * P], kT[:, h, 0:w], tables[:, MASK, S - w:S],
                              [v[:, j, h * VH:(h + 1) * VH] for j in range(i + 1)], i * MH + h))
    attend(nc, chip, units, QK ** -0.5, VH, lambda g: ocat[:, g, 0:512], low, total)
    with stage(nc, "v_step") as (v_step,):
        with nc.Block() as block:
            @block.vector
            def _(dve):
                done = Steps(dve, v_step)
                done(dve.reciprocal(total[:, 0:TT * MH], total[:, 0:TT * MH]))
                done.wait()
                for t in range(TT):
                    o = ocat[:, t, 0:512].rearrange("p (h v) -> p h v", h=MH)
                    done(dve.tensor_tensor(o, o, total[:, t * MH:(t + 1) * MH].rearrange("p (h o) -> p h o", o=1)
                                           .to_broadcast([P, MH, VH]), ALU.mult))
                done.wait()


def _diff(nc, chip, dqT, dkT, dv, ocat, low, total, tables, lam):
    with ExitStack() as ctx:
        sb = lambda name, shape: ctx.enter_context(buffer(nc, name, shape, F32))
        bias = sb("diff_bias", [P, DH, S])
        o = sb("diff_o", [P, 2, TT, DH * DV])
        st = sb("diff_stats", [P, 4, TT * DH])
        scale = HS ** -0.5
        with stage(nc, "biased") as (biased,):
            with nc.Block() as block:
                @block.vector
                def _(dve):
                    for h in range(DH):
                        slope = 2.0 ** (-8.0 * (h + 1) / DH)
                        dve.tensor_scalar(bias[:, h, :], tables[:, DIST, :], -slope / scale, None,
                                          ALU.mult).then_inc(biased, 1)
                    dve.wait_ge(biased, DH)
        units = []
        for i in range(TT):
            w = (i + 1) * P
            for s_ in range(2):
                r = slice(s_ * HS, (s_ + 1) * HS)
                for h in range(DH):
                    units.append(Unit(dqT[r, h, i * P:(i + 1) * P], dkT[r, h, 0:w], bias[:, h, S - w:S],
                                      [dv[:, j, h * DV:(h + 1) * DV] for j in range(i + 1)],
                                      s_ * TT * DH + i * DH + h))
        attend(nc, chip, units, scale, DV, lambda g: o[:, g % 2, g // 2, :], low, total)
        n = TT * DH
        with stage(nc, "v_step", "mean_ready", "root_ready") as (v_step, mean_ready, root_ready):
            with nc.Block() as block:
                @block.scalar
                def _(act):
                    act.wait_ge(mean_ready, 1)
                    act.activation(st[:, 2, :], st[:, 1, :], ACT.Sqrt).then_inc(root_ready, 1)

                @block.vector
                def _(dve):
                    done = Steps(dve, v_step)
                    flat = lambda s_: o[:, s_].rearrange("p t (h v) -> p (t h) v", v=DV)
                    wide = lambda ap: ap.rearrange("p (n o) -> p n o", o=1).to_broadcast([P, n, DV])
                    done(dve.reciprocal(total[:, 0:2 * n], total[:, 0:2 * n]))
                    done.wait()
                    done(dve.tensor_scalar(total[:, n:2 * n], total[:, n:2 * n], lam[:, 0:1], None, ALU.mult))
                    done(dve.tensor_tensor(flat(0), flat(0), wide(total[:, 0:n]), ALU.mult))
                    done.wait()
                    done(dve.tensor_tensor(flat(1), flat(1), wide(total[:, n:2 * n]), ALU.mult))
                    done.wait()
                    done(dve.tensor_tensor(flat(0), flat(0), flat(1), ALU.add))
                    done.wait()
                    done(dve.tensor_tensor(flat(1), flat(0), flat(0), ALU.mult))
                    done.wait()
                    done(dve.tensor_reduce(st[:, 0, :], flat(1), AX.X, ALU.add))
                    done.wait()
                    dve.tensor_scalar(st[:, 1, :], st[:, 0, :], 1.0 / DV, NORM_EPS, ALU.mult,
                                      ALU.add).then_inc(mean_ready, 1)
                    dve.wait_ge(root_ready, 1)
                    done(dve.reciprocal(st[:, 3, :], st[:, 2, :]))
                    done.wait()
                    for t in range(TT):
                        done(dve.tensor_tensor(
                            ocat[:, t, 512:1024].rearrange("p (h v) -> p h v", v=DV), flat(0)[:, t * DH:(t + 1) * DH],
                            wide(st[:, 3, :])[:, t * DH:(t + 1) * DH], ALU.mult))
                    done.wait()


ND = GROUPS * GH


def odd_mixer(nc, chip, A):
    with ExitStack() as ctx:
        sb = lambda name, shape, c=ctx: c.enter_context(buffer(nc, name, shape, F32))
        ocat = sb("od_out", [P, TT, 512])
        v = sb("od_v", [P, TT, D])
        qk = sb("od_qk", [P, 16, S])
        with ExitStack() as split_ctx:
            parts = split_ctx.enter_context(buffer(nc, "h_parts", [P, 2, KD, S], F32R))
            norm_transpose(nc, chip, NORM_EPS, A["od_pre_row"], parts)
            stream_product(nc, chip, lambda k: A["od_w_v"][k], KD, parts=parts,
                           out_of=lambda t, half: v[:, t, half * 512:(half + 1) * 512])
            feature_projection(nc, chip, parts, A["od_w_qk"], 16, lambda m: qk[:, m, :])
        _dilated(nc, chip, A, qk, v, ocat)
        _stick(nc, chip, A, qk, v, ocat)
        turn_tokens(nc, chip, lambda n, t: ocat[:, t, n * P:(n + 1) * P], 4, lambda n: chip.hT[:, n, :],
                    lambda n: None)
    stream_product(nc, chip, lambda k: of_rows(A["od_w_out"], k), 4, x_of=lambda k: of_tiles(chip.hT, k),
                   norm_row=A["od_post_row"])


def _dilated(nc, chip, A, qk, v, ocat):
    with ExitStack() as ctx:
        sb = lambda name, shape: ctx.enter_context(buffer(nc, name, shape, F32))
        bias = sb("dil_bias", [P, ND, S])
        tables = sb("dil_tables", [P, GROUPS, S])
        o = sb("dil_o", [P, TT, ND * HS])
        low, total = sb("dil_low", [P, TT, ND]), sb("dil_total", [P, TT, ND])
        wts = sb("dil_weights", [P, TT, ND])
        small = sb("dil_small", [P, 2, TT, GH])
        scale = HS ** -0.5
        with stage(nc, "loaded", "biased") as (loaded, biased):
            with nc.Block() as block:
                @block.sync
                def _(sp):
                    sp.dma_start(tables[:], A["tables"][:, DIL0:DIL0 + GROUPS, :]).then_inc(loaded, 16)

                @block.vector
                def _(dve):
                    dve.wait_ge(loaded, 16)
                    for n in range(ND):
                        slope = 2.0 ** (-8.0 * (n + 1) / ND)
                        dve.tensor_scalar(bias[:, n, :], tables[:, n // GH, :], -slope / scale, None,
                                          ALU.mult).then_inc(biased, 1)
                    dve.wait_ge(biased, ND)
        units = []
        for i in range(TT):
            for n in range(ND):
                first = max(0, i - 1) if n < GH else 0
                w = (i + 1 - first) * P
                r = slice(n % 2 * HS, n % 2 * HS + HS)
                units.append(Unit(qk[r, n // 2, i * P:(i + 1) * P], qk[r, 6 + n // 2, first * P:(i + 1) * P],
                                  bias[:, n, S - w:S], [v[:, j, n * HS:(n + 1) * HS] for j in range(first, i + 1)],
                                  i * ND + n))
        flat = o[:].rearrange("p t n -> p (t n)")
        attend(nc, chip, units, scale, HS, lambda g: flat[:, g * 512:(g + 1) * 512],
               low[:].rearrange("p t n -> p (t n)"), total[:].rearrange("p t n -> p (t n)"))
        with stage(nc, "v_step", "apart", "exped") as (v_step, apart, exped):
            with nc.Block() as block:
                @block.vector
                def _(dve):
                    done = Steps(dve, v_step)
                    of = lambda ap, g: ap[:, :, g * GH:(g + 1) * GH]
                    lo, den = small[:, 0], small[:, 1]
                    done(dve.tensor_tensor(lo, of(low, 0), of(low, 1), ALU.min))
                    done.wait()
                    done(dve.tensor_tensor(lo, lo, of(low, 2), ALU.min))
                    done.wait()
                    for g in range(GROUPS):
                        dve.tensor_tensor(of(wts, g), lo, of(low, g), ALU.subtract).then_inc(apart, 1)
                    dve.wait_ge(exped, 1)
                    done(dve.tensor_tensor(total[:], total[:], wts[:], ALU.mult))
                    done.wait()
                    done(dve.tensor_tensor(den, of(total, 0), of(total, 1), ALU.add))
                    done.wait()
                    done(dve.tensor_tensor(den, den, of(total, 2), ALU.add))
                    done.wait()
                    done(dve.reciprocal(den, den))
                    done.wait()
                    for g in range(GROUPS):
                        done(dve.tensor_tensor(of(wts, g), of(wts, g), den, ALU.mult))
                    done.wait()
                    for t in range(TT):
                        ot = o[:, t].rearrange("p (n v) -> p n v", v=HS)
                        done(dve.tensor_tensor(ot, ot, wts[:, t].rearrange("p (n o) -> p n o", o=1)
                                               .to_broadcast([P, ND, HS]), ALU.mult))
                    done.wait()
                    q = GH * HS
                    done(dve.tensor_tensor(ocat[:, :, 0:q], o[:, :, 0:q], o[:, :, q:2 * q], ALU.add))
                    done.wait()
                    done(dve.tensor_tensor(ocat[:, :, 0:q], ocat[:, :, 0:q], o[:, :, 2 * q:3 * q], ALU.add))
                    done.wait()

                @block.scalar
                def _(act):
                    act.wait_ge(apart, GROUPS)
                    act.activation(wts[:], wts[:], ACT.Exp).then_inc(exped, 1)


def _stick(nc, chip, A, qk, v, ocat):
    units = [(i, pair) for i in range(TT)[::-1] for pair in range(2)]
    N = len(units)
    with ExitStack() as ctx:
        sb = lambda name, shape: ctx.enter_context(buffer(nc, name, shape, F32))
        strict = sb("strict_table", [P, 1, S])
        ones = sb("stick_ones", [P, S])
        z, mag, keep, after = (sb("stick_" + n, [P, 2, 2, S]) for n in ("z", "mag", "keep", "after"))
        probT = sb("stick_pT", [P, 2, S])
        scale = HS ** -0.5
        with stage(nc, "loaded", "scored", "z_out", "logged", "a_step", "v_step", "arg_ready", "a_exped", "masked",
                   "turned", "turned_out", "weighted", "kept") as \
                (loaded, scored, z_out, logged, a_step, v_step, arg_ready, a_exped, masked, turned, turned_out,
                 weighted, kept):
            with nc.Block() as block:
                @block.sync
                def _(sp):
                    sp.dma_start(strict[:], A["tables"][:, STRICT:STRICT + 1, :]).then_inc(loaded, 16)

                @block.tensor
                def _(pe):
                    def logits(u):
                        i, pair = units[u]
                        w = (i + 1) * P
                        if u >= 2:
                            pe.wait_ge(z_out, u - 1)
                        for h in range(2):
                            r = slice(h * HS, h * HS + HS)
                            last = pe.matmul(chip.ps[:, u % 2 * 2 + h, 0:w], qk[r, 12 + pair, i * P:(i + 1) * P],
                                             qk[r, 14 + pair, 0:w], start=True, stop=True)
                        last.then_inc(scored, 1)

                    def turn(u, h):
                        n = 2 * u + h
                        if n >= 2:
                            pe.wait_ge(turned_out, n - 1)
                        for j in range(units[u][0] + 1):
                            last = pe.transpose(chip.ps[:, 4 + n % 2, j * P:(j + 1) * P],
                                                z[:, u % 2, h, j * P:(j + 1) * P], chip.ident[:])
                        last.then_inc(turned, 1)

                    def weigh(u, h):
                        n, (i, pair) = 2 * u + h, units[u]
                        pe.wait_ge(turned_out, n + 1)
                        if pair == 0 and h == 0 and u >= 4:
                            pe.wait_ge(kept, u // 2 - 1)
                        at = ND * HS + (2 * pair + h) * HS
                        for j in range(i + 1):
                            last = pe.matmul(chip.ps[:, 6 + i % 2, (2 * pair + h) * HS:(2 * pair + h + 1) * HS],
                                             probT[:, n % 2, j * P:(j + 1) * P], v[:, j, at:at + HS],
                                             start=j == 0, stop=j == i)
                        last.then_inc(weighted, 1)

                    logits(0)
                    logits(1)
                    for u in range(N):
                        pe.wait_ge(masked, u + 1)
                        turn(u, 0)
                        turn(u, 1)
                        if u + 2 < N:
                            logits(u + 2)
                        weigh(u, 0)
                        weigh(u, 1)

                @block.scalar
                def _(act):
                    step = Steps(act, a_step)

                    def take_logits(u):
                        w = (units[u][0] + 1) * P
                        act.wait_ge(scored, u + 1)
                        if u >= 2:
                            act.wait_ge(turned, 2 * (u - 1))
                        ps = chip.ps[:, u % 2 * 2:u % 2 * 2 + 2, 0:w]
                        m = mag[:, u % 2, :, 0:w]
                        step(act.activation(m, ps, ACT.Abs, scale=scale))
                        act.activation(z[:, u % 2, :, 0:w], ps, ACT.Copy, scale=scale).then_inc(z_out, 1)
                        step.wait()
                        step(act.activation(m, m, ACT.Exp, scale=-1.0))
                        step.wait()
                        act.activation(m, m, ACT.Ln, bias=1.0).then_inc(logged, 1)

                    take_logits(0)
                    take_logits(1)
                    for u in range(N):
                        i, pair = units[u]
                        w = (i + 1) * P
                        act.wait_ge(arg_ready, u + 1)
                        act.activation(z[:, u % 2, :, 0:w], z[:, u % 2, :, 0:w], ACT.Exp).then_inc(a_exped, 1)
                        if pair == 0 and u:
                            act.wait_ge(weighted, 2 * u)
                            act.activation(ocat[:, i + 1, 256:512], chip.ps[:, 6 + (i + 1) % 2, 0:256],
                                           ACT.Copy).then_inc(kept, 1)
                        if u + 2 < N:
                            take_logits(u + 2)
                    act.wait_ge(weighted, 2 * N)
                    act.activation(ocat[:, 0, 256:512], chip.ps[:, 6, 0:256], ACT.Copy).then_inc(kept, 1)
                    act.wait_ge(kept, TT)

                @block.vector
                def _(dve):
                    done = Steps(dve, v_step)

                    def argument(u):
                        w = (units[u][0] + 1) * P
                        zz, mm, kk, aa = (t[:, u % 2, :, 0:w] for t in (z, mag, keep, after))
                        own = strict[:, :, S - w:S].to_broadcast([P, 2, w])
                        dve.wait_ge(logged, u + 1)
                        dve.wait_ge(z_out, u + 1)
                        done(dve.scalar_tensor_tensor(out=mm, in0=zz, scalar=0.0, in1=mm, op0=ALU.max, op1=ALU.add))
                        done.wait()
                        done(dve.tensor_tensor(kk, mm, own, ALU.mult))
                        done(dve.tensor_tensor(zz, zz, mm, ALU.subtract))
                        done.wait()
                        for h in range(2):
                            done(dve.tensor_tensor_scan(after[:, u % 2, h, 0:w][:, ::-1], ones[:, 0:w],
                                                        keep[:, u % 2, h, 0:w][:, ::-1], 0.0, ALU.mult, ALU.add))
                        done(dve.tensor_tensor(zz, zz, kk, ALU.add))
                        done.wait()
                        dve.tensor_tensor(zz, zz, aa, ALU.subtract).then_inc(arg_ready, 1)

                    done(dve.memset(ones[:], 1.0))
                    dve.wait_ge(loaded, 16)
                    argument(0)
                    for u in range(N):
                        w = (units[u][0] + 1) * P
                        zz = z[:, u % 2, :, 0:w]
                        dve.wait_ge(a_exped, u + 1)
                        dve.tensor_tensor(zz, zz, strict[:, :, S - w:S].to_broadcast([P, 2, w]),
                                          ALU.mult).then_inc(masked, 1)
                        if u + 1 < N:
                            argument(u + 1)
                        for h in range(2):
                            n = 2 * u + h
                            dve.wait_ge(turned, n + 1)
                            if n >= 2:
                                dve.wait_ge(weighted, n - 1)
                            dve.tensor_copy(probT[:, n % 2, 0:w], chip.ps[:, 4 + n % 2, 0:w]).then_inc(turned_out, 1)


FF = 2816
FT = FF // P
WPAIR = 2


def conv_ffn(nc, chip, A, layer):
    with ExitStack() as ctx:
        hid = ctx.enter_context(buffer(nc, "hiddenT", [P, FT, S], F32))
        with ExitStack() as split_ctx:
            parts = split_ctx.enter_context(buffer(nc, "h_parts", [P, 2, KD, S], F32R))
            norm_transpose(nc, chip, NORM_EPS, A["ffn_pre_rows"][layer], parts)
            _ffn_up(nc, chip, A, layer, parts, hid)
        stream_product(nc, chip, lambda k: of_rows(A["ffn_w_down"][layer], k), FT, x_of=lambda k: of_tiles(hid, k),
                       norm_row=A["ffn_post_rows"][layer])


def _ffn_up(nc, chip, A, layer, parts, hid):
    with ExitStack() as ctx:
        sb = lambda name, shape, dt=F32: ctx.enter_context(buffer(nc, name, shape, dt))
        ring = sb("up_ring", [P, WPAIR, 2, KD, P])
        wp = sb("up_parts", [P, WPAIR, 2, 2, KD, P], F32R)
        conv = sb("conv", [P, WPAIR, 2, S])
        with stage(nc, "w0", "w1", "large", "small", "product", "centre", "one_back", "two_back", "gated", "hidden") as \
                (w0, w1, large, small, product, centre, one_back, two_back, gated, hidden):
            w = (w0, w1)
            turns = FT // WPAIR

            def tap(side, f, back):
                return chip.cols[:, bass.ds(f + (COLS["conv_w"][0] + (3 * layer + 2 - back) * 2 * FT + side * FT), 1)]

            def w_parts(j):
                return wp[:, j, 0], wp[:, j, 1]

            with nc.Block() as block:
                @block.sync
                def _(sp):
                    def load(i, first=False):
                        for j in range(WPAIR):
                            if not first:
                                sp.wait_ge(small, i * WPAIR + (j + 1 - WPAIR))
                            sp.dma_start(ring[:, j], A["ffn_w_up"][layer, bass.ds(i * WPAIR + j, 1)]
                                         .rearrange("o p s k n -> p (o s) k n")).then_inc(w[j], 16)

                    load(0, True)
                    with sp.Fori(1, turns) as i:
                        load(i)

                @block.tensor
                def _(pe):
                    def products(i, first=False):
                        for j in range(WPAIR):
                            pe.wait_ge(small, i * WPAIR + (j + 1))
                            if not first:
                                pe.wait_ge(two_back, i * 2 * WPAIR + (2 * j + 2 - 2 * WPAIR))
                            wide = w_parts(j)
                            for side in range(2):
                                for k in range(KD):
                                    last = split_product(pe, chip.ps[:, 2 * j + side, :],
                                                         (wide[0][:, side, k, :], wide[1][:, side, k, :]),
                                                         (parts[:, 0, k, :], parts[:, 1, k, :]), k == 0, k == KD - 1)
                                last.then_inc(product, 1)

                    products(0, True)
                    with pe.Fori(1, turns) as i:
                        products(i)

                @block.scalar
                def _(act):
                    def split(i, j, first=False):
                        act.wait_ge(w[j], i * 16 + 16)
                        if not first:
                            act.wait_ge(product, i * 2 * WPAIR + (2 * j + 2 - 2 * WPAIR))
                        large_part(act, w_parts(j), ring[:, j]).then_inc(large, 1)

                    def centre_and_gate(i, j, first=False):
                        f = i * WPAIR + (j - WPAIR)
                        if not first:
                            act.wait_ge(hidden, i * WPAIR + (j + 1 - 2 * WPAIR))
                        for side in range(2):
                            act.wait_ge(product, i * 2 * WPAIR + (2 * j + side + 1 - 2 * WPAIR))
                            act.activation(conv[:, j, side, :], chip.ps[:, 2 * j + side, :], ACT.Identity,
                                           scale=tap(side, f, 0),
                                           bias=chip.cols[:, bass.ds(f + (COLS["conv_b"][0] + layer * 2 * FT
                                                                          + side * FT), 1)]).then_inc(centre, 1)
                        act.wait_ge(two_back, i * 2 * WPAIR + (2 * j + 1 - 2 * WPAIR))
                        act.activation(conv[:, j, 0, :], conv[:, j, 0, :], ACT.Silu).then_inc(gated, 1)

                    for j in range(WPAIR):
                        split(0, j, True)
                    for j in range(WPAIR):
                        split(1, j)
                        centre_and_gate(1, j, True)
                    with act.Fori(2, turns) as i:
                        for j in range(WPAIR):
                            split(i, j)
                            centre_and_gate(i, j)
                    for j in range(WPAIR):
                        centre_and_gate(turns, j)

                @block.vector
                def _(dve):
                    def split(i, j):
                        dve.wait_ge(large, i * WPAIR + (j + 1))
                        small_part(dve, w_parts(j), ring[:, j]).then_inc(small, 1)

                    def taps_and_product(i, j):
                        f = i * WPAIR + (j - WPAIR)
                        for side in range(2):
                            c, ps = conv[:, j, side, :], chip.ps[:, 2 * j + side, :]
                            dve.wait_ge(centre, i * 2 * WPAIR + (2 * j + side + 1 - 2 * WPAIR))
                            dve.scalar_tensor_tensor(out=c[:, 1:S], in0=ps[:, 0:S - 1], scalar=tap(side, f, 1),
                                                     in1=c[:, 1:S], op0=ALU.mult, op1=ALU.add).then_inc(one_back, 1)
                            dve.wait_ge(one_back, i * 2 * WPAIR + (2 * j + side + 1 - 2 * WPAIR))
                            dve.scalar_tensor_tensor(out=c[:, 2:S], in0=ps[:, 0:S - 2], scalar=tap(side, f, 2),
                                                     in1=c[:, 2:S], op0=ALU.mult, op1=ALU.add).then_inc(two_back, 1)
                        dve.wait_ge(two_back, i * 2 * WPAIR + (2 * j + 2 - 2 * WPAIR))
                        dve.wait_ge(gated, i * WPAIR + (j + 1 - WPAIR))
                        dve.tensor_tensor(hid[:, bass.ds(f, 1), :].rearrange("p o s -> p (o s)"),
                                          conv[:, j, 0, :], conv[:, j, 1, :], ALU.mult).then_inc(hidden, 1)

                    for j in range(WPAIR):
                        split(0, j)
                    with dve.Fori(1, turns) as i:
                        for j in range(WPAIR):
                            split(i, j)
                            taps_and_product(i, j)
                    for j in range(WPAIR):
                        taps_and_product(turns, j)
                    dve.wait_ge(hidden, FT)


UPTO = 99


def build(nc, A, out):
    STAGES.clear()
    with ExitStack() as ctx:
        chip = Chip(nc, ctx)
        load_constants(nc, chip, A)
        if UPTO not in (20, 30, 40, 50):
            rwkv_block(nc, chip, A)
        if UPTO not in (1, 30, 40, 50):
            expert_block(nc, chip, A)
        if UPTO == 30 or UPTO > 90:
            even_mixer(nc, chip, A)
        if UPTO == 40 or UPTO > 90:
            conv_ffn(nc, chip, A, 0)
        if UPTO == 50 or UPTO > 90:
            odd_mixer(nc, chip, A)
        if UPTO > 90:
            conv_ffn(nc, chip, A, 1)
        with stage(nc, "stored") as (stored,):
            with nc.Block() as block:
                @block.sync
                def _(sp):
                    sp.dma_start(out.rearrange("(t p) d -> p t d", p=P), chip.x[:]).then_inc(stored, 16)
                    sp.wait_ge(stored, 16)


def pack_columns(vectors):
    return np.concatenate([np.ascontiguousarray(v.reshape(-1, P).T) for v in vectors], axis=1)


def tiles_of_columns(w, widths):
    k = w.shape[0] // P
    out, at = np.zeros((len(widths), P, k, P), w.dtype), 0
    for i, n in enumerate(widths):
        out[i, :, :, :n] = w[:, at:at + n].reshape(k, P, n).transpose(1, 0, 2)
        at += n
    return out


def rows(w):
    return np.ascontiguousarray(w.reshape(-1, P, w.shape[1]).transpose(1, 0, 2))


def lay_out(i):
    f = lambda n: np.asarray(i[n])
    a = {}
    a["x"] = f("x")[0]
    in1 = [P] * 15 + [32] + [P] * 4
    a["w_in"] = tiles_of_columns(f("w_in")[0], in1)
    mu = np.zeros((2, SHIFTED * P), np.float32)
    mu[:, :1952] = f("shift_mu")[0]
    a["w_up"] = f("w_up")[0].reshape(P, RD)
    a["a_up"] = f("a_up")[0].reshape(P, RD)
    a["g_up"] = f("g_up")[0]
    a["pool_w"] = np.ascontiguousarray(f("pool_w")[0].transpose(1, 0, 2))
    inv = np.zeros((1, 4 * S), np.float32)
    t = np.arange(S)
    for g, win in enumerate((2, 4, 8, 16)):
        inv[0, g * S:(g + 1) * S] = 1.0 / (np.clip(t + win // 2, 0, S) - np.clip(t - win // 2, 0, S))
    a["pool_inv"] = inv
    a["w_out"] = f("w_out")[0].reshape(KD, P, D)
    a["peer_wq"] = tiles_of_columns(f("peer_wq")[0], [P] * 16)
    a["peer_keys"] = np.ascontiguousarray(f("peer_keys")[0].reshape(16, P, P).transpose(2, 0, 1))
    a["peer_u"], a["peer_v"] = f("peer_u")[0], f("peer_v")[0]
    a["norm1_row"], a["norm2_row"], a["norm_f_row"] = f("norm1_w")[0], f("norm2_w")[0], f("norm_f_w")
    a["cols"] = pack_columns([
        mu[0], mu[1], f("w0")[0], f("a0")[0], f("k_k")[0], f("k_a")[0], f("r_k")[0],
        f("ln_x_w")[0], f("ln_x_b")[0], f("pool_scale")[0], f("ev_cq_g_2")[0],
        f("ev_ckv_g_2")[0], f("ev_subln_g_2")[0],
        f("ffn_conv_w_2"), f("ffn_conv_b_2")])
    a.update(lay_out_attention(f))
    return a


def lay_out_attention(f):
    a = {}
    w = f("ev_w_in_2")[0]
    a["ev_w_tok"] = np.concatenate([w[:, 0:384], w[:, 416 + 1024:416 + 1536]], axis=1).reshape(KD, P, 896)
    a["ev_pre_row"], a["od_pre_row"], a["ffn_pre_rows"] = f("ev_pre_g_2")[0], f("od_pre_g_2")[0], f("ffn_pre_g_2")
    half = QR // 2
    swap = np.r_[half:QR, 0:half]
    kr = w[:, 384:416]
    a["ev_w_qk"] = tiles_of_columns(np.concatenate([w[:, 416:416 + 1024], kr, kr[:, swap]], axis=1), [P] * 8 + [32, 32])
    uq = f("ev_w_uq_2")[0].reshape(256, MH, QK)
    rope_cols = uq[:, :, QN:]
    a["ev_w_uq"] = rows(np.concatenate([rope_cols, uq[:, :, :QN]], axis=2).reshape(256, MH * QK))
    a["ev_w_us"] = rows(np.ascontiguousarray(rope_cols[:, :, swap]).reshape(256, MH * QR))
    ukv = f("ev_w_ukv_2")[0].reshape(P, MH, QN + VH)
    uk = np.zeros((P, MH, QK), np.float32)
    uk[:, :, QR:] = ukv[:, :, :QN]
    a["ev_w_uk"] = uk.reshape(P, MH * QK)
    a["ev_w_uv"] = np.ascontiguousarray(ukv[:, :, QN:]).reshape(P, MH * VH)
    a["ev_lam"] = np.concatenate([f(n)[0] for n in ("ev_lam_q1_2", "ev_lam_k1_2", "ev_lam_q2_2", "ev_lam_k2_2")])
    a["ev_w_out"] = f("ev_w_out_2")[0].reshape(KD, P, D)
    a["ev_post_row"] = f("ev_post_g_2")[0]
    w = f("od_w_in_2")[0]
    a["od_w_qk"] = tiles_of_columns(np.concatenate([w[:, 0:1536], w[:, 2304:2816]], axis=1), [P] * 16)
    a["od_w_v"] = np.concatenate([w[:, 1536:2304], w[:, 2816:3072]], axis=1).reshape(KD, P, D)
    a["od_w_out"] = f("od_w_out_2")[0].reshape(4, P, D)
    a["od_post_row"] = f("od_post_g_2")[0]
    up = f("ffn_w_up_2")
    a["ffn_w_up"] = np.ascontiguousarray(up.reshape(2, KD, P, 2, FT, P).transpose(0, 4, 2, 3, 1, 5))
    a["ffn_w_down"] = f("ffn_w_down_2").reshape(2, FT, P, D)
    a["ffn_post_rows"] = f("ffn_post_g_2")
    ang = (np.arange(S, dtype=np.float32)[None, :]
           * (np.float32(10000.0) ** (-np.arange(half, dtype=np.float32) / half))[:, None]).astype(np.float32)
    cos, sin = np.cos(ang), np.sin(ang)
    a["rope"] = np.stack([np.r_[cos, cos], np.r_[-sin, sin]], axis=1).astype(np.float32)
    dist = (np.arange(P)[:, None] + (S - P) - np.arange(S)[None, :]).astype(np.float32)
    far = np.float32(1e32)
    t = [np.where(dist >= 0, 0, NEG), np.where(dist >= 0, dist, far)]
    for wdt, dil in ((128, 1), (512, 4), (2048, 16)):
        t.append(np.where((dist >= 0) & (dist <= wdt) & (dist % dil == 0), dist, far))
    t.append(dist > 0)
    a["tables"] = np.stack(t, axis=1).astype(np.float32)
    return a


def kernel(**inputs):
    import numpy as _np
    import concourse.bacc as _bacc
    from concourse import mybir as _mybir
    from concourse.bass_utils import run_bass_kernel_spmd as _run

    nc = _bacc.Bacc("TRN2", target_bir_lowering=False, num_devices=1)
    arrays, A = {}, {}
    for name, a in lay_out(inputs).items():
        arrays[f"in_{name}_dram"] = _np.ascontiguousarray(a)
        A[name] = nc.dram_tensor(f"in_{name}_dram", a.shape, _mybir.dt.from_np(a.dtype), kind="ExternalInput").ap()
    A["scratch"] = nc.dram_tensor("rwkv_scratch", (8, 3, P, S), F32, kind="Internal").ap()
    out = nc.dram_tensor("out_0_dram", (S, D), F32, kind="ExternalOutput").ap()
    build(nc, A, out)
    r = _run(nc, [arrays], core_ids=[0])
    return r.results[0]["out_0_dram"].reshape(1, S, D)
```

```python
from contextlib import ExitStack, contextmanager

import numpy as np
import concourse.bass as bass
from concourse import mybir

F32 = mybir.dt.float32
F32R = mybir.dt.float32r
U32 = mybir.dt.uint32
ALU = mybir.AluOpType
ACT = mybir.ActivationFunctionType
AX = mybir.AxisListType

P = 128
S = 512
TT = S // P
D = 1024
KD = D // P
RD = 512
PR = RD // P
HS = 64
LORA = 64
C = 64
NCH = S // C
DECAY = float(np.exp(-0.5))
GN_EPS = 64e-5
RMS_EPS = 1e-5
NORM_EPS = 1e-6
NEG = -1e30
IN1_TILES = 20
SHIFTED = 16


def buffer(nc, name, shape, dt=F32):
    return nc.sbuf_tensor(f"{name}_{len(STAGES)}", shape, dt)


class Steps:

    def __init__(self, eng, sem, base=0):
        self.eng, self.sem, self.n, self.base = eng, sem, 0, base

    def __call__(self, ins):
        self.n += 1
        ins.then_inc(self.sem, 1)
        return self.n

    def wait(self):
        self.eng.wait_ge(self.sem, self.base + self.n)


STAGES = []


HELD = []
HELD_LIMIT = 120


def clear_finished(nc):
    nc.clear_and_free_semaphores([sem for h in HELD if h[1] for sem in h[0]])
    nc.all_engine_barrier()
    HELD[:] = [h for h in HELD if not h[1]]


@contextmanager
def stage(nc, *names):
    if sum(len(h[0]) for h in HELD) + len(names) > HELD_LIMIT:
        clear_finished(nc)
    STAGES.append(names)
    held = [[nc.alloc_semaphore(f"s{len(STAGES)}_{n}") for n in names], False]
    HELD.append(held)
    yield held[0]
    held[1] = True


COLS = {}


def _cols():
    at = 0
    for name, n in (("mu0", SHIFTED), ("mu1", SHIFTED), ("w0", 8), ("a0", 8), ("k_k", 4),
                    ("k_a", 4), ("r_k", 4), ("ln_x_w", 4), ("ln_x_b", 4), ("pool_scale", 4),
                    ("cq_g", 2), ("ckv_g", 1), ("subln_g", 1), ("conv_w", 2 * 3 * 44), ("conv_b", 2 * 44)):
        COLS[name] = (at, n)
        at += n
    return at


NCOLS = _cols()


class Chip:

    def __init__(self, nc, ctx):
        sb = lambda name, shape, dt=F32: ctx.enter_context(buffer(nc, name, shape, dt))
        self.x = sb("x_res", [P, TT, D])
        self.hT = sb("hT", [P, KD, S])
        self.cols = sb("cols", [P, NCOLS])
        self.ident = sb("ident", [P, P])
        self.stack2 = sb("stack2", [P, HS])
        self.ps = ctx.enter_context(nc.psum_tensor("ps", [P, 8, 512], F32))

    def col(self, name, i=0, n=1):
        at, _ = COLS[name]
        return self.cols[:, at + i:at + i + n]


def load_constants(nc, chip, A):
    with stage(nc, "constants_loaded", "constants_step") as (loaded, step):
        with nc.Block() as block:
            @block.sync
            def _(sp):
                sp.dma_start(chip.x[:], A["x"].rearrange("(t p) d -> p t d", p=P)).then_inc(loaded, 16)
                sp.dma_start(chip.cols[:], A["cols"]).then_inc(loaded, 16)
                sp.wait_ge(loaded, 32)

            @block.gpsimd
            def _(pool):
                done = Steps(pool, step)
                done(pool.memset(chip.ident[:], 0.0))
                done(pool.memset(chip.stack2[:], 0.0))
                done.wait()
                done(pool.affine_select(out=chip.ident[:], in_=chip.ident[:], compare_op=ALU.not_equal, fill=1.0,
                                        base=0, pattern=[[-1, P]], channel_multiplier=1))
                done(pool.affine_select(out=chip.stack2[:], in_=chip.stack2[:], compare_op=ALU.not_equal,
                                        fill=1.0, base=0, pattern=[[-1, HS]], channel_multiplier=1))
                done.wait()
                done(pool.affine_select(out=chip.stack2[:], in_=chip.stack2[:], compare_op=ALU.not_equal,
                                        fill=1.0, base=-HS, pattern=[[-1, HS]], channel_multiplier=1))
                done.wait()


def in_order(xT, t):
    return xT[:, t * P:(t + 1) * P]


def by_4(xT, t):
    return xT[:, t:S:4]


def split_product(pe, out, a, b, start, stop, skip=False):
    pe.matmul(out, a[0], b[0], start=start, stop=False, skip_group_check=skip)
    pe.matmul(out, a[0], b[1], start=False, stop=False, skip_group_check=skip)
    return pe.matmul(out, a[1], b[0], start=False, stop=stop, skip_group_check=skip)


def large_part(act, parts, src):
    return act.activation(parts[0], src, ACT.Copy)


def small_part(dve, parts, src):
    return dve.tensor_tensor(parts[1], src, parts[0].bitcast(F32), ALU.subtract)


def norm_transpose(nc, chip, eps, gain_row, parts, keep=None, ahead=None):
    with ExitStack() as ctx:
        h = keep if keep is not None else ctx.enter_context(buffer(nc, "norm_h", [P, TT, D], F32))
        junk = ctx.enter_context(buffer(nc, "norm_squares", [P, D], F32))
        gain = ctx.enter_context(buffer(nc, "norm_gain", [P, D], F32))
        st = ctx.enter_context(buffer(nc, "norm_stats", [P, 4, TT], F32))
        with stage(nc, "gain_in", "squares", "mean_ready", "root_ready", "v_step", "normed", "turned", "large",
                   "small") as (gain_in, squares, mean_ready, root_ready, v_step, normed, turned, large, small):
            def turned_tile(t):
                return chip.ps[:, 2 * t:2 * t + 2, :].rearrange("p b (k n) -> p (b k) n", n=P)

            def tile_parts(t):
                return [parts[:, i, :, t * P:(t + 1) * P] for i in range(2)]

            with nc.Block() as block:
                @block.sync
                def _(sp):
                    sp.dma_start(gain[:], gain_row.partition_broadcast(P)).then_inc(gain_in, 16)
                    if ahead is not None:
                        ahead(sp)

                @block.scalar
                def _(act):
                    def square(t):
                        if t:
                            act.wait_ge(squares, t)
                        act.activation(junk[:], chip.x[:, t, :], ACT.Square,
                                       accum_out=st[:, 0, t:t + 1]).then_inc(squares, 1)

                    square(0)
                    for t in range(TT):
                        if t + 1 < TT:
                            square(t + 1)
                        act.wait_ge(mean_ready, t + 1)
                        act.activation(st[:, 2, t:t + 1], st[:, 1, t:t + 1], ACT.Sqrt).then_inc(root_ready, 1)
                    for t in range(TT):
                        act.wait_ge(turned, t + 1)
                        large_part(act, tile_parts(t), turned_tile(t)).then_inc(large, 1)

                @block.vector
                def _(dve):
                    done = Steps(dve, v_step)

                    def mean(t):
                        dve.wait_ge(squares, t + 1)
                        dve.tensor_scalar(st[:, 1, t:t + 1], st[:, 0, t:t + 1], 1.0 / D, eps, ALU.mult,
                                          ALU.add).then_inc(mean_ready, 1)

                    mean(0)
                    for t in range(TT):
                        if t + 1 < TT:
                            mean(t + 1)
                        dve.wait_ge(root_ready, t + 1)
                        done(dve.reciprocal(st[:, 3, t:t + 1], st[:, 2, t:t + 1]))
                        done.wait()
                        if t == 0:
                            dve.wait_ge(gain_in, 16)
                        dve.scalar_tensor_tensor(out=h[:, t, :], in0=chip.x[:, t, :], scalar=st[:, 3, t:t + 1],
                                                 in1=gain[:], op0=ALU.mult, op1=ALU.mult).then_inc(normed, 1)
                    for t in range(TT):
                        dve.wait_ge(large, t + 1)
                        small_part(dve, tile_parts(t), turned_tile(t)).then_inc(small, 1)
                    dve.wait_ge(small, TT)

                @block.tensor
                def _(pe):
                    for t in range(TT):
                        pe.wait_ge(normed, t + 1)
                        for k in range(KD):
                            last = pe.transpose(chip.ps[:, 2 * t + k // 4, k % 4 * P:(k % 4 + 1) * P],
                                                h[:, t, k * P:(k + 1) * P], chip.ident[:])
                        last.then_inc(turned, 1)


WRING = 4


@contextmanager
def row_ring(nc, w_of, width=D):
    with ExitStack() as ctx:
        raw = ctx.enter_context(buffer(nc, "row_ring", [P, 2, width], F32))
        with stage(nc, "w0", "w1") as w:
            def load(sp, i, j):
                sp.dma_start(raw[:, j], w_of(i * 2 + j)).then_inc(w[j], 16)

            yield raw, w, load, lambda sp: [load(sp, 0, j) for j in range(2)]


@contextmanager
def weight_ring(nc, w_dram):
    with ExitStack() as ctx:
        ring = ctx.enter_context(buffer(nc, "w_ring", [P, WRING, KD, P], F32))
        with stage(nc, *[f"w{i}" for i in range(WRING)]) as w:
            def load(sp, m):
                sp.dma_start(ring[:, m % WRING], w_dram[m]).then_inc(w[m % WRING], 16)

            yield ring, w, load, lambda sp: [load(sp, m) for m in range(WRING)]


def split_weights(nc, ctx):
    return ctx.enter_context(buffer(nc, "w_parts", [P, 2, 2, KD, P], F32R))


def project_in_1(nc, chip, b, parts, ring, w, load):
    with ExitStack() as ctx:
        wp = split_weights(nc, ctx)
        rest = ctx.enter_context(buffer(nc, "mu_rest", [P, SHIFTED], F32))
        dst = ([b.rT[:, i, :] for i in range(4)] + [b.kT[:, i, :] for i in range(4)]
               + [b.vT[:, i, :] for i in range(4)] + [b.loraT[:, i, :] for i in range(4)])
        with stage(nc, "rest_ready", "large", "small", "product", "scaled", "shifted",
                   "prev", "pooled") as (rest_ready, large, small, product, scaled, shifted, prev, pooled):
            def w_parts(m):
                return wp[:, m % 2, 0], wp[:, m % 2, 1]

            with nc.Block() as block:
                @block.sync
                def _(sp):
                    for m in range(WRING, IN1_TILES):
                        sp.wait_ge(small, m - WRING + 1)
                        load(sp, m)

                @block.tensor
                def _(pe):
                    for m in range(IN1_TILES):
                        pe.wait_ge(small, m + 1)
                        if m >= 8:
                            if m - 8 < SHIFTED:
                                pe.wait_ge(shifted, m - 7)
                            else:
                                pe.wait_ge(pooled, m - 7 - SHIFTED)
                        wide = w_parts(m)
                        for k in range(KD):
                            last = split_product(pe, chip.ps[:, m % 8, :], (wide[0][:, k, :], wide[1][:, k, :]),
                                                 (parts[:, 0, k, :], parts[:, 1, k, :]), k == 0, k == KD - 1)
                        last.then_inc(product, 1)

                @block.scalar
                def _(act):
                    def split(m):
                        act.wait_ge(w[m % WRING], 16 * (m // WRING + 1))
                        if m >= 2:
                            act.wait_ge(product, m - 1)
                        large_part(act, w_parts(m), ring[:, m % WRING]).then_inc(large, 1)

                    split(0)
                    act.wait_ge(rest_ready, 2)
                    for m in range(IN1_TILES):
                        if m + 1 < IN1_TILES:
                            split(m + 1)
                        act.wait_ge(product, m + 1)
                        if m < SHIFTED:
                            act.activation(dst[m], chip.ps[:, m % 8, :], ACT.Copy,
                                           scale=rest[:, m:m + 1]).then_inc(scaled, 1)
                        else:
                            act.activation(b.poolT[:, m - SHIFTED, 8:8 + S], chip.ps[:, m % 8, :],
                                           ACT.Copy).then_inc(pooled, 1)
                    act.wait_ge(pooled, 4)

                @block.vector
                def _(dve):
                    dve.tensor_tensor(rest[:], chip.col("mu0", 0, SHIFTED), chip.col("mu1", 0, SHIFTED),
                                      ALU.add).then_inc(rest_ready, 1)
                    dve.wait_ge(rest_ready, 1)
                    dve.tensor_scalar(rest[:], rest[:], -1.0, 1.0, ALU.mult, ALU.add).then_inc(rest_ready, 1)

                    def split(m):
                        dve.wait_ge(large, m + 1)
                        small_part(dve, w_parts(m), ring[:, m % WRING]).then_inc(small, 1)

                    split(0)
                    for m in range(IN1_TILES):
                        if m + 1 < IN1_TILES:
                            split(m + 1)
                        if m >= SHIFTED:
                            continue
                        o, ps = dst[m], chip.ps[:, m % 8, :]
                        dve.wait_ge(scaled, m + 1)
                        dve.scalar_tensor_tensor(out=o[:, 1:S], in0=ps[:, 0:S - 1], scalar=chip.col("mu0", m),
                                                 in1=o[:, 1:S], op0=ALU.mult, op1=ALU.add).then_inc(prev, 1)
                        dve.wait_ge(prev, m + 1)
                        dve.scalar_tensor_tensor(out=o[:, 0:S - 1], in0=ps[:, 1:S], scalar=chip.col("mu1", m),
                                                 in1=o[:, 0:S - 1], op0=ALU.mult, op1=ALU.add).then_inc(shifted, 1)
                    dve.wait_ge(shifted, SHIFTED)


def rwkv_inputs(nc, chip, A, b, yT):
    W = S + 16
    with ExitStack() as ctx:
        sb = lambda name, shape: ctx.enter_context(buffer(nc, name, shape, F32))
        ups = sb("ups", [P, 2, RD])
        gup = sb("gup", [P, 2, RD])
        sq = sb("kk_square", [P, PR, S])
        rr = sb("r_rk", [P, PR, S])
        oma = sb("one_less_ka", [P, PR])
        halves = sb("halves", [P, P])
        sums = sb("window_sums", [P, 2, W])
        inv = sb("window_inverse", [P, 4, S])
        pw = sb("pool_w", [P, 4, P])
        cell = sb("signal_cell", [P, 1])
        with stage(nc, "loras_loaded", "a_step", "v_step", "squared", "summed", "rooted", "low_ready", "up_done",
                   "sig_done", "gate_done", "gate_out", "bonus_in", "bonus_sum", "kept", "spilled", "halves_ready",
                   "windows_loaded", "p_step", "means_ready", "mixed", "pool_taken") as \
                (loaded, a_step, v_step, squared, summed, rooted, low_ready, up_done, sig_done, gate_done,
                 gate_out, bonus_in, bonus_sum, kept, spilled, halves_ready, windows_loaded, p_step, means_ready,
                 mixed, pool_taken):
            with nc.Block() as block:
                @block.sync
                def _(sp):
                    sp.dma_start(ups[:, 0, :], A["w_up"]).then_inc(loaded, 16)
                    sp.dma_start(ups[:, 1, :], A["a_up"]).then_inc(loaded, 16)
                    sp.dma_start(gup[:, 0, :], A["g_up"][0:P]).then_inc(loaded, 16)
                    sp.dma_start(gup[0:32, 1, :], A["g_up"][P:P + 32]).then_inc(loaded, 16)
                    sp.dma_start(inv[:].rearrange("p g t -> p (g t)"),
                                 A["pool_inv"][0].partition_broadcast(P)).then_inc(windows_loaded, 16)
                    sp.dma_start(pw[:], A["pool_w"]).then_inc(windows_loaded, 16)
                    sp.wait_ge(kept, 1)
                    sp.dma_start(A["scratch"][:, 2].rearrange("d p s -> p d s"), b.kd[:]).then_inc(spilled, 16)
                    sp.wait_ge(sig_done, 16)
                    sp.dma_start(A["scratch"][:, 0].rearrange("d p s -> p d s"), b.decay[:]).then_inc(spilled, 16)
                    sp.wait_ge(kept, 2)
                    sp.dma_start(A["scratch"][:, 1].rearrange("d p s -> p d s"), b.a[:]).then_inc(spilled, 16)
                    sp.wait_ge(spilled, 48)

                @block.scalar
                def _(act):
                    act.activation(b.loraT[:, 0, :], b.loraT[:, 0, :], ACT.Tanh).then_inc(low_ready, 1)
                    act.activation(b.loraT[:, 2:4, :], b.loraT[:, 2:4, :], ACT.Sigmoid).then_inc(low_ready, 1)
                    for i in range(PR):
                        act.wait_ge(summed, i + 1)
                        act.activation(sq[:, i, :], chip.ps[:, 4 + i, :], ACT.Sqrt).then_inc(rooted, 1)
                    for n in range(16):
                        act.wait_ge(up_done, n + 1)
                        out = (b.a if n < 8 else b.decay)[:, n % 8, :]
                        act.activation(out, chip.ps[:, n % 4, :], ACT.Sigmoid,
                                       bias=chip.col("a0" if n < 8 else "w0", n % 8)).then_inc(sig_done, 1)
                    for i in range(PR):
                        act.wait_ge(gate_done, i + 1)
                        act.activation(b.gateT[:, i, :], chip.ps[:, i, :], ACT.Copy).then_inc(gate_out, 1)
                    for g in range(4):
                        act.wait_ge(mixed, g + 1)
                        act.activation(yT[:, 4 + g, :], chip.ps[:, g, :], ACT.Copy,
                                       scale=chip.col("pool_scale", g)).then_inc(pool_taken, 1)
                    act.wait_ge(pool_taken, 4)

                @block.gpsimd
                def _(pool):
                    pool.memset(halves[0:HS, 0:HS], 1.0).then_inc(halves_ready, 1)
                    pool.memset(halves[HS:P, HS:P], 1.0).then_inc(halves_ready, 1)
                    pool.memset(halves[0:HS, HS:P], 0.0).then_inc(halves_ready, 1)
                    pool.memset(halves[HS:P, 0:HS], 0.0).then_inc(halves_ready, 1)
                    pool.wait_ge(halves_ready, 4)
                    done = Steps(pool, p_step)
                    done(pool.memset(b.poolT[:, :, 0:8], 0.0))
                    done(pool.memset(b.poolT[:, :, S + 8:W], 0.0))
                    done(pool.memset(sums[:], 0.0))
                    done.wait()
                    pool.wait_ge(windows_loaded, 32)
                    for g in range(4):
                        src = b.poolT[:, g, :]
                        for lv in range(g + 1):
                            lo, hi = (1, 0) if lv == 0 else (1 << (lv - 1), 1 << (lv - 1))
                            dst = sums[:, lv % 2, :]
                            done(pool.tensor_tensor(dst[:, 8:8 + S] if lv == g else dst[:, lo:W - hi],
                                                    src[:, 8 - lo:8 - lo + S] if lv == g else src[:, 0:W - hi - lo],
                                                    src[:, 8 + hi:8 + hi + S] if lv == g else src[:, lo + hi:W],
                                                    ALU.add))
                            done.wait()
                            src = dst
                        done(pool.tensor_tensor(sums[:, g % 2, 8:8 + S], src[:, 8:8 + S], inv[:, g, :], ALU.mult))
                        done.wait()
                        pool.tensor_tensor(b.poolT[:, g, 8:8 + S], sums[:, g % 2, 8:8 + S], b.poolT[:, g, 8:8 + S],
                                           ALU.subtract).then_inc(means_ready, 1)
                        pool.wait_ge(means_ready, g + 1)
                        if g < 3:
                            done(pool.memset(sums[:], 0.0))
                            done.wait()

                @block.tensor
                def _(pe):
                    pe.wait_ge(halves_ready, 4)
                    for i in range(PR):
                        pe.wait_ge(squared, i + 1)
                        pe.matmul(chip.ps[:, 4 + i, :], halves[:], sq[:, i, :], start=True,
                                  stop=True).then_inc(summed, 1)
                    pe.wait_ge(loaded, 64)
                    pe.wait_ge(low_ready, 2)
                    for n in range(16):
                        d, i = n // 4 % 2, n % 4
                        if n >= 4:
                            pe.wait_ge(sig_done, n - 3)
                        what = 1 - n // 8
                        pe.matmul(chip.ps[:, n % 4, :], ups[d * LORA:(d + 1) * LORA, what, i * P:(i + 1) * P],
                                  b.loraT[d * LORA:(d + 1) * LORA, what, :], start=True,
                                  stop=True).then_inc(up_done, 1)
                    pe.wait_ge(sig_done, 16)
                    for i in range(PR):
                        pe.matmul(chip.ps[:, i, :], gup[:, 0, i * P:(i + 1) * P], b.loraT[:, 2, :], start=True,
                                  stop=False)
                        pe.matmul(chip.ps[:, i, :], gup[0:32, 1, i * P:(i + 1) * P], b.loraT[0:32, 3, :],
                                  start=False, stop=True).then_inc(gate_done, 1)
                    pe.wait_ge(rooted, PR)
                    for i in range(PR):
                        pe.wait_ge(bonus_in, i + 1)
                        pe.matmul(chip.ps[:, 4 + i, :], halves[:], rr[:, i, :], start=True,
                                  stop=True).then_inc(bonus_sum, 1)
                    pe.wait_ge(windows_loaded, 32)
                    pe.wait_ge(gate_out, PR)
                    for g in range(4):
                        pe.wait_ge(means_ready, g + 1)
                        pe.matmul(chip.ps[:, g, :], pw[:, g, :], b.poolT[:, g, 8:8 + S], start=True,
                                  stop=True).then_inc(mixed, 1)

                @block.vector
                def _(dve):
                    done = Steps(dve, v_step)
                    for i in range(PR):
                        done(dve.tensor_scalar(b.kk[:, i, :], b.kT[:, i, :], chip.col("k_k", i), None, ALU.mult))
                    done(dve.tensor_scalar(oma[:], chip.col("k_a", 0, 4), -1.0, 1.0, ALU.mult, ALU.add))
                    done.wait()
                    for i in range(PR):
                        dve.tensor_tensor(sq[:, i, :], b.kk[:, i, :], b.kk[:, i, :], ALU.mult).then_inc(squared, 1)
                    for i in range(PR):
                        done(dve.tensor_scalar(rr[:, i, :], b.rT[:, i, :], chip.col("r_k", i), None, ALU.mult))
                    dve.wait_ge(rooted, PR)
                    done(dve.tensor_scalar(sq[:], sq[:], 1e-12, None, ALU.max))
                    done.wait()
                    done(dve.reciprocal(sq[:], sq[:]))
                    done.wait()
                    done(dve.tensor_tensor(b.kk[:], b.kk[:], sq[:], ALU.mult))
                    for n in range(8):
                        dve.wait_ge(sig_done, n + 1)
                        done(dve.tensor_scalar(b.kd[:, n, :], b.a[:, n, :], chip.col("k_a", n % 4),
                                               oma[:, n % 4:n % 4 + 1], ALU.mult, ALU.add))
                        done.wait()
                        done(dve.tensor_tensor(b.kd[:, n, :], b.kd[:, n, :], b.kT[:, n % 4, :], ALU.mult))
                    done.wait()
                    dve.memset(cell[:], 0.0).then_inc(kept, 1)
                    for n in range(8):
                        done(dve.tensor_tensor(b.a[:, n, :], b.a[:, n, :], b.kk[:, n % 4, :], ALU.mult))
                    done.wait()
                    dve.memset(cell[:], 0.0).then_inc(kept, 1)
                    for i in range(PR):
                        done(dve.tensor_tensor(sq[:, i, :], b.kd[:, i, :], b.kd[:, 4 + i, :], ALU.add))
                        done.wait()
                        dve.tensor_tensor(rr[:, i, :], rr[:, i, :], sq[:, i, :], ALU.mult).then_inc(bonus_in, 1)
                    for i in range(PR):
                        dve.wait_ge(bonus_sum, i + 1)
                        done(dve.tensor_tensor(b.bonusT[:, i, :], chip.ps[:, 4 + i, :], b.vT[:, i, :], ALU.mult))
                    done.wait()


def recurrence(nc, chip, b, A, rev):
    with ExitStack() as ctx:
        sb = lambda name, shape: ctx.enter_context(buffer(nc, name, shape, F32))
        M1 = sb("M1", [P, PR, NCH, P])
        M2 = sb("M2", [P, PR, NCH, P])
        C1 = sb("C1", [P, NCH, PR, HS])
        C2 = sb("C2", [P, NCH, PR, HS])
        with ExitStack() as inner:
            _chunks(nc, chip, b, A, rev, M1, M2, C1, C2, lambda n, s: inner.enter_context(buffer(nc, n, s, F32)))
        _chain(nc, chip, b, rev, M1, M2, C1, C2, sb)


ROUNDS = 14
DVE_IDLE = (8, 10)
ACT_IDLE = (6, 11, 12, 13)


def signals(idle, n):
    whole, part = divmod(n + 1, 2 * ROUNDS)
    return whole * 2 * (ROUNDS - len(idle)) + sum(m // 2 not in idle for m in range(part))


def _chunks(nc, chip, b, A, rev, M1, M2, C1, C2, sb):
    E = {n: sb("E" + n, [P, NCH, P]) for n in ("alpha", "beta", "kappa", "beta_end", "kappa_end", "v")}
    cum = sb("cum", [P, S])
    grow = sb("grow", [P, 3, S])
    start = sb("chunk_start", [P, S])
    strict = sb("strict", [P, P])
    incl = sb("incl", [P, P])
    near = sb("near", [P, 2, P])
    far = sb("far", [P, 2, P])
    pend = sb("chunk_decay", [P, 2, NCH])
    blk = M2[:, 0, 0, :]
    fed = sb("fed", [P, 2, 3, S])
    B = []
    for i in range(2):
        B.append({n: sb(f"{n}{i}", [P, 4, w]) for n, w in (
            ("DD", 2 * P), ("Fn", P), ("Fm", P), ("QB", 2 * P), ("BT", P), ("Qv", P), ("kT_", P),
            ("V", HS), ("XA", HS + P), ("R", P))})
        w = B[-1]
        whole = w["DD"][:].rearrange("p u f -> p (u f)")
        w["Dn"] = whole[:, 0:4 * P].rearrange("p (u f) -> p u f", u=4)
        w["Dm"] = whole[:, 4 * P:8 * P].rearrange("p (u f) -> p u f", u=4)
        w["WA"] = whole[:, 0:4 * (HS + P)].rearrange("p (u f) -> p u f", u=4)
        w["RT"] = w["BT"]
    ps = chip.ps
    with stage(nc, "mask_step", "start_ready", "masks_ready", "summed", "grown", "prepared", "pe_round",
               "dve_round", "act_round", "v_step", "fed0", "fed1") as \
            (mask_step, start_ready, masks_ready, summed, grown, prepared, pe_round, dve_round, act_round,
             v_step, fed0, fed1):
        ends = 0 if rev else C - 1

        def chunked(ap):
            return ap.rearrange("p (c t) -> p c t", t=C)

        def wait_fed(eng, g):
            eng.wait_ge((fed0, fed1)[g % 2], 16 * (g // 2 + 1))

        def prepare(eng, done, g):
            eng.wait_ge(grown, 3 * g + 3)
            bb, kd = fed[:, g % 2, 1, :], fed[:, g % 2, 2, :]
            for dst, s_, w in ((E["alpha"][:], b.kk[:, g, :], 2), (E["beta"][:], bb, 1),
                               (E["kappa"][:], kd, 1), (M1[:, g], b.rT[:, g, :], 0)):
                for h in range(2):
                    r = slice(h * HS, (h + 1) * HS)
                    done(eng.tensor_tensor(dst[r, :, r], chunked(s_[r]), chunked(grow[r, w, :]), ALU.mult))
            for h in range(2):
                r = slice(h * HS, (h + 1) * HS)
                done(eng.tensor_copy(E["v"][r, :, r], chunked(b.vT[r, g, :])))
            done.wait()
            done(eng.tensor_copy(pend[:, g % 2, :], grow[:, 0, ends:S:C]))
            done.wait()
            end = pend[:, g % 2, :].rearrange("p (c o) -> p c o", o=1).to_broadcast([P, NCH, P])
            eng.tensor_tensor(E["beta_end"][:], E["beta"][:], end, ALU.mult).then_inc(prepared, 1)
            eng.tensor_tensor(E["kappa_end"][:], E["kappa"][:], end, ALU.mult).then_inc(prepared, 1)

        def bc(m):
            return m.rearrange("p (o f) -> p o f", o=1).to_broadcast([P, 4, P])

        def banks(i, k, w=P):
            if w == P:
                return ps[:, 4 * i + k, :].rearrange("p (u f) -> p u f", u=4)
            return ps[:, 4 * i + k:4 * i + k + 2, :].rearrange("p b (u f) -> p (b u) f", u=2)

        def quad(i, k, u, w):
            if w == P:
                return ps[:, 4 * i + k, u * P:(u + 1) * P]
            return ps[:, 4 * i + k + u // 2, (u % 2) * 2 * P:(u % 2) * 2 * P + w]

        with nc.Block() as block:
            @block.gpsimd
            def _(pool):
                done = Steps(pool, mask_step)
                done(pool.memset(start[:], 1.0))
                done.wait()
                pool.memset(start[:, (C - 1 if rev else 0):S:C], 0.0).then_inc(start_ready, 1)
                done(pool.memset(strict[:], 1.0))
                done(pool.memset(incl[:], 1.0))
                done(pool.memset(far[:, 1, :], 1.0))
                done(pool.memset(blk, 1.0))
                done.wait()
                sg = -1 if rev else 1
                for m, op, s_ in ((strict[:], ALU.is_gt, sg), (incl[:], ALU.is_ge, sg), (far[:, 1, :], ALU.is_gt, -sg)):
                    done(pool.affine_select(out=m, in_=m, compare_op=op, fill=0.0, base=0, pattern=[[s_, P]],
                                            channel_multiplier=-s_))
                v = blk.rearrange("p (g f) -> p g f", f=16)
                done(pool.affine_select(out=v, in_=v, compare_op=ALU.is_ge, fill=0.0, base=0,
                                        pattern=[[-16, 8], [0, 16]], channel_multiplier=1))
                done.wait()
                done(pool.affine_select(out=v, in_=v, compare_op=ALU.is_ge, fill=0.0, base=15,
                                        pattern=[[16, 8], [0, 16]], channel_multiplier=-1))
                done.wait()
                done(pool.tensor_tensor(near[:, 0, :], strict[:], blk, ALU.mult))
                done(pool.tensor_tensor(near[:, 1, :], far[:, 1, :], blk, ALU.mult))
                done.wait()
                done(pool.tensor_tensor(far[:, 0, :], strict[:], near[:, 0, :], ALU.subtract))
                done(pool.tensor_tensor(far[:, 1, :], far[:, 1, :], near[:, 1, :], ALU.subtract))
                done.wait()
                pool.memset(M1[:, 1:PR], 0.0).then_inc(masks_ready, 1)
                pool.wait_ge(masks_ready, 1)
                for g in range(1, PR):
                    wait_fed(pool, g)
                    pool.wait_ge(pe_round, 2 * ROUNDS * (g - 1) + 6)
                    pool.wait_ge(prepared, 2 * g)
                    prepare(pool, done, g)

            @block.sync
            def _(sp):
                for g in range(PR):
                    if g >= 2:
                        sp.wait_ge(prepared, 2 * (g - 1))
                    sp.dma_start(fed[:, g % 2], A["scratch"][(4 if rev else 0) + g].rearrange("n p s -> p n s"))\
                        .then_inc((fed0, fed1)[g % 2], 16)

            @block.vector
            def _(dve):
                done = Steps(dve, v_step)

                def sum_up(g):
                    wait_fed(dve, g)
                    if g:
                        dve.wait_ge(prepared, 2 * g)
                    decay = fed[:, g % 2, 0, :]
                    flip = slice(None, None, -1) if rev else slice(None)
                    dve.tensor_tensor_scan(cum[:, flip], start[:, flip], decay[:, flip], 0.0, ALU.mult,
                                           ALU.add).then_inc(summed, 1)
                    dve.wait_ge(summed, 2 * g + 1)
                    dve.tensor_tensor(grow[:, 2, :], cum[:], decay, ALU.subtract).then_inc(summed, 1)

                for n in E:
                    done(dve.memset(E[n][:], 0.0))
                done(dve.memset(M1[:, 0], 0.0))
                dve.wait_ge(start_ready, 1)
                sum_up(0)
                done.wait()
                prepare(dve, done, 0)
                dve.wait_ge(masks_ready, 1)
                for g in range(PR):
                    for r in range(ROUNDS):
                        if r == 4 and g + 1 < PR:
                            sum_up(g + 1)
                        for i in range(2):
                            n = (g * ROUNDS + r) * 2 + i
                            dve.wait_ge(pe_round, n + 1)
                            w, c0 = B[i], 4 * i
                            fin = None
                            if r == 0:
                                done(dve.tensor_tensor(w["Dn"][:], banks(i, 0, 256)[:, :, 0:P], bc(near[:, 0, :]), ALU.mult))
                                done(dve.tensor_tensor(w["Fn"][:], banks(i, 0, 256)[:, :, 0:P], bc(far[:, 0, :]), ALU.mult))
                                done(dve.tensor_tensor(w["Dm"][:], banks(i, 2), bc(near[:, 1, :]), ALU.mult))
                                done(dve.tensor_tensor(w["Fm"][:], banks(i, 2), bc(far[:, 1, :]), ALU.mult))
                                done.wait()
                                done(dve.tensor_tensor(w["R"][:], bc(chip.ident[:]), w["Dn"][:], ALU.subtract))
                                fin = dve.tensor_tensor(w["QB"][:, :, 0:P], banks(i, 0, 256)[:, :, P:256], bc(incl[:]), ALU.mult)
                            elif r == 1:
                                done(dve.tensor_tensor(w["BT"][:], banks(i, 0, 256)[:, :, 0:P], bc(strict[:]), ALU.mult))
                                fin = dve.tensor_tensor(w["Qv"][:], banks(i, 0, 256)[:, :, P:256], bc(incl[:]), ALU.mult)
                            elif r == 2:
                                fin = dve.tensor_copy(w["V"][:], ps[:, 4 * i + 1, 0:4 * HS].rearrange("p (u f) -> p u f", u=4))
                            elif r == 3:
                                fin = dve.tensor_copy(w["Dn"][:], banks(i, 0))
                            elif r in (4, 5):
                                done(dve.tensor_tensor(w["R"][:], w["R"][:], banks(i, 2), ALU.add))
                                if r == 4:
                                    fin = dve.tensor_copy(w["Dn"][:], banks(i, 0))
                                else:
                                    fin = dve.tensor_copy(w["XA"][:, :, 0:HS], ps[:, 4 * i + 3, 0:4 * HS].rearrange("p (u f) -> p u f", u=4))
                            elif r == 6:
                                fin = dve.tensor_tensor(w["R"][:], w["R"][:], banks(i, 2), ALU.add)
                            elif r == 7:
                                done(dve.tensor_copy(w["Dn"][:], banks(i, 0)))
                                fin = dve.tensor_tensor(w["Fn"][:], bc(chip.ident[:]), banks(i, 0), ALU.subtract)
                            elif r == 9:
                                fin = dve.tensor_tensor(w["Fn"][:], w["Fn"][:], banks(i, 0), ALU.add)
                            elif r == 11:
                                fin = dve.tensor_scalar(w["WA"][:], banks(i, 0, 256)[:, :, 0:HS + P], -1.0, None, ALU.mult)
                            elif r == 12:
                                done(dve.tensor_tensor(M1[:, g, c0:c0 + 4, :], banks(i, 0, 256)[:, :, 0:P],
                                                       M1[:, g, c0:c0 + 4, :], ALU.add))
                                for u in range(4):
                                    pe_col = pend[:, g % 2, c0 + u:c0 + u + 1]
                                    fin = dve.scalar_tensor_tensor(
                                        out=M2[:, g, c0 + u, :], in0=chip.ident[:], scalar=pe_col,
                                        in1=quad(i, 0, u, 256)[:, P:256], op0=ALU.mult, op1=ALU.add)
                                    if u < 3:
                                        done(fin)
                            elif r == 13:
                                done(dve.tensor_copy(C1[:, c0:c0 + 4, g, :], ps[:, 4 * i, 0:256].rearrange("p (u f) -> p u f", u=4)))
                                fin = dve.tensor_copy(C2[:, c0:c0 + 4, g, :], ps[:, 4 * i + 1, 0:256].rearrange("p (u f) -> p u f", u=4))
                            if r not in DVE_IDLE:
                                fin.then_inc(dve_round, 1)

            @block.scalar
            def _(act):
                def grow_up(g):
                    act.wait_ge(summed, 2 * g + 2)
                    act.activation(grow[:, 0, :], cum[:], ACT.Exp, scale=-DECAY).then_inc(grown, 1)
                    act.activation(grow[:, 1, :], cum[:], ACT.Exp, scale=DECAY).then_inc(grown, 1)
                    act.activation(grow[:, 2, :], grow[:, 2, :], ACT.Exp, scale=-DECAY).then_inc(grown, 1)

                grow_up(0)
                for g in range(PR):
                    for r in range(ROUNDS):
                        if r == 5 and g + 1 < PR:
                            grow_up(g + 1)
                        for i in range(2):
                            n = (g * ROUNDS + r) * 2 + i
                            act.wait_ge(pe_round, n + 1)
                            w = B[i]
                            cp = lambda o, s_: act.activation(o, s_, ACT.Copy)
                            if r == 0:
                                fin = cp(w["XA"][:, :, HS:HS + P], banks(i, 3))
                            elif r == 1:
                                fin = cp(w["QB"][:, :, P:2 * P], banks(i, 2))
                            elif r == 2:
                                fin = cp(w["kT_"][:], banks(i, 0))
                            elif r == 3:
                                fin = cp(w["Dm"][:], banks(i, 1))
                            elif r in (4, 5):
                                fin = cp(w["Dm"][:], banks(i, 1))
                            elif r == 7:
                                fin = cp(w["Dm"][:], banks(i, 1))
                            elif r == 8:
                                fin = cp(w["Fm"][:], banks(i, 0))
                            elif r == 9:
                                fin = cp(w["RT"][:], banks(i, 1))
                            elif r == 10:
                                fin = cp(w["R"][:], banks(i, 0))
                            if r not in ACT_IDLE:
                                fin.then_inc(act_round, 1)

            @block.tensor
            def _(pe):
                for g in range(PR):
                    pe.wait_ge(prepared, 2 * g + 2)
                    for r in range(ROUNDS):
                        for i in range(2):
                            n = (g * ROUNDS + r) * 2 + i
                            if n >= 2:
                                pe.wait_ge(dve_round, signals(DVE_IDLE, n - 2))
                                pe.wait_ge(act_round, signals(ACT_IDLE, n - 2))
                            w = B[i]
                            last = None
                            for u in range(4):
                                c = 4 * i + u
                                al, be, ka, rh = E["alpha"][:, c, :], E["beta"][:, c, :], E["kappa"][:, c, :], M1[:, g, c, :]

                                def mm(dst, lhsT, rhs, start=True, stop=True):
                                    return pe.matmul(dst, lhsT, rhs, start=start, stop=stop)

                                def q(k, width=P):
                                    return quad(i, k, u, width)

                                X = lambda name: w[name][:, u, :]
                                if r == 0:
                                    mm(quad(i, 0, u, 256)[:, 0:P], be, al)
                                    mm(quad(i, 0, u, 256)[:, P:256], be, rh)
                                    mm(q(2), al, be)
                                    last = pe.transpose(q(3), al, chip.ident[:])
                                elif r == 1:
                                    mm(quad(i, 0, u, 256)[:, 0:P], ka, al)
                                    mm(quad(i, 0, u, 256)[:, P:256], ka, rh)
                                    last = pe.transpose(q(2), E["beta_end"][:, c, :], chip.ident[:])
                                elif r == 2:
                                    pe.transpose(q(0), E["kappa_end"][:, c, :], chip.ident[:])
                                    last = mm(ps[:, 4 * i + 1, u * HS:(u + 1) * HS], E["v"][:, c, :], chip.stack2[:])
                                elif r == 3:
                                    mm(q(0), X("Dm"), X("Dn"))
                                    last = mm(q(1), X("Dn"), X("Dm"))
                                elif r == 4:
                                    mm(q(0), X("Dm"), X("Dn"))
                                    mm(q(1), X("Dn"), X("Dm"))
                                    last = mm(q(2), X("Dm"), X("R"))
                                elif r == 5:
                                    mm(ps[:, 4 * i + 3, u * HS:(u + 1) * HS], X("BT"), X("V"))
                                    mm(q(1), X("Dn"), X("Dm"))
                                    last = mm(q(2), X("Dm"), X("R"))
                                elif r == 6:
                                    last = mm(q(2), X("Dm"), X("R"))
                                elif r == 7:
                                    mm(q(0), X("Fm"), X("R"))
                                    last = mm(q(1), X("R"), X("Fm"))
                                elif r == 8:
                                    last = mm(q(0), X("Dn"), X("Dm"))
                                elif r == 9:
                                    mm(q(0), X("Fm"), X("Fn"))
                                    last = pe.transpose(q(1), X("R"), chip.ident[:])
                                elif r == 10:
                                    last = mm(q(0), X("RT"), X("Fn"))
                                elif r == 11:
                                    last = mm(quad(i, 0, u, 256)[:, 0:HS + P], X("R"), X("XA"))
                                elif r == 12:
                                    last = mm(quad(i, 0, u, 256), w["WA"][:, u, HS:HS + P], X("QB"))
                                elif r == 13:
                                    o1 = ps[:, 4 * i, u * HS:(u + 1) * HS]
                                    mm(o1, X("Qv"), X("V"), stop=False)
                                    mm(o1, w["QB"][:, u, 0:P], w["WA"][:, u, 0:HS], start=False)
                                    o2 = ps[:, 4 * i + 1, u * HS:(u + 1) * HS]
                                    mm(o2, X("kT_"), X("V"), stop=False)
                                    last = mm(o2, w["QB"][:, u, P:2 * P], w["WA"][:, u, 0:HS], start=False)
                            last.then_inc(pe_round, 1)


def _chain(nc, chip, b, rev, M1, M2, C1, C2, sb):
    st = sb("states", [P, NCH, PR, HS])
    order = list(range(NCH))[::-1] if rev else list(range(NCH))
    with stage(nc, "stepped", "state_ready", "out_ready", "out_taken", "v_step") as \
            (stepped, state_ready, out_ready, out_taken, v_step):
        def wide(t):
            return t.rearrange("p (g v) -> p g v", g=PR)

        with nc.Block() as block:
            @block.tensor
            def _(pe):
                for n, c in enumerate(order):
                    pe.wait_ge(state_ready, n + 1)
                    if n + 1 < NCH:
                        for g in range(PR):
                            last = pe.matmul(chip.ps[:, n % 2, g * HS:(g + 1) * HS], M2[:, g, c, :], st[:, n, g, :],
                                             start=True, stop=True)
                        last.then_inc(stepped, 1)
                    if n >= 4:
                        pe.wait_ge(out_taken, n - 3)
                    for g in range(PR):
                        last = pe.matmul(chip.ps[:, 2 + n % 4, g * HS:(g + 1) * HS], M1[:, g, c, :], st[:, n, g, :],
                                         start=True, stop=True)
                    last.then_inc(out_ready, 1)

            @block.vector
            def _(dve):
                done = Steps(dve, v_step)
                dve.memset(st[:, 0], 0.0).then_inc(state_ready, 1)
                if rev:
                    done(dve.tensor_tensor(C1[:], C1[:], b.out, ALU.add))
                for n, c in enumerate(order):
                    if n + 1 < NCH:
                        dve.wait_ge(stepped, n + 1)
                        dve.tensor_tensor(st[:, n + 1], wide(chip.ps[:, n % 2, 0:PR * HS]), C2[:, c],
                                          ALU.add).then_inc(state_ready, 1)
                    if n == 0 and rev:
                        done.wait()
                    dve.wait_ge(out_ready, n + 1)
                    dve.tensor_tensor(b.out[:, c], wide(chip.ps[:, 2 + n % 4, 0:PR * HS]), C1[:, c],
                                      ALU.add).then_inc(out_taken, 1)
                dve.wait_ge(out_taken, NCH)


def rwkv_output(nc, chip, A, b, yT, ahead):
    NU = NCH * PR
    with ExitStack() as ctx:
        sb = lambda name, shape: ctx.enter_context(buffer(nc, name, shape, F32))
        sq = sb("out_sq", [P, NU, HS])
        OE = sb("out_E", [P, NU, P])
        st = sb("out_stats", [P, 4, NU])
        with stage(nc, "v_step", "var_ready", "root_ready", "zeroed", "normed", "turned", "affine", "gated") as \
                (v_step, var_ready, root_ready, zeroed, normed, turned, affine, gated):
            with nc.Block() as block:
                @block.sync
                def _(sp):
                    ahead(sp)

                @block.gpsimd
                def _(pool):
                    pool.memset(OE[0:HS, :, HS:P], 0.0).then_inc(zeroed, 1)
                    pool.memset(OE[HS:P, :, 0:HS], 0.0).then_inc(zeroed, 1)
                    pool.wait_ge(zeroed, 2)

                @block.vector
                def _(dve):
                    done = Steps(dve, v_step)
                    o = b.out.rearrange("p c g v -> p (c g) v")
                    spread = lambda r: st[:, r, :].rearrange("p (u o) -> p u o", o=1).to_broadcast([P, NU, HS])
                    done(dve.tensor_reduce(st[:, 0, :], o, AX.X, ALU.add))
                    done.wait()
                    done(dve.tensor_scalar(st[:, 0, :], st[:, 0, :], 1.0 / HS, None, ALU.mult))
                    done.wait()
                    done(dve.tensor_tensor(o, o, spread(0), ALU.subtract))
                    done.wait()
                    done(dve.tensor_tensor(sq[:], o, o, ALU.mult))
                    done.wait()
                    done(dve.tensor_reduce(st[:, 1, :], sq[:], AX.X, ALU.add))
                    done.wait()
                    dve.tensor_scalar(st[:, 2, :], st[:, 1, :], 1.0 / HS, GN_EPS, ALU.mult,
                                      ALU.add).then_inc(var_ready, 1)
                    dve.wait_ge(root_ready, 1)
                    done(dve.reciprocal(st[:, 1, :], st[:, 3, :]))
                    done.wait()
                    dve.wait_ge(zeroed, 2)
                    for h in range(2):
                        r = slice(h * HS, (h + 1) * HS)
                        dve.tensor_tensor(OE[r, :, r], o[r], spread(1)[r], ALU.mult).then_inc(normed, 1)
                    for g in range(PR):
                        dve.wait_ge(affine, g + 1)
                        done(dve.tensor_tensor(yT[:, g, :], yT[:, g, :], b.bonusT[:, g, :], ALU.add))
                        done.wait()
                        done(dve.tensor_tensor(yT[:, g, :], yT[:, g, :], b.gateT[:, g, :], ALU.mult))
                    done.wait()

                @block.scalar
                def _(act):
                    act.wait_ge(var_ready, 1)
                    act.activation(st[:, 3, :], st[:, 2, :], ACT.Sqrt).then_inc(root_ready, 1)
                    for g in range(PR):
                        act.wait_ge(turned, g + 1)
                        act.activation(yT[:, g, :], chip.ps[:, g, :], ACT.Identity, scale=chip.col("ln_x_w", g),
                                       bias=chip.col("ln_x_b", g)).then_inc(affine, 1)

                @block.tensor
                def _(pe):
                    pe.wait_ge(normed, 2)
                    for g in range(PR):
                        for c in range(NCH):
                            last = pe.matmul(chip.ps[:, g, c * C:(c + 1) * C], OE[:, c * PR + g, :], chip.stack2[:],
                                             start=True, stop=True)
                        last.then_inc(turned, 1)


def stream_product(nc, chip, ring, n_k, halves=((0, 512), (512, 1024)), x_of=None, parts=None, out_of=None,
                   norm_row=None, x_again=None, pieces=None, ahead=None, store=None):
    if pieces is None:
        pieces = [(lo, hi, in_order) for lo, hi in halves]
    shared = len(pieces) > len(halves)

    def place(t, lo, hi):
        half = 0 if hi <= halves[0][1] else 1
        at = lo - halves[half][0]
        return chip.ps[:, 2 * t + half, at:at + hi - lo]

    raw, w, load, _ = ring
    width = halves[1][1]
    turns = n_k // 2
    per = 1 if parts is not None else 2
    with ExitStack() as ctx:
        wp = ctx.enter_context(buffer(nc, "stream_w_parts", [P, 2, 2, width], F32R))
        xp = ctx.enter_context(buffer(nc, "stream_x_parts", [P, 2, 2, S if per == 2 else 2], F32R))
        gain = ctx.enter_context(buffer(nc, "post_gain", [P, D if norm_row is not None else 2], F32))
        junk = ctx.enter_context(buffer(nc, "post_squares", [P, D if norm_row is not None else 2], F32))
        y = ctx.enter_context(buffer(nc, "post_normed", [P, TT, D if norm_row is not None else 2], F32))
        st = ctx.enter_context(buffer(nc, "post_stats", [P, 4, TT], F32))
        zero = ctx.enter_context(buffer(nc, "zero_parts", [P, P if shared else 2], F32R))
        with stage(nc, "stored", "zeroed", "gain_in", "x_in", "large", "small", "product", "taken_a", "taken_v", "squares", "mean_ready",
                   "root_ready", "v_step", "normed", "added") as \
                (stored, zeroed, gain_in, x_in, large, small, product, taken_a, taken_v, squares, mean_ready, root_ready, v_step,
                 normed, added):
            def w_parts(j):
                return wp[:, j, 0, :], wp[:, j, 1, :]

            def x_parts(j):
                return xp[:, j, 0, :], xp[:, j, 1, :]

            def loop(eng, turn, last_apart=False):
                turn(0, first=True)
                end = turns - 1 if last_apart else turns
                if parts is not None or end < 4:
                    for i in range(1, end):
                        turn(i)
                else:
                    with eng.Fori(1, end) as i:
                        turn(i)
                if last_apart:
                    turn(turns - 1, last=True)

            with nc.Block() as block:
                @block.sync
                def _(sp):
                    def load_turn(i):
                        for j in range(2):
                            sp.wait_ge(small, i * 2 * per + (j + 1 - 2) * per)
                            load(sp, i, j)

                    if x_again is not None:
                        sp.dma_start(chip.x[:], x_again).then_inc(x_in, 16)
                    if norm_row is not None:
                        sp.dma_start(gain[:], norm_row.partition_broadcast(P)).then_inc(gain_in, 16)
                    if parts is not None or turns < 4:
                        for i in range(1, turns):
                            load_turn(i)
                    else:
                        with sp.Fori(1, turns) as i:
                            load_turn(i)
                    if ahead is not None:
                        ahead(sp)
                    if store is not None:
                        for t in range(TT):
                            if t < TT // 2:
                                sp.wait_ge(added, t + 1)
                            else:
                                sp.wait_ge(taken_v, t + 1 - TT // 2)
                            sp.dma_start(store[t * P:(t + 1) * P, :], chip.x[:, t, :]).then_inc(stored, 16)
                        sp.wait_ge(stored, 16 * TT)

                @block.tensor
                def _(pe):
                    def turn(i, first=False, last=False):
                        for j in range(2):
                            pe.wait_ge(small, i * 2 * per + (j + 1) * per)
                            for t in range(TT):
                                for lo, hi, order in pieces:
                                    if parts is None:
                                        x = [order(part, t) for part in x_parts(j)]
                                    else:
                                        x = [order(parts[:, part, 2 * i + j, :], t) for part in range(2)]
                                    ins = split_product(pe, place(t, lo, hi), x, [part[:, lo:hi] for part in w_parts(j)],
                                                        first and j == 0 and not shared, last and j == 1 and not shared,
                                                        shared)
                            if not (shared and last and j == 1):
                                ins.then_inc(product, 1)

                    def products_with_zero(**flags):
                        for n in range(2 * TT):
                            last = pe.matmul(chip.ps[:, n, :], zero[:], zero[:, 0:1].to_broadcast([P, 512]),
                                             skip_group_check=True, **flags)
                        return last

                    if shared:
                        pe.wait_ge(zeroed, 1)
                        products_with_zero(start=True, stop=False)
                    loop(pe, turn, last_apart=True)
                    if shared:
                        products_with_zero(start=False, stop=True).then_inc(product, 1)

                @block.scalar
                def _(act):
                    def split(i, first=False):
                        for j in range(2):
                            act.wait_ge(w[j], i * 16 + 16)
                            if not first:
                                act.wait_ge(product, i * 2 + (j + 1 - 2))
                            large_part(act, w_parts(j), raw[:, j, :]).then_inc(large, 1)
                            if per == 2:
                                large_part(act, x_parts(j), x_of(i * 2 + j)).then_inc(large, 1)

                    loop(act, split)
                    act.wait_ge(product, n_k)
                    if out_of is not None:
                        lo, hi = halves[0]
                        for t in range(TT):
                            act.activation(out_of(t, 0), chip.ps[:, 2 * t, 0:hi - lo], ACT.Copy).then_inc(taken_a, 1)
                        act.wait_ge(taken_a, TT)
                    elif norm_row is not None:
                        for t in range(TT):
                            if t:
                                act.wait_ge(squares, t)
                            act.activation(junk[:], chip.ps[:, 2 * t:2 * t + 2, :].rearrange("p b n -> p (b n)"),
                                           ACT.Square, accum_out=st[:, 0, t:t + 1]).then_inc(squares, 1)
                            if t:
                                act.wait_ge(mean_ready, t)
                                act.activation(st[:, 2, t - 1:t], st[:, 1, t - 1:t], ACT.Sqrt).then_inc(root_ready, 1)
                        act.wait_ge(mean_ready, TT)
                        act.activation(st[:, 2, TT - 1:TT], st[:, 1, TT - 1:TT], ACT.Sqrt).then_inc(root_ready, 1)

                @block.vector
                def _(dve):
                    done = Steps(dve, v_step)

                    def split(i, first=False):
                        for j in range(2):
                            dve.wait_ge(large, i * 2 * per + (j * per + 1))
                            small_part(dve, w_parts(j), raw[:, j, :]).then_inc(small, 1)
                            if per == 2:
                                dve.wait_ge(large, i * 2 * per + (j * per + 2))
                                small_part(dve, x_parts(j), x_of(i * 2 + j)).then_inc(small, 1)

                    if shared:
                        dve.tensor_scalar(zero[:], chip.ident[:], 0.0, None, ALU.mult).then_inc(zeroed, 1)
                    loop(dve, split)
                    if norm_row is None:
                        dve.wait_ge(product, n_k)
                        if x_again is not None:
                            dve.wait_ge(x_in, 16)
                        lo, hi = halves[1]
                        for t in range(TT):
                            if out_of is not None:
                                dve.tensor_copy(out_of(t, 1), chip.ps[:, 2 * t + 1, 0:hi - lo]).then_inc(taken_v, 1)
                            else:
                                xt = chip.x[:, t, :].rearrange("p (b n) -> p b n", b=2)
                                dve.tensor_tensor(xt, xt, chip.ps[:, 2 * t:2 * t + 2, :], ALU.add).then_inc(taken_v, 1)
                        dve.wait_ge(taken_v, TT)
                        return

                    def mean(t):
                        dve.wait_ge(squares, t + 1)
                        dve.tensor_scalar(st[:, 1, t:t + 1], st[:, 0, t:t + 1], 1.0 / D, NORM_EPS, ALU.mult,
                                          ALU.add).then_inc(mean_ready, 1)

                    mean(0)
                    for t in range(TT):
                        if t + 1 < TT:
                            mean(t + 1)
                        dve.wait_ge(root_ready, t + 1)
                        done(dve.reciprocal(st[:, 3, t:t + 1], st[:, 2, t:t + 1]))
                        done.wait()
                        if t == 0:
                            dve.wait_ge(gain_in, 16)
                        dve.scalar_tensor_tensor(out=y[:, t, :], in0=chip.ps[:, 2 * t:2 * t + 2, :]
                                                 .rearrange("p b n -> p (b n)"), scalar=st[:, 3, t:t + 1], in1=gain[:],
                                                 op0=ALU.mult, op1=ALU.mult).then_inc(normed, 1)
                    for t in range(TT // 2, TT):
                        dve.wait_ge(normed, t + 1)
                        dve.tensor_tensor(chip.x[:, t, :], chip.x[:, t, :], y[:, t, :], ALU.add).then_inc(taken_v, 1)
                    dve.wait_ge(taken_v, TT // 2)

                @block.gpsimd
                def _(pool):
                    if norm_row is not None:
                        for t in range(TT // 2):
                            pool.wait_ge(normed, t + 1)
                            pool.tensor_tensor(chip.x[:, t, :], chip.x[:, t, :], y[:, t, :], ALU.add).then_inc(added, 1)
                        pool.wait_ge(added, TT // 2)


def of_rows(w, k):
    return w[bass.ds(k, 1)].rearrange("o p n -> p (o n)")


def of_tiles(xT, k):
    return xT[:, bass.ds(k, 1), :].rearrange("p o s -> p (o s)")


class Obj:
    pass


def rwkv_block(nc, chip, A):
    with ExitStack() as ctx:
        sb = lambda name, shape, c=ctx: c.enter_context(buffer(nc, name, shape, F32))
        b = Obj()
        yT = chip.hT[:]
        b.out = chip.hT[:, 0:4, :].rearrange("p k (c v) -> p (k c) v", v=HS).rearrange("p (c g) v -> p c g v", g=PR)
        spare = chip.x[:].rearrange("p t d -> p (t d)")
        b.gateT = spare[:, 0:PR * S].rearrange("p (g s) -> p g s", g=PR)
        b.bonusT = spare[:, PR * S:2 * PR * S].rearrange("p (g s) -> p g s", g=PR)
        b.rT, b.vT, b.kk = (sb(n, [P, PR, S]) for n in ("rT", "vT", "kkT"))
        with ExitStack() as early:
            b.kT, b.loraT = sb("kT", [P, PR, S], early), sb("loraT", [P, 4, S], early)
            b.poolT = sb("poolT", [P, 4, S + 16], early)
            with ExitStack() as split_ctx:
                parts = split_ctx.enter_context(buffer(nc, "h_parts", [P, 2, KD, S], F32R))
                with weight_ring(nc, A["w_in"]) as (ring, w, load, ahead):
                    norm_transpose(nc, chip, RMS_EPS, A["norm1_row"], parts, ahead=ahead)
                    project_in_1(nc, chip, b, parts, ring, w, load)
            b.decay, b.a, b.kd = (sb(n, [P, 8, S], early) for n in ("decayT", "aT", "kdT"))
            rwkv_inputs(nc, chip, A, b, yT)
        for rev in (False, True):
            recurrence(nc, chip, b, A, rev)
        with row_ring(nc, lambda k: of_rows(A["w_out"], k)) as ring:
            rwkv_output(nc, chip, A, b, yT, ring[-1])
            stream_product(nc, chip, ring, KD, x_of=lambda k: of_tiles(chip.hT, k),
                           x_again=A["x"].rearrange("(t p) d -> p t d", p=P))


PH = 8
TOPK = 16
SLOTS = PH * TOPK
NKEYS = 128
RING = 16


class Choice:
    STEPS = 28

    def __init__(self, dve, sb, scores, idx, gate, iota):
        self.dve, self.scores, self.idx, self.gate, self.iota = dve, scores, idx, gate, iota
        self.mine = sb("scores_now", [P, 2, NKEYS])
        self.left = sb("scores_left", [P, 2, NKEYS])
        self.top = sb("top", [P, 2, TOPK])
        self.topi = sb("top_index", [P, 2, TOPK], U32)
        self.topf = sb("top_index_f", [P, 2, TOPK])
        self.cand = sb("cand", [P, 1, TOPK * TOPK])
        self.candl = sb("cand_left", [P, 1, TOPK * TOPK])
        self.best = sb("best", [P, 1, TOPK])
        self.pos = sb("best_pos", [P, 1, TOPK], U32)
        self.part = sb("pos_part", [P, 2, TOPK], U32)
        self.partf = sb("pos_part_f", [P, 2, TOPK])
        self.same = sb("pos_same", [P, 2, TOPK, TOPK])
        self.chosen = sb("chosen", [P, 2, TOPK])
        self.gatekeeper = sb("choice_gatekeeper", [P, 1])

    def let_through(self):
        self.dve.tensor_copy(self.gatekeeper[:], self.iota[:, 0:1])

    def top16(self, done, values, rest, n, out, index):
        dve = self.dve
        self.let_through()
        for j in range(n):
            done(dve.max(out[:, j, 0:8], values[:, j, :]))
        done.wait()
        self.let_through()
        for j in range(n):
            done(dve.match_replace(rest[:, j, :], out[:, j, 0:8], values[:, j, :], -3e38))
            done(dve.max_index(index[:, j, 0:8], out[:, j, 0:8], values[:, j, :]))
        done.wait()
        self.let_through()
        for j in range(n):
            done(dve.max(out[:, j, 8:16], rest[:, j, :]))
        done.wait()
        self.let_through()
        for j in range(n):
            done(dve.max_index(index[:, j, 8:16], out[:, j, 8:16], rest[:, j, :]))
        done.wait()

    def sides(self, done, t, h):
        done(self.dve.tensor_copy(self.mine[:].rearrange("p a n -> p (a n)"),
                                  self.scores[:, t, bass.ds(h * (2 * NKEYS), 2 * NKEYS)]))
        done.wait()
        self.top16(done, self.mine, self.left, 2, self.top, self.topi)

    def pairs(self, done, t, h):
        dve = self.dve
        done(dve.tensor_copy(self.topf[:], self.topi[:]))
        a = self.top[:, 0, :].rearrange("p (k o) -> p k o", o=1).to_broadcast([P, TOPK, TOPK])
        c = self.top[:, 1, :].rearrange("p (o k) -> p o k", o=1).to_broadcast([P, TOPK, TOPK])
        done(dve.tensor_tensor(self.cand[:, 0, :].rearrange("p (a b) -> p a b", b=TOPK), a, c, ALU.add))
        done.wait()
        self.top16(done, self.cand, self.candl, 1, self.best, self.pos)

    def names(self, done, t, h, picked):
        dve = self.dve
        done(dve.tensor_scalar(self.gate[:, t, bass.ds(h * TOPK, TOPK)], self.best[:, 0, :], self.best[:, 0, 0:1], None,
                               ALU.subtract))
        done(dve.tensor_scalar(self.part[:, 0, :], self.pos[:, 0, :], 4, None, ALU.logical_shift_right))
        done(dve.tensor_scalar(self.part[:, 1, :], self.pos[:, 0, :], 15, None, ALU.bitwise_and))
        done.wait()
        done(dve.tensor_copy(self.partf[:], self.part[:]))
        done.wait()
        for side in range(2):
            done(dve.tensor_tensor(self.same[:, side], self.partf[:, side, :].rearrange("p (k o) -> p k o", o=1)
                                   .to_broadcast([P, TOPK, TOPK]), self.iota[:].rearrange("p (o a) -> p o a", o=1)
                                   .to_broadcast([P, TOPK, TOPK]), ALU.is_equal))
        done.wait()
        for side in range(2):
            done(dve.tensor_tensor(self.same[:, side], self.same[:, side], self.topf[:, side, :]
                                   .rearrange("p (o a) -> p o a", o=1).to_broadcast([P, TOPK, TOPK]), ALU.mult))
        done.wait()
        done(dve.tensor_reduce(self.chosen[:].rearrange("p s k -> p (s k)"),
                               self.same[:].rearrange("p s k a -> p (s k) a"), AX.X, ALU.add))
        done.wait()
        done(dve.scalar_tensor_tensor(out=self.chosen[:, 0, :], in0=self.chosen[:, 0, :], scalar=float(NKEYS),
                                      in1=self.chosen[:, 1, :], op0=ALU.mult, op1=ALU.add))
        done.wait()
        dve.tensor_copy(self.idx[:, t, bass.ds(h * TOPK, TOPK)], self.chosen[:, 0, :]).then_inc(picked, 1)


def expert_scores(nc, chip, A, parts, scores, idx, gate, iota, ring, w, load):
    with ExitStack() as ctx:
        sb = lambda name, shape, dt=F32: ctx.enter_context(buffer(nc, name, shape, dt))
        keys = sb("keys", [P, 2 * PH, NKEYS])
        q = lambda m: chip.hT[:, m % KD, :]
        wp = split_weights(nc, ctx)
        with stage(nc, "keys_in", "iota_ready", "large", "small", "q_done", "q_out", "s_done", "s_out", "picked",
                   "v_step") as (keys_in, iota_ready, large, small, q_done, q_out, s_done, s_out, picked, v_step):
            def w_parts(m):
                return wp[:, m % 2, 0], wp[:, m % 2, 1]

            def bank(h, side):
                return chip.ps[:, 4 + h % 2 * 2 + side, :]

            with nc.Block() as block:
                @block.sync
                def _(sp):
                    sp.dma_start(keys[:], A["peer_keys"]).then_inc(keys_in, 16)
                    for m in range(WRING, 2 * PH):
                        sp.wait_ge(small, m - WRING + 1)
                        load(sp, m)

                @block.tensor
                def _(pe):
                    for m in range(2 * PH + 1):
                        if m < 2 * PH:
                            pe.wait_ge(small, m + 1)
                            if m >= 4:
                                pe.wait_ge(q_out, m - 3)
                            wide = w_parts(m)
                            for k in range(KD):
                                last = split_product(pe, chip.ps[:, m % 4, :], (wide[0][:, k, :], wide[1][:, k, :]),
                                                     (parts[:, 0, k, :], parts[:, 1, k, :]), k == 0, k == KD - 1)
                            last.then_inc(q_done, 1)
                        if m and m % 2 == 0:
                            h = m // 2 - 1
                            pe.wait_ge(q_out, 2 * h + 2)
                            if h == 0:
                                pe.wait_ge(keys_in, 16)
                            if h >= 2:
                                pe.wait_ge(s_out, 2 * h - 2)
                            for side in range(2):
                                for t in range(TT):
                                    last = pe.matmul(bank(h, side)[:, t * P:(t + 1) * P],
                                                     q(2 * h + side)[:, t * P:(t + 1) * P], keys[:, 2 * h + side, :],
                                                     start=True, stop=True)
                                last.then_inc(s_done, 1)

                @block.scalar
                def _(act):
                    for m in range(2 * PH + 3):
                        if m < 2 * PH:
                            act.wait_ge(w[m % WRING], 16 * (m // WRING + 1))
                            if m >= 2:
                                act.wait_ge(q_done, m - 1)
                            large_part(act, w_parts(m), ring[:, m % WRING]).then_inc(large, 1)
                        if 1 <= m <= 2 * PH:
                            act.wait_ge(q_done, m)
                            if m > KD:
                                act.wait_ge(s_done, m - KD)
                            act.activation(q(m - 1), chip.ps[:, (m - 1) % 4, :], ACT.Copy).then_inc(q_out, 1)
                        if m >= 4 and m % 2 == 0:
                            h = m // 2 - 2
                            for side in range(2):
                                n = 2 * h + side
                                act.wait_ge(s_done, n + 1)
                                act.activation(scores[:, :, n * NKEYS:(n + 1) * NKEYS],
                                               bank(h, side).rearrange("p (t n) -> p t n", t=TT),
                                               ACT.Copy).then_inc(s_out, 1)
                    act.wait_ge(s_out, 2 * PH)

                @block.gpsimd
                def _(pool):
                    pool.iota(iota[:], pattern=[[1, TOPK]], base=0, channel_multiplier=0,
                              allow_small_or_imprecise_dtypes=True).then_inc(iota_ready, 1)
                    for m in range(2 * PH):
                        pool.wait_ge(large, m + 1)
                        if m:
                            pool.wait_ge(small, m)
                        small_part(pool, w_parts(m), ring[:, m % WRING]).then_inc(small, 1)
                    pool.wait_ge(small, 2 * PH)

                @block.vector
                def _(dve):
                    choice = Choice(dve, sb, scores, idx, gate, iota)
                    dve.wait_ge(iota_ready, 1)
                    for h in range(PH - 1):
                        dve.wait_ge(s_out, 2 * h + 2)
                        done = Steps(dve, v_step, h * Choice.STEPS)
                        choice.sides(done, 0, h)
                        choice.pairs(done, 0, h)
                        choice.names(done, 0, h, picked)
                    dve.wait_ge(picked, PH - 1)


PASSES = tuple((kind, t) for t in range(TT) for kind in "uv")
TURNS = SLOTS // RING
HALF = RING // 2
ADDED = (3, 7, 11, 15)
MULTIPLIED = tuple(s for s in range(RING) if s not in ADDED)


def experts(nc, chip, A, h2, scores, idx, gate, iota):
    with ExitStack() as ctx:
        sb = lambda name, shape, dt=F32: ctx.enter_context(buffer(nc, name, shape, dt))
        ring = sb("row_ring", [P, RING, D])
        now = sb("idx_now", [P, RING], U32)
        dots = sb("dots_now", [P, RING])
        dot = sb("dots", [P, TT, SLOTS])
        coef = sb("coef", [P, TT, SLOTS])
        diag = sb("diag", [P, RING, P])
        zero = sb("zero", [P, P])
        sums = sb("gate_sum", [P, PH])
        gatekeeper = sb("gatekeeper", [P, 1], U32)
        gain = sb("norm_f_gain", [P, D])
        junk = sb("norm_f_squares", [P, D])
        st = sb("norm_f_stats", [P, 4, TT])
        with stage(nc, *[f"row{i}" for i in range(RING)], "picked", "v_step", "idx_now_ready", "u_used",
                   "v_multiplied", "v_added", "dots_kept", "exped", "gelu_done", "coef_ready", "diag_ready", "zeroed",
                   "summed", "x_taken", "gain_in", "squared", "mean_ready", "rooted") as \
                (*row, picked, v_step, idx_ready, u_used, v_multiplied, v_added, dots_kept, exped, gelu_done,
                 coef_ready, diag_ready, zeroed, summed, x_taken, gain_in, squared, mean_ready, rooted):
            users = {"u": ((u_used, RING),), "v": ((v_multiplied, len(MULTIPLIED)), (v_added, len(ADDED)))}

            with nc.Block() as block:
                @block.sync
                def _(sp):
                    sp.dma_start(gain[:], A["norm_f_row"].partition_broadcast(P)).then_inc(gain_in, 16)

                @block.gpsimd
                def _(pool):
                    def turn(n, i, first=False):
                        kind, t = PASSES[n]
                        for half in range(2):
                            lo = half * HALF
                            if not first:
                                for used, per in users[kind]:
                                    pool.wait_ge(used, i * per + (t * TURNS * per - per + (half + 1) * per // 2))
                            if n:
                                for used, per in users["v" if kind == "u" else "u"]:
                                    turns = TURNS * (t if kind == "u" else t + 1)
                                    pool.wait_ge(used, turns * per - per + (half + 1) * per // 2)
                            if n == 0 and half == 0 and not first:
                                pool.wait_ge(picked, 1)
                            if n and kind == "u" and half == 0:
                                pool.wait_ge(picked, i + (t * PH - PH + 2))
                            pool.tensor_copy(now[:, lo:lo + HALF], idx[:, t, bass.ds(i * RING + lo, HALF)]) \
                                .then_inc(idx_ready, 1)
                            pool.wait_ge(idx_ready, i * 4 + (n * TURNS * 4 + half * 2 + 1))
                            pool.tensor_tensor(gatekeeper[:], now[:, lo:lo + 1], now[:, lo:lo + 1],
                                               ALU.add).then_inc(idx_ready, 1)
                            for s in range(lo, lo + HALF):
                                pool.indirect_dma_start(
                                    ring[:, s, :], None, A["peer_u"] if kind == "u" else A["peer_v"],
                                    bass.IndirectOffsetOnAxis(ap=now[:, s:s + 1], axis=0)).then_inc(row[s], 16)

                    for n, (kind, t) in enumerate(PASSES):
                        if t == 0:
                            turn(n, 0, first=True)
                            with pool.Fori(1, TURNS) as i:
                                turn(n, i)
                        else:
                            with pool.Fori(0, TURNS) as i:
                                turn(n, i)

                @block.vector
                def _(dve):
                    choice = Choice(dve, sb, scores, idx, gate, iota)
                    steps = 0

                    def dot_rows(n, t, i):
                        for s in range(RING):
                            dve.wait_ge(row[s], i * 16 + 16 * (n * TURNS + 1))
                            dve.tensor_tensor_reduce(ring[:, s, :], ring[:, s, :], h2[:, t, :], 1.0, 0.0, ALU.mult,
                                                     ALU.add, dots[:, s:s + 1]).then_inc(u_used, 1)
                        dve.wait_ge(u_used, i * RING + (t * SLOTS + RING))
                        dve.tensor_copy(dot[:, t, bass.ds(i * RING, RING)], dots[:]).then_inc(dots_kept, 1)
                        dve.wait_ge(dots_kept, i + (t * TURNS + 1))

                    def add_row(n, t, i, j):
                        s = ADDED[j]
                        dve.wait_ge(row[s], i * 16 + 16 * (n * TURNS + 1))
                        if j:
                            dve.wait_ge(v_added, i * len(ADDED) + (t * TURNS * len(ADDED) + j))
                        dve.scalar_tensor_tensor(out=chip.x[:, t, :], in0=ring[:, s, :],
                                                 scalar=coef[:, t, bass.ds(i * RING + s, 1)], in1=chip.x[:, t, :],
                                                 op0=ALU.mult, op1=ALU.add).then_inc(v_added, 1)

                    def weights(t):
                        done = Steps(dve, v_step, steps)
                        g = gate[:, t, :].rearrange("p (h k) -> p h k", h=PH)
                        dve.wait_ge(exped, t + 1)
                        done(dve.tensor_reduce(sums[:], g, AX.X, ALU.add))
                        done.wait()
                        done(dve.reciprocal(sums[:], sums[:]))
                        done.wait()
                        done(dve.tensor_tensor(g, g, sums[:].rearrange("p (h o) -> p h o", o=1)
                                               .to_broadcast([P, PH, TOPK]), ALU.mult))
                        done.wait()
                        dve.wait_ge(gelu_done, t + 1)
                        dve.tensor_tensor(coef[:, t, :], coef[:, t, :], gate[:, t, :], ALU.mult).then_inc(coef_ready, 1)
                        dve.wait_ge(coef_ready, t + 1)
                        return done.n

                    def take(t):
                        dve.wait_ge(summed, t + 1)
                        xt = chip.x[:, t, :].rearrange("p (b n) -> p b n", b=2)
                        dve.tensor_tensor(xt, xt, chip.ps[:, t % 2 * 2:t % 2 * 2 + 2, :], ALU.add).then_inc(x_taken, 1)

                    def mean(t):
                        dve.wait_ge(squared, t + 1)
                        dve.tensor_scalar(st[:, 1, t:t + 1], st[:, 0, t:t + 1], 1.0 / D, RMS_EPS, ALU.mult,
                                          ALU.add).then_inc(mean_ready, 1)

                    def norm(t):
                        done = Steps(dve, v_step, steps)
                        dve.wait_ge(rooted, t + 1)
                        done(dve.reciprocal(st[:, 3, t:t + 1], st[:, 2, t:t + 1]))
                        done.wait()
                        dve.wait_ge(gain_in, 16)
                        done(dve.scalar_tensor_tensor(out=chip.x[:, t, :], in0=chip.x[:, t, :], scalar=st[:, 3, t:t + 1],
                                                      in1=gain[:], op0=ALU.mult, op1=ALU.mult))
                        done.wait()
                        return done.n

                    dve.memset(zero[:], 0.0).then_inc(zeroed, 1)
                    done = Steps(dve, v_step)
                    choice.sides(done, 0, PH - 1)
                    choice.pairs(done, 0, PH - 1)
                    choice.names(done, 0, PH - 1, picked)
                    assert done.n == Choice.STEPS
                    steps += Choice.STEPS
                    for t in range(TT):
                        with dve.Fori(0, TURNS) as i:
                            dot_rows(2 * t, t, i)
                        steps += weights(t)
                        if t:
                            take(t - 1)
                        if t >= 2:
                            mean(t - 2)
                        with dve.Fori(0, TURNS) as i:
                            n = 2 * t + 1
                            add_row(n, t, i, 0)
                            if t + 1 < TT:
                                done = Steps(dve, v_step, i * Choice.STEPS + steps)
                                choice.sides(done, t + 1, i)
                                add_row(n, t, i, 1)
                                choice.pairs(done, t + 1, i)
                                add_row(n, t, i, 2)
                                choice.names(done, t + 1, i, picked)
                            else:
                                add_row(n, t, i, 1)
                                add_row(n, t, i, 2)
                            add_row(n, t, i, 3)
                            dve.wait_ge(v_added, i * len(ADDED) + (t * TURNS + 1) * len(ADDED))
                        if t + 1 < TT:
                            steps += PH * Choice.STEPS
                        if t >= 3:
                            steps += norm(t - 3)
                    take(TT - 1)
                    mean(TT - 2)
                    steps += norm(TT - 3)
                    steps += norm(TT - 2)
                    mean(TT - 1)
                    steps += norm(TT - 1)

                @block.scalar
                def _(act):
                    per = len(MULTIPLIED)

                    def square(t):
                        act.wait_ge(x_taken, t + 1)
                        if t:
                            act.wait_ge(squared, t)
                        act.activation(junk[:], chip.x[:, t, :], ACT.Square, accum_out=st[:, 0, t:t + 1]).then_inc(squared, 1)

                    def root(t):
                        act.wait_ge(mean_ready, t + 1)
                        act.activation(st[:, 2, t:t + 1], st[:, 1, t:t + 1], ACT.Sqrt).then_inc(rooted, 1)

                    for n, (kind, t) in enumerate(PASSES):
                        if kind == "u" and t >= 2:
                            square(t - 2)
                            if t >= 3:
                                root(t - 3)
                        if kind == "u":
                            act.wait_ge(picked, PH * t + 1)
                            act.activation(gate[:, t, :], gate[:, t, :], ACT.Exp).then_inc(exped, 1)
                            act.wait_ge(dots_kept, TURNS * (t + 1))
                            act.activation(coef[:, t, :], dot[:, t, :], ACT.Gelu).then_inc(gelu_done, 1)
                            continue
                        act.wait_ge(coef_ready, t + 1)

                        def build(i, first=False):
                            for j, s in enumerate(MULTIPLIED):
                                if not first:
                                    act.wait_ge(v_multiplied, i * per + (t * TURNS * per - per + j + 1))
                                act.activation(diag[:, s, :], chip.ident[:], ACT.Copy,
                                               scale=coef[:, t, bass.ds(i * RING + s, 1)]).then_inc(diag_ready, 1)

                        if t == 0:
                            build(0, True)
                            with act.Fori(1, TURNS) as i:
                                build(i)
                        else:
                            with act.Fori(0, TURNS) as i:
                                build(i)
                    act.wait_ge(diag_ready, TURNS * per * TT)
                    root(TT - 3)
                    square(TT - 2)
                    root(TT - 2)
                    square(TT - 1)
                    root(TT - 1)

                @block.tensor
                def _(pe):
                    per = len(MULTIPLIED)
                    pe.wait_ge(zeroed, 1)

                    def product_with_zero(bank, **flags):
                        for b2 in range(2):
                            last = pe.matmul(chip.ps[:, bank + b2, :], zero[:], chip.ident[:, 0:1]
                                             .to_broadcast([P, 512]), skip_group_check=True, **flags)
                        return last

                    for n, (kind, t) in enumerate(PASSES):
                        if kind == "u":
                            continue
                        bank = t % 2 * 2
                        if t >= 2:
                            pe.wait_ge(x_taken, t - 1)
                        product_with_zero(bank, start=True, stop=False)
                        with pe.Fori(0, TURNS) as i:
                            for j, s in enumerate(MULTIPLIED):
                                pe.wait_ge(row[s], i * 16 + 16 * (n * TURNS + 1))
                                pe.wait_ge(diag_ready, i * per + (t * TURNS * per + j + 1))
                                for b2 in range(2):
                                    last = pe.matmul(chip.ps[:, bank + b2, :], diag[:, s, :],
                                                     ring[:, s, b2 * 512:(b2 + 1) * 512], start=False, stop=False,
                                                     skip_group_check=True)
                                last.then_inc(v_multiplied, 1)
                        product_with_zero(bank, start=False, stop=True).then_inc(summed, 1)


def expert_block(nc, chip, A):
    with ExitStack() as ctx:
        sb = lambda name, shape, dt=F32: ctx.enter_context(buffer(nc, name, shape, dt))
        idx = sb("expert_idx", [P, TT, SLOTS], U32)
        gate = sb("expert_gate", [P, TT, SLOTS])
        h2 = sb("h2", [P, TT, D])
        scores = sb("scores", [P, TT, 2 * PH * NKEYS])
        iota = sb("iota16", [P, TOPK])
        with ExitStack() as split_ctx:
            parts = split_ctx.enter_context(buffer(nc, "h_parts", [P, 2, KD, S], F32R))
            with weight_ring(nc, A["peer_wq"]) as (ring, w, load, ahead):
                norm_transpose(nc, chip, RMS_EPS, A["norm2_row"], parts, keep=h2, ahead=ahead)
                expert_scores(nc, chip, A, parts, scores, idx, gate, iota, ring, w, load)
        experts(nc, chip, A, h2, scores, idx, gate, iota)


MH, QN, QR, VH = 8, 64, 32, 64
QK = QN + QR
DH, DV = 4, 128
GROUPS, GH = 3, 4
LAM_INIT = 0.8 - 0.6
MASK, DIST, DIL0, STRICT = 0, 1, 2, 5


def feature_projection(nc, chip, parts, weights, n_tiles, out_of, rows_of=lambda m: P):
    ring, w, load, _ = weights
    with ExitStack() as ctx:
        wp = split_weights(nc, ctx)
        with stage(nc, "large", "small", "product", "out_a", "out_v") as \
                (large, small, product, out_a, out_v):
            def w_parts(m):
                return wp[:, m % 2, 0], wp[:, m % 2, 1]

            with nc.Block() as block:
                @block.sync
                def _(sp):
                    for m in range(WRING, n_tiles):
                        sp.wait_ge(small, m - WRING + 1)
                        load(sp, m)

                @block.tensor
                def _(pe):
                    for m in range(n_tiles):
                        pe.wait_ge(small, m + 1)
                        if m >= 8:
                            pe.wait_ge(out_v if m % 2 else out_a, m // 2 - 3)
                        wide = w_parts(m)
                        for k in range(KD):
                            last = split_product(pe, chip.ps[:, m % 8, :], (wide[0][:, k, :], wide[1][:, k, :]),
                                                 (parts[:, 0, k, :], parts[:, 1, k, :]), k == 0, k == KD - 1)
                        last.then_inc(product, 1)

                @block.scalar
                def _(act):
                    for m in range(n_tiles + 1):
                        if m < n_tiles:
                            act.wait_ge(w[m % WRING], 16 * (m // WRING + 1))
                            if m >= 2:
                                act.wait_ge(product, m - 1)
                            large_part(act, w_parts(m), ring[:, m % WRING]).then_inc(large, 1)
                        if m % 2:
                            act.wait_ge(product, m)
                            act.activation(out_of(m - 1), chip.ps[0:rows_of(m - 1), (m - 1) % 8, :],
                                           ACT.Copy).then_inc(out_a, 1)
                    act.wait_ge(out_a, (n_tiles + 1) // 2)

                @block.vector
                def _(dve):
                    for m in range(n_tiles + 1):
                        if m < n_tiles:
                            dve.wait_ge(large, m + 1)
                            small_part(dve, w_parts(m), ring[:, m % WRING]).then_inc(small, 1)
                        if m and m % 2 == 0:
                            dve.wait_ge(product, m)
                            dve.tensor_copy(out_of(m - 1), chip.ps[0:rows_of(m - 1), (m - 1) % 8, :]).then_inc(out_v, 1)
                    dve.wait_ge(out_v, n_tiles // 2)


class Unit:

    def __init__(self, q, k, bias, values, stat):
        self.q, self.k, self.bias, self.values, self.stat = q, k, bias, values, stat
        self.width = k.shape[1]


def attend(nc, chip, units, scale, width, dst_of, low, total):
    N, G = len(units), 512 // width if len(units) % (512 // width) == 0 else 256 // width
    with ExitStack() as ctx:
        sb = lambda name, shape: ctx.enter_context(buffer(nc, name, shape, F32))
        neg = sb("neg_logits", [P, 3, S])
        prob = sb("probs", [P, 3, S])
        probT = sb("probsT", [P, 2, S])
        with stage(nc, "scored", "masked", "exped", "turned", "turned_out", "weighted", "kept") as \
                (scored, masked, exped, turned, turned_out, weighted, kept):
            with nc.Block() as block:
                @block.tensor
                def _(pe):
                    for n in range(N + 3):
                        if n < N:
                            u = units[n]
                            if n >= 3:
                                pe.wait_ge(masked, n - 2)
                            pe.matmul(chip.ps[:, n % 3, 0:u.width], u.q, u.k, start=True,
                                      stop=True).then_inc(scored, 1)
                        m = n - 2
                        if 0 <= m < N:
                            pe.wait_ge(exped, m + 1)
                            if m >= 2:
                                pe.wait_ge(turned_out, m - 1)
                            for j in range(units[m].width // P):
                                last = pe.transpose(chip.ps[:, 3 + m % 2, j * P:(j + 1) * P],
                                                    prob[:, m % 3, j * P:(j + 1) * P], chip.ident[:])
                            last.then_inc(turned, 1)
                        m = n - 3
                        if 0 <= m < N:
                            pe.wait_ge(turned_out, m + 1)
                            if m % G == 0 and m >= 2 * G:
                                pe.wait_ge(kept, m // G - 1)
                            vs = units[m].values
                            for j, v in enumerate(vs):
                                last = pe.matmul(chip.ps[:, 6 + m // G % 2, m % G * width:(m % G + 1) * width],
                                                 probT[:, m % 2, j * P:(j + 1) * P], v, start=j == 0,
                                                 stop=j == len(vs) - 1)
                            last.then_inc(weighted, 1)

                @block.vector
                def _(dve):
                    for n in range(N + 2):
                        if n < N:
                            u = units[n]
                            dve.wait_ge(scored, n + 1)
                            if n >= 3:
                                dve.wait_ge(exped, n - 2)
                            dve.tensor_tensor_reduce(neg[:, n % 3, 0:u.width], chip.ps[:, n % 3, 0:u.width], u.bias,
                                                     -scale, 3e38, ALU.add, ALU.min,
                                                     low[:, u.stat:u.stat + 1]).then_inc(masked, 1)
                        m = n - 2
                        if 0 <= m < N:
                            w = units[m].width
                            dve.wait_ge(turned, m + 1)
                            if m >= 2:
                                dve.wait_ge(weighted, m - 1)
                            dve.tensor_copy(probT[:, m % 2, 0:w], chip.ps[:, 3 + m % 2, 0:w]).then_inc(turned_out, 1)

                @block.scalar
                def _(act):
                    for n in range(N + 4):
                        if n < N:
                            u = units[n]
                            act.wait_ge(masked, n + 1)
                            if n >= 3:
                                act.wait_ge(turned, n - 2)
                            act.activation(prob[:, n % 3, 0:u.width], neg[:, n % 3, 0:u.width], ACT.Exp, scale=-1.0,
                                           bias=low[:, u.stat:u.stat + 1],
                                           accum_out=total[:, u.stat:u.stat + 1]).then_inc(exped, 1)
                        m = n - 4
                        if m >= 0 and m % G == G - 1:
                            act.wait_ge(weighted, m + 1)
                            act.activation(dst_of(m // G), chip.ps[:, 6 + m // G % 2, 0:G * width],
                                           ACT.Copy).then_inc(kept, 1)
                    act.wait_ge(kept, N // G)


def turn_tokens(nc, chip, src_of, n_tiles, dst_of, gain_of, ahead=None):
    with stage(nc, "turned", "out_a", "out_v") as (turned, out_a, out_v):
        with nc.Block() as block:
            @block.sync
            def _(sp):
                if ahead is not None:
                    ahead(sp)

            @block.tensor
            def _(pe):
                for n in range(n_tiles):
                    for t in range(TT):
                        last = pe.transpose(chip.ps[:, n % 8, t * P:(t + 1) * P], src_of(n, t), chip.ident[:])
                    last.then_inc(turned, 1)

            @block.scalar
            def _(act):
                for n in range(0, n_tiles, 2):
                    act.wait_ge(turned, n + 1)
                    g = gain_of(n)
                    act.activation(dst_of(n), chip.ps[:, n % 8, :], ACT.Copy, scale=1.0 if g is None else g)\
                        .then_inc(out_a, 1)
                act.wait_ge(out_a, (n_tiles + 1) // 2)

            @block.vector
            def _(dve):
                for n in range(1, n_tiles, 2):
                    dve.wait_ge(turned, n + 1)
                    g = gain_of(n)
                    dve.tensor_scalar(dst_of(n), chip.ps[:, n % 8, :], 1.0 if g is None else g, None,
                                      ALU.mult).then_inc(out_v, 1)
                dve.wait_ge(out_v, n_tiles // 2)


def even_mixer(nc, chip, A):
    with row_ring(nc, lambda k: of_rows(A["ev_w_out"], k)) as ring:
        _even_heads(nc, chip, A, ring[-1])
        stream_product(nc, chip, ring, KD, x_of=lambda k: of_tiles(chip.hT, k), norm_row=A["ev_post_row"])


def _even_heads(nc, chip, A, ahead):
    with ExitStack() as ctx:
        sb = lambda name, shape, c=ctx: c.enter_context(buffer(nc, name, shape, F32))
        ocat = sb("ev_out", [P, TT, D])
        low, total = sb("ev_low", [P, 64]), sb("ev_total", [P, 64])
        lam = sb("ev_lam", [P, 4])
        tables = sb("ev_tables", [P, 2, S])
        dqT, dkT, dv = sb("dqT", [P, DH, S]), sb("dkT", [P, DH, S]), sb("dv", [P, TT, DH * DV])
        with ExitStack() as mla:
            c_tok = sb("c_tok", [P, TT, 384], mla)
            krT = sb("krT", [32, 2, S], mla)
            with ExitStack() as split_ctx:
                parts = split_ctx.enter_context(buffer(nc, "h_parts", [P, 2, KD, S], F32R))
                with weight_ring(nc, A["ev_w_qk"]) as next_ring:
                    with row_ring(nc, lambda k: A["ev_w_tok"][k], 896) as rows_in:
                        norm_transpose(nc, chip, NORM_EPS, A["ev_pre_row"], parts, ahead=rows_in[-1])
                        stream_product(nc, chip, rows_in, KD, ((0, 384), (384, 896)), parts=parts,
                                       out_of=lambda t, half: dv[:, t, :] if half else c_tok[:, t, :],
                                       ahead=next_ring[-1])
                    feature_projection(nc, chip, parts, next_ring, 10,
                                       lambda m: (dqT, dkT)[m // 4][:, m % 4, :] if m < 8 else krT[:, m - 8, :],
                                       lambda m: P if m < 8 else 32)
            _mla(nc, chip, A, mla, c_tok, krT, ocat, low, total, tables, lam)
        _diff(nc, chip, dqT, dkT, dv, ocat, low, total, tables, lam)
        turn_tokens(nc, chip, lambda n, t: ocat[:, t, n * P:(n + 1) * P], KD, lambda n: chip.hT[:, n, :],
                    lambda n: None if n < 4 else lam[:, 3:4], ahead)


def _mla(nc, chip, A, ctx, c_tok, krT, ocat, low, total, tables, lam):
    sb = lambda name, shape, c=ctx: c.enter_context(buffer(nc, name, shape, F32))
    cT = sb("cT", [P, 3, S])
    v = sb("mla_v", [P, TT, MH * VH])
    qT, kT = sb("mla_qT", [QK, MH, S]), sb("mla_kT", [QK, MH, S])
    with ExitStack() as own:
        wuq = sb("w_uq", [P, 2, MH * QK], own)
        wus = sb("w_uq_swapped", [P, 2, MH * QR], own)
        wuk = sb("w_uk", [P, MH * QK], own)
        wuv = sb("w_uv", [P, MH * VH], own)
        rot = sb("rope_tables", [QR, 2, S], own)
        turn = sb("rope_turn", [QR, 2, S], own)
        kr = sb("rope_k", [QR, S], own)
        st = sb("c_stats", [P, 4, 2 * TT], own)
        junk = sb("c_junk", [P, 256], own)
        lv = sb("lam_vectors", [P, 4 * HS], own)
        lj = sb("lam_products", [P, HS], own)
        with stage(nc, "loaded", "squares", "mean_ready", "root_ready", "v_step", "lam_dots", "lam_exps") as \
                (loaded, squares, mean_ready, root_ready, v_step, lam_dots, lam_exps):
            with nc.Block() as block:
                @block.sync
                def _(sp):
                    sp.dma_start(lv[:], A["ev_lam"].partition_broadcast(P)).then_inc(loaded, 16)
                    sp.dma_start(tables[:], A["tables"][:, MASK:DIST + 1, :]).then_inc(loaded, 16)
                    sp.wait_ge(loaded, 32)

                @block.scalar
                def _(act):
                    for t in range(TT):
                        for part in range(2):
                            n = 2 * t + part
                            if n:
                                act.wait_ge(squares, n)
                            sl = slice(0, 256) if part == 0 else slice(256, 384)
                            act.activation(junk[:, 0:sl.stop - sl.start], c_tok[:, t, sl], ACT.Square,
                                           accum_out=st[:, 0, part * TT + t:part * TT + t + 1]).then_inc(squares, 1)
                    act.wait_ge(mean_ready, 2)
                    act.activation(st[:, 2, :], st[:, 1, :], ACT.Sqrt).then_inc(root_ready, 1)
                    act.wait_ge(lam_dots, 2)
                    act.activation(lam[:, 1:3], lam[:, 1:3], ACT.Exp).then_inc(lam_exps, 1)

                @block.vector
                def _(dve):
                    done = Steps(dve, v_step)
                    dve.wait_ge(squares, 2 * TT)
                    for part, n in ((0, 256), (1, 128)):
                        r = slice(part * TT, (part + 1) * TT)
                        dve.tensor_scalar(st[:, 1, r], st[:, 0, r], 1.0 / n, NORM_EPS, ALU.mult,
                                          ALU.add).then_inc(mean_ready, 1)
                    dve.wait_ge(root_ready, 1)
                    done(dve.reciprocal(st[:, 3, :], st[:, 2, :]))
                    done.wait()
                    for t in range(TT):
                        for part, sl in ((0, slice(0, 256)), (1, slice(256, 384))):
                            done(dve.tensor_scalar(c_tok[:, t, sl], c_tok[:, t, sl],
                                                   st[:, 3, part * TT + t:part * TT + t + 1], None, ALU.mult))
                    dve.wait_ge(loaded, 32)
                    for j in range(2):
                        a, c = lv[:, 2 * j * HS:(2 * j + 1) * HS], lv[:, (2 * j + 1) * HS:(2 * j + 2) * HS]
                        if j:
                            dve.wait_ge(lam_dots, j)
                        dve.tensor_tensor_reduce(lj[:], a, c, 1.0, 0.0, ALU.mult, ALU.add,
                                                 lam[:, 1 + j:2 + j]).then_inc(lam_dots, 1)
                    dve.wait_ge(lam_exps, 1)
                    done(dve.tensor_tensor(lam[:, 0:1], lam[:, 2:3], lam[:, 1:2], ALU.subtract))
                    done.wait()
                    done(dve.tensor_scalar(lam[:, 0:1], lam[:, 0:1], LAM_INIT, None, ALU.subtract))
                    done(dve.tensor_scalar(lam[:, 3:4], chip.col("subln_g"), 1.0 - LAM_INIT, None, ALU.mult))
                    done.wait()
        turn_tokens(nc, chip, lambda n, t: c_tok[:, t, n * P:(n + 1) * P], 3, lambda n: cT[:, n, :],
                    lambda n: chip.col("cq_g", n) if n < 2 else chip.col("ckv_g"))
        with stage(nc, "loaded", "product", "copied", "v_step", "key_turned", "values_out") as \
                (loaded, product, copied, v_step, key_turned, values_out):
            with nc.Block() as block:
                @block.sync
                def _(sp):
                    for dst, src in ((wuq, "ev_w_uq"), (wus, "ev_w_us"), (wuk, "ev_w_uk"), (wuv, "ev_w_uv"), (rot, "rope")):
                        sp.dma_start(dst[:], A[src]).then_inc(loaded, 16)

                @block.tensor
                def _(pe):
                    pe.wait_ge(loaded, 80)
                    for m in range(2):
                        for k in range(2):
                            pe.matmul(chip.ps[:, 3 * m + 1, :], wus[:, k, m * P:(m + 1) * P], cT[:, k, :],
                                      start=k == 0, stop=k == 1)
                    for h in range(MH):
                        if h >= 2:
                            pe.wait_ge(copied, 3 * (h - 1))
                        b0 = h % 2 * 3
                        for k in range(2):
                            pe.matmul(chip.ps[0:QK, b0, :], wuq[:, k, h * QK:(h + 1) * QK], cT[:, k, :],
                                      start=k == 0, stop=k == 1)
                        pe.matmul(chip.ps[0:QK, b0 + 2, :], wuk[:, h * QK:(h + 1) * QK], cT[:, 2, :], start=True,
                                  stop=True).then_inc(product, 1)
                    for t in range(TT):
                        if t >= 2:
                            pe.wait_ge(values_out, t - 1)
                        pe.matmul(chip.ps[:, 6 + t % 2, :], cT[:, 2, t * P:(t + 1) * P], wuv[:], start=True,
                                  stop=True).then_inc(product, 1)

                @block.scalar
                def _(act):
                    for h in range(MH):
                        act.wait_ge(product, h + 1)
                        b0 = h % 2 * 3
                        act.activation(qT[:, h, :], chip.ps[0:QK, b0, :], ACT.Copy).then_inc(copied, 1)
                        act.activation(kT[:, h, :], chip.ps[0:QK, b0 + 2, :], ACT.Copy).then_inc(copied, 1)
                        if h >= 2:
                            act.wait_ge(v_step, 3 * (h - 1) + 3)
                        act.activation(turn[:, h % 2, :], chip.ps[h % 4 * QR:(h % 4 + 1) * QR, h // 4 * 3 + 1, :],
                                       ACT.Copy).then_inc(copied, 1)
                    for t in range(TT):
                        act.wait_ge(product, MH + t + 1)
                        act.activation(v[:, t, :], chip.ps[:, 6 + t % 2, :], ACT.Copy).then_inc(values_out, 1)
                    act.wait_ge(values_out, TT)

                @block.vector
                def _(dve):
                    done = Steps(dve, v_step)
                    dve.wait_ge(loaded, 80)
                    done(dve.tensor_tensor(krT[:, 0, :], krT[:, 0, :], rot[:, 0, :], ALU.mult))
                    done(dve.tensor_tensor(krT[:, 1, :], krT[:, 1, :], rot[:, 1, :], ALU.mult))
                    done.wait()
                    done(dve.tensor_tensor(kr[:], krT[:, 0, :], krT[:, 1, :], ALU.add))
                    for h in range(MH):
                        dve.wait_ge(copied, 3 * h + 3)
                        if h == 0:
                            done.wait()
                        done(dve.tensor_tensor(turn[:, h % 2, :], turn[:, h % 2, :], rot[:, 1, :], ALU.mult))
                        done(dve.tensor_tensor(qT[0:QR, h, :], qT[0:QR, h, :], rot[:, 0, :], ALU.mult))
                        done.wait()
                        done(dve.tensor_tensor(qT[0:QR, h, :], qT[0:QR, h, :], turn[:, h % 2, :], ALU.add))
                        dve.tensor_copy(kT[0:QR, h, :], kr[:]).then_inc(key_turned, 1)
                    done.wait()
                    dve.wait_ge(key_turned, MH)
    units = []
    for i in range(TT):
        w = (i + 1) * P
        for h in range(MH):
            units.append(Unit(qT[:, h, i * P:(i + 1) * P], kT[:, h, 0:w], tables[:, MASK, S - w:S],
                              [v[:, j, h * VH:(h + 1) * VH] for j in range(i + 1)], i * MH + h))
    attend(nc, chip, units, QK ** -0.5, VH, lambda g: ocat[:, g, 0:512], low, total)
    with stage(nc, "v_step") as (v_step,):
        with nc.Block() as block:
            @block.vector
            def _(dve):
                done = Steps(dve, v_step)
                done(dve.reciprocal(total[:, 0:TT * MH], total[:, 0:TT * MH]))
                done.wait()
                for t in range(TT):
                    o = ocat[:, t, 0:512].rearrange("p (h v) -> p h v", h=MH)
                    done(dve.tensor_tensor(o, o, total[:, t * MH:(t + 1) * MH].rearrange("p (h o) -> p h o", o=1)
                                           .to_broadcast([P, MH, VH]), ALU.mult))
                done.wait()


def _diff(nc, chip, dqT, dkT, dv, ocat, low, total, tables, lam):
    with ExitStack() as ctx:
        sb = lambda name, shape: ctx.enter_context(buffer(nc, name, shape, F32))
        bias = sb("diff_bias", [P, DH, S])
        o = sb("diff_o", [P, 2, TT, DH * DV])
        st = sb("diff_stats", [P, 4, TT * DH])
        scale = HS ** -0.5
        with stage(nc, "biased") as (biased,):
            with nc.Block() as block:
                @block.vector
                def _(dve):
                    for h in range(DH):
                        slope = 2.0 ** (-8.0 * (h + 1) / DH)
                        dve.tensor_scalar(bias[:, h, :], tables[:, DIST, :], -slope / scale, None,
                                          ALU.mult).then_inc(biased, 1)
                    dve.wait_ge(biased, DH)
        units = []
        for i in range(TT):
            w = (i + 1) * P
            for s_ in range(2):
                r = slice(s_ * HS, (s_ + 1) * HS)
                for h in range(DH):
                    units.append(Unit(dqT[r, h, i * P:(i + 1) * P], dkT[r, h, 0:w], bias[:, h, S - w:S],
                                      [dv[:, j, h * DV:(h + 1) * DV] for j in range(i + 1)],
                                      s_ * TT * DH + i * DH + h))
        attend(nc, chip, units, scale, DV, lambda g: o[:, g % 2, g // 2, :], low, total)
        n = TT * DH
        with stage(nc, "v_step", "mean_ready", "root_ready") as (v_step, mean_ready, root_ready):
            with nc.Block() as block:
                @block.scalar
                def _(act):
                    act.wait_ge(mean_ready, 1)
                    act.activation(st[:, 2, :], st[:, 1, :], ACT.Sqrt).then_inc(root_ready, 1)

                @block.vector
                def _(dve):
                    done = Steps(dve, v_step)
                    flat = lambda s_: o[:, s_].rearrange("p t (h v) -> p (t h) v", v=DV)
                    wide = lambda ap: ap.rearrange("p (n o) -> p n o", o=1).to_broadcast([P, n, DV])
                    done(dve.reciprocal(total[:, 0:2 * n], total[:, 0:2 * n]))
                    done.wait()
                    done(dve.tensor_scalar(total[:, n:2 * n], total[:, n:2 * n], lam[:, 0:1], None, ALU.mult))
                    done(dve.tensor_tensor(flat(0), flat(0), wide(total[:, 0:n]), ALU.mult))
                    done.wait()
                    done(dve.tensor_tensor(flat(1), flat(1), wide(total[:, n:2 * n]), ALU.mult))
                    done.wait()
                    done(dve.tensor_tensor(flat(0), flat(0), flat(1), ALU.add))
                    done.wait()
                    done(dve.tensor_tensor(flat(1), flat(0), flat(0), ALU.mult))
                    done.wait()
                    done(dve.tensor_reduce(st[:, 0, :], flat(1), AX.X, ALU.add))
                    done.wait()
                    dve.tensor_scalar(st[:, 1, :], st[:, 0, :], 1.0 / DV, NORM_EPS, ALU.mult,
                                      ALU.add).then_inc(mean_ready, 1)
                    dve.wait_ge(root_ready, 1)
                    done(dve.reciprocal(st[:, 3, :], st[:, 2, :]))
                    done.wait()
                    for t in range(TT):
                        done(dve.tensor_tensor(
                            ocat[:, t, 512:1024].rearrange("p (h v) -> p h v", v=DV), flat(0)[:, t * DH:(t + 1) * DH],
                            wide(st[:, 3, :])[:, t * DH:(t + 1) * DH], ALU.mult))
                    done.wait()


ND = GROUPS * GH


def odd_mixer(nc, chip, A):
    with row_ring(nc, lambda k: of_rows(A["od_w_out"], k)) as ring:
        _odd_heads(nc, chip, A, ring[-1])
        stream_product(nc, chip, ring, 4, x_of=lambda k: of_tiles(chip.hT, k), norm_row=A["od_post_row"])


def _odd_heads(nc, chip, A, ahead):
    with ExitStack() as ctx:
        sb = lambda name, shape, c=ctx: c.enter_context(buffer(nc, name, shape, F32))
        ocat = sb("od_out", [P, TT, 512])
        v = sb("od_v", [P, TT, D])
        qk = sb("od_qk", [P, 16, S])
        with ExitStack() as split_ctx:
            parts = split_ctx.enter_context(buffer(nc, "h_parts", [P, 2, KD, S], F32R))
            with weight_ring(nc, A["od_w_qk"]) as next_ring:
                with row_ring(nc, lambda k: A["od_w_v"][k]) as rows_in:
                    norm_transpose(nc, chip, NORM_EPS, A["od_pre_row"], parts, ahead=rows_in[-1])
                    stream_product(nc, chip, rows_in, KD, parts=parts, ahead=next_ring[-1],
                                   out_of=lambda t, half: v[:, t, half * 512:(half + 1) * 512],
                                   pieces=[(0, 256, in_order), (256, 512, by_4), (512, 768, by_4),
                                           (768, 1024, in_order)])
                feature_projection(nc, chip, parts, next_ring, 16, lambda m: qk[:, m, :])
        o = sb("dil_o", [P, TT, ND * HS])
        stats = sb("dil_stats", [P, TT, ND, 2])
        _dilated(nc, chip, A, qk, v, o, stats)
        _stick(nc, chip, A, qk, v, ocat, o, stats)
        _dilated_sum(nc, chip, o, stats, ocat)
        turn_tokens(nc, chip, lambda n, t: ocat[:, t, n * P:(n + 1) * P], 4, lambda n: chip.hT[:, n, :],
                    lambda n: None, ahead)


def _dilated(nc, chip, A, qk, v, o, stats):
    with ExitStack() as ctx:
        sb = lambda name, shape: ctx.enter_context(buffer(nc, name, shape, F32))
        near = sb("dil_near_bias", [P, GH, 2 * P])
        apart = sb("dil_apart_bias", [P, ND - GH, P])
        tables = sb("dil_tables", [P, GROUPS, S])
        scale = HS ** -0.5
        with stage(nc, "loaded", "biased") as (loaded, biased):
            with nc.Block() as block:
                @block.sync
                def _(sp):
                    sp.dma_start(tables[:], A["tables"][:, DIL0:DIL0 + GROUPS, :]).then_inc(loaded, 16)

                @block.vector
                def _(dve):
                    dve.wait_ge(loaded, 16)
                    for n in range(ND):
                        slope = 2.0 ** (-8.0 * (n + 1) / ND)
                        dst, src = (near[:, n, :], tables[:, 0, S - 2 * P:S]) if n < GH else \
                            (apart[:, n - GH, :], tables[:, n // GH, 0:P])
                        dve.tensor_scalar(dst, src, -slope / scale, None, ALU.mult).then_inc(biased, 1)
                    dve.wait_ge(biased, ND)
        units = []
        for i in range(TT):
            for n in range(ND):
                r = slice(n % 2 * HS, n % 2 * HS + HS)
                q, k, stat = qk[r, n // 2, :], qk[r, 6 + n // 2, :], (i * ND + n) * 2
                if n < GH:
                    first = max(0, i - 1)
                    w = (i + 1 - first) * P
                    units.append(Unit(q[:, i * P:(i + 1) * P], k[:, first * P:(i + 1) * P], near[:, n, 2 * P - w:2 * P],
                                      [v[:, j, n * HS:(n + 1) * HS] for j in range(first, i + 1)], stat))
                else:
                    units.append(Unit(by_4(q, i), by_4(k, i), apart[:, n - GH, :], [v[:, i, n * HS:(n + 1) * HS]], stat))
        flat, st = o[:].rearrange("p t n -> p (t n)"), stats[:].rearrange("p t n s -> p (t n s)")
        attend(nc, chip, units, scale, HS, lambda g: flat[:, g * 512:(g + 1) * 512], st, st[:, 1:])


def tokens_again(sp, A, o, stats, out_of, back):
    for buf, dram, n in ((o, A["dil_scratch"], HS), (stats, A["stat_scratch"], 2)):
        if buf is stats:
            buf = buf.rearrange("p t n s -> p t (n s)")
        sp.dma_start(dram.rearrange("(m t) f -> m t f", t=TT), buf[:, :, GH * n:3 * GH * n]).then_inc(out_of, 16)
    sp.wait_ge(out_of, 32)
    for buf, dram, n in ((o, A["dil_scratch"], HS), (stats, A["stat_scratch"], 2)):
        if buf is stats:
            buf = buf.rearrange("p t n s -> p t (n s)")
        sp.dma_start(buf[:, :, GH * n:3 * GH * n], dram.rearrange("(t p) f -> p t f", p=P)).then_inc(back, 16)
    sp.wait_ge(back, 32)


def _dilated_sum(nc, chip, o, stats, ocat):
    with ExitStack() as ctx:
        sb = lambda name, shape: ctx.enter_context(buffer(nc, name, shape, F32))
        wts = sb("dil_weights", [P, TT, ND])
        small = sb("dil_small", [P, 2, TT, GH])
        low, total = stats[:, :, :, 0], stats[:, :, :, 1]
        with stage(nc, "v_step", "apart", "exped") as (v_step, apart, exped):
            with nc.Block() as block:
                @block.vector
                def _(dve):
                    done = Steps(dve, v_step)
                    of = lambda ap, g: ap[:, :, g * GH:(g + 1) * GH]
                    lo, den = small[:, 0], small[:, 1]
                    done(dve.tensor_tensor(lo, of(low, 0), of(low, 1), ALU.min))
                    done.wait()
                    done(dve.tensor_tensor(lo, lo, of(low, 2), ALU.min))
                    done.wait()
                    for g in range(GROUPS):
                        dve.tensor_tensor(of(wts, g), lo, of(low, g), ALU.subtract).then_inc(apart, 1)
                    dve.wait_ge(exped, 1)
                    done(dve.tensor_tensor(total, total, wts[:], ALU.mult))
                    done.wait()
                    done(dve.tensor_tensor(den, of(total, 0), of(total, 1), ALU.add))
                    done.wait()
                    done(dve.tensor_tensor(den, den, of(total, 2), ALU.add))
                    done.wait()
                    done(dve.reciprocal(den, den))
                    done.wait()
                    for g in range(GROUPS):
                        done(dve.tensor_tensor(of(wts, g), of(wts, g), den, ALU.mult))
                    done.wait()
                    for t in range(TT):
                        ot = o[:, t].rearrange("p (n v) -> p n v", v=HS)
                        done(dve.tensor_tensor(ot, ot, wts[:, t].rearrange("p (n o) -> p n o", o=1)
                                               .to_broadcast([P, ND, HS]), ALU.mult))
                    done.wait()
                    q = GH * HS
                    done(dve.tensor_tensor(ocat[:, :, 0:q], o[:, :, 0:q], o[:, :, q:2 * q], ALU.add))
                    done.wait()
                    done(dve.tensor_tensor(ocat[:, :, 0:q], ocat[:, :, 0:q], o[:, :, 2 * q:3 * q], ALU.add))
                    done.wait()

                @block.scalar
                def _(act):
                    act.wait_ge(apart, GROUPS)
                    act.activation(wts[:], wts[:], ACT.Exp).then_inc(exped, 1)


def _stick(nc, chip, A, qk, v, ocat, o, stats):
    units = [(i, pair) for i in range(TT)[::-1] for pair in range(2)]
    N = len(units)
    with ExitStack() as ctx:
        sb = lambda name, shape: ctx.enter_context(buffer(nc, name, shape, F32))
        strict = sb("strict_table", [P, 1, S])
        ones = sb("stick_ones", [P, S])
        z, mag, keep, after = (sb("stick_" + n, [P, 2, 2, S]) for n in ("z", "mag", "keep", "after"))
        probT = sb("stick_pT", [P, 2, S])
        scale = HS ** -0.5
        with stage(nc, "loaded", "scored", "z_out", "logged", "a_step", "v_step", "arg_ready", "a_exped", "masked",
                   "turned", "turned_out", "weighted", "kept", "put_down", "back") as \
                (loaded, scored, z_out, logged, a_step, v_step, arg_ready, a_exped, masked, turned, turned_out,
                 weighted, kept, put_down, back):
            with nc.Block() as block:
                @block.sync
                def _(sp):
                    sp.dma_start(strict[:], A["tables"][:, STRICT:STRICT + 1, :]).then_inc(loaded, 16)
                    tokens_again(sp, A, o[:], stats[:], put_down, back)

                @block.tensor
                def _(pe):
                    def logits(u):
                        i, pair = units[u]
                        w = (i + 1) * P
                        if u >= 2:
                            pe.wait_ge(z_out, u - 1)
                        for h in range(2):
                            r = slice(h * HS, h * HS + HS)
                            last = pe.matmul(chip.ps[:, u % 2 * 2 + h, 0:w], qk[r, 12 + pair, i * P:(i + 1) * P],
                                             qk[r, 14 + pair, 0:w], start=True, stop=True)
                        last.then_inc(scored, 1)

                    def turn(u, h):
                        n = 2 * u + h
                        if n >= 2:
                            pe.wait_ge(turned_out, n - 1)
                        for j in range(units[u][0] + 1):
                            last = pe.transpose(chip.ps[:, 4 + n % 2, j * P:(j + 1) * P],
                                                z[:, u % 2, h, j * P:(j + 1) * P], chip.ident[:])
                        last.then_inc(turned, 1)

                    def weigh(u, h):
                        n, (i, pair) = 2 * u + h, units[u]
                        pe.wait_ge(turned_out, n + 1)
                        if pair == 0 and h == 0 and u >= 4:
                            pe.wait_ge(kept, u // 2 - 1)
                        at = ND * HS + (2 * pair + h) * HS
                        for j in range(i + 1):
                            last = pe.matmul(chip.ps[:, 6 + i % 2, (2 * pair + h) * HS:(2 * pair + h + 1) * HS],
                                             probT[:, n % 2, j * P:(j + 1) * P], v[:, j, at:at + HS],
                                             start=j == 0, stop=j == i)
                        last.then_inc(weighted, 1)

                    logits(0)
                    logits(1)
                    for u in range(N):
                        pe.wait_ge(masked, u + 1)
                        turn(u, 0)
                        turn(u, 1)
                        if u + 2 < N:
                            logits(u + 2)
                        weigh(u, 0)
                        weigh(u, 1)

                @block.scalar
                def _(act):
                    step = Steps(act, a_step)

                    def take_logits(u):
                        w = (units[u][0] + 1) * P
                        act.wait_ge(scored, u + 1)
                        if u >= 2:
                            act.wait_ge(turned, 2 * (u - 1))
                        ps = chip.ps[:, u % 2 * 2:u % 2 * 2 + 2, 0:w]
                        m = mag[:, u % 2, :, 0:w]
                        step(act.activation(m, ps, ACT.Abs, scale=scale))
                        act.activation(z[:, u % 2, :, 0:w], ps, ACT.Copy, scale=scale).then_inc(z_out, 1)
                        step.wait()
                        step(act.activation(m, m, ACT.Exp, scale=-1.0))
                        step.wait()
                        act.activation(m, m, ACT.Ln, bias=1.0).then_inc(logged, 1)

                    take_logits(0)
                    take_logits(1)
                    for u in range(N):
                        i, pair = units[u]
                        w = (i + 1) * P
                        act.wait_ge(arg_ready, u + 1)
                        act.activation(z[:, u % 2, :, 0:w], z[:, u % 2, :, 0:w], ACT.Exp).then_inc(a_exped, 1)
                        if pair == 0 and u:
                            act.wait_ge(weighted, 2 * u)
                            act.activation(ocat[:, i + 1, 256:512], chip.ps[:, 6 + (i + 1) % 2, 0:256],
                                           ACT.Copy).then_inc(kept, 1)
                        if u + 2 < N:
                            take_logits(u + 2)
                    act.wait_ge(weighted, 2 * N)
                    act.activation(ocat[:, 0, 256:512], chip.ps[:, 6, 0:256], ACT.Copy).then_inc(kept, 1)
                    act.wait_ge(kept, TT)

                @block.vector
                def _(dve):
                    done = Steps(dve, v_step)

                    def argument(u):
                        w = (units[u][0] + 1) * P
                        zz, mm, kk, aa = (t[:, u % 2, :, 0:w] for t in (z, mag, keep, after))
                        own = strict[:, :, S - w:S].to_broadcast([P, 2, w])
                        dve.wait_ge(logged, u + 1)
                        dve.wait_ge(z_out, u + 1)
                        done(dve.scalar_tensor_tensor(out=mm, in0=zz, scalar=0.0, in1=mm, op0=ALU.max, op1=ALU.add))
                        done.wait()
                        done(dve.tensor_tensor(kk, mm, own, ALU.mult))
                        done(dve.tensor_tensor(zz, zz, mm, ALU.subtract))
                        done.wait()
                        for h in range(2):
                            done(dve.tensor_tensor_scan(after[:, u % 2, h, 0:w][:, ::-1], ones[:, 0:w],
                                                        keep[:, u % 2, h, 0:w][:, ::-1], 0.0, ALU.mult, ALU.add))
                        done(dve.tensor_tensor(zz, zz, kk, ALU.add))
                        done.wait()
                        dve.tensor_tensor(zz, zz, aa, ALU.subtract).then_inc(arg_ready, 1)

                    done(dve.memset(ones[:], 1.0))
                    dve.wait_ge(loaded, 16)
                    argument(0)
                    for u in range(N):
                        w = (units[u][0] + 1) * P
                        zz = z[:, u % 2, :, 0:w]
                        dve.wait_ge(a_exped, u + 1)
                        dve.tensor_tensor(zz, zz, strict[:, :, S - w:S].to_broadcast([P, 2, w]),
                                          ALU.mult).then_inc(masked, 1)
                        if u + 1 < N:
                            argument(u + 1)
                        for h in range(2):
                            n = 2 * u + h
                            dve.wait_ge(turned, n + 1)
                            if n >= 2:
                                dve.wait_ge(weighted, n - 1)
                            dve.tensor_copy(probT[:, n % 2, 0:w], chip.ps[:, 4 + n % 2, 0:w]).then_inc(turned_out, 1)


FF = 2816
FT = FF // P
WPAIR = 2


def conv_ffn(nc, chip, A, layer, store=None):
    with ExitStack() as ctx:
        hid = ctx.enter_context(buffer(nc, "hiddenT", [P, FT, S], F32))
        down = ctx.enter_context(row_ring(nc, lambda k: of_rows(A["ffn_w_down"][layer], k)))
        with ExitStack() as split_ctx:
            parts = split_ctx.enter_context(buffer(nc, "h_parts", [P, 2, KD, S], F32R))
            ring = split_ctx.enter_context(buffer(nc, "up_ring", [P, WPAIR, 2, KD, P], F32))
            with stage(nc, "w0", "w1") as w:
                def load(sp, i, j):
                    sp.dma_start(ring[:, j], A["ffn_w_up"][layer, bass.ds(i * WPAIR + j, 1)]
                                 .rearrange("o p s k n -> p (o s) k n")).then_inc(w[j], 16)

                norm_transpose(nc, chip, NORM_EPS, A["ffn_pre_rows"][layer], parts,
                               ahead=lambda sp: [load(sp, 0, j) for j in range(WPAIR)])
                _ffn_up(nc, chip, layer, parts, hid, ring, w, load, down[-1])
        stream_product(nc, chip, down, FT, x_of=lambda k: of_tiles(hid, k), norm_row=A["ffn_post_rows"][layer],
                       store=store)


def _ffn_up(nc, chip, layer, parts, hid, ring, w, load, ahead):
    with ExitStack() as ctx:
        sb = lambda name, shape, dt=F32: ctx.enter_context(buffer(nc, name, shape, dt))
        wp = sb("up_parts", [P, WPAIR, 2, 2, KD, P], F32R)
        conv = sb("conv", [P, WPAIR, 2, S])
        with stage(nc, "large", "small", "product", "centre", "one_back", "two_back", "gated", "hidden") as \
                (large, small, product, centre, one_back, two_back, gated, hidden):
            turns = FT // WPAIR

            def tap(side, f, back):
                return chip.cols[:, bass.ds(f + (COLS["conv_w"][0] + (3 * layer + 2 - back) * 2 * FT + side * FT), 1)]

            def w_parts(j):
                return wp[:, j, 0], wp[:, j, 1]

            with nc.Block() as block:
                @block.sync
                def _(sp):
                    with sp.Fori(1, turns) as i:
                        for j in range(WPAIR):
                            sp.wait_ge(small, i * WPAIR + (j + 1 - WPAIR))
                            load(sp, i, j)
                    ahead(sp)

                @block.tensor
                def _(pe):
                    def products(i, first=False):
                        for j in range(WPAIR):
                            pe.wait_ge(small, i * WPAIR + (j + 1))
                            if not first:
                                pe.wait_ge(two_back, i * 2 * WPAIR + (2 * j + 2 - 2 * WPAIR))
                            wide = w_parts(j)
                            for side in range(2):
                                for k in range(KD):
                                    last = split_product(pe, chip.ps[:, 2 * j + side, :],
                                                         (wide[0][:, side, k, :], wide[1][:, side, k, :]),
                                                         (parts[:, 0, k, :], parts[:, 1, k, :]), k == 0, k == KD - 1)
                                last.then_inc(product, 1)

                    products(0, True)
                    with pe.Fori(1, turns) as i:
                        products(i)

                @block.scalar
                def _(act):
                    def split(i, j, first=False):
                        act.wait_ge(w[j], i * 16 + 16)
                        if not first:
                            act.wait_ge(product, i * 2 * WPAIR + (2 * j + 2 - 2 * WPAIR))
                        large_part(act, w_parts(j), ring[:, j]).then_inc(large, 1)

                    def centre_and_gate(i, j, first=False):
                        f = i * WPAIR + (j - WPAIR)
                        if not first:
                            act.wait_ge(hidden, i * WPAIR + (j + 1 - 2 * WPAIR))
                        for side in range(2):
                            act.wait_ge(product, i * 2 * WPAIR + (2 * j + side + 1 - 2 * WPAIR))
                            act.activation(conv[:, j, side, :], chip.ps[:, 2 * j + side, :], ACT.Identity,
                                           scale=tap(side, f, 0),
                                           bias=chip.cols[:, bass.ds(f + (COLS["conv_b"][0] + layer * 2 * FT
                                                                          + side * FT), 1)]).then_inc(centre, 1)
                        act.wait_ge(two_back, i * 2 * WPAIR + (2 * j + 1 - 2 * WPAIR))
                        act.activation(conv[:, j, 0, :], conv[:, j, 0, :], ACT.Silu).then_inc(gated, 1)

                    for j in range(WPAIR):
                        split(0, j, True)
                    for j in range(WPAIR):
                        split(1, j)
                        centre_and_gate(1, j, True)
                    with act.Fori(2, turns) as i:
                        for j in range(WPAIR):
                            split(i, j)
                            centre_and_gate(i, j)
                    for j in range(WPAIR):
                        centre_and_gate(turns, j)

                @block.vector
                def _(dve):
                    def split(i, j):
                        dve.wait_ge(large, i * WPAIR + (j + 1))
                        small_part(dve, w_parts(j), ring[:, j]).then_inc(small, 1)

                    def taps_and_product(i, j):
                        f = i * WPAIR + (j - WPAIR)
                        for side in range(2):
                            c, ps = conv[:, j, side, :], chip.ps[:, 2 * j + side, :]
                            dve.wait_ge(centre, i * 2 * WPAIR + (2 * j + side + 1 - 2 * WPAIR))
                            dve.scalar_tensor_tensor(out=c[:, 1:S], in0=ps[:, 0:S - 1], scalar=tap(side, f, 1),
                                                     in1=c[:, 1:S], op0=ALU.mult, op1=ALU.add).then_inc(one_back, 1)
                            dve.wait_ge(one_back, i * 2 * WPAIR + (2 * j + side + 1 - 2 * WPAIR))
                            dve.scalar_tensor_tensor(out=c[:, 2:S], in0=ps[:, 0:S - 2], scalar=tap(side, f, 2),
                                                     in1=c[:, 2:S], op0=ALU.mult, op1=ALU.add).then_inc(two_back, 1)
                        dve.wait_ge(two_back, i * 2 * WPAIR + (2 * j + 2 - 2 * WPAIR))
                        dve.wait_ge(gated, i * WPAIR + (j + 1 - WPAIR))
                        dve.tensor_tensor(hid[:, bass.ds(f, 1), :].rearrange("p o s -> p (o s)"),
                                          conv[:, j, 0, :], conv[:, j, 1, :], ALU.mult).then_inc(hidden, 1)

                    for j in range(WPAIR):
                        split(0, j)
                    with dve.Fori(1, turns) as i:
                        for j in range(WPAIR):
                            split(i, j)
                            taps_and_product(i, j)
                    for j in range(WPAIR):
                        taps_and_product(turns, j)
                    dve.wait_ge(hidden, FT)


def build(nc, A, out):
    STAGES.clear()
    HELD.clear()
    with ExitStack() as ctx:
        chip = Chip(nc, ctx)
        load_constants(nc, chip, A)
        rwkv_block(nc, chip, A)
        expert_block(nc, chip, A)
        even_mixer(nc, chip, A)
        conv_ffn(nc, chip, A, 0)
        odd_mixer(nc, chip, A)
        conv_ffn(nc, chip, A, 1, store=out)
    clear_finished(nc)


def pack_columns(vectors):
    return np.concatenate([np.ascontiguousarray(v.reshape(-1, P).T) for v in vectors], axis=1)


def tiles_of_columns(w, widths):
    k = w.shape[0] // P
    out, at = np.zeros((len(widths), P, k, P), w.dtype), 0
    for i, n in enumerate(widths):
        out[i, :, :, :n] = w[:, at:at + n].reshape(k, P, n).transpose(1, 0, 2)
        at += n
    return out


def rows(w):
    return np.ascontiguousarray(w.reshape(-1, P, w.shape[1]).transpose(1, 0, 2))


def lay_out(i):
    f = lambda n: np.asarray(i[n])
    a = {}
    a["x"] = f("x")[0]
    in1 = [P] * 15 + [32] + [P] * 4
    a["w_in"] = tiles_of_columns(f("w_in")[0], in1)
    mu = np.zeros((2, SHIFTED * P), np.float32)
    mu[:, :1952] = f("shift_mu")[0]
    a["w_up"] = f("w_up")[0].reshape(P, RD)
    a["a_up"] = f("a_up")[0].reshape(P, RD)
    a["g_up"] = f("g_up")[0]
    a["pool_w"] = np.ascontiguousarray(f("pool_w")[0].transpose(1, 0, 2))
    inv = np.zeros((1, 4 * S), np.float32)
    t = np.arange(S)
    for g, win in enumerate((2, 4, 8, 16)):
        inv[0, g * S:(g + 1) * S] = 1.0 / (np.clip(t + win // 2, 0, S) - np.clip(t - win // 2, 0, S))
    a["pool_inv"] = inv
    a["w_out"] = f("w_out")[0].reshape(KD, P, D)
    a["peer_wq"] = tiles_of_columns(f("peer_wq")[0], [P] * 16)
    a["peer_keys"] = np.ascontiguousarray(f("peer_keys")[0].reshape(16, P, P).transpose(2, 0, 1))
    a["peer_u"], a["peer_v"] = f("peer_u")[0], f("peer_v")[0]
    a["norm1_row"], a["norm2_row"], a["norm_f_row"] = f("norm1_w")[0], f("norm2_w")[0], f("norm_f_w")
    a["cols"] = pack_columns([
        mu[0], mu[1], f("w0")[0], f("a0")[0], f("k_k")[0], f("k_a")[0], f("r_k")[0],
        f("ln_x_w")[0], f("ln_x_b")[0], f("pool_scale")[0], f("ev_cq_g_2")[0],
        f("ev_ckv_g_2")[0], f("ev_subln_g_2")[0],
        f("ffn_conv_w_2"), f("ffn_conv_b_2")])
    a.update(lay_out_attention(f))
    return a


def lay_out_attention(f):
    a = {}
    w = f("ev_w_in_2")[0]
    a["ev_w_tok"] = np.concatenate([w[:, 0:384], w[:, 416 + 1024:416 + 1536]], axis=1).reshape(KD, P, 896)
    a["ev_pre_row"], a["od_pre_row"], a["ffn_pre_rows"] = f("ev_pre_g_2")[0], f("od_pre_g_2")[0], f("ffn_pre_g_2")
    half = QR // 2
    swap = np.r_[half:QR, 0:half]
    kr = w[:, 384:416]
    a["ev_w_qk"] = tiles_of_columns(np.concatenate([w[:, 416:416 + 1024], kr, kr[:, swap]], axis=1), [P] * 8 + [32, 32])
    uq = f("ev_w_uq_2")[0].reshape(256, MH, QK)
    rope_cols = uq[:, :, QN:]
    a["ev_w_uq"] = rows(np.concatenate([rope_cols, uq[:, :, :QN]], axis=2).reshape(256, MH * QK))
    a["ev_w_us"] = rows(np.ascontiguousarray(rope_cols[:, :, swap]).reshape(256, MH * QR))
    ukv = f("ev_w_ukv_2")[0].reshape(P, MH, QN + VH)
    uk = np.zeros((P, MH, QK), np.float32)
    uk[:, :, QR:] = ukv[:, :, :QN]
    a["ev_w_uk"] = uk.reshape(P, MH * QK)
    a["ev_w_uv"] = np.ascontiguousarray(ukv[:, :, QN:]).reshape(P, MH * VH)
    a["ev_lam"] = np.concatenate([f(n)[0] for n in ("ev_lam_q1_2", "ev_lam_k1_2", "ev_lam_q2_2", "ev_lam_k2_2")])
    a["ev_w_out"] = f("ev_w_out_2")[0].reshape(KD, P, D)
    a["ev_post_row"] = f("ev_post_g_2")[0]
    w = f("od_w_in_2")[0]
    a["od_w_qk"] = tiles_of_columns(np.concatenate([w[:, 0:1536], w[:, 2304:2816]], axis=1), [P] * 16)
    a["od_w_v"] = np.concatenate([w[:, 1536:2304], w[:, 2816:3072]], axis=1).reshape(KD, P, D)
    a["od_w_out"] = f("od_w_out_2")[0].reshape(4, P, D)
    a["od_post_row"] = f("od_post_g_2")[0]
    up = f("ffn_w_up_2")
    a["ffn_w_up"] = np.ascontiguousarray(up.reshape(2, KD, P, 2, FT, P).transpose(0, 4, 2, 3, 1, 5))
    a["ffn_w_down"] = f("ffn_w_down_2").reshape(2, FT, P, D)
    a["ffn_post_rows"] = f("ffn_post_g_2")
    ang = (np.arange(S, dtype=np.float32)[None, :]
           * (np.float32(10000.0) ** (-np.arange(half, dtype=np.float32) / half))[:, None]).astype(np.float32)
    cos, sin = np.cos(ang), np.sin(ang)
    a["rope"] = np.stack([np.r_[cos, cos], np.r_[-sin, sin]], axis=1).astype(np.float32)
    dist = (np.arange(P)[:, None] + (S - P) - np.arange(S)[None, :]).astype(np.float32)
    far = np.float32(1e32)
    t = [np.where(dist >= 0, 0, NEG), np.where(dist >= 0, dist, far)]
    t.append(np.where((dist >= 0) & (dist <= P), dist, far))
    for every in (1, 4):
        q, k = np.arange(P)[:, None], np.arange(S)[None, :]
        t.append(np.where((q >= k) & ((q - k) % every == 0), (q - k) * 4, far))
    t.append(dist > 0)
    a["tables"] = np.stack(t, axis=1).astype(np.float32)
    return a


def kernel(**inputs):
    import numpy as _np
    import concourse.bacc as _bacc
    from concourse import mybir as _mybir
    from concourse.bass_utils import run_bass_kernel_spmd as _run

    nc = _bacc.Bacc("TRN2", target_bir_lowering=False, num_devices=1)
    arrays, A = {}, {}
    for name, a in lay_out(inputs).items():
        arrays[f"in_{name}_dram"] = _np.ascontiguousarray(a)
        A[name] = nc.dram_tensor(f"in_{name}_dram", a.shape, _mybir.dt.from_np(a.dtype), kind="ExternalInput").ap()
    A["scratch"] = nc.dram_tensor("rwkv_scratch", (8, 3, P, S), F32, kind="Internal").ap()
    A["dil_scratch"] = nc.dram_tensor("dilated_scratch", (S, 2 * GH * HS), F32, kind="Internal").ap()
    A["stat_scratch"] = nc.dram_tensor("dilated_stat_scratch", (S, 2 * GH * 2), F32, kind="Internal").ap()
    out = nc.dram_tensor("out_0_dram", (S, D), F32, kind="ExternalOutput").ap()
    build(nc, A, out)
    r = _run(nc, [arrays], core_ids=[0])
    return r.results[0]["out_0_dram"].reshape(1, S, D)
```
